# Optimizing a Trainium2 kernel written in Bass

```python
import math
import jax, jax.numpy as jnp
from jax import lax
import numpy as np
import jax
import jax.numpy as jnp

D_MODEL = 1024
BATCH = 1
SEQ = 512
DEPTH = 4

N_MIXERS = 3
D_INNER = D_MODEL
PLE_DIM = 256
CONV_WIDTH = 3
SSM_GROUP = 16
SSM_STATE = 64
SSM_GROUPS = D_INNER // SSM_GROUP
DT_MIN = 1e-3
DT_MAX = 1e-1
RWKV_HEAD = 64
RWKV_HEADS = D_INNER // RWKV_HEAD
DECAY_LORA = 64
ICLR_LORA = 64
RWKV_GN_EPS = 64e-5
LN_EPS = 1e-5
DN_ALPHA = (2 * DEPTH) ** 0.25
DN_BETA = (8 * DEPTH) ** -0.25
N_CONV = (DEPTH + 2) // 3
N_SSM = (DEPTH + 1) // 3
N_RWKV = DEPTH // 3


def layer_norm(h, g, b, eps=LN_EPS):
    h32 = h.astype(jnp.float32)
    mu = h32.mean(-1, keepdims=True)
    var = jnp.square(h32 - mu).mean(-1, keepdims=True)
    return ((h32 - mu) * lax.rsqrt(var + eps) * g.astype(jnp.float32) + b.astype(jnp.float32)).astype(h.dtype)

def token_shift(x):
    return jnp.pad(x, ((0, 0), (1, 0), (0, 0)))[:, :-1]

def short_conv_mixer(x, w_in, conv_k, w_out):
    bg, cg, h, z = jnp.split(x @ w_in, 4, axis=-1)
    u = cg * h
    conv = lax.conv_general_dilated(
        u, conv_k[:, None, :].astype(u.dtype), window_strides=(1,),
        padding=[(CONV_WIDTH - 1, 0)], dimension_numbers=("NWC", "WIO", "NWC"),
        feature_group_count=D_INNER)
    return (bg * conv * jax.nn.silu(z)) @ w_out

def _ssm_combine(left, right):
    a_l, b_l = left
    a_r, b_r = right
    return a_r * a_l, a_r * b_l + b_r

def s5_mixer(x, w_in, lam_re, lam_im, log_dt, b_re, b_im, c_re, c_im, d_skip, w_glu, b_glu, w_out):
    f32 = jnp.float32
    u, z = jnp.split(x @ w_in, 2, axis=-1)
    bsz, seqlen, _ = u.shape
    ug = u.astype(f32).reshape(bsz, seqlen, SSM_GROUPS, SSM_GROUP)
    lam = lax.complex(lam_re.astype(f32), lam_im.astype(f32))
    dt = jnp.exp(log_dt.astype(f32))[:, None]
    a_bar = jnp.exp(lam * dt)
    b_mat = lax.complex(b_re.astype(f32), b_im.astype(f32))
    b_bar = ((a_bar - 1.0) / lam)[..., None] * b_mat
    c_mat = lax.complex(c_re.astype(f32), c_im.astype(f32))
    bu = jnp.einsum("blgh,gph->blgp", ug, b_bar)
    a_seq = jnp.broadcast_to(a_bar, bu.shape)
    states = lax.associative_scan(_ssm_combine, (a_seq, bu), axis=1)[1]
    y = jnp.einsum("blgp,ghp->blgh", states, c_mat).real + d_skip.astype(f32).reshape(SSM_GROUPS, SSM_GROUP) * ug
    y = jax.nn.gelu(y.reshape(bsz, seqlen, D_INNER).astype(x.dtype))
    y = y * jax.nn.sigmoid(y @ w_glu + b_glu)
    return (y * jax.nn.silu(z)) @ w_out

def _rwkv_step(state, inp):
    r_t, w_t, k_t, v_t, kk_t, a_t = inp
    sa = jnp.einsum("bhvk,bhk->bhv", state, -kk_t)
    state = (state * w_t[:, :, None, :] + sa[..., None] * (kk_t * a_t)[:, :, None, :]
             + v_t[..., None] * k_t[:, :, None, :])
    out = jnp.einsum("bhvk,bhk->bhv", state, r_t)
    return state, out

def rwkv7_mixer(x, mu, w_rkvz, w0, w1, w2, a0, a1, a2, k_k, k_a, r_k, lnx_g, lnx_b, w_out):
    f32 = jnp.float32
    bsz, seqlen, _ = x.shape
    dx = token_shift(x) - x
    xs = x[None] + dx[None] * mu[:, None, None, :]
    r, k, v, z = jnp.einsum("nbld,nde->nble", xs[:4], w_rkvz)
    xw, xa = xs[4], xs[5]
    w_log = -jax.nn.softplus(-(w0 + jnp.tanh(xw @ w1) @ w2)) - 0.5
    decay = jnp.exp(-jnp.exp(w_log.astype(f32)))
    a = jax.nn.sigmoid(a0 + (xa @ a1) @ a2).astype(f32)
    heads = lambda t: t.astype(f32).reshape(bsz, seqlen, RWKV_HEADS, RWKV_HEAD)
    kk = heads(k * k_k)
    kk = kk / jnp.maximum(jnp.linalg.norm(kk, axis=-1, keepdims=True), 1e-12)
    k = heads(k * (1.0 + (a.astype(k.dtype) - 1.0) * k_a))
    r, v, decay, a = heads(r), heads(v), heads(decay), heads(a)
    seq_first = lambda t: jnp.moveaxis(t, 1, 0)
    s0 = jnp.zeros((bsz, RWKV_HEADS, RWKV_HEAD, RWKV_HEAD), f32)
    _, out = lax.scan(_rwkv_step, s0, tuple(seq_first(t) for t in (r, decay, k, v, kk, a)))
    out = jnp.moveaxis(out, 0, 1)
    mu_o = out.mean(-1, keepdims=True)
    var_o = jnp.square(out - mu_o).mean(-1, keepdims=True)
    out = ((out - mu_o) * lax.rsqrt(var_o + RWKV_GN_EPS)).reshape(bsz, seqlen, D_INNER)
    out = out * lnx_g.astype(f32) + lnx_b.astype(f32)
    bonus = jnp.sum(r * k * r_k.astype(f32), axis=-1, keepdims=True) * v
    out = (out + bonus.reshape(bsz, seqlen, D_INNER)).astype(x.dtype)
    return (out * jax.nn.silu(z)) @ w_out

def first_inputs(seed: int = 0) -> dict:
    key = jax.random.key(seed)
    ks = iter(jax.random.split(key, 48))
    nrm = lambda shape, s: jax.random.normal(next(ks), shape, jnp.float32) * s
    D, E, G, P, H, N = D_MODEL, D_INNER, SSM_GROUPS, SSM_STATE, RWKV_HEADS, RWKV_HEAD
    ramp = jnp.linspace(0.0, 1.0, E, dtype=jnp.float32) ** 0.85
    inp = {}
    inp["x"] = nrm((BATCH, SEQ, D), 1.0)
    inp["p"] = nrm((DEPTH, BATCH, SEQ, PLE_DIM), 1.0)
    inp["conv_w_in"] = nrm((N_CONV, D, 4 * E), D ** -0.5)
    inp["conv_k"] = nrm((N_CONV, CONV_WIDTH, E), CONV_WIDTH ** -0.5)
    inp["conv_w_out"] = nrm((N_CONV, E, D), E ** -0.5 * DN_BETA)
    inp["ssm_w_in"] = nrm((N_SSM, D, 2 * E), D ** -0.5)
    inp["ssm_lam_re"] = -0.5 + nrm((N_SSM, G, P), 0.01)
    inp["ssm_lam_im"] = math.pi * jnp.arange(P, dtype=jnp.float32) + nrm((N_SSM, G, P), 0.01)
    inp["ssm_log_dt"] = jax.random.uniform(next(ks), (N_SSM, G), jnp.float32, math.log(DT_MIN), math.log(DT_MAX))
    inp["ssm_b_re"] = nrm((N_SSM, G, P, SSM_GROUP), (2 * SSM_GROUP) ** -0.5)
    inp["ssm_b_im"] = nrm((N_SSM, G, P, SSM_GROUP), (2 * SSM_GROUP) ** -0.5)
    inp["ssm_c_re"] = nrm((N_SSM, G, SSM_GROUP, P), (2 * P) ** -0.5)
    inp["ssm_c_im"] = nrm((N_SSM, G, SSM_GROUP, P), (2 * P) ** -0.5)
    inp["ssm_d"] = nrm((N_SSM, E), 1.0)
    inp["ssm_w_glu"] = nrm((N_SSM, E, E), E ** -0.5)
    inp["ssm_b_glu"] = nrm((N_SSM, E), 0.01)
    inp["ssm_w_out"] = nrm((N_SSM, E, D), E ** -0.5 * DN_BETA)
    inp["rwkv_mu"] = jax.random.uniform(next(ks), (N_RWKV, 6, D), jnp.float32)
    inp["rwkv_w_rkvz"] = nrm((N_RWKV, 4, D, E), D ** -0.5)
    inp["rwkv_w0"] = -6.0 + 5.0 * ramp + nrm((N_RWKV, E), 0.1)
    inp["rwkv_w1"] = nrm((N_RWKV, D, DECAY_LORA), D ** -0.5)
    inp["rwkv_w2"] = nrm((N_RWKV, DECAY_LORA, E), 0.1 * DECAY_LORA ** -0.5)
    inp["rwkv_a0"] = nrm((N_RWKV, E), 0.1)
    inp["rwkv_a1"] = nrm((N_RWKV, D, ICLR_LORA), D ** -0.5)
    inp["rwkv_a2"] = nrm((N_RWKV, ICLR_LORA, E), 0.1 * ICLR_LORA ** -0.5)
    inp["rwkv_k_k"] = 0.85 + nrm((N_RWKV, E), 0.05)
    inp["rwkv_k_a"] = 1.0 + nrm((N_RWKV, E), 0.05)
    inp["rwkv_r_k"] = nrm((N_RWKV, H, N), 0.1)
    inp["rwkv_lnx_g"] = 1.0 + nrm((N_RWKV, E), 0.05)
    inp["rwkv_lnx_b"] = nrm((N_RWKV, E), 0.01)
    inp["rwkv_w_out"] = nrm((N_RWKV, E, D), E ** -0.5 * DN_BETA)
    inp["ple_proj"] = nrm((DEPTH, PLE_DIM, D), PLE_DIM ** -0.5)
    inp["ple_gate"] = nrm((DEPTH, D, D), D ** -0.5)
    inp["ln_g"] = 1.0 + nrm((DEPTH, D), 0.05)
    inp["ln_b"] = nrm((DEPTH, D), 0.01)
    return inp

def first_block(x, p, conv_w_in, conv_k, conv_w_out,
              ssm_w_in, ssm_lam_re, ssm_lam_im, ssm_log_dt, ssm_b_re, ssm_b_im, ssm_c_re, ssm_c_im,
              ssm_d, ssm_w_glu, ssm_b_glu, ssm_w_out,
              rwkv_mu, rwkv_w_rkvz, rwkv_w0, rwkv_w1, rwkv_w2, rwkv_a0, rwkv_a1, rwkv_a2,
              rwkv_k_k, rwkv_k_a, rwkv_r_k, rwkv_lnx_g, rwkv_lnx_b, rwkv_w_out,
              ple_proj, ple_gate, ln_g, ln_b):
    for i in range(DEPTH):
        kind, j = i % N_MIXERS, i // N_MIXERS
        if kind == 0:
            y = short_conv_mixer(x, conv_w_in[j], conv_k[j], conv_w_out[j])
        elif kind == 1:
            y = s5_mixer(x, ssm_w_in[j], ssm_lam_re[j], ssm_lam_im[j], ssm_log_dt[j],
                         ssm_b_re[j], ssm_b_im[j], ssm_c_re[j], ssm_c_im[j], ssm_d[j],
                         ssm_w_glu[j], ssm_b_glu[j], ssm_w_out[j])
        else:
            y = rwkv7_mixer(x, rwkv_mu[j], rwkv_w_rkvz[j], rwkv_w0[j], rwkv_w1[j], rwkv_w2[j],
                            rwkv_a0[j], rwkv_a1[j], rwkv_a2[j], rwkv_k_k[j], rwkv_k_a[j],
                            rwkv_r_k[j], rwkv_lnx_g[j], rwkv_lnx_b[j], rwkv_w_out[j])
        r = DN_ALPHA * x + y
        r = r + (p[i] @ ple_proj[i]) * jax.nn.sigmoid(r @ ple_gate[i])
        x = layer_norm(r, ln_g[i], ln_b[i])
    return x


DEPTH_2 = 2

D_MIX = D_MODEL
GROUP_WIDTH = D_MIX // 4
MLA_V_DIM = 64
MLA_HEADS = GROUP_WIDTH // MLA_V_DIM
MLA_NOPE_DIM = 64
MLA_ROPE_DIM = 32
MLA_QK_DIM = MLA_NOPE_DIM + MLA_ROPE_DIM
MLA_Q_LORA = 3 * D_MODEL // 16
MLA_KV_LORA = D_MODEL // 8
ROPE_THETA = 10000.0
ATTN_BLOCK = 128
POOL_WINDOWS = (2, 4, 8, 16)
POOL_GROUP = GROUP_WIDTH // len(POOL_WINDOWS)
HGRN_DK = 64
HGRN_DV = 64
HGRN_HEADS = GROUP_WIDTH // HGRN_DV
HGRN_CHUNK = 128
CONV_CH = GROUP_WIDTH
CONV_K = 31
N_EXPERT_GROUPS = 4
EXPERTS_PER_GROUP = 8
N_EXPERTS = N_EXPERT_GROUPS * EXPERTS_PER_GROUP
TOP_K = 2
D_EXPERT = D_MODEL // 2
MOE_BLOCK = 128
EPS = 1e-6
IN_SIZES = (MLA_Q_LORA, MLA_KV_LORA, MLA_ROPE_DIM, GROUP_WIDTH,
            HGRN_HEADS * HGRN_DK, HGRN_HEADS * HGRN_DK, HGRN_HEADS * HGRN_DV, HGRN_HEADS * HGRN_DV,
            2 * CONV_CH)
IN_COLS = sum(IN_SIZES)
IN_OFFSETS = tuple(int(v) for v in np.cumsum(IN_SIZES)[:-1])


def rms_norm(x, g):
    xf = x.astype(jnp.float32)
    y = xf * lax.rsqrt(jnp.mean(xf * xf, axis=-1, keepdims=True) + EPS)
    return (y * g.astype(jnp.float32)).astype(x.dtype)

def layer_norm_2(x, g, b):
    xf = x.astype(jnp.float32)
    mu = jnp.mean(xf, axis=-1, keepdims=True)
    var = jnp.mean(jnp.square(xf - mu), axis=-1, keepdims=True)
    y = (xf - mu) * lax.rsqrt(var + EPS)
    return (y * g.astype(jnp.float32) + b.astype(jnp.float32)).astype(x.dtype)

def rope_tables(positions):
    half = MLA_ROPE_DIM // 2
    inv_freq = ROPE_THETA ** (-jnp.arange(half, dtype=jnp.float32) / half)
    ang = positions.astype(jnp.float32)[..., None] * inv_freq
    return jnp.cos(ang)[:, :, None, :], jnp.sin(ang)[:, :, None, :]

def apply_rope(x, cos, sin):
    x1, x2 = jnp.split(x, 2, axis=-1)
    cos = cos.astype(x.dtype)
    sin = sin.astype(x.dtype)
    return jnp.concatenate([x1 * cos - x2 * sin, x1 * sin + x2 * cos], axis=-1)

def causal_attention(q, k, v):
    B, S, H, Dq = q.shape
    nb = S // ATTN_BLOCK
    qb = q.reshape(B, nb, ATTN_BLOCK, H, Dq).transpose(1, 0, 2, 3, 4)
    starts = jnp.arange(nb, dtype=jnp.int32) * ATTN_BLOCK
    kpos = jnp.arange(S, dtype=jnp.int32)
    scale = MLA_QK_DIM ** -0.5

    def block(args):
        qi, st = args
        s = jnp.einsum('bqhd,bkhd->bhqk', qi, k).astype(jnp.float32) * scale
        qpos = st + jnp.arange(ATTN_BLOCK, dtype=jnp.int32)
        s = jnp.where(kpos[None, :] <= qpos[:, None], s, -1e30)
        p = jax.nn.softmax(s, axis=-1).astype(v.dtype)
        return jnp.einsum('bhqk,bkhd->bqhd', p, v)

    o = lax.map(block, (qb, starts))
    return o.transpose(1, 0, 2, 3, 4).reshape(B, S, H, v.shape[-1])

def mla_mixer(cq, ckv, krope, cos, sin, q_a_g, w_uq, kv_a_g, w_ukv, q_g, k_g):
    B, S, _ = cq.shape
    q = (rms_norm(cq, q_a_g) @ w_uq).reshape(B, S, MLA_HEADS, MLA_QK_DIM)
    kv = (rms_norm(ckv, kv_a_g) @ w_ukv).reshape(B, S, MLA_HEADS, MLA_NOPE_DIM + MLA_V_DIM)
    k_nope, v = jnp.split(kv, [MLA_NOPE_DIM], axis=-1)
    k_rope = jnp.broadcast_to(krope[:, :, None, :], (B, S, MLA_HEADS, MLA_ROPE_DIM))
    k = jnp.concatenate([k_nope, k_rope], axis=-1)
    q = rms_norm(q, q_g)
    k = rms_norm(k, k_g)
    q = jnp.concatenate([q[..., :MLA_NOPE_DIM], apply_rope(q[..., MLA_NOPE_DIM:], cos, sin)], axis=-1)
    k = jnp.concatenate([k[..., :MLA_NOPE_DIM], apply_rope(k[..., MLA_NOPE_DIM:], cos, sin)], axis=-1)
    o = causal_attention(q, k, v)
    return o.reshape(B, S, MLA_HEADS * MLA_V_DIM)

def pool_mixer(u, w_pool, scale):
    B, S, _ = u.shape
    uf = u.astype(jnp.float32).reshape(B, S, len(POOL_WINDOWS), POOL_GROUP)
    cs = jnp.cumsum(uf, axis=1)
    t1 = jnp.arange(1, S + 1, dtype=jnp.float32)
    outs = []
    for gi, w in enumerate(POOL_WINDOWS):
        csg = cs[:, :, gi]
        lag = jnp.pad(csg, ((0, 0), (w, 0), (0, 0)))[:, :S]
        mean = (csg - lag) / jnp.minimum(t1, w)[None, :, None]
        outs.append(mean - uf[:, :, gi])
    pooled = jnp.stack(outs, axis=2).astype(u.dtype)
    y = jnp.einsum('bsgc,gcd->bsgd', pooled, w_pool)
    return y.reshape(B, S, GROUP_WIDTH) * scale

def gated_recurrence_chunked(q, k, v, logf):
    B, S, H, DK = q.shape
    DV = v.shape[-1]
    nc = S // HGRN_CHUNK

    def to_chunks(a):
        return a.reshape(B, nc, HGRN_CHUNK, H, a.shape[-1]).transpose(1, 0, 3, 2, 4)

    causal = jnp.tril(jnp.ones((HGRN_CHUNK, HGRN_CHUNK), dtype=bool))

    def step(state, inp):
        qc, kc, vc, lc = inp
        b = jnp.cumsum(lc, axis=2)
        o_inter = jnp.einsum('bhtd,bhdv->bhtv', qc * jnp.exp(b), state)
        diff = b[:, :, :, None, :] - b[:, :, None, :, :]
        decay = jnp.exp(jnp.where(causal[:, :, None], diff, -jnp.inf))
        a = jnp.einsum('bhtd,bhtsd,bhsd->bhts', qc, decay, kc)
        o_intra = jnp.einsum('bhts,bhsv->bhtv', a, vc)
        b_last = b[:, :, -1:, :]
        new_state = jnp.exp(b_last[:, :, 0, :])[..., None] * state + \
            jnp.einsum('bhsd,bhsv->bhdv', kc * jnp.exp(b_last - b), vc)
        return new_state, o_inter + o_intra

    state0 = jnp.zeros((B, H, DK, DV), jnp.float32)
    _, o = lax.scan(step, state0, (to_chunks(q), to_chunks(k), to_chunks(v), to_chunks(logf)))
    return o.transpose(1, 0, 3, 2, 4).reshape(B, S, H, DV)

def hgrn2_mixer(hq, hf, hi, hg, lb, out_g):
    B, S, _ = hq.shape
    q = jax.nn.silu(hq.astype(jnp.float32)).reshape(B, S, HGRN_HEADS, HGRN_DK)
    zf = hf.astype(jnp.float32).reshape(B, S, HGRN_HEADS, HGRN_DK)
    lbh = lb.reshape(HGRN_HEADS, HGRN_DK)
    logf = jnp.logaddexp(jnp.log(lbh), jnp.log1p(-lbh) + jax.nn.log_sigmoid(zf))
    k = -jnp.expm1(logf)
    v = hi.astype(jnp.float32).reshape(B, S, HGRN_HEADS, HGRN_DV)
    o = gated_recurrence_chunked(q, k, v, logf)
    g = hg.astype(jnp.float32).reshape(B, S, HGRN_HEADS, HGRN_DV)
    o = rms_norm(o, out_g) * jax.nn.silu(g)
    return o.reshape(B, S, GROUP_WIDTH).astype(hq.dtype)

def conformer_conv_mixer(u2, dw_w, dw_b, ln_g, ln_b):
    a, gate = jnp.split(u2, 2, axis=-1)
    u = a * jax.nn.sigmoid(gate)
    u = lax.conv_general_dilated(
        u, dw_w[:, None, :].astype(u.dtype), window_strides=(1,), padding=[(CONV_K - 1, 0)],
        dimension_numbers=('NWC', 'WIO', 'NWC'), feature_group_count=CONV_CH) + dw_b
    u = layer_norm_2(u, ln_g, ln_b)
    return jax.nn.silu(u)

def token_mixer(h, cos, sin, lb, w_in, q_a_g, w_uq, kv_a_g, w_ukv, q_g, k_g, w_pool, pool_scale,
                hgrn_out_g, dw_w, dw_b, ln_g, ln_b, w_out):
    z = h @ w_in
    cq, ckv, krope, u_pool, hq, hf, hi, hg, u_conv = jnp.split(z, list(IN_OFFSETS), axis=-1)
    y_mla = mla_mixer(cq, ckv, krope, cos, sin, q_a_g, w_uq, kv_a_g, w_ukv, q_g, k_g)
    y_pool = pool_mixer(u_pool, w_pool, pool_scale)
    y_hgrn = hgrn2_mixer(hq, hf, hi, hg, lb, hgrn_out_g)
    y_conv = conformer_conv_mixer(u_conv, dw_w, dw_b, ln_g, ln_b)
    y = jnp.concatenate([y_mla, y_pool, y_hgrn, y_conv], axis=-1)
    return y @ w_out

def hierarchical_moe(h, rg_w, rg_b, re_w, re_b, w1, w3, w2):
    B, S, D = h.shape
    N = B * S
    xf = h.reshape(N, D)
    g_logits = (xf @ rg_w).astype(jnp.float32) + rg_b
    g_prob = jax.nn.softmax(g_logits, axis=-1)
    g_idx = jnp.argmax(g_logits, axis=-1).astype(jnp.int32)
    g_w = jnp.take_along_axis(g_prob, g_idx[:, None], axis=-1)
    e_logits = ((xf @ re_w).astype(jnp.float32) + re_b).reshape(N, N_EXPERT_GROUPS, EXPERTS_PER_GROUP)
    e_logits = jnp.take_along_axis(e_logits, g_idx[:, None, None], axis=1)[:, 0]
    top_l, top_i = lax.top_k(e_logits, TOP_K)
    e_w = jax.nn.softmax(top_l, axis=-1) * g_w
    expert_id = (g_idx[:, None] * EXPERTS_PER_GROUP + top_i).reshape(-1).astype(jnp.int32)
    weight = e_w.reshape(-1)
    token = jnp.repeat(jnp.arange(N, dtype=jnp.int32), TOP_K)
    A = N * TOP_K
    order = jnp.argsort(expert_id)
    e_sorted = expert_id[order]
    tok_sorted = token[order]
    w_sorted = weight[order]
    counts = jax.ops.segment_sum(jnp.ones((A,), jnp.int32), expert_id, num_segments=N_EXPERTS)
    start = jnp.cumsum(counts) - counts
    padded = (counts + MOE_BLOCK - 1) // MOE_BLOCK * MOE_BLOCK
    padded_end = jnp.cumsum(padded)
    padded_start = padded_end - padded
    dest = padded_start[e_sorted] + jnp.arange(A, dtype=jnp.int32) - start[e_sorted]
    n_rows = (-(-A // MOE_BLOCK) + N_EXPERTS) * MOE_BLOCK
    n_blocks = n_rows // MOE_BLOCK
    row_tok = jnp.full((n_rows,), N, jnp.int32).at[dest].set(tok_sorted)
    row_w = jnp.zeros((n_rows,), jnp.float32).at[dest].set(w_sorted)
    blk_start = jnp.arange(n_blocks, dtype=jnp.int32) * MOE_BLOCK
    blk_expert = jnp.minimum(jnp.searchsorted(padded_end, blk_start, side='right'), N_EXPERTS - 1)
    x_pad = jnp.concatenate([xf, jnp.zeros((1, D), xf.dtype)], axis=0)

    def run_block(args):
        toks, wts, e = args
        xb = x_pad[toks]
        hb = jax.nn.silu(xb @ w1[e]) * (xb @ w3[e])
        return (hb @ w2[e]) * wts[:, None].astype(xb.dtype)

    yb = lax.map(run_block, (row_tok.reshape(n_blocks, MOE_BLOCK), row_w.reshape(n_blocks, MOE_BLOCK), blk_expert))
    y = jnp.zeros((N + 1, D), h.dtype).at[row_tok].add(yb.reshape(n_rows, D).astype(h.dtype))
    return y[:N].reshape(B, S, D)

def second_inputs(seed: int = 0) -> dict:
    key = jax.random.key(seed)
    ks = jax.random.split(key, 32)
    f32 = jnp.float32
    L, D = DEPTH_2, D_MODEL

    def nrm(k, shape, scale):
        return jax.random.normal(k, shape, f32) * scale

    def gain(k, shape):
        return 1.0 + 0.02 * jax.random.normal(k, shape, f32)

    return {
        'x': nrm(ks[0], (BATCH, SEQ, D), 1.0),
        'c': nrm(ks[1], (BATCH, D), 1.0),
        'positions': jnp.arange(SEQ, dtype=jnp.int32)[None, :] + jax.random.randint(ks[2], (BATCH, 1), 0, 4096, dtype=jnp.int32),
        'w_ada': nrm(ks[3], (L, D, 6 * D), 0.5 * D ** -0.5),
        'b_ada': nrm(ks[4], (L, 6 * D), 0.02),
        'norm1_g': gain(ks[5], (L, D)),
        'norm2_g': gain(ks[6], (L, D)),
        'w_in': nrm(ks[7], (L, D, IN_COLS), D ** -0.5),
        'q_a_norm_g': gain(ks[8], (L, MLA_Q_LORA)),
        'w_uq': nrm(ks[9], (L, MLA_Q_LORA, MLA_HEADS * MLA_QK_DIM), MLA_Q_LORA ** -0.5),
        'kv_a_norm_g': gain(ks[10], (L, MLA_KV_LORA)),
        'w_ukv': nrm(ks[11], (L, MLA_KV_LORA, MLA_HEADS * (MLA_NOPE_DIM + MLA_V_DIM)), MLA_KV_LORA ** -0.5),
        'q_norm_g': gain(ks[12], (L, MLA_QK_DIM)),
        'k_norm_g': gain(ks[13], (L, MLA_QK_DIM)),
        'w_pool': nrm(ks[14], (L, len(POOL_WINDOWS), POOL_GROUP, POOL_GROUP), POOL_GROUP ** -0.5),
        'pool_scale': 1.0 + 0.1 * jax.random.normal(ks[15], (L, GROUP_WIDTH), f32),
        'hgrn_lb_logits': nrm(ks[16], (DEPTH_2, HGRN_HEADS * HGRN_DK), 1.0),
        'hgrn_out_norm_g': gain(ks[17], (L, HGRN_DV)),
        'conv_dw_w': nrm(ks[18], (L, CONV_K, CONV_CH), CONV_K ** -0.5),
        'conv_dw_b': nrm(ks[19], (L, CONV_CH), 0.02),
        'conv_ln_g': gain(ks[20], (L, CONV_CH)),
        'conv_ln_b': nrm(ks[21], (L, CONV_CH), 0.02),
        'w_out': nrm(ks[22], (L, D_MIX, D), D_MIX ** -0.5),
        'router_group_w': nrm(ks[23], (L, D, N_EXPERT_GROUPS), D ** -0.5),
        'router_group_b': nrm(ks[24], (L, N_EXPERT_GROUPS), 0.01),
        'router_expert_w': nrm(ks[25], (L, D, N_EXPERTS), D ** -0.5),
        'router_expert_b': nrm(ks[26], (L, N_EXPERTS), 0.01),
        'w1': nrm(ks[27], (L, N_EXPERTS, D, D_EXPERT), D ** -0.5),
        'w3': nrm(ks[28], (L, N_EXPERTS, D, D_EXPERT), D ** -0.5),
        'w2': nrm(ks[29], (L, N_EXPERTS, D_EXPERT, D), D_EXPERT ** -0.5),
    }

def second_block(x, c, positions, w_ada, b_ada, norm1_g, norm2_g, w_in, q_a_norm_g, w_uq, kv_a_norm_g, w_ukv,
              q_norm_g, k_norm_g, w_pool, pool_scale, hgrn_lb_logits, hgrn_out_norm_g, conv_dw_w, conv_dw_b,
              conv_ln_g, conv_ln_b, w_out, router_group_w, router_group_b, router_expert_w, router_expert_b,
              w1, w3, w2):
    cos, sin = rope_tables(positions)
    lb_cum = jnp.cumsum(jax.nn.softmax(hgrn_lb_logits.astype(jnp.float32), axis=0), axis=0)
    lower_bounds = lb_cum - lb_cum[0:1]
    c_act = jax.nn.silu(c)
    for l in range(DEPTH_2):
        mod = (c_act @ w_ada[l] + b_ada[l])[:, None, :]
        sh1, sc1, g1, sh2, sc2, g2 = jnp.split(mod, 6, axis=-1)
        h = rms_norm(x, norm1_g[l]) * (1 + sc1) + sh1
        x = x + g1 * token_mixer(h, cos, sin, lower_bounds[l], w_in[l], q_a_norm_g[l], w_uq[l], kv_a_norm_g[l],
                                 w_ukv[l], q_norm_g[l], k_norm_g[l], w_pool[l], pool_scale[l], hgrn_out_norm_g[l],
                                 conv_dw_w[l], conv_dw_b[l], conv_ln_g[l], conv_ln_b[l], w_out[l])
        h = rms_norm(x, norm2_g[l]) * (1 + sc2) + sh2
        x = x + g2 * hierarchical_moe(h, router_group_w[l], router_group_b[l], router_expert_w[l],
                                      router_expert_b[l], w1[l], w3[l], w2[l])
    return x


def setup_inputs(seed=0):
    out = dict(first_inputs(seed))
    for name, value in second_inputs(seed + 1).items():
        if name != "x":
            out[name + "_2"] = value
    return out


def reference(
    x, p, conv_w_in, conv_k, conv_w_out, ssm_w_in, ssm_lam_re, ssm_lam_im, ssm_log_dt, ssm_b_re,
    ssm_b_im, ssm_c_re, ssm_c_im, ssm_d, ssm_w_glu, ssm_b_glu, ssm_w_out, rwkv_mu, rwkv_w_rkvz,
    rwkv_w0, rwkv_w1, rwkv_w2, rwkv_a0, rwkv_a1, rwkv_a2, rwkv_k_k, rwkv_k_a, rwkv_r_k,
    rwkv_lnx_g, rwkv_lnx_b, rwkv_w_out, ple_proj, ple_gate, ln_g, ln_b, c_2, positions_2,
    w_ada_2, b_ada_2, norm1_g_2, norm2_g_2, w_in_2, q_a_norm_g_2, w_uq_2, kv_a_norm_g_2,
    w_ukv_2, q_norm_g_2, k_norm_g_2, w_pool_2, pool_scale_2, hgrn_lb_logits_2,
    hgrn_out_norm_g_2, conv_dw_w_2, conv_dw_b_2, conv_ln_g_2, conv_ln_b_2, w_out_2,
    router_group_w_2, router_group_b_2, router_expert_w_2, router_expert_b_2, w1_2, w3_2, w2_2,
):
    x = first_block(
        x, p, conv_w_in, conv_k, conv_w_out, ssm_w_in, ssm_lam_re, ssm_lam_im, ssm_log_dt,
        ssm_b_re, ssm_b_im, ssm_c_re, ssm_c_im, ssm_d, ssm_w_glu, ssm_b_glu, ssm_w_out, rwkv_mu,
        rwkv_w_rkvz, rwkv_w0, rwkv_w1, rwkv_w2, rwkv_a0, rwkv_a1, rwkv_a2, rwkv_k_k, rwkv_k_a,
        rwkv_r_k, rwkv_lnx_g, rwkv_lnx_b, rwkv_w_out, ple_proj, ple_gate, ln_g, ln_b,
    )
    return second_block(
        x, c_2, positions_2, w_ada_2, b_ada_2, norm1_g_2, norm2_g_2, w_in_2, q_a_norm_g_2,
        w_uq_2, kv_a_norm_g_2, w_ukv_2, q_norm_g_2, k_norm_g_2, w_pool_2, pool_scale_2,
        hgrn_lb_logits_2, hgrn_out_norm_g_2, conv_dw_w_2, conv_dw_b_2, conv_ln_g_2, conv_ln_b_2,
        w_out_2, router_group_w_2, router_group_b_2, router_expert_w_2, router_expert_b_2, w1_2,
        w3_2, w2_2,
    )


_drawn_inputs = setup_inputs


def setup_inputs(seed=0):
    import zlib

    import numpy as np

    out = dict(_drawn_inputs(seed))
    spreads = {}
    factors = {'ssm_lam_re': 64.0,
     'ssm_lam_im': 64.0,
     'ssm_log_dt': 64.0,
     'ssm_b_re': 64.0,
     'ssm_b_im': 64.0,
     'ssm_c_re': 64.0,
     'ssm_c_im': 64.0,
     'ssm_b_glu': 8.0,
     'rwkv_w1': 8.0,
     'rwkv_w2': 8.0,
     'rwkv_a0': 5.763,
     'rwkv_a1': 6.464,
     'rwkv_a2': 5.617,
     'rwkv_k_k': 5.26,
     'rwkv_k_a': 5.544,
     'rwkv_lnx_g': 6.281,
     'rwkv_lnx_b': 8.0,
     'norm1_g_2': 5.986,
     'norm2_g_2': 3.258,
     'q_a_norm_g_2': 8.0,
     'kv_a_norm_g_2': 8.0,
     'q_norm_g_2': 8.0,
     'k_norm_g_2': 8.0,
     'hgrn_lb_logits_2': 3.384,
     'hgrn_out_norm_g_2': 7.632,
     'conv_dw_b_2': 5.986,
     'conv_ln_g_2': 27.255,
     'conv_ln_b_2': 23.988,
     'router_group_b_2': 8.0,
     'router_expert_b_2': 6.034}
    for name, (base, spread) in spreads.items():
        noise = np.random.default_rng([zlib.crc32(name.encode()), seed]).standard_normal(out[name].shape)
        drawn = base * np.exp(spread * noise) if base else spread * noise
        out[name] = jnp.asarray(drawn.astype(out[name].dtype))
    for name, factor in factors.items():
        out[name] = (out[name] * factor).astype(out[name].dtype)
    return out
```

```python
from contextlib import ExitStack, contextmanager

import numpy as np

import concourse.bass as bass
from concourse import mybir

F32 = mybir.dt.float32
I32 = mybir.dt.int32
ALU = mybir.AluOpType
ACT = mybir.ActivationFunctionType
AX = mybir.AxisListType

P = 128
D = 1024
DC = D // P
T = 512
TC = T // P
DEPTH = 4
ALPHA = float((2 * DEPTH) ** 0.25)
LN_EPS = 1e-5
GN_EPS = 64e-5
EPS = 1e-6
SLOTS = 6
SLOT = 4096
TWO_PI = 2.0 * np.pi
ROUND = 12582912.0
PI_A = 6.28125
PI_B = 0.0019350051879882812
PI_C = float(TWO_PI - 6.28125 - 0.0019350051879882812)


class Steps:

    def __init__(self, eng, sem, base=0):
        self.eng, self.sem, self.n, self.base = eng, sem, 0, base

    def __call__(self, ins, wait=True):
        ins.then_inc(self.sem, 1)
        self.n += 1
        if wait:
            self.eng.wait_ge(self.sem, self.base + self.n)


class Kernel:
    def __init__(self, nc, ctx, ins, out):
        self.nc, self.ctx, self.ins, self.out = nc, ctx, ins, out
        sb = lambda name, shape, dt=F32: ctx.enter_context(nc.sbuf_tensor(name, shape, dt))
        self.sb = sb
        self.ring = sb("weight_ring", [P, SLOTS, SLOT])
        self.X = sb("residual", [P, DC, T])
        self.A = sb("work_a", [P, DC, T])
        self.B = sb("work_b", [P, DC, T])
        self.C = sb("work_c", [P, DC, T])
        self.cols = sb("column_params", [P, ins["cols"].shape[1]])
        self.tmp = sb("tmp", [P, 6, T])
        self.c_act = sb("c_act", [P, DC])
        self.mod = sb("modulation", [P, 2, 48])
        self.row_w = sb("row_weights", [P, 2, TC])
        self.row_slot = sb("row_slots", [P, 2, TC])
        self.row_index = sb("row_indices", [P, 2, TC], I32)
        self.block_expert = sb("block_experts", [1, NE + 8], I32)
        self.lb = sb("lower_bound", [P, 10])
        self.ps = ctx.enter_context(nc.psum_tensor("banks", [P, 8, 512], F32))
        sem = lambda name: ctx.enter_context(nc.semaphore(name))
        self.weights_loaded = [sem(f"weights_loaded_{i}") for i in range(SLOTS)]
        self.weights_used = sem("weights_used")
        self.dev_ready = sem("deviation_ready")
        self.y_copied = sem("expert_rows_copied")
        self.rows_fetched = [sem(f"rows_fetched_{t}") for t in range(TC)]
        self.output_stored = sem("output_stored")
        self.signals = [[sem(f"stage_{h}_{i}") for i in range(14)] for h in range(2)]
        self.stage_no = 0
        self.queue = []
        self.first = {}
        self.issued = self.used = 0

    def slot(self, n):
        return self.ring[:, n % SLOTS, :]

    def want(self, name, src, kc, cols):
        self.first.setdefault(name, len(self.queue))
        self.queue.append((src, kc, cols))

    def want_halves(self, name, src, kc=DC):
        for q in range(src.shape[1] // 512):
            self.want(name, src[:, q * 512:(q + 1) * 512], kc, 512)

    def chunk(self, n):
        _, kc, cols = self.queue[n]
        return self.slot(n)[:, 0:kc * cols].rearrange("p (k n) -> p k n", k=kc)

    def feed(self, sp, consumed):
        self.used += consumed
        while self.issued < min(len(self.queue), self.used + SLOTS):
            n = self.issued
            src, kc, cols = self.queue[n]
            if src is None:
                break
            if n >= SLOTS:
                sp.wait_ge(self.weights_used, n - SLOTS + 1)
            sp.dma_start(self.chunk(n), src.rearrange("(k p) n -> p k n", p=P)).then_inc(
                self.weights_loaded[n % SLOTS], 16)
            self.issued += 1

    def loaded(self, pe, n):
        pe.wait_ge(self.weights_loaded[n % SLOTS], 16 * (n // SLOTS + 1))

    @contextmanager
    def stage(self, signals):
        mine = self.signals[self.stage_no % 2]
        other = self.signals[(self.stage_no + 1) % 2]
        self.stage_no += 1
        with self.nc.Block() as block:
            if self.stage_no > 1:
                @block.gpsimd
                def _(pool):
                    for s in other:
                        pool.sem_clear(s)
            yield (block, *mine[:signals])


def col(k, name, i, n=P):
    at = k.where[name]
    return k.cols[0:n, at + i:at + i + 1]


def plan_weights(k):
    i = k.ins
    for layer in range(DEPTH):
        j = layer // 3
        if layer % 3 == 0:
            for q in range(2):
                for part in (1, 2, 0, 3):
                    at = part * D + q * 512
                    k.want(f"conv_in{j}", i["conv_w_in"][j][:, at:at + 512], DC, 512)
            w_out = i["conv_w_out"][j]
        elif layer % 3 == 1:
            k.want_halves("ssm_in", i["ssm_w_in"][0])
            k.want_halves("ssm_glu", i["ssm_w_glu"][0])
            w_out = i["ssm_w_out"][0]
        else:
            for n in range(4):
                k.want_halves("rwkv_in", i["rwkv_w_rkvz"][0, n])
            w_out = i["rwkv_w_out"][0]
        k.want_halves(f"out{layer}", w_out)
        k.want(f"out{layer}", i["ple_proj"][layer], 2, D)
        k.want_halves(f"out{layer}", i["ple_gate"][layer])
    for l in range(2):
        k.want_halves(f"ada{l}", i["w_ada_2"][l])
    for l in range(2):
        plan_mixer(k, l)
        plan_experts(k, l)


def accumulate(k, pe, bank, n, m, src, kc, size=P):
    w = k.chunk(n)
    for c in range(kc):
        last = pe.matmul(bank, w[:, c, m:m + size], src[:, c, :], start=(c == 0), stop=(c == kc - 1))
    return last


def load_constants(k):
    with k.stage(1) as (block, landed):
        @block.sync
        def _(sp):
            k.feed(sp, 0)

        @block.scalar
        def _(act):
            loads = [(k.X[:, :, :], k.ins["x_t"].rearrange("(c p) t -> p c t", p=P)),
                     (k.cols[:, :], k.ins["cols"])]
            at = 0
            for dst, n in k.const_tiles:
                loads.append((dst, k.ins["consts"][:, at:at + n]))
                at += n
            for dst, src in loads:
                act.dma_start(dst, src).then_inc(landed, 16)
            act.wait_ge(landed, 16 * len(loads))


def short_conv(k, layer):
    first = k.first[f"conv_in{layer}"]
    with k.stage(6) as (block, product_ready, cg_copied, gate_ready, unit_done, dve_step, act_step):
        @block.sync
        def _(sp):
            k.feed(sp, 8)

        @block.tensor
        def _(pe):
            for q in range(2):
                for m in range(4):
                    unit = 4 * q + m
                    if unit >= 2:
                        pe.wait_ge(unit_done, unit - 1)
                    for w in range(4):
                        if m == 0:
                            k.loaded(pe, first + 4 * q + w)
                        accumulate(k, pe, k.ps[:, 4 * (unit % 2) + w, :], first + 4 * q + w, m * P, k.X, DC)\
                            .then_inc(product_ready, 1)

        @block.scalar
        def _(act):
            for unit in range(8):
                half = unit % 2
                act.wait_ge(product_ready, 4 * unit + 1)
                if unit >= 2:
                    act.wait_ge(unit_done, unit - 1)
                act.activation(k.tmp[:, 3 * half, :], k.ps[:, 4 * half, :], ACT.Copy).then_inc(cg_copied, 1)
                act.wait_ge(product_ready, 4 * unit + 4)
                act.activation(k.tmp[:, 3 * half + 1, :], k.ps[:, 4 * half + 3, :], ACT.Silu).then_inc(gate_ready, 1)

        @block.vector
        def _(dve):
            step = Steps(dve, dve_step)
            tap = [[col(k, f"conv_k{layer}_{w}", u) for u in range(DC)] for w in range(3)]
            for unit in range(8):
                half = unit % 2
                u, out = k.tmp[:, 3 * half + 2, :], k.A[:, unit, :]
                dve.wait_ge(cg_copied, unit + 1)
                dve.wait_ge(product_ready, 4 * unit + 2)
                step(dve.tensor_tensor(u, k.tmp[:, 3 * half, :], k.ps[:, 4 * half + 1, :], ALU.mult))
                step(dve.tensor_scalar(out, u, tap[2][unit], None, ALU.mult))
                step(dve.scalar_tensor_tensor(out[:, 1:T], u[:, 0:T - 1], tap[1][unit], out[:, 1:T], ALU.mult, ALU.add))
                step(dve.scalar_tensor_tensor(out[:, 2:T], u[:, 0:T - 2], tap[0][unit], out[:, 2:T], ALU.mult, ALU.add))
                dve.wait_ge(product_ready, 4 * unit + 3)
                step(dve.tensor_tensor(out, out, k.ps[:, 4 * half + 2, :], ALU.mult))
                dve.wait_ge(gate_ready, unit + 1)
                step(dve.tensor_tensor(out, out, k.tmp[:, 3 * half + 1, :], ALU.mult))
                dve.sem_inc(unit_done, 1)
                if unit % 4 == 3:
                    dve.sem_inc(k.weights_used, 4)


def output_and_gate(k, layer, src, r):
    first = k.first[f"out{layer}"]
    p_t = k.tmp[:, 4:6, :]
    with k.stage(6) as (block, p_loaded, mixed, summed, gated, gate_ready, dve_step):
        @block.sync
        def _(sp):
            sp.dma_start(p_t, k.ins["p_t"][layer].rearrange("(c p) t -> p c t", p=P)).then_inc(p_loaded, 16)
            k.feed(sp, 5)

        @block.tensor
        def _(pe):
            for m in range(DC):
                if m % 4 == 0:
                    k.loaded(pe, first + m // 4)
                if m >= 4:
                    pe.wait_ge(summed, m - 3)
                accumulate(k, pe, k.ps[:, m % 4, :], first + m // 4, m % 4 * P, src, DC).then_inc(mixed, 1)
            pe.wait_ge(p_loaded, 16)
            k.loaded(pe, first + 2)
            pe.wait_ge(summed, DC)
            for m in range(DC):
                if m % 4 == 0:
                    k.loaded(pe, first + 3 + m // 4)
                if m >= 2:
                    pe.wait_ge(summed, DC + m - 1)
                accumulate(k, pe, k.ps[:, 4 + m % 2, :], first + 3 + m // 4, m % 4 * P, r, DC).then_inc(gated, 1)
                accumulate(k, pe, k.ps[:, 6 + m % 2, :], first + 2, m * P, p_t, 2).then_inc(gated, 1)

        @block.scalar
        def _(act):
            for m in range(DC):
                act.wait_ge(gated, 2 * m + 1)
                if m >= 2:
                    act.wait_ge(summed, DC + m - 1)
                act.activation(k.tmp[:, m % 2, :], k.ps[:, 4 + m % 2, :], ACT.Sigmoid).then_inc(gate_ready, 1)

        @block.vector
        def _(dve):
            step = Steps(dve, dve_step)
            for m in range(DC):
                dve.wait_ge(mixed, m + 1)
                dve.scalar_tensor_tensor(r[:, m, :], k.X[:, m, :], ALPHA, k.ps[:, m % 4, :], ALU.mult, ALU.add)\
                    .then_inc(summed, 1)
                if m % 4 == 3:
                    dve.sem_inc(k.weights_used, 1)
            for m in range(DC):
                dve.wait_ge(gate_ready, m + 1)
                dve.wait_ge(gated, 2 * m + 2)
                step(dve.tensor_tensor(k.tmp[:, 2, :], k.tmp[:, m % 2, :], k.ps[:, 6 + m % 2, :], ALU.mult))
                step(dve.tensor_tensor(k.X[:, m, :], r[:, m, :], k.tmp[:, 2, :], ALU.add))
                dve.sem_inc(summed, 1)
            dve.sem_inc(k.weights_used, 3)


def layer_norm(k, layer):
    with k.stage(5) as (block, sums, centred, squared, deviation, dve_step):
        @block.sync
        def _(sp):
            k.feed(sp, 0)

        @block.tensor
        def _(pe):
            for c in range(DC):
                last = pe.matmul(k.ps[:, 0, :], k.ones[:, :], k.X[:, c, :], start=(c == 0), stop=(c == DC - 1))
            last.then_inc(sums, 1)
            for c in range(DC):
                pe.wait_ge(squared, c + 1)
                last = pe.matmul(k.ps[:, 1, :], k.ones[:, :], k.B[:, c, :], start=(c == 0), stop=(c == DC - 1))
            last.then_inc(sums, 1)

        @block.scalar
        def _(act):
            for c in range(DC):
                act.wait_ge(centred, c + 1)
                act.activation(k.B[:, c, :], k.A[:, c, :], ACT.Square).then_inc(squared, 1)
            act.wait_ge(sums, 2)
            act.activation(k.tmp[:, 0, :], k.ps[:, 1, :], ACT.Sqrt, bias=col(k, "ln_eps", 0), scale=1.0 / D)\
                .then_inc(deviation, 1)

        @block.vector
        def _(dve):
            step = Steps(dve, dve_step)
            dve.wait_ge(sums, 1)
            for c in range(DC):
                dve.scalar_tensor_tensor(k.A[:, c, :], k.ps[:, 0, :], -1.0 / D, k.X[:, c, :], ALU.mult, ALU.add)\
                    .then_inc(centred, 1)
            dve.wait_ge(deviation, 1)
            step(dve.reciprocal(k.tmp[:, 1, :], k.tmp[:, 0, :]))
            for c in range(DC):
                step(dve.tensor_tensor(k.A[:, c, :], k.A[:, c, :], k.tmp[:, 1, :], ALU.mult))
                step(dve.tensor_scalar(k.X[:, c, :], k.A[:, c, :], col(k, f"ln_g{layer}", c),
                                       col(k, f"ln_b{layer}", c), ALU.mult, ALU.add))


def store_output(k):
    stored = k.output_stored
    with k.stage(0) as (block,):
        @block.sync
        def _(sp):
            sp.dma_start(k.out.rearrange("(c p) t -> p c t", p=P), k.X[:, :, :]).then_inc(stored, 16)
            sp.wait_ge(stored, 16)


def reduce_angle(dve, step, angle, turns, scratch):
    step(dve.tensor_scalar(turns, angle, 1.0 / TWO_PI, ROUND, ALU.mult, ALU.add))
    step(dve.tensor_scalar(turns, turns, ROUND, None, ALU.subtract))
    step(dve.scalar_tensor_tensor(scratch, turns, -PI_A, angle, ALU.mult, ALU.add))
    step(dve.scalar_tensor_tensor(scratch, turns, -PI_B, scratch, ALU.mult, ALU.add))
    step(dve.scalar_tensor_tensor(scratch, turns, -PI_C, scratch, ALU.mult, ALU.add))
    step(dve.tensor_scalar(turns, scratch, 1.0 / TWO_PI, 0.5, ALU.mult, ALU.min))
    step(dve.tensor_scalar(turns, turns, -0.5, None, ALU.max))


TURN = 6.283185
G2 = 32


def ssm_project(k, name, halves, base, dst, func):
    first = k.first[name] + base
    with k.stage(3) as (block, product_ready, evacuated, act_step):
        @block.sync
        def _(sp):
            k.feed(sp, halves)

        @block.tensor
        def _(pe):
            for m in range(4 * halves):
                if m % 4 == 0:
                    k.loaded(pe, first + m // 4)
                if m >= 4:
                    pe.wait_ge(evacuated, m - 3)
                accumulate(k, pe, k.ps[:, m % 4, :], first + m // 4, m % 4 * P, k.X, DC).then_inc(product_ready, 1)

        @block.scalar
        def _(act):
            for m in range(4 * halves):
                act.wait_ge(product_ready, m + 1)
                act.activation(dst[:, m, :], k.ps[:, m % 4, :], func).then_inc(evacuated, 1)
                if m % 4 == 3:
                    act.sem_inc(k.weights_used, 1)


def ssm_scan(k):
    par_names = "re im dt rho turn a_re a_im den k_re k_im s0 s1".split()
    with ExitStack() as own:
        sb = lambda name, shape: own.enter_context(k.nc.sbuf_tensor(name, shape, F32))
        par = sb("ssm_params", [P, len(par_names), G2])
        raw = sb("ssm_raw", [P, 3, G2])
        bmat = sb("ssm_bmat", [P, 2, DC, P])
        cmat = sb("ssm_cmat", [P, 2, G2, 32])
        q = {name: par[:, i, :] for i, name in enumerate(par_names)}
        lr, li, log_dt = raw[:, 0, :], raw[:, 1, :], raw[:, 2, :]
        cf = k.tmp[:, 0:4, :].rearrange("p a (g h) -> p a g h", h=32)

        with k.stage(4) as (block, landed, dve_step, act_step, ready):
            @block.sync
            def _(sp):
                sp.dma_start(raw[:, :, :], k.ins["ssm_raw"].rearrange("p (a g) -> p a g", a=3)).then_inc(landed, 16)
                sp.dma_start(bmat[:, :, :, :], k.ins["ssm_b"].rearrange("p (a c n) -> p a c n", a=2, c=DC)).then_inc(landed, 16)
                sp.dma_start(cmat[:, :, :, :], k.ins["ssm_c"].rearrange("p (a g n) -> p a g n", a=2, g=G2)).then_inc(landed, 16)
                k.feed(sp, 0)

            @block.scalar
            def _(act):
                act.wait_ge(landed, 48)
                act.activation(q["dt"], log_dt, ACT.Exp).then_inc(act_step, 1)
                act.wait_ge(ready, 1)
                act.activation(q["rho"], q["re"], ACT.Exp).then_inc(act_step, 1)
                act.wait_ge(ready, 2)
                act.activation(q["s0"], q["turn"], ACT.Sin, scale=TURN).then_inc(act_step, 1)
                act.activation(q["s1"], q["k_re"], ACT.Sin, scale=-TURN, bias=col(k, "half_pi", 0)).then_inc(act_step, 1)

            @block.vector
            def _(dve):
                step = Steps(dve, dve_step)
                dve.wait_ge(act_step, 1)
                step(dve.tensor_tensor(q["re"], lr, q["dt"], ALU.mult))
                step(dve.tensor_tensor(q["im"], li, q["dt"], ALU.mult))
                dve.sem_inc(ready, 1)
                reduce_angle(dve, step, q["im"], q["turn"], q["k_re"])
                step(dve.scalar_tensor_tensor(q["k_re"], q["turn"], -1.0, q["turn"], ALU.mult, ALU.max))
                dve.sem_inc(ready, 1)
                dve.wait_ge(act_step, 4)
                step(dve.tensor_tensor(q["a_im"], q["rho"], q["s0"], ALU.mult))
                step(dve.tensor_tensor(q["a_re"], q["rho"], q["s1"], ALU.mult))
                step(dve.tensor_scalar(q["a_re"], q["a_re"], -1.0, None, ALU.add))
                step(dve.tensor_tensor(q["den"], lr, lr, ALU.mult))
                step(dve.tensor_tensor(q["s0"], li, li, ALU.mult))
                step(dve.tensor_tensor(q["den"], q["den"], q["s0"], ALU.add))
                step(dve.reciprocal(q["den"], q["den"]))
                step(dve.tensor_tensor(q["k_re"], q["a_re"], lr, ALU.mult))
                step(dve.tensor_tensor(q["s0"], q["a_im"], li, ALU.mult))
                step(dve.tensor_tensor(q["k_re"], q["k_re"], q["s0"], ALU.add))
                step(dve.tensor_tensor(q["k_re"], q["k_re"], q["den"], ALU.mult))
                step(dve.tensor_tensor(q["k_im"], q["a_im"], lr, ALU.mult))
                step(dve.tensor_tensor(q["s0"], q["a_re"], li, ALU.mult))
                step(dve.tensor_tensor(q["k_im"], q["k_im"], q["s0"], ALU.subtract))
                step(dve.tensor_tensor(q["k_im"], q["k_im"], q["den"], ALU.mult))
                for h in range(2):
                    g = slice(16 * h, 16 * h + 16)
                    kr = q["k_re"][:, g].unsqueeze(2).to_broadcast([P, 16, 32])
                    ki = q["k_im"][:, g].unsqueeze(2).to_broadcast([P, 16, 32])
                    cr, ci = cmat[:, 0, g, :], cmat[:, 1, g, :]
                    step(dve.tensor_tensor(cf[:, 0], cr, kr, ALU.mult))
                    step(dve.tensor_tensor(cf[:, 1], ci, ki, ALU.mult))
                    step(dve.tensor_tensor(cf[:, 2], cr, ki, ALU.mult))
                    step(dve.tensor_tensor(cf[:, 3], ci, kr, ALU.mult))
                    step(dve.tensor_tensor(cr, cf[:, 0], cf[:, 1], ALU.subtract))
                    step(dve.scalar_tensor_tensor(ci, cf[:, 2], -1.0, cf[:, 3], ALU.mult, ALU.subtract))

        u = k.tmp[:, 0, :]
        frac = [k.tmp[:, 1, :], k.tmp[:, 2, :]]
        size = [k.tmp[:, 3, :], k.tmp[:, 4, :]]
        sine, cosine = frac, size
        prod = k.C[:, 0:4, :]
        rot = [k.C[:, 4, :], k.C[:, 5, :]]
        scr = k.tmp[:, 5, :]
        scan = [k.C[:, 6, :], k.C[:, 7, :]]
        with ExitStack() as more:
            sb2 = lambda name, shape: more.enter_context(k.nc.sbuf_tensor(name, shape, F32))
            bc = sb2("ssm_b_chunk", [P, 2, P])
            cc = sb2("ssm_c_chunk", [P, 2, 4, 32])
            pc = sb2("ssm_param_chunk", [P, 4, 2])
            dc = sb2("ssm_d_chunk", [P, 1])
            with k.stage(10) as (block, chunk_ready, angle_ready, table_ready, bu_ready, bu_read, products_ready,
                                 products_used, y_ready, dve_step, act_step):
                STEPS = 4 * 16 + 1

                @block.sync
                def _(sp):
                    k.feed(sp, 0)

                @block.scalar
                def _(act):
                    with act.Fori(0, DC) as c:
                        act.wait_ge(y_ready, c * 2 + 1)
                        act.activation(u, k.B[:, bass.ds(c, 1), :], ACT.Copy).then_inc(chunk_ready, 1)
                        act.activation(bc[:, :, :], bmat[:, :, bass.ds(c, 1), :], ACT.Copy).then_inc(chunk_ready, 1)
                        act.activation(cc[:, :, :, :], cmat[:, :, bass.ds(c * 4, 4), :], ACT.Copy).then_inc(chunk_ready, 1)
                        act.activation(pc[:, :, 0], q["rho"][:, bass.ds(c * 4, 4)], ACT.Copy).then_inc(chunk_ready, 1)
                        act.activation(pc[:, :, 1], q["turn"][:, bass.ds(c * 4, 4)], ACT.Copy).then_inc(chunk_ready, 1)
                        act.activation(dc[:, :], k.cols[:, bass.ds(c + k.where["ssm_d"], 1)], ACT.Copy).then_inc(chunk_ready, 1)
                        for j in range(4):
                            act.wait_ge(angle_ready, c * 4 + (j + 1))
                            act.activation(sine[j % 2], frac[j % 2], ACT.Sin, scale=TURN).then_inc(table_ready, 1)
                            act.activation(cosine[j % 2], size[j % 2], ACT.Sin, scale=-TURN, bias=col(k, "half_pi", 0))\
                                .then_inc(table_ready, 1)

                @block.tensor
                def _(pe):
                    pe.sem_inc(products_used, 1)
                    with pe.Fori(0, DC) as c:
                        pe.wait_ge(chunk_ready, c * 6 + 6)

                        def inputs(j):
                            lo = 32 * j
                            for i in range(2):
                                pe.matmul(k.ps[:, 2 * (j % 2) + i, :], bc[lo:lo + 32, i, :], u[lo:lo + 32, :],
                                          start=True, stop=True).then_inc(bu_ready, 1)

                        inputs(0)
                        for j in range(4):
                            if j < 3:
                                if j >= 1:
                                    pe.wait_ge(bu_read, c * 4 + j)
                                inputs(j + 1)
                            pe.wait_ge(products_ready, c * 4 + (j + 1))
                            for i in range(4):
                                last = pe.matmul(k.ps[32 * j:32 * j + 32, 4, :], cc[:, [0, 0, 1, 1][i], j, :],
                                                 prod[:, i, :], start=(i == 0), stop=(i == 3))
                            last.then_inc(products_used, 1)

                @block.vector
                def _(dve):
                    dve.sem_inc(y_ready, 1)
                    with dve.Fori(0, DC) as c:
                        step = Steps(dve, dve_step, c * STEPS)
                        dve.wait_ge(chunk_ready, c * 6 + 6)

                        def angles(j):
                            step(dve.tensor_scalar(frac[j % 2], k.trow[:, :], pc[:, j, 1:2], None, ALU.mult))
                            step(dve.tensor_scalar(scr, frac[j % 2], ROUND, ROUND, ALU.add, ALU.subtract))
                            step(dve.tensor_tensor(frac[j % 2], frac[j % 2], scr, ALU.subtract))
                            step(dve.scalar_tensor_tensor(size[j % 2], frac[j % 2], -1.0, frac[j % 2], ALU.mult, ALU.max))
                            dve.sem_inc(angle_ready, 1)

                        angles(0)
                        for j in range(4):
                            if j < 3:
                                angles(j + 1)
                            co, si = cosine[j % 2], sine[j % 2]
                            bu = [k.ps[:, 2 * (j % 2) + i, :] for i in range(2)]
                            dve.wait_ge(table_ready, c * 8 + 2 * (j + 1))
                            dve.wait_ge(bu_ready, c * 8 + 2 * (j + 1))
                            step(dve.tensor_tensor(rot[0], co, bu[0], ALU.mult))
                            step(dve.tensor_tensor(scr, si, bu[1], ALU.mult))
                            step(dve.tensor_tensor(rot[0], rot[0], scr, ALU.add))
                            step(dve.tensor_tensor(rot[1], co, bu[1], ALU.mult))
                            step(dve.tensor_tensor(scr, si, bu[0], ALU.mult))
                            dve.sem_inc(bu_read, 1)
                            step(dve.tensor_tensor(rot[1], rot[1], scr, ALU.subtract))
                            rho = pc[:, j, 0:1].to_broadcast([P, T])
                            step(dve.tensor_tensor_scan(scan[0], rho, rot[0], 0.0, ALU.mult, ALU.add))
                            step(dve.tensor_tensor_scan(scan[1], rho, rot[1], 0.0, ALU.mult, ALU.add))
                            dve.wait_ge(products_used, c * 4 + (j + 1))
                            step(dve.tensor_tensor(prod[:, 0, :], co, scan[0], ALU.mult))
                            step(dve.scalar_tensor_tensor(prod[:, 1, :], si, -1.0, scan[1], ALU.mult, ALU.mult))
                            step(dve.tensor_tensor(prod[:, 2, :], si, scan[0], ALU.mult))
                            step(dve.tensor_tensor(prod[:, 3, :], co, scan[1], ALU.mult))
                            dve.sem_inc(products_ready, 1)
                        dve.wait_ge(products_used, c * 4 + 5)
                        dve.sem_inc(y_ready, 1)
                        step(dve.scalar_tensor_tensor(k.A[:, bass.ds(c, 1), :], u, dc[:, :], k.ps[:, 4, :], ALU.mult, ALU.add))
                        dve.sem_inc(y_ready, 1)
                        assert step.n == STEPS, step.n

    with k.stage(1) as (block, act_step):
        @block.scalar
        def _(act):
            for c in range(DC):
                act.activation(k.A[:, c, :], k.A[:, c, :], ACT.Gelu_apprx_tanh).then_inc(act_step, 1)
            act.wait_ge(act_step, DC)


def ssm_glu(k):
    first = k.first["ssm_glu"]
    with k.stage(4) as (block, product_ready, gate_ready, bank_free, dve_step):
        @block.sync
        def _(sp):
            k.feed(sp, 2)

        @block.tensor
        def _(pe):
            for m in range(DC):
                if m % 4 == 0:
                    k.loaded(pe, first + m // 4)
                if m >= 4:
                    pe.wait_ge(gate_ready, m - 3)
                accumulate(k, pe, k.ps[:, m % 4, :], first + m // 4, m % 4 * P, k.A, DC).then_inc(product_ready, 1)

        @block.scalar
        def _(act):
            for m in range(DC):
                act.wait_ge(product_ready, m + 1)
                if m >= 4:
                    act.wait_ge(bank_free, m - 3)
                act.activation(k.tmp[:, m % 4, :], k.ps[:, m % 4, :], ACT.Sigmoid, bias=col(k, "ssm_b_glu", m))\
                    .then_inc(gate_ready, 1)
                if m % 4 == 3:
                    act.sem_inc(k.weights_used, 1)

        @block.vector
        def _(dve):
            step = Steps(dve, dve_step)
            for m in range(DC):
                step(dve.tensor_tensor(k.B[:, m, :], k.A[:, m, :], k.C[:, m, :], ALU.mult))
                dve.wait_ge(gate_ready, m + 1)
                step(dve.tensor_tensor(k.B[:, m, :], k.B[:, m, :], k.tmp[:, m % 4, :], ALU.mult))
                dve.sem_inc(bank_free, 1)


def ssm_mixer(k):
    ssm_project(k, "ssm_in", 2, 0, k.B, ACT.Copy)
    ssm_scan(k)
    ssm_project(k, "ssm_in", 2, 2, k.C, ACT.Silu)
    ssm_glu(k)


class Phases:

    def __init__(self, sem, names, start=0):
        self.sem, self.names, self.told, self.start = sem, names, 0, start

    def at(self, i, name):
        return i * len(self.names) + (self.names.index(name) + 1 + self.start)

    def place(self, name):
        assert self.names[self.told] == name, (self.names[self.told], name)
        self.told += 1

    def wait(self, eng, i, name):
        eng.wait_ge(self.sem, self.at(i, name))

    def done(self, eng, name):
        self.place(name)
        eng.sem_inc(self.sem, 1)

    def last(self, ins, name):
        self.place(name)
        ins.then_inc(self.sem, 1)


HEADS = 16
L = 64
NL = T // L
DECAY = -float(np.exp(-0.5))
LEVELS = 6


def rwkv_project(k, scratch):
    first = k.first["rwkv_in"]
    with ExitStack() as own:
        sb = lambda name, shape: own.enter_context(k.nc.sbuf_tensor(name, shape, F32))
        w1 = sb("lora_down", [P, 2, DC, 64])
        w2 = sb("lora_up", [64, 2, D])
        low = sb("lora_mid", [64, T])
        xs = [k.A, k.B]
        with k.stage(10) as (block, landed, mixed, product_ready, staged, low_ready, dve_step, *stored):
            @block.sync
            def _(sp):
                k.feed(sp, 8)

            @block.vector
            def _(dve):
                step = Steps(dve, dve_step)
                for c in range(DC):
                    step(dve.tensor_tensor(k.C[:, c, 1:T], k.X[:, c, 0:T - 1], k.X[:, c, 1:T], ALU.subtract))
                    step(dve.tensor_scalar(k.C[:, c, 0:1], k.X[:, c, 0:1], -1.0, None, ALU.mult))
                for n in range(6):
                    if n >= 2:
                        dve.wait_ge(product_ready, DC * (n - 1) + (n == 5))
                    for c in range(DC):
                        step(dve.scalar_tensor_tensor(xs[n % 2][:, c, :], k.C[:, c, :], col(k, f"rwkv_mu{n}", c),
                                                      k.X[:, c, :], ALU.mult, ALU.add))
                        dve.sem_inc(mixed, 1)

            @block.tensor
            def _(pe):
                for n in range(4):
                    pe.wait_ge(mixed, DC * (n + 1))
                    for m in range(DC):
                        o = n * DC + m
                        if m % 4 == 0:
                            k.loaded(pe, first + o // 4)
                        if o >= 4:
                            pe.wait_ge(staged, o - 3)
                        accumulate(k, pe, k.ps[:, o % 4, :], first + o // 4, m % 4 * P, xs[n % 2], DC)\
                            .then_inc(product_ready, 1)
                pe.wait_ge(landed, 64)
                for n in (4, 5):
                    pe.wait_ge(mixed, DC * (n + 1))
                    if n == 5:
                        pe.wait_ge(low_ready, 1)
                    for c in range(DC):
                        last = pe.matmul(k.ps[0:64, 4, :], w1[:, n - 4, c, :], xs[n % 2][:, c, :],
                                         start=(c == 0), stop=(c == DC - 1))
                    last.then_inc(product_ready, 1)
                    pe.wait_ge(low_ready, n - 3)
                    for m in range(DC):
                        o = n * DC + m
                        pe.wait_ge(staged, o - 3)
                        pe.matmul(k.ps[:, o % 4, :], w2[:, n - 4, m * P:(m + 1) * P], low[:, :], start=True, stop=True)\
                            .then_inc(product_ready, 1)

            @block.scalar
            def _(act):
                for i, name in enumerate(("w", "a")):
                    act.dma_start(w1[:, i, :, :], k.ins[f"rwkv_{name}1"].rearrange("(c p) n -> p c n", p=P))\
                        .then_inc(landed, 16)
                    act.dma_start(w2[:, i, :], k.ins[f"rwkv_{name}2"]).then_inc(landed, 16)
                for n in range(6):
                    if n >= 4:
                        act.wait_ge(product_ready, DC * n + (n - 3))
                        act.activation(low[:, :], k.ps[0:64, 4, :], ACT.Tanh if n == 4 else ACT.Copy).then_inc(low_ready, 1)
                    for m in range(DC):
                        o = n * DC + m
                        act.wait_ge(product_ready, o + 1 + max(0, n - 3))
                        if o >= 4:
                            act.wait_ge(stored[o % 4], 16 * (o // 4))
                        if n < 4:
                            ins = act.activation(k.tmp[:, o % 4, :], k.ps[:, o % 4, :], ACT.Silu if n == 3 else ACT.Copy)
                        else:
                            ins = act.activation(k.tmp[:, o % 4, :], k.ps[:, o % 4, :], ACT.Sigmoid,
                                                 bias=col(k, "rwkv_w0" if n == 4 else "rwkv_a0", m))
                        ins.then_inc(staged, 1)
                        act.wait_ge(staged, o + 1)
                        act.dma_start(scratch[m, :, n, :], k.tmp[:, o % 4, :]).then_inc(stored[o % 4], 16)
                        if n < 4 and m % 4 == 3:
                            act.sem_inc(k.weights_used, 1)
                for s in stored:
                    act.wait_ge(s, 16 * 6 * DC // 4)


def rwkv_heads(k, scratch):
    with ExitStack() as own:
        sb = lambda name, shape: own.enter_context(k.nc.sbuf_tensor(name, shape, F32))
        ld = sb("pair_inputs", [P, 6, T])
        hc = sb("pair_params", [P, 8])
        S = sb("state", [P, P])
        SA = sb("removed", [P, 2, 64])
        WL = sb("chunk_decay", [P, NL])
        r_, k_, v_, z_, sw, a_ = (ld[:, n, :] for n in range(6))
        k_k, k_a, r_k, gn_g, gn_b = (hc[:, n:n + 1] for n in range(5))
        bonus = sw
        alpha, beta, key, query = (k.B[:, n, :] for n in range(4))
        blocks = lambda tile: tile.rearrange("p (a b) -> p a b", b=P)
        alpha_t, beta_t, key_t, v_t = (blocks(k.B[:, 4 + n, :]) for n in range(4))
        RB = [blocks(k.C[:, 0, :]), blocks(k.C[:, 1, :])]
        RK = [blocks(k.C[:, 2, :]), blocks(k.C[:, 3, :])]
        P1T = k.C[:, 4, :]
        P2 = k.C[:, 5, :].rearrange("p (a h v) -> p a h v", h=2, v=64)
        Ti, TT = blocks(k.C[:, 6, :]), blocks(k.C[:, 7, :])
        NT, NTl, Y, AK = (blocks(k.tmp[:, n, :]) for n in range(4))
        G = k.tmp[:, 4, 0:256].rearrange("p (a v) -> p a v", v=64)
        sum_, sum_before, e_query, e_beta, e_alpha, kk = (k.tmp[:, n, :] for n in range(6))
        square, norm = k.C[:, 6, :], k.C[:, 7, :]
        out, centred, out_sq, dev = (k.tmp[:, n, :] for n in range(4))
        bank = lambda n: k.ps[:, n, :]
        mats = lambda n: blocks(k.ps[:, n, :])
        mask = lambda name: k.mask[name][:, :].unsqueeze(1).to_broadcast([P, TC, P])

        with k.stage(6) as (block, pair_loaded, pe_done, act_done, dve_done, dve_step, act_step):
            per_head = lambda h: [f"Y{h}{l}" for l in range(1, LEVELS)] + [f"G{h}", f"P2{h}"]
            AP_ = Phases(act_done, ["exps", "kk_sq", "kk_norm", "by_time"] + per_head(0) + per_head(1) + ["out", "out_sq", "dev"])
            VP = Phases(dve_done, ["sums", "kk", "bonus", "hats"]
                        + [f"lvl{h}{l}" for h in range(2) for l in range(LEVELS)]
                        + [n for c in range(NL) for n in (f"sa{c}", f"s{c}")] + ["centred", "gated"], start=1)
            TP = Phases(pe_done, ["kk_sum", "bonus", "by_time"]
                        + [n for h in range(2) for n in [f"mats{h}"] + [m for l in range(1, LEVELS) for m in (f"y{h}{l}", f"upd{h}{l}")] + [f"g{h}", f"p2{h}"]]
                        + [n for c in range(NL) for n in (f"sa{c}", f"u{c}")] + ["mean", "var"])
            STEPS = 2 + 1 + 1 + 2 + 1 + 3 + 5 + 1 + 1 + 2 * (8 + 5 * 2 + 4) + NL * 3 + 6

            @block.sync
            def _(sp):
                k.feed(sp, 0)
                with sp.Fori(0, DC) as i:
                    sp.wait_ge(dve_done, i * len(VP.names) + 1)
                    sp.dma_start(ld[:, :, :], scratch[bass.ds(i, 1), :, :, :]).then_inc(pair_loaded, 16)
                    sp.dma_start(hc[:, :], k.ins["rwkv_pairs"][bass.ds(i, 1), :, :]).then_inc(pair_loaded, 16)

            @block.tensor
            def _(pe):
                with pe.Fori(0, DC) as i:
                    AP_.wait(pe, i, "kk_sq")
                    TP.last(pe.matmul(bank(0), k.pairs[:, :], square, start=True, stop=True), "kk_sum")
                    VP.wait(pe, i, "bonus")
                    TP.last(pe.matmul(bank(6), k.pairs[:, :], square, start=True, stop=True), "bonus")
                    VP.wait(pe, i, "hats")
                    for n, src in enumerate((alpha, beta, key, v_)):
                        for t in range(TC):
                            ins = pe.transpose(k.ps[:, 1 + n, t * P:(t + 1) * P], src[:, t * P:(t + 1) * P], k.ident[:, :])
                    TP.last(ins, "by_time")
                    AP_.wait(pe, i, "by_time")
                    for h in range(2):
                        lo = 64 * h
                        if h:
                            AP_.wait(pe, i, "P20")
                        for n, (left, right) in enumerate(((beta, alpha), (alpha, beta), (key, alpha), (beta, query), (key, query))):
                            for t in range(TC):
                                ts = slice(t * P, (t + 1) * P)
                                ins = pe.matmul(k.ps[:, 1 + n, ts], left[lo:lo + 64, ts], right[lo:lo + 64, ts], start=True, stop=True)
                        TP.last(ins, f"mats{h}")
                        for l in range(1, LEVELS):
                            VP.wait(pe, i, f"lvl{h}{l - 1}")
                            for t in range(TC):
                                ins = pe.matmul(mats(6)[:, t, :], NTl[:, t, :], Ti[:, t, :], start=True, stop=True)
                            TP.last(ins, f"y{h}{l}")
                            AP_.wait(pe, i, f"Y{h}{l}")
                            for t in range(TC):
                                pe.matmul(mats(7)[:, t, :], TT[:, t, :], Y[:, t, :], start=True, stop=True)
                            for t in range(TC):
                                ins = pe.matmul(mats(0)[:, t, :], Y[:, t, :], TT[:, t, :], start=True, stop=True)
                            TP.last(ins, f"upd{h}{l}")
                        VP.wait(pe, i, f"lvl{h}{LEVELS - 1}")
                        for t in range(TC):
                            pe.matmul(k.ps[lo:lo + 64, 1, t * P:(t + 1) * P], alpha_t[:, t, lo:lo + 64], TT[:, t, :], start=True, stop=True)
                        for t in range(TC):
                            ins = pe.matmul(k.ps[:, 2, 64 * t:64 * t + 64], AK[:, t, :], v_t[:, t, lo:lo + 64], start=True, stop=True)
                        TP.last(ins, f"g{h}")
                        AP_.wait(pe, i, f"G{h}")
                        for t in range(TC):
                            ins = pe.matmul(k.ps[:, 3, 64 * t:64 * t + 64], TT[:, t, :], G[:, t, :], start=True, stop=True)
                        TP.last(ins, f"p2{h}")
                    AP_.wait(pe, i, "P21")
                    for c in range(NL):
                        t, lo = c // 2, 64 * (c % 2)
                        rows, cs = slice(lo, lo + 64), slice(64 * c, 64 * c + 64)
                        if c:
                            VP.wait(pe, i, f"s{c - 1}")
                        TP.last(pe.matmul(k.ps[rows, 4, 0:P], P1T[:, cs], S[:, :], start=True, stop=True), f"sa{c}")
                        VP.wait(pe, i, f"sa{c}")
                        pe.matmul(k.ps[:, 5, cs], S[:, :], query[:, cs], start=True, stop=False)
                        for h in range(2):
                            hs = slice(64 * h, 64 * h + 64)
                            pe.matmul(k.ps[hs, 5, cs], SA[rows, h, :], RB[h][rows, t, rows], start=False, stop=False)
                            pe.matmul(k.ps[hs, 5, cs], v_t[rows, t, hs], RK[h][rows, t, rows], start=False, stop=True)
                        pe.matmul(k.ps[:, 6, 0:P], beta_t[rows, t, :], SA[rows, :, :], start=True, stop=False)
                        ins = pe.matmul(k.ps[:, 6, 0:P], key_t[rows, t, :], v_t[rows, t, :], start=False, stop=True)
                        TP.last(ins, f"u{c}")
                    AP_.wait(pe, i, "out")
                    TP.last(pe.matmul(bank(0), k.pairs[:, :], out, start=True, stop=True), "mean")
                    AP_.wait(pe, i, "out_sq")
                    TP.last(pe.matmul(bank(1), k.pairs[:, :], out_sq, start=True, stop=True), "var")

            @block.scalar
            def _(act):
                with act.Fori(0, DC) as i:
                    VP.wait(act, i, "sums")
                    act.activation(e_query, sum_, ACT.Exp, scale=DECAY)
                    act.activation(e_beta, sum_, ACT.Exp, scale=-DECAY)
                    AP_.last(act.activation(e_alpha, sum_before, ACT.Exp, scale=DECAY), "exps")
                    VP.wait(act, i, "kk")
                    AP_.last(act.activation(square, kk, ACT.Square), "kk_sq")
                    TP.wait(act, i, "kk_sum")
                    AP_.last(act.activation(norm, bank(0), ACT.Sqrt), "kk_norm")
                    TP.wait(act, i, "by_time")
                    for n in range(4):
                        ins = act.activation(k.B[:, 4 + n, :], bank(1 + n), ACT.Copy)
                    AP_.last(ins, "by_time")
                    for h in range(2):
                        lo = 64 * h
                        for l in range(1, LEVELS):
                            TP.wait(act, i, f"y{h}{l}")
                            AP_.last(act.activation(Y[:, :, :], mats(6), ACT.Copy), f"Y{h}{l}")
                        TP.wait(act, i, f"g{h}")
                        act.activation(P1T[lo:lo + 64, :], k.ps[lo:lo + 64, 1, :], ACT.Copy)
                        AP_.last(act.activation(k.tmp[:, 4, 0:256], k.ps[:, 2, 0:256], ACT.Copy), f"G{h}")
                        TP.wait(act, i, f"p2{h}")
                        AP_.last(act.activation(P2[:, :, h, :], k.ps[:, 3, 0:256].rearrange("p (a v) -> p a v", v=64), ACT.Copy), f"P2{h}")
                    TP.wait(act, i, f"u{NL - 1}")
                    AP_.last(act.activation(out, bank(5), ACT.Copy), "out")
                    VP.wait(act, i, "centred")
                    AP_.last(act.activation(out_sq, centred, ACT.Square), "out_sq")
                    TP.wait(act, i, "var")
                    AP_.last(act.activation(dev, bank(1), ACT.Sqrt, scale=1.0 / 64, bias=col(k, "gn_eps", 0)), "dev")

            @block.vector
            def _(dve):
                dve.sem_inc(dve_done, 1)
                with dve.Fori(0, DC) as i:
                    step = Steps(dve, dve_step, i * STEPS)
                    dve.wait_ge(pair_loaded, i * 32 + 32)
                    step(dve.tensor_tensor_scan(sum_, k.seg[L][:, :], sw, 0.0, ALU.mult, ALU.add))
                    step(dve.tensor_tensor(sum_before, sum_, sw, ALU.subtract))
                    VP.done(dve, "sums")
                    step(dve.tensor_scalar(kk, k_, k_k, None, ALU.mult))
                    VP.done(dve, "kk")
                    step(dve.memset(S[:, :], 0.0))
                    step(dve.tensor_scalar(k.C[:, 0, :], a_, -1.0, k_a, ALU.add, ALU.mult))
                    step(dve.scalar_tensor_tensor(k_, k.C[:, 0, :], 1.0, k_, ALU.add, ALU.mult))
                    AP_.wait(dve, i, "kk_norm")
                    step(dve.scalar_tensor_tensor(square, r_, r_k, k_, ALU.mult, ALU.mult))
                    VP.done(dve, "bonus")
                    step(dve.tensor_scalar(norm, norm, 1e-12, None, ALU.max))
                    step(dve.reciprocal(norm, norm))
                    step(dve.tensor_tensor(kk, kk, norm, ALU.mult))
                    step(dve.scalar_tensor_tensor(alpha, kk, -1.0, e_alpha, ALU.mult, ALU.mult))
                    step(dve.tensor_tensor(beta, kk, a_, ALU.mult))
                    step(dve.tensor_tensor(beta, beta, e_beta, ALU.mult))
                    step(dve.tensor_tensor(key, k_, e_beta, ALU.mult))
                    step(dve.tensor_tensor(query, r_, e_query, ALU.mult))
                    VP.done(dve, "hats")
                    step(dve.tensor_copy(WL[:, :], e_query[:, L - 1:T:L]))
                    TP.wait(dve, i, "bonus")
                    step(dve.tensor_tensor(bonus, bank(6), v_, ALU.mult))
                    for h in range(2):
                        TP.wait(dve, i, f"mats{h}")
                        step(dve.tensor_tensor(NT, mats(1), mask("before"), ALU.mult))
                        step(dve.tensor_tensor(Ti, mats(2), mask("first_lower"), ALU.mult))
                        step(dve.tensor_tensor(AK, mats(3), mask("before"), ALU.mult))
                        step(dve.tensor_tensor(RB[h], mats(4), mask("upto"), ALU.mult))
                        step(dve.tensor_tensor(RK[h], mats(5), mask("upto"), ALU.mult))
                        step(dve.tensor_tensor(Ti, Ti, mask("ident"), ALU.add))
                        step(dve.tensor_tensor(TT, NT, mask("level0"), ALU.mult))
                        step(dve.tensor_tensor(TT, TT, mask("ident"), ALU.add))
                        for l in range(1, LEVELS):
                            step(dve.tensor_tensor(NTl, NT, mask(f"level{l}"), ALU.mult))
                            VP.done(dve, f"lvl{h}{l - 1}")
                            TP.wait(dve, i, f"upd{h}{l}")
                            if l < LEVELS - 1:
                                step(dve.tensor_tensor(Ti, Ti, mats(7), ALU.add))
                            step(dve.tensor_tensor(TT, TT, mats(0), ALU.add))
                        VP.done(dve, f"lvl{h}{LEVELS - 1}")
                    AP_.wait(dve, i, "P21")
                    for c in range(NL):
                        t, lo = c // 2, 64 * (c % 2)
                        rows = slice(lo, lo + 64)
                        TP.wait(dve, i, f"sa{c}")
                        step(dve.tensor_tensor(SA[rows, :, :], k.ps[rows, 4, 0:128].rearrange("p (h v) -> p h v", h=2),
                                               P2[rows, t, :, :], ALU.add))
                        VP.done(dve, f"sa{c}")
                        TP.wait(dve, i, f"u{c}")
                        step(dve.tensor_tensor(S[:, :], S[:, :], k.ps[:, 6, 0:P], ALU.add))
                        step(dve.scalar_tensor_tensor(S[:, :], S[:, :], WL[:, c:c + 1], k.pairs[:, :], ALU.mult, ALU.mult))
                        VP.done(dve, f"s{c}")
                    TP.wait(dve, i, "mean")
                    step(dve.scalar_tensor_tensor(centred, bank(0), -1.0 / 64, out, ALU.mult, ALU.add))
                    VP.done(dve, "centred")
                    AP_.wait(dve, i, "dev")
                    step(dve.reciprocal(dev, dev))
                    step(dve.tensor_tensor(centred, centred, dev, ALU.mult))
                    step(dve.tensor_scalar(centred, centred, gn_g, gn_b, ALU.mult, ALU.add))
                    step(dve.tensor_tensor(centred, centred, bonus, ALU.add))
                    step(dve.tensor_tensor(k.A[:, bass.ds(i, 1), :], centred, z_, ALU.mult))
                    VP.done(dve, "gated")
                    assert step.n == STEPS, step.n


def rwkv_mixer(k):
    scratch = k.nc.dram_tensor("rwkv_scratch", (DC, P, 6, T), F32, kind="Internal").ap()
    rwkv_project(k, scratch)
    rwkv_heads(k, scratch)


MLA_H, QK, ROPE = 4, 96, 32
IN_COLS = 2144
CONV_K = 31
MOD = {"sh1": 0, "sc1": 8, "g1": 16, "sh2": 24, "sc2": 32, "g2": 40}
SMALL = {"w_uq": (0, 768), "w_ukv": (768, 512), "swap": (1280, P), "strip": (1408, 896),
         "pool_inv": (2304, 1024), "w_pool": (3328, 128)}
SMALL_COLS = 3456


def plan_mixer(k, l):
    w_in = k.ins["w_in_2"][l]
    k.want(f"small{l}", k.ins["small"][l], 1, SMALL_COLS)
    k.want(f"mla{l}", w_in[:, 0:352], DC, 352)
    k.want(f"pool{l}", w_in[:, 352:608], DC, 256)
    k.want(f"hgrn{l}", w_in[:, 608:1120], DC, 512)
    k.want(f"hgrn{l}", w_in[:, 1120:1632], DC, 512)
    k.want(f"conv{l}", w_in[:, 1632:2144], DC, 512)
    k.want_halves(f"out_2{l}", k.ins["w_out_2"][l])


def small(k, l, name):
    at, n = SMALL[name]
    return k.slot(k.first[f"small{l}"])[:, at:at + n]


def modulation(k):
    with k.stage(4) as (block, ready, product_ready, bank_free, dve_step):
        @block.sync
        def _(sp):
            k.feed(sp, 24)

        @block.scalar
        def _(act):
            act.activation(k.c_act[:, :], k.cols[:, k.where["c"]:k.where["c"] + DC], ACT.Silu).then_inc(ready, 1)

        @block.tensor
        def _(pe):
            pe.wait_ge(ready, 1)
            for l in range(2):
                for n in range(12):
                    i = k.first[f"ada{l}"] + n
                    k.loaded(pe, i)
                    for m in range(4):
                        for c in range(DC):
                            last = pe.matmul(k.ps[:, l, 4 * n + m:4 * n + m + 1], k.chunk(i)[:, c, m * P:(m + 1) * P],
                                             k.c_act[:, c:c + 1], start=(c == 0), stop=(c == DC - 1))
                    last.then_inc(product_ready, 1)

        @block.vector
        def _(dve):
            step = Steps(dve, dve_step)
            for l in range(2):
                for n in range(12):
                    dve.wait_ge(product_ready, 12 * l + n + 1)
                    dve.sem_inc(k.weights_used, 1)
                at = k.where[f"b_ada{l}"]
                step(dve.tensor_tensor(k.mod[:, l, :], k.ps[:, l, 0:48], k.cols[:, at:at + 48], ALU.add))
                for i, name in enumerate(("norm1", "norm2")):
                    g = k.cols[:, k.where[f"{name}_g{l}"]:][:, 0:DC]
                    sc = k.mod[:, l, MOD[f"sc{i + 1}"]:][:, 0:DC]
                    step(dve.scalar_tensor_tensor(sc, sc, 1.0, g, ALU.add, ALU.mult))


def mod(k, l, name, c):
    at = MOD[name] + c
    return k.mod[:, l, at:at + 1]


def modulated_norm(k, l, i):
    with k.stage(5) as (block, squared, summed, deviation, dve_step, act_step):
        @block.sync
        def _(sp):
            k.feed(sp, 0)

        @block.tensor
        def _(pe):
            for c in range(DC):
                pe.wait_ge(squared, c + 1)
                last = pe.matmul(k.ps[:, 0, :], k.ones[:, :], k.B[:, c, :], start=(c == 0), stop=(c == DC - 1))
            last.then_inc(summed, 1)

        @block.scalar
        def _(act):
            for c in range(DC):
                act.activation(k.B[:, c, :], k.X[:, c, :], ACT.Square).then_inc(squared, 1)
            act.wait_ge(summed, 1)
            act.activation(k.tmp[:, 0, :], k.ps[:, 0, :], ACT.Sqrt, bias=col(k, "eps", 0), scale=1.0 / D)\
                .then_inc(deviation, 1)

        @block.vector
        def _(dve):
            step = Steps(dve, dve_step)
            dve.wait_ge(deviation, 1)
            step(dve.reciprocal(k.tmp[:, 1, :], k.tmp[:, 0, :]))
            for c in range(DC):
                step(dve.scalar_tensor_tensor(k.A[:, c, :], k.X[:, c, :], mod(k, l, f"sc{i}", c), k.tmp[:, 1, :],
                                              ALU.mult, ALU.mult))
                step(dve.tensor_scalar(k.A[:, c, :], k.A[:, c, :], mod(k, l, f"sh{i}", c), None, ALU.add))


def mla(k, l):
    n0 = k.first[f"mla{l}"]
    tile = lambda n: k.tmp[:, n, :]
    ckv, cq = tile(2), [tile(0), k.tmp[0:64, 1, :]]
    w_uq, w_ukv, swap = small(k, l, "w_uq"), small(k, l, "w_ukv"), small(k, l, "swap")
    strip = small(k, l, "strip")
    q, key = [k.B[:, h, :] for h in range(4)], [k.B[:, 4 + h, :] for h in range(4)]
    v_t = k.tmp[:, 4:6, :].rearrange("p a b -> p (a b)").rearrange("p (t n) -> p t n", t=TC)
    with ExitStack() as own:
        rope = own.enter_context(k.nc.sbuf_tensor(f"rope{l}", [QK, 2, T], F32))

        with k.stage(7) as (block, landed, product_ready, act_done, dve_done, sums_ready, dve_step, act_step):
            AP_ = Phases(act_done, ["latents", "squares", "devs", "tables"])
            VP = Phases(dve_done, ["turns", "normed"])

            @block.sync
            def _(sp):
                sp.dma_start(k.C[0:QK, 7, :].bitcast(I32), k.ins["positions"].to_broadcast([QK, T])).then_inc(landed, 16)
                k.feed(sp, 0)

            @block.tensor
            def _(pe):
                k.loaded(pe, n0)
                w = k.chunk(n0)
                for out, lo, size in ((k.ps[:, 0, :], 0, 128), (k.ps[0:64, 1, :], 128, 64), (k.ps[:, 2, :], 192, 128),
                                      (k.ps[64:96, 3, :], 320, 32)):
                    for c in range(DC):
                        last = pe.matmul(out, w[:, c, lo:lo + size], k.A[:, c, :], start=(c == 0), stop=(c == DC - 1))
                    last.then_inc(product_ready, 1)
                AP_.wait(pe, 0, "squares")
                pe.matmul(k.ps[:, 4, :], k.ones[:, :], k.C[:, 0, :], start=True, stop=False)
                pe.matmul(k.ps[:, 4, :], k.ones[0:64, :], k.C[0:64, 1, :], start=False, stop=True)
                pe.matmul(k.ps[:, 5, :], k.ones[:, :], k.C[:, 2, :], start=True, stop=True).then_inc(sums_ready, 1)

            @block.scalar
            def _(act):
                act.wait_ge(product_ready, 3)
                act.activation(cq[0], k.ps[:, 0, :], ACT.Copy)
                act.activation(cq[1], k.ps[0:64, 1, :], ACT.Copy)
                act.activation(ckv, k.ps[:, 2, :], ACT.Copy)
                act.wait_ge(product_ready, 4)
                for h in range(MLA_H):
                    ins = act.activation(key[h][64:96, :], k.ps[64:96, 3, :], ACT.Copy)
                AP_.last(ins, "latents")
                act.activation(k.C[:, 0, :], k.ps[:, 0, :], ACT.Square)
                act.activation(k.C[0:64, 1, :], k.ps[0:64, 1, :], ACT.Square)
                AP_.last(act.activation(k.C[:, 2, :], k.ps[:, 2, :], ACT.Square), "squares")
                act.wait_ge(sums_ready, 1)
                act.activation(k.C[:, 3, :], k.ps[:, 4, :], ACT.Sqrt, bias=col(k, "eps", 0), scale=1.0 / 192)
                AP_.last(act.activation(k.C[:, 4, :], k.ps[:, 5, :], ACT.Sqrt, bias=col(k, "eps", 0), scale=1.0 / 128), "devs")
                VP.wait(act, 0, "turns")
                act.activation(rope[:, 1, :], k.C[0:QK, 5, :], ACT.Sin, scale=TURN)
                AP_.last(act.activation(rope[:, 0, :], k.C[0:QK, 6, :], ACT.Sin, scale=-TURN,
                                        bias=col(k, "half_pi", 0, QK)), "tables")

            @block.vector
            def _(dve):
                step = Steps(dve, dve_step)
                dve.wait_ge(landed, 16)
                angle, turns, scr = k.C[0:QK, 5, :], k.C[0:QK, 6, :], k.tmp[0:QK, 3, :]
                step(dve.tensor_copy(angle, k.C[0:QK, 7, :].bitcast(I32)))
                step(dve.tensor_scalar(angle, angle, col(k, "rope_freq", 0, QK), None, ALU.mult))
                reduce_angle(dve, step, angle, turns, scr)
                step(dve.tensor_scalar(angle, turns, col(k, "rope_sign", 0, QK), None, ALU.mult))
                step(dve.scalar_tensor_tensor(scr, turns, -1.0, turns, ALU.mult, ALU.max))
                step(dve.tensor_copy(turns, scr))
                VP.done(dve, "turns")
                AP_.wait(dve, 0, "devs")
                step(dve.reciprocal(k.C[:, 3, :], k.C[:, 3, :]))
                step(dve.reciprocal(k.C[:, 4, :], k.C[:, 4, :]))
                step(dve.scalar_tensor_tensor(cq[0], cq[0], col(k, f"q_a_g{l}", 0), k.C[:, 3, :], ALU.mult, ALU.mult))
                step(dve.scalar_tensor_tensor(cq[1], cq[1], col(k, f"q_a_g{l}", 1, 64), k.C[0:64, 3, :], ALU.mult, ALU.mult))
                step(dve.scalar_tensor_tensor(ckv, ckv, col(k, f"kv_a_g{l}", 0), k.C[:, 4, :], ALU.mult, ALU.mult))
                VP.done(dve, "normed")

        items = [(t, h) for h in range(MLA_H) for t in ("q", "k")]
        with k.stage(7) as (block, product_ready, copied, squared, sum_ready, dve_done, swap_ready, dve_step):
            @block.sync
            def _(sp):
                k.feed(sp, 0)

            @block.tensor
            def _(pe):
                k.loaded(pe, k.first[f"small{l}"])
                def product(i):
                    t, h = items[i]
                    if t == "q":
                        pe.matmul(k.ps[0:QK, i % 2, :], w_uq[:, QK * h:QK * (h + 1)], cq[0], start=True, stop=False)
                        ins = pe.matmul(k.ps[0:QK, i % 2, :], w_uq[0:64, 384 + QK * h:384 + QK * (h + 1)], cq[1], start=False, stop=True)
                    else:
                        ins = pe.matmul(k.ps[0:64, i % 2, :], w_ukv[:, P * h:P * h + 64], ckv, start=True, stop=True)
                    ins.then_inc(product_ready, 1)
                for i in range(8):
                    if i >= 2:
                        pe.wait_ge(copied, i - 1)
                    product(i)
                    pe.wait_ge(squared, i + 1)
                    pe.matmul(k.ps[0:QK, 2, :], k.ones[0:QK, 0:QK], k.C[0:QK, 2 + i % 2, :], start=True, stop=True)\
                        .then_inc(sum_ready, 1)
                    pe.wait_ge(dve_done, 2 * i + 1)
                    x = (q if items[i][0] == "q" else key)[items[i][1]]
                    pe.matmul(k.ps[0:QK, 3, :], swap[0:QK, 0:QK], x[0:QK, :], start=True, stop=True).then_inc(swap_ready, 1)
                    pe.wait_ge(dve_done, 2 * i + 2)
                vw = w_ukv.rearrange("p (h n) -> p h n", h=4)
                for t in range(TC):
                    ins = pe.matmul(k.ps[:, 4 + t // 2, 256 * (t % 2):256 * (t % 2) + 256], ckv[:, t * P:(t + 1) * P],
                                    vw[:, :, 64:128], start=True, stop=True)
                ins.then_inc(product_ready, 1)

            @block.scalar
            def _(act):
                for i, (t, h) in enumerate(items):
                    act.wait_ge(product_ready, i + 1)
                    if t == "q":
                        act.activation(q[h][0:QK, :], k.ps[0:QK, i % 2, :], ACT.Copy).then_inc(copied, 1)
                    else:
                        act.activation(key[h][0:64, :], k.ps[0:64, i % 2, :], ACT.Copy).then_inc(copied, 1)
                    act.wait_ge(copied, i + 1)
                    x = (q if t == "q" else key)[h]
                    act.activation(k.C[0:QK, 2 + i % 2, :], x[0:QK, :], ACT.Square).then_inc(squared, 1)
                    act.wait_ge(sum_ready, i + 1)
                    if i >= 2:
                        act.wait_ge(dve_done, 2 * i - 3)
                    act.activation(k.C[0:QK, 4 + i % 2, :], k.ps[0:QK, 2, :], ACT.Sqrt, bias=col(k, "eps", 0, QK),
                                   scale=1.0 / QK).then_inc(k.dev_ready, 1)
                act.wait_ge(product_ready, 9)
                act.activation(v_t, k.ps[:, 4:6, :].rearrange("p a b -> p (a b)").rearrange("p (t n) -> p t n", t=TC), ACT.Copy)\
                    .then_inc(copied, 1)
                act.wait_ge(copied, 9)

            @block.vector
            def _(dve):
                step = Steps(dve, dve_step)
                for i, (t, h) in enumerate(items):
                    x = (q if t == "q" else key)[h][0:QK, :]
                    rstd = k.C[0:QK, 4 + i % 2, :]
                    dve.wait_ge(k.dev_ready, 8 * l + i + 1)
                    step(dve.reciprocal(rstd, rstd))
                    step(dve.scalar_tensor_tensor(x, x, col(k, f"{t}_g{l}", 0, QK), rstd, ALU.mult, ALU.mult))
                    dve.sem_inc(dve_done, 1)
                    dve.wait_ge(swap_ready, i + 1)
                    step(dve.tensor_tensor(k.C[0:QK, 6, :], k.ps[0:QK, 3, :], rope[:, 1, :], ALU.mult))
                    step(dve.tensor_tensor(x, x, rope[:, 0, :], ALU.mult))
                    step(dve.tensor_tensor(x, x, k.C[0:QK, 6, :], ALU.add))
                    dve.sem_inc(dve_done, 1)

    with ExitStack() as own:
        mx = own.enter_context(k.nc.sbuf_tensor(f"softmax_stats{l}", [P, 2, 4], F32))
        todo = [(h, qt) for h in range(MLA_H) for qt in range(TC)]
        with k.stage(9) as (block, scores_ready, scaled, probs_ready, probs_scaled, turned, turned_copied, out_ready, dve_step, copied):
            @block.sync
            def _(sp):
                k.feed(sp, 0)

            @block.tensor
            def _(pe):
                def scores(i):
                    h, qt = todo[i]
                    if i >= 2:
                        pe.wait_ge(scaled, i - 1)
                    pe.matmul(k.ps[:, i % 2, 0:P * (qt + 1)], q[h][0:QK, qt * P:(qt + 1) * P], key[h][0:QK, 0:P * (qt + 1)],
                              start=True, stop=True).then_inc(scores_ready, 1)
                scores(0)
                for i, (h, qt) in enumerate(todo):
                    if i + 1 < len(todo):
                        scores(i + 1)
                    pe.wait_ge(probs_scaled, i + 1)
                    if i >= 2:
                        pe.wait_ge(turned_copied, i - 1)
                    for j in range(qt + 1):
                        ins = pe.transpose(k.ps[:, 2 + i % 2, j * P:(j + 1) * P], k.tmp[:, i % 2, j * P:(j + 1) * P], k.ident[:, :])
                    ins.then_inc(turned, 1)
                    pe.wait_ge(turned_copied, i + 1)
                    hs = slice(64 * (h % 2), 64 * (h % 2) + 64)
                    for j in range(qt + 1):
                        ins = pe.matmul(k.ps[hs, 4 + h // 2, qt * P:(qt + 1) * P], v_t[:, j, 64 * h:64 * h + 64],
                                        k.tmp[:, 2 + i % 2, j * P:(j + 1) * P], start=(j == 0), stop=(j == qt))
                    ins.then_inc(out_ready, 1)

            @block.scalar
            def _(act):
                def copy_turned(i):
                    act.wait_ge(turned, i + 1)
                    if i >= 2:
                        act.wait_ge(out_ready, i - 1)
                    n = P * (todo[i][1] + 1)
                    act.activation(k.tmp[:, 2 + i % 2, 0:n], k.ps[:, 2 + i % 2, 0:n], ACT.Copy).then_inc(turned_copied, 1)
                for i, (h, qt) in enumerate(todo):
                    act.wait_ge(scaled, i + 1)
                    s = k.tmp[:, i % 2, 0:P * (qt + 1)]
                    act.activation(s, s, ACT.Exp, bias=mx[:, i % 2, 0:1], accum_out=mx[:, i % 2, 1:2]).then_inc(probs_ready, 1)
                    if i:
                        copy_turned(i - 1)
                copy_turned(len(todo) - 1)
                act.wait_ge(out_ready, len(todo))
                for j in range(2):
                    act.activation(k.C[:, j, :], k.ps[:, 4 + j, :], ACT.Copy).then_inc(copied, 1)
                act.wait_ge(copied, 2)

            @block.vector
            def _(dve):
                step = Steps(dve, dve_step)
                def normalise(i):
                    dve.wait_ge(probs_ready, i + 1)
                    s = k.tmp[:, i % 2, 0:P * (todo[i][1] + 1)]
                    step(dve.reciprocal(mx[:, i % 2, 2:3], mx[:, i % 2, 1:2]))
                    step(dve.tensor_scalar(s, s, mx[:, i % 2, 2:3], None, ALU.mult))
                    dve.sem_inc(probs_scaled, 1)
                for i, (h, qt) in enumerate(todo):
                    n = P * (qt + 1)
                    dve.wait_ge(scores_ready, i + 1)
                    if i >= 2:
                        dve.wait_ge(turned, i - 1)
                    step(dve.scalar_tensor_tensor(k.tmp[:, i % 2, 0:n], k.ps[:, i % 2, 0:n], QK ** -0.5,
                                                  strip[:, 512 - n:512], ALU.mult, ALU.add))
                    step(dve.tensor_reduce(mx[:, i % 2, 0:1], k.tmp[:, i % 2, 0:n], AX.X, ALU.max, negate=True))
                    dve.sem_inc(scaled, 1)
                    if i:
                        normalise(i - 1)
                normalise(len(todo) - 1)


def pool_mixer(k, l):
    n0 = k.first[f"pool{l}"]
    inv = small(k, l, "pool_inv").rearrange("p (a t) -> p a t", a=2)
    w_pool = small(k, l, "w_pool").rearrange("p (a n) -> p a n", a=2)
    with k.stage(5) as (block, product_ready, copied, pooled_ready, mixed, dve_step):
        @block.sync
        def _(sp):
            k.feed(sp, 3)

        @block.tensor
        def _(pe):
            k.loaded(pe, n0)
            for m in range(2):
                accumulate(k, pe, k.ps[:, m, :], n0, m * P, k.A, DC).then_inc(product_ready, 1)
            pe.wait_ge(pooled_ready, 1)
            for g in range(4):
                gs = slice(64 * (g % 2), 64 * (g % 2) + 64)
                ins = pe.matmul(k.ps[gs, 2 + g // 2, :], w_pool[gs, g // 2, :], k.B[gs, g // 2, :], start=True, stop=True)
            ins.then_inc(mixed, 1)

        @block.scalar
        def _(act):
            for m in range(2):
                act.wait_ge(product_ready, m + 1)
                act.activation(k.B[:, m, :], k.ps[:, m, :], ACT.Copy).then_inc(copied, 1)

        @block.vector
        def _(dve):
            step = Steps(dve, dve_step)
            dve.wait_ge(copied, 2)

            def widen(dst, src, lag, rows):
                step(dve.tensor_copy(dst[rows, 0:lag], src[rows, 0:lag]))
                step(dve.tensor_tensor(dst[rows, lag:T], src[rows, lag:T], src[rows, 0:T - lag], ALU.add))

            tile = lambda n: k.B[:, n, :]
            every, low, high = slice(0, P), slice(0, 64), slice(64, P)
            widen(tile(2), tile(0), 1, every)
            widen(tile(4), tile(2), 2, high)
            widen(tile(3), tile(1), 1, every)
            widen(tile(5), tile(3), 2, every)
            widen(tile(6), tile(5), 4, every)
            widen(tile(7), tile(6), 8, high)
            for rows, wide, m in ((low, 2, 0), (high, 4, 0), (low, 6, 1), (high, 7, 1)):
                step(dve.tensor_tensor(k.B[rows, wide, :], k.B[rows, wide, :], inv[rows, m, :], ALU.mult))
                step(dve.tensor_tensor(k.B[rows, m, :], k.B[rows, wide, :], k.B[rows, m, :], ALU.subtract))
            dve.sem_inc(pooled_ready, 1)
            dve.wait_ge(mixed, 1)
            dve.sem_inc(k.weights_used, 3)
            for m in range(2):
                step(dve.tensor_scalar(k.C[:, 2 + m, :], k.ps[:, 2 + m, :], col(k, f"pool_scale{l}", m), None, ALU.mult))


def conformer(k, l):
    n0 = k.first[f"conv{l}"]
    with k.stage(6) as (block, product_ready, gate_ready, vector_ready, stats_ready, squared, dve_step):
        @block.sync
        def _(sp):
            k.feed(sp, 1)

        @block.tensor
        def _(pe):
            k.loaded(pe, n0)
            for m in range(4):
                accumulate(k, pe, k.ps[:, m, :], n0, m * P, k.A, DC).then_inc(product_ready, 1)
            pe.wait_ge(vector_ready, 1)
            for m in range(2):
                ins = pe.matmul(k.ps[:, 4, :], k.ones[:, :], k.B[:, 2 + m, :], start=(m == 0), stop=(m == 1))
            ins.then_inc(stats_ready, 1)
            pe.wait_ge(squared, 2)
            for m in range(2):
                ins = pe.matmul(k.ps[:, 5, :], k.ones[:, :], k.B[:, 4 + m, :], start=(m == 0), stop=(m == 1))
            ins.then_inc(stats_ready, 1)

        @block.scalar
        def _(act):
            for m in range(2):
                act.wait_ge(product_ready, m + 3)
                act.activation(k.tmp[:, m, :], k.ps[:, 2 + m, :], ACT.Sigmoid).then_inc(gate_ready, 1)
            for m in range(2):
                act.wait_ge(vector_ready, m + 2)
                act.activation(k.B[:, 4 + m, :], k.B[:, 2 + m, :], ACT.Square).then_inc(squared, 1)
            act.wait_ge(stats_ready, 2)
            act.activation(k.tmp[:, 2, :], k.ps[:, 5, :], ACT.Sqrt, bias=col(k, "eps", 0), scale=1.0 / 256).then_inc(squared, 1)
            for m in range(2):
                act.wait_ge(vector_ready, m + 4)
                act.activation(k.C[:, 6 + m, :], k.B[:, 2 + m, :], ACT.Silu).then_inc(squared, 1)
            act.wait_ge(squared, 5)

        @block.vector
        def _(dve):
            step = Steps(dve, dve_step)
            for m in range(2):
                dve.wait_ge(gate_ready, m + 1)
                step(dve.tensor_tensor(k.B[:, m, :], k.tmp[:, m, :], k.ps[:, m, :], ALU.mult))
            dve.sem_inc(k.weights_used, 1)
            taps = lambda m, j: col(k, f"dw_w{l}_{j}", m)
            for m in range(2):
                acc, u = k.B[:, 2 + m, :], k.B[:, m, :]
                step(dve.tensor_scalar(acc, u, taps(m, CONV_K - 1), col(k, f"dw_b{l}", m), ALU.mult, ALU.add))
                for lag in range(1, CONV_K):
                    step(dve.scalar_tensor_tensor(acc[:, lag:T], u[:, 0:T - lag], taps(m, CONV_K - 1 - lag), acc[:, lag:T],
                                                  ALU.mult, ALU.add))
            dve.sem_inc(vector_ready, 1)
            dve.wait_ge(stats_ready, 1)
            for m in range(2):
                step(dve.scalar_tensor_tensor(k.B[:, 2 + m, :], k.ps[:, 4, :], -1.0 / 256, k.B[:, 2 + m, :], ALU.mult, ALU.add))
                dve.sem_inc(vector_ready, 1)
            dve.wait_ge(squared, 3)
            step(dve.reciprocal(k.tmp[:, 2, :], k.tmp[:, 2, :]))
            for m in range(2):
                step(dve.tensor_tensor(k.B[:, 2 + m, :], k.B[:, 2 + m, :], k.tmp[:, 2, :], ALU.mult))
                step(dve.tensor_scalar(k.B[:, 2 + m, :], k.B[:, 2 + m, :], col(k, f"cln_g{l}", m), col(k, f"cln_b{l}", m),
                                       ALU.mult, ALU.add))
                dve.sem_inc(vector_ready, 1)


def hgrn(k, l):
    n0 = k.first[f"hgrn{l}"]
    q, key, b = k.B[:, 0:2, :], k.B[:, 2:4, :], k.B[:, 4:6, :]
    v_t = k.tmp[:, 4:6, :].rearrange("p a b -> p (a b)").rearrange("p (t n) -> p t n", t=TC)
    g = k.C[:, 6:8, :]
    blocks = lambda tile: tile.rearrange("p (a b) -> p a b", b=P)
    with k.stage(5) as (block, product_ready, act_done, dve_done, dve_step, copied):
        AP_ = Phases(act_done, ["start"] + [f"{x}{m}" for m in range(2) for x in ("e", "ln", "e2", "ln2")])
        VP = Phases(dve_done, ["bounds"] + [f"{x}{m}" for m in range(2) for x in ("z", "d")])

        @block.sync
        def _(sp):
            k.feed(sp, 2)

        @block.tensor
        def _(pe):
            k.loaded(pe, n0)
            for m in range(4):
                accumulate(k, pe, k.ps[:, m, :], n0, m * P, k.A, DC).then_inc(product_ready, 1)
            k.loaded(pe, n0 + 1)
            for m in range(2):
                accumulate(k, pe, k.ps[:, 6 + m, :], n0 + 1, 256 + m * P, k.A, DC).then_inc(product_ready, 1)
            for t in range(TC):
                for c in range(DC):
                    ins = pe.matmul(k.ps[:, 4 + t // 2, 256 * (t % 2):256 * (t % 2) + 256], k.A[:, c, t * P:(t + 1) * P],
                                    k.chunk(n0 + 1)[:, c, 0:256], start=(c == 0), stop=(c == DC - 1))
            ins.then_inc(product_ready, 1)

        @block.scalar
        def _(act):
            act.wait_ge(product_ready, 2)
            act.activation(q, k.ps[:, 0:2, :], ACT.Silu).then_inc(copied, 1)
            act.wait_ge(product_ready, 4)
            act.activation(key, k.ps[:, 2:4, :], ACT.Sigmoid, scale=-1.0).then_inc(copied, 1)
            act.wait_ge(product_ready, 6)
            act.activation(g, k.ps[:, 6:8, :], ACT.Silu).then_inc(copied, 1)
            act.wait_ge(product_ready, 7)
            act.activation(v_t, k.ps[:, 4:6, :].rearrange("p a b -> p (a b)").rearrange("p (t n) -> p t n", t=TC), ACT.Copy)\
                .then_inc(copied, 1)
            act.wait_ge(copied, 4)
            VP.wait(act, 0, "bounds")
            if l:
                act.activation(k.lb[:, 0:2], k.lb[:, 4:6], ACT.Sigmoid)
                ins = act.activation(k.lb[:, 2:4], k.lb[:, 4:6], ACT.Sigmoid, scale=-1.0)
                ins.then_inc(copied, 1)
                act.wait_ge(copied, 5)
                act.activation(k.lb[:, 6:8], k.lb[:, 2:4], ACT.Ln).then_inc(copied, 1)
                AP_.last(act.activation(k.lb[:, 8:10], k.lb[:, 0:2], ACT.Ln), "start")
            else:
                AP_.done(act, "start")
            for m in range(2):
                VP.wait(act, 0, f"z{m}")
                AP_.last(act.activation(k.tmp[:, 0, :], k.tmp[:, 0, :], ACT.Exp), f"e{m}")
                act.wait_ge(act_done, AP_.at(0, f"e{m}"))
                AP_.last(act.activation(k.tmp[:, 0, :], k.tmp[:, 0, :], ACT.Ln, bias=1.0), f"ln{m}")
                VP.wait(act, 0, f"d{m}")
                if l:
                    AP_.last(act.activation(k.tmp[:, 2, :], k.tmp[:, 2, :], ACT.Exp), f"e2{m}")
                    act.wait_ge(act_done, AP_.at(0, f"e2{m}"))
                    AP_.last(act.activation(k.tmp[:, 2, :], k.tmp[:, 2, :], ACT.Ln, bias=1.0), f"ln2{m}")
                else:
                    AP_.done(act, f"e2{m}")
                    AP_.done(act, f"ln2{m}")

        @block.vector
        def _(dve):
            step = Steps(dve, dve_step)
            at = k.where["lb_logits"]
            step(dve.tensor_tensor(k.lb[:, 4:6], k.cols[:, at + 2:at + 4], k.cols[:, at:at + 2], ALU.subtract))
            VP.done(dve, "bounds")
            dve.wait_ge(copied, 4)
            dve.sem_inc(k.weights_used, 2)
            AP_.wait(dve, 0, "start")
            for m in range(2):
                t0, t1, t2 = k.tmp[:, 0, :], k.tmp[:, 1, :], k.tmp[:, 2, :]
                z = k.ps[:, 2 + m, :]
                step(dve.tensor_copy(t1, z))
                step(dve.scalar_tensor_tensor(t0, t1, -1.0, t1, ALU.mult, ALU.min))
                VP.done(dve, f"z{m}")
                step(dve.tensor_scalar(t1, t1, 0.0, None, ALU.min))
                AP_.wait(dve, 0, f"ln{m}")
                step(dve.tensor_tensor(t1, t1, t0, ALU.subtract))
                if l:
                    step(dve.tensor_scalar(t1, t1, k.lb[:, 6 + m:7 + m], None, ALU.add))
                    step(dve.tensor_scalar(t0, t1, -1.0, k.lb[:, 8 + m:9 + m], ALU.mult, ALU.add))
                    step(dve.scalar_tensor_tensor(t2, t0, -1.0, t0, ALU.mult, ALU.min))
                    VP.done(dve, f"d{m}")
                    step(dve.scalar_tensor_tensor(t1, t0, 0.0, t1, ALU.max, ALU.add))
                    AP_.wait(dve, 0, f"ln2{m}")
                    step(dve.tensor_tensor(t1, t1, t2, ALU.add))
                    step(dve.tensor_scalar(key[:, m, :], key[:, m, :], k.lb[:, 2 + m:3 + m], None, ALU.mult))
                else:
                    VP.done(dve, f"d{m}")
                step(dve.tensor_tensor_scan(b[:, m, :], k.seg[128][:, :], t1, 0.0, ALU.mult, ALU.add))
                AP_.wait(dve, 0, f"ln2{m}")

    with ExitStack() as own:
        S = own.enter_context(k.nc.sbuf_tensor(f"hgrn_state{l}", [P, P], F32))
        last_decay = own.enter_context(k.nc.sbuf_tensor(f"hgrn_last{l}", [P, TC], F32))
        AT = [blocks(k.B[:, 6, :]), blocks(k.B[:, 7, :])]
        E, qx, kx, part = (k.tmp[:, n, :] for n in range(4))
        with k.stage(5) as (block, pe_done, act_done, dve_done, dve_step, _):
            names = lambda *n: [f"{x}{m}" for m in range(2) for x in n]
            AP_ = Phases(act_done, names(*[f"E{v}_" for v in range(7)], "inter_", "turned_", "out_", "sq_", "dev_"))
            VP = Phases(dve_done, names("diag_", *[y for v in range(7) for y in (f"d{v}_", f"x{v}_")], "inter_", "hats_", *[f"s{c}_" for c in range(TC)], "fin_"))
            TP = Phases(pe_done, names("diag_", *[f"a{v}_" for v in range(7)], "turned_", *[f"u{c}_" for c in range(TC)], "sum_"))

            @block.sync
            def _(sp):
                k.feed(sp, 0)

            @block.tensor
            def _(pe):
                def pairwise(left, right, banks):
                    for h in range(2):
                        hs = slice(64 * h, 64 * h + 64)
                        for t in range(TC):
                            ts = slice(t * P, (t + 1) * P)
                            ins = pe.matmul(k.ps[:, banks + h, ts], left[hs, ts], right[hs, ts], start=True, stop=True)
                    return ins
                for m in range(2):
                    if m:
                        VP.wait(pe, 0, "fin_0")
                    TP.last(pairwise(key[:, m, :], q[:, m, :], 0), f"diag_{m}")
                    for v in range(7):
                        VP.wait(pe, 0, f"x{v}_{m}")
                        TP.last(pairwise(kx, qx, 2 if v % 2 == 0 else 0), f"a{v}_{m}")
                    VP.wait(pe, 0, f"hats_{m}")
                    for t in range(TC):
                        ins = pe.transpose(k.ps[:, 4, t * P:(t + 1) * P], kx[:, t * P:(t + 1) * P], k.ident[:, :])
                    TP.last(ins, f"turned_{m}")
                    AP_.wait(pe, 0, f"turned_{m}")
                    kt = blocks(part)
                    for c in range(TC):
                        cs = slice(c * P, (c + 1) * P)
                        if c:
                            VP.wait(pe, 0, f"s{c - 1}_{m}")
                        pe.matmul(k.ps[:, 5, cs], S[:, :], qx[:, cs], start=True, stop=False)
                        for h in range(2):
                            pe.matmul(k.ps[64 * h:64 * h + 64, 5, cs], v_t[:, c, P * m + 64 * h:P * m + 64 * h + 64], AT[h][:, c, :],
                                      start=False, stop=True)
                        TP.last(pe.matmul(k.ps[:, 6, 0:P], kt[:, c, :], v_t[:, c, P * m:P * m + P], start=True, stop=True), f"u{c}_{m}")
                    AP_.wait(pe, 0, f"sq_{m}")
                    TP.last(pe.matmul(k.ps[:, 7, :], k.pairs[:, :], kx, start=True, stop=True), f"sum_{m}")

            @block.scalar
            def _(act):
                for m in range(2):
                    for v in range(7):
                        VP.wait(act, 0, f"d{v}_{m}")
                        AP_.last(act.activation(E, E, ACT.Exp), f"E{v}_{m}")
                    VP.wait(act, 0, f"inter_{m}")
                    act.activation(qx, b[:, m, :], ACT.Exp)
                    act.activation(last_decay[:, :], b[:, m, P - 1:T:P], ACT.Exp)
                    AP_.last(act.activation(E, E, ACT.Exp), f"inter_{m}")
                    TP.wait(act, 0, f"turned_{m}")
                    AP_.last(act.activation(part, k.ps[:, 4, :], ACT.Copy), f"turned_{m}")
                    TP.wait(act, 0, f"u{TC - 1}_{m}")
                    AP_.last(act.activation(E, k.ps[:, 5, :], ACT.Copy), f"out_{m}")
                    AP_.last(act.activation(kx, k.ps[:, 5, :], ACT.Square), f"sq_{m}")
                    TP.wait(act, 0, f"sum_{m}")
                    AP_.last(act.activation(qx, k.ps[:, 7, :], ACT.Sqrt, bias=col(k, "eps", 0), scale=1.0 / 64), f"dev_{m}")

            @block.vector
            def _(dve):
                step = Steps(dve, dve_step)
                mask = lambda name: k.mask[name][:, :].unsqueeze(1).to_broadcast([P, TC, P])
                for m in range(2):
                    step(dve.memset(S[:, :], 0.0))
                    VP.done(dve, f"diag_{m}")
                    def gather(v, bank):
                        for h in range(2):
                            step(dve.tensor_tensor(blocks(part), blocks(k.ps[:, bank + h, :]), mask(f"level{v}"), ALU.mult))
                            step(dve.tensor_tensor(AT[h], AT[h], blocks(part), ALU.add))
                    for v in range(7):
                        size = 2 ** (v + 1)
                        wide = lambda ap: ap.rearrange("p (a b) -> p a b", b=size)
                        ref = wide(b[:, m, :])[:, :, size // 2 - 1:size // 2].to_broadcast([P, T // size, size])
                        step(dve.tensor_tensor(wide(E), wide(b[:, m, :]), ref, ALU.subtract))
                        step(dve.scalar_tensor_tensor(E, E, -1.0, E, ALU.mult, ALU.min))
                        VP.done(dve, f"d{v}_{m}")
                        if v == 0:
                            TP.wait(dve, 0, f"diag_{m}")
                            for h in range(2):
                                step(dve.tensor_tensor(AT[h], blocks(k.ps[:, h, :]), mask("ident"), ALU.mult))
                        else:
                            TP.wait(dve, 0, f"a{v - 1}_{m}")
                            gather(v - 1, 2 if (v - 1) % 2 == 0 else 0)
                        AP_.wait(dve, 0, f"E{v}_{m}")
                        step(dve.tensor_tensor(qx, q[:, m, :], E, ALU.mult))
                        step(dve.tensor_tensor(kx, key[:, m, :], E, ALU.mult))
                        VP.done(dve, f"x{v}_{m}")
                    last = blocks(b[:, m, :])[:, :, P - 1:P].to_broadcast([P, TC, P])
                    step(dve.tensor_tensor(blocks(E), last, blocks(b[:, m, :]), ALU.subtract))
                    TP.wait(dve, 0, f"a6_{m}")
                    gather(6, 2)
                    VP.done(dve, f"inter_{m}")
                    AP_.wait(dve, 0, f"inter_{m}")
                    step(dve.tensor_tensor(qx, qx, q[:, m, :], ALU.mult))
                    step(dve.tensor_tensor(kx, key[:, m, :], E, ALU.mult))
                    VP.done(dve, f"hats_{m}")
                    for c in range(TC):
                        TP.wait(dve, 0, f"u{c}_{m}")
                        step(dve.scalar_tensor_tensor(S[:, :], S[:, :], last_decay[:, c:c + 1], k.ps[:, 6, 0:P], ALU.mult, ALU.add))
                        step(dve.tensor_tensor(S[:, :], S[:, :], k.pairs[:, :], ALU.mult))
                        VP.done(dve, f"s{c}_{m}")
                    AP_.wait(dve, 0, f"dev_{m}")
                    step(dve.reciprocal(qx, qx))
                    step(dve.scalar_tensor_tensor(E, E, col(k, f"hgrn_g{l}", 0), qx, ALU.mult, ALU.mult))
                    step(dve.tensor_tensor(k.C[:, 4 + m, :], E, g[:, m, :], ALU.mult))
                    VP.done(dve, f"fin_{m}")


def mixer_output(k, l):
    n0 = k.first[f"out_2{l}"]
    with k.stage(2) as (block, product_ready, dve_step):
        @block.sync
        def _(sp):
            k.feed(sp, 2)

        @block.tensor
        def _(pe):
            for m in range(DC):
                if m % 4 == 0:
                    k.loaded(pe, n0 + m // 4)
                if m >= 4:
                    pe.wait_ge(dve_step, m - 3)
                accumulate(k, pe, k.ps[:, m % 4, :], n0 + m // 4, m % 4 * P, k.C, DC).then_inc(product_ready, 1)

        @block.vector
        def _(dve):
            step = Steps(dve, dve_step)
            for m in range(DC):
                dve.wait_ge(product_ready, m + 1)
                step(dve.scalar_tensor_tensor(k.X[:, m, :], k.ps[:, m % 4, :], mod(k, l, "g1", m), k.X[:, m, :], ALU.mult, ALU.add))
                if m % 4 == 3:
                    dve.sem_inc(k.weights_used, 1)


EG, EPG = 4, 8
NE = EG * EPG
F = 512
BLOCKS = NE + 7


def plan_experts(k, l):
    for b in range(2):
        for name in ("w1_2", "w3_2"):
            k.want(f"experts{l}", k.ins[name][l, b], DC, F)
        k.want(f"experts{l}", k.ins["w2_2"][l, b], F // P, D)
    for b in range(2, BLOCKS):
        for _ in range(3):
            k.want(f"experts{l}", None, 0, 0)


def routing(k, l):
    h_tok = k.B[:, :, :].rearrange("p a b -> p (a b)").rearrange("p (t d) -> p t d", t=TC)
    with ExitStack() as own:
        sb = lambda name, shape: own.enter_context(k.nc.sbuf_tensor(f"{name}{l}", shape, F32))
        rw = sb("router_w", [P, DC, 36])
        rb = sb("router_b", [P, 36])
        c = k.C[:, :, :].rearrange("p a b -> p (a b)")
        at = [0]

        def tile(*shape):
            n = int(np.prod(shape))
            ap = c[:, at[0]:at[0] + n]
            at[0] += n
            if len(shape) == 2:
                return ap.rearrange("p (a b) -> p a b", a=shape[0])
            if len(shape) == 3:
                return ap.rearrange("p (a b c) -> p a b c", a=shape[0], b=shape[1])
            return ap
        logit, gl_e, one_g = tile(TC, 36), tile(TC, EG), tile(TC, EG)
        small4, small8 = tile(TC, EG), tile(TC, EPG)
        stat = [tile(TC, 1) for _ in range(8)]
        by_group, sel, sel2 = tile(TC, EG, EPG), tile(TC, EPG), tile(TC, EPG)
        one = [tile(TC, EPG), tile(TC, EPG)]
        OH = [tile(TC, NE), tile(TC, NE)]
        M, R, Q, t1, t2 = (tile(TC, NE) for _ in range(5))
        cnt, nov, st, end, off = (tile(NE) for _ in range(5))
        ind, ind2 = tile(8, NE), tile(8, NE)
        eid = tile(8)
        erow = k.trow[:, 0:NE]

        with k.stage(8) as (block, landed, turned, copied, logits_ready, exps, ranks, dve_step, dve_done):
            @block.sync
            def _(sp):
                sp.dma_start(rw[:, :, :], k.ins["router_w"][l].rearrange("(c p) n -> p c n", p=P)).then_inc(landed, 16)
                sp.dma_start(rb[:, :], k.ins["router_b"][l:l + 1, :].to_broadcast([P, 36])).then_inc(landed, 16)
                k.feed(sp, 0)

            @block.tensor
            def _(pe):
                pe.wait_ge(landed, 32)
                for t in range(TC):
                    for c_ in range(DC):
                        ins = pe.matmul(k.ps[:, 7, 36 * t:36 * t + 36], k.A[:, c_, t * P:(t + 1) * P], rw[:, c_, :],
                                        start=(c_ == 0), stop=(c_ == DC - 1))
                ins.then_inc(logits_ready, 1)
                for i in range(2 * TC):
                    t, half = divmod(i, 2)
                    if i >= 4:
                        pe.wait_ge(copied, i - 3)
                    for j in range(4):
                        ins = pe.transpose(k.ps[:, i % 4, j * P:(j + 1) * P], k.A[:, 4 * half + j, t * P:(t + 1) * P], k.ident[:, :])
                    ins.then_inc(turned, 1)
                pe.wait_ge(dve_done, 2)
                for t in range(TC):
                    for u in range(t):
                        pe.matmul(k.ps[:, 6, NE * t:NE * (t + 1)], k.ones[:, :], M[:, u, :], start=(u == 0), stop=False)
                    pe.matmul(k.ps[:, 6, NE * t:NE * (t + 1)], k.mask["sooner"][:, :], M[:, t, :], start=(t == 0), stop=True)
                for u in range(TC):
                    ins = pe.matmul(k.ps[:, 6, NE * TC:NE * (TC + 1)], k.ones[:, :], M[:, u, :], start=(u == 0), stop=(u == TC - 1))
                ins.then_inc(ranks, 1)

            @block.scalar
            def _(act):
                for i in range(2 * TC):
                    t, half = divmod(i, 2)
                    act.wait_ge(turned, i + 1)
                    act.activation(h_tok[:, t, 512 * half:512 * half + 512], k.ps[:, i % 4, :], ACT.Copy).then_inc(copied, 1)
                act.wait_ge(dve_done, 1)
                act.activation(gl_e, gl_e, ACT.Exp).then_inc(exps, 1)
                act.activation(stat[3], stat[3], ACT.Exp).then_inc(exps, 1)
                act.wait_ge(copied, 2 * TC)

            @block.vector
            def _(dve):
                step = Steps(dve, dve_step)
                wide = lambda ap, n: ap.to_broadcast([P, TC, n])
                row = lambda ap, n: ap.unsqueeze(1).to_broadcast([P, TC, n])

                def first_of(x, top, n, scratch, out):
                    step(dve.tensor_tensor(scratch, x, wide(top, n), ALU.is_equal))
                    step(dve.tensor_scalar(scratch, scratch, -64.0, 64.0, ALU.mult, ALU.add))
                    step(dve.tensor_tensor(scratch, scratch, row(k.trow[:, 0:n], n), ALU.add))
                    step(dve.tensor_reduce(stat[7], scratch, AX.X, ALU.min))
                    step(dve.tensor_tensor(out, row(k.trow[:, 0:n], n), wide(stat[7], n), ALU.is_equal))

                dve.wait_ge(logits_ready, 1)
                step(dve.tensor_tensor(logit, k.ps[:, 7, 0:36 * TC].rearrange("p (t n) -> p t n", t=TC), row(rb[:, :], 36), ALU.add))
                gl = logit[:, :, 0:EG]
                step(dve.tensor_reduce(stat[0], gl, AX.X, ALU.max))
                first_of(gl, stat[0], EG, small4, one_g)
                step(dve.tensor_tensor(gl_e, gl, wide(stat[0], EG), ALU.subtract))
                el = logit[:, :, EG:36].rearrange("p t (g e) -> p t g e", g=EG)
                for g in range(EG):
                    step(dve.tensor_tensor(by_group[:, :, g, :], el[:, :, g, :], wide(one_g[:, :, g:g + 1], EPG), ALU.mult))
                step(dve.tensor_tensor(sel, by_group[:, :, 0, :], by_group[:, :, 1, :], ALU.add))
                step(dve.tensor_tensor(sel, sel, by_group[:, :, 2, :], ALU.add))
                step(dve.tensor_tensor(sel, sel, by_group[:, :, 3, :], ALU.add))
                step(dve.tensor_reduce(stat[1], sel, AX.X, ALU.max))
                first_of(sel, stat[1], EPG, small8, one[0])
                step(dve.scalar_tensor_tensor(sel2, one[0], -1e30, sel, ALU.mult, ALU.add))
                step(dve.tensor_reduce(stat[2], sel2, AX.X, ALU.max))
                first_of(sel2, stat[2], EPG, small8, one[1])
                step(dve.tensor_tensor(stat[3], stat[2], stat[1], ALU.subtract))
                dve.sem_inc(dve_done, 1)
                for i in range(2):
                    for g in range(EG):
                        step(dve.tensor_tensor(OH[i][:, :, EPG * g:EPG * (g + 1)], one[i], wide(one_g[:, :, g:g + 1], EPG), ALU.mult))
                step(dve.tensor_tensor(M, OH[0], OH[1], ALU.add))
                dve.sem_inc(dve_done, 1)
                dve.wait_ge(exps, 2)
                step(dve.tensor_reduce(stat[4], gl_e, AX.X, ALU.add))
                step(dve.tensor_scalar(stat[5], stat[3], 1.0, None, ALU.add))
                step(dve.tensor_tensor(stat[4], stat[4], stat[5], ALU.mult))
                step(dve.reciprocal(stat[4], stat[4]))
                step(dve.tensor_copy(k.row_w[:, 0, :].unsqueeze(2), stat[4]))
                step(dve.tensor_tensor(k.row_w[:, 1, :].unsqueeze(2), stat[4], stat[3], ALU.mult))
                dve.wait_ge(ranks, 1)
                step(dve.tensor_copy(R, k.ps[:, 6, 0:NE * TC].rearrange("p (t e) -> p t e", t=TC)))
                step(dve.tensor_copy(cnt, k.ps[:, 6, NE * TC:NE * (TC + 1)]))
                for x, y, cmp in ((R, Q, ALU.is_ge), (cnt, nov, ALU.is_gt)):
                    step(dve.tensor_scalar(y, x, 128.0, None, cmp))
                    for edge in (256.0, 384.0):
                        step(dve.scalar_tensor_tensor(y, x, edge, y, cmp, ALU.add))
                step(dve.tensor_tensor_scan(end, k.ones[:, 0:NE], nov, 0.0, ALU.mult, ALU.add))
                step(dve.tensor_tensor(st, end, nov, ALU.subtract))
                step(dve.tensor_tensor(off, st, erow, ALU.subtract))
                step(dve.tensor_scalar(off, off, float(NE - 1), None, ALU.add))
                step(dve.tensor_tensor(t1, Q, row(off, NE), ALU.add))
                step(dve.scalar_tensor_tensor(t1, Q, 0.0, t1, ALU.is_gt, ALU.mult))
                step(dve.tensor_tensor(t1, t1, row(erow, NE), ALU.add))
                step(dve.scalar_tensor_tensor(t1, t1, 128.0, R, ALU.mult, ALU.add))
                step(dve.scalar_tensor_tensor(t1, Q, -128.0, t1, ALU.mult, ALU.add))
                for i in range(2):
                    step(dve.tensor_tensor(t2, t1, OH[i], ALU.mult))
                    step(dve.tensor_reduce(k.row_slot[:, i, :].unsqueeze(2), t2, AX.X, ALU.add))
                step(dve.tensor_copy(k.row_index[:, :, :], k.row_slot[:, :, :]))
                wide8 = lambda ap: ap.unsqueeze(1).to_broadcast([P, 8, NE])
                jcol = k.trow[:, 0:8].unsqueeze(2).to_broadcast([P, 8, NE])
                step(dve.tensor_tensor(ind, wide8(st), jcol, ALU.is_le))
                step(dve.tensor_tensor(ind2, wide8(end), jcol, ALU.is_gt))
                step(dve.tensor_tensor(ind, ind, ind2, ALU.mult))
                step(dve.tensor_tensor(ind, ind, wide8(erow), ALU.mult))
                step(dve.tensor_reduce(eid, ind, AX.X, ALU.add))
                step(dve.tensor_copy(k.block_expert[:, 0:NE], erow[0:1, :]))
                step(dve.tensor_copy(k.block_expert[:, NE:NE + 8], eid[0:1, :]))


def experts(k, l, rows_out):
    n0 = k.first[f"experts{l}"]
    h_tok = k.B[:, :, :].rearrange("p a b -> p (a b)").rearrange("p (t d) -> p t d", t=TC)
    flat = lambda lo: k.C[:, lo:lo + 2, :].rearrange("p a b -> p (a b)")
    xb = [flat(0).rearrange("p (c r) -> p c r", c=DC), flat(2).rearrange("p (c r) -> p c r", c=DC)]
    yb = [flat(4), flat(6)]
    pick, gate, hidden, hidden_t, row_no = (k.tmp[:, n, :] for n in (0, 1, 2, 3, 4))
    blocks = lambda ap: ap.rearrange("p (a b) -> p a b", b=P)
    last = BLOCKS - 1
    with k.stage(12) as (block, picked, gathered, x_ready, up_ready, gate_ready, hidden_ready, turned, turned_copied,
                         y_ready, stored0, stored1, dve_step):
        y_copied = k.y_copied
        slot = lambda p, j: k.slot(n0 + 3 * p + j)
        stored = [stored0, stored1]

        @block.sync
        def _(sp):
            def load(b, i, p):
                expert = sp.value_load(k.block_expert[0:1, bass.ds(b, 1)], min_val=0, max_val=NE - 1)
                for j, (name, kc) in enumerate((("w1_2", DC), ("w3_2", DC), ("w2_2", F // P))):
                    n = n0 + 3 * p + j
                    sp.wait_ge(k.weights_used, i * 6 + (n + 1))
                    src = k.ins[name][l][bass.ds(expert, 1), :, :].rearrange("o (k p) n -> p (o k) n", p=P)
                    sp.dma_start(k.slot(n)[:, :].rearrange("p (k n) -> p k n", k=kc), src)\
                        .then_inc(k.weights_loaded[n % SLOTS], 16)
            k.feed(sp, 0)
            with sp.Fori(0, (BLOCKS - 3) // 2) as i:
                load(i * 2 + 2, i, 0)
                load(i * 2 + 3, i, 1)
            load(last, (BLOCKS - 3) // 2, 0)
            k.issued = n0 + 3 * BLOCKS
            k.used = n0 + 3 * BLOCKS
            k.feed(sp, 0)

        @block.tensor
        def _(pe):
            def gather(b, p):
                pe.wait_ge(picked, b + 1)
                for half in range(2):
                    for c in range(4):
                        for t in range(TC):
                            ins = pe.matmul(k.ps[:, half, c * P:(c + 1) * P], h_tok[:, t, (4 * half + c) * P:(4 * half + c + 1) * P],
                                            pick[:, t * P:(t + 1) * P], start=(t == 0), stop=(t == TC - 1))
                    ins.then_inc(gathered, 1)

            def up(b, i, p):
                pe.wait_ge(x_ready, b * 2 + 2)
                for j in range(2):
                    n = n0 + 3 * p + j
                    pe.wait_ge(k.weights_loaded[n % SLOTS], i * 16 + 16 * (n // SLOTS + 1))
                    w = k.slot(n).rearrange("p (k n) -> p k n", k=DC)
                    if j == 0:
                        pe.wait_ge(hidden_ready, b + 1)
                    for c in range(DC):
                        ins = pe.matmul(k.ps[:, 2 + j, :], xb[p][:, c, :], w[:, c, :], start=(c == 0), stop=(c == DC - 1))
                    ins.then_inc(up_ready, 1)

            def down(b, i, p):
                n = n0 + 3 * p + 2
                pe.wait_ge(hidden_ready, b + 2)
                for j in range(4):
                    ins = pe.transpose(k.ps[:, 4, j * P:(j + 1) * P], hidden[:, j * P:(j + 1) * P], k.ident[:, :])
                ins.then_inc(turned, 1)
                pe.wait_ge(k.weights_loaded[n % SLOTS], i * 16 + 16 * (n // SLOTS + 1))
                pe.wait_ge(y_copied, b * 2 + (2 * BLOCKS * l + 1))
                pe.wait_ge(turned_copied, b + 1)
                w = k.slot(n).rearrange("p (k n) -> p k n", k=F // P)
                for half in range(2):
                    for f in range(F // P):
                        ins = pe.matmul(k.ps[:, 5 + half, :], hidden_t[:, f * P:(f + 1) * P], w[:, f, 512 * half:512 * half + 512],
                                        start=(f == 0), stop=(f == F // P - 1))
                    ins.then_inc(y_ready, 1)

            pe.sem_inc(turned, 1)
            pe.sem_inc(y_ready, 1)
            gather(0, 0)
            with pe.Fori(0, BLOCKS // 2) as i:
                for p in range(2):
                    up(i * 2 + p, i, p)
                    gather(i * 2 + (p + 1), 1 - p)
                    down(i * 2 + p, i, p)
            up(last, BLOCKS // 2, 0)
            down(last, BLOCKS // 2, 0)

        @block.scalar
        def _(act):
            def take(b, p):
                for half in range(2):
                    act.wait_ge(gathered, b * 2 + (half + 1))
                    act.activation(xb[p][:, 4 * half:4 * half + 4, :], blocks(k.ps[:, half, :]), ACT.Copy).then_inc(x_ready, 1)

            def gates(b, p):
                act.wait_ge(up_ready, b * 2 + 1)
                act.wait_ge(hidden_ready, b + 1)
                act.activation(gate, k.ps[:, 2, :], ACT.Silu).then_inc(gate_ready, 1)

            def finish(b, i, p):
                act.wait_ge(turned, b + 2)
                act.wait_ge(y_ready, b * 2 + 1)
                act.activation(hidden_t, k.ps[:, 4, :], ACT.Copy).then_inc(turned_copied, 1)
                act.wait_ge(stored[p], i * 16 + 16)
                for half in range(2):
                    act.wait_ge(y_ready, b * 2 + (half + 2))
                    act.activation(yb[p][:, 512 * half:512 * half + 512], k.ps[:, 5 + half, :], ACT.Copy).then_inc(y_copied, 1)
                act.sem_inc(k.weights_used, 3)
                act.wait_ge(y_copied, b * 2 + (2 * BLOCKS * l + 3))
                act.dma_start(rows_out[bass.ds(b, 1), :, :].rearrange("o p d -> p (o d)"), yb[p]).then_inc(stored[p], 16)

            if l == 0:
                act.sem_inc(y_copied, 1)
            act.sem_inc(stored[0], 16)
            act.sem_inc(stored[1], 16)
            take(0, 0)
            with act.Fori(0, BLOCKS // 2) as i:
                for p in range(2):
                    gates(i * 2 + p, p)
                    take(i * 2 + (p + 1), 1 - p)
                    finish(i * 2 + p, i, p)
            gates(last, 0)
            finish(last, BLOCKS // 2, 0)
            act.wait_ge(stored[0], 16 * (BLOCKS // 2 + 2))
            act.wait_ge(stored[1], 16 * (BLOCKS // 2 + 1))

        @block.vector
        def _(dve):
            slots = lambda i: k.row_slot[:, i, :].unsqueeze(2).to_broadcast([P, TC, P])
            rows = row_no[:, 0:P].unsqueeze(1).to_broadcast([P, TC, P])
            other = k.tmp[:, 5, :]

            def choose(step, b):
                step(dve.tensor_tensor(blocks(other), rows, slots(0), ALU.is_equal))
                dve.wait_ge(gathered, b * 2)
                step(dve.tensor_tensor(blocks(pick), rows, slots(1), ALU.is_equal))
                step(dve.tensor_tensor(pick, pick, other, ALU.add))
                dve.sem_inc(picked, 1)
                step(dve.tensor_scalar(row_no[:, 0:P], row_no[:, 0:P], float(P), None, ALU.add))

            def hide(step, b):
                dve.wait_ge(gate_ready, b + 1)
                dve.wait_ge(up_ready, b * 2 + 2)
                dve.wait_ge(turned, b + 1)
                step(dve.tensor_tensor(hidden, gate, k.ps[:, 3, :], ALU.mult))
                dve.sem_inc(hidden_ready, 1)

            step = Steps(dve, dve_step)
            step(dve.tensor_copy(row_no[:, 0:P], k.trow[:, 0:P]))
            dve.sem_inc(hidden_ready, 1)
            choose(step, 0)
            done = step.n
            with dve.Fori(0, BLOCKS // 2) as i:
                step = Steps(dve, dve_step, i * 10 + done)
                for p in range(2):
                    choose(step, i * 2 + (p + 1))
                    hide(step, i * 2 + p)
                assert step.n == 10
            step = Steps(dve, dve_step, 10 * (BLOCKS // 2) + done)
            hide(step, last)


def combine(k, l, rows_out):
    row = [k.A[:, :, :].rearrange("p a b -> p (a b)").rearrange("p (t d) -> p t d", t=TC),
           k.C[:, :, :].rearrange("p a b -> p (a b)").rearrange("p (t d) -> p t d", t=TC)]
    source = rows_out.rearrange("b p d -> (b p) d")
    fetched = k.rows_fetched
    with k.stage(3) as (block, mixed, turned, dve_step):
        @block.sync
        def _(sp):
            k.feed(sp, 0)

        @block.gpsimd
        def _(pool):
            for t in range(TC):
                for i in range(2):
                    pool.indirect_dma_start(row[i][:, t, :], None, source,
                                            bass.IndirectOffsetOnAxis(ap=k.row_index[:, i, t:t + 1], axis=0)).then_inc(fetched[t], 16)

        @block.vector
        def _(dve):
            step = Steps(dve, dve_step)
            for t in range(TC):
                dve.wait_ge(fetched[t], 32 * (l + 1))
                step(dve.tensor_scalar(row[0][:, t, :], row[0][:, t, :], k.row_w[:, 0, t:t + 1], None, ALU.mult))
                step(dve.scalar_tensor_tensor(row[0][:, t, :], row[1][:, t, :], k.row_w[:, 1, t:t + 1], row[0][:, t, :],
                                              ALU.mult, ALU.add))
            dve.sem_inc(mixed, 1)
            for c in range(DC):
                dve.wait_ge(turned, c + 1)
                step(dve.scalar_tensor_tensor(k.X[:, c, :], k.ps[:, c % 4, :], mod(k, l, "g2", c), k.X[:, c, :], ALU.mult, ALU.add))

        @block.tensor
        def _(pe):
            pe.wait_ge(mixed, 1)
            for c in range(DC):
                if c >= 4:
                    pe.wait_ge(dve_step, 2 * TC + c - 3)
                for t in range(TC):
                    ins = pe.transpose(k.ps[:, c % 4, t * P:(t + 1) * P], row[0][:, t, c * P:(c + 1) * P], k.ident[:, :])
                ins.then_inc(turned, 1)


def mixture(k, l):
    modulated_norm(k, l, 2)
    routing(k, l)
    rows_out = k.nc.dram_tensor(f"expert_rows{l}", (BLOCKS, P, D), F32, kind="Internal").ap()
    experts(k, l, rows_out)
    combine(k, l, rows_out)


def columns(x):
    out = {}

    def put(name, v):
        v = np.asarray(v).reshape(-1)
        pad = -len(v) % P
        if pad:
            v = np.concatenate([v, np.zeros(pad, v.dtype)])
        out[name] = v.reshape(-1, P).T

    for j in range(2):
        for w in range(3):
            put(f"conv_k{j}_{w}", x["conv_k"][j, w])
    for i in range(DEPTH):
        put(f"ln_g{i}", x["ln_g"][i])
        put(f"ln_b{i}", x["ln_b"][i])
    for n in range(6):
        put(f"rwkv_mu{n}", x["rwkv_mu"][0, n])
    put("rwkv_w0", x["rwkv_w0"])
    put("rwkv_a0", x["rwkv_a0"])
    put("c", x["c_2"])
    put("eps", np.full(P, EPS, np.float32))
    half = ROPE // 2
    freq = np.zeros(P, np.float32)
    freq[64:96] = np.tile((np.float32(10000.0) ** (-np.arange(half, dtype=np.float32) / half)).astype(np.float32), 2)
    put("rope_freq", freq)
    put("rope_sign", np.where(np.arange(P) < 80, -1.0, 1.0).astype(np.float32))
    put("lb_logits", x["hgrn_lb_logits_2"])
    for l in range(2):
        for name, key in (("b_ada", "b_ada"), ("norm1_g", "norm1_g"), ("norm2_g", "norm2_g"), ("q_a_g", "q_a_norm_g"),
                          ("kv_a_g", "kv_a_norm_g"), ("q_g", "q_norm_g"), ("k_g", "k_norm_g"), ("pool_scale", "pool_scale"),
                          ("dw_b", "conv_dw_b"), ("cln_g", "conv_ln_g"), ("cln_b", "conv_ln_b")):
            put(f"{name}{l}", x[f"{key}_2"][l])
        put(f"hgrn_g{l}", np.tile(x["hgrn_out_norm_g_2"][l], 2))
        for j in range(CONV_K):
            put(f"dw_w{l}_{j}", x["conv_dw_w_2"][l, j])
    put("gn_eps", np.full(P, GN_EPS, np.float32))
    put("ssm_d", x["ssm_d"])
    put("ssm_b_glu", x["ssm_b_glu"])
    put("half_pi", np.full(P, np.pi / 2, np.float32))
    put("ln_eps", np.full(P, LN_EPS, np.float32))
    return out


def ssm_layouts(x):
    tile = lambda v: np.asarray(v)[0].reshape(32, P).T
    log_dt = np.broadcast_to(x["ssm_log_dt"][0][:, None], (64, 64))
    raw = [tile(x["ssm_lam_re"]), tile(x["ssm_lam_im"]), log_dt.reshape(32, P).T]
    b = np.zeros((P, 2, DC, P), np.float32)
    c = np.zeros((P, 2, 32, 32), np.float32)
    for part, (bn, cn) in enumerate((("ssm_b_re", "ssm_c_re"), ("ssm_b_im", "ssm_c_im"))):
        for g in range(64):
            j, half = divmod(g, 2)
            row = 32 * (j % 4) + 16 * half
            b[row:row + 16, part, j // 4, 64 * half:64 * half + 64] = x[bn][0, g].T
            c[64 * half:64 * half + 64, part, j, 16 * half:16 * half + 16] = x[cn][0, g].T
    return {"ssm_raw": np.concatenate(raw, axis=1), "ssm_b": b.reshape(P, -1), "ssm_c": c.reshape(P, -1)}


def small_layouts(x):
    out = np.zeros((2, P, SMALL_COLS), np.float32)
    where = lambda name: slice(SMALL[name][0], SMALL[name][0] + SMALL[name][1])
    swap = np.zeros((P, P), np.float32)
    for i in range(64, 80):
        swap[i, i + 16] = swap[i + 16, i] = 1.0
    strip = np.zeros((P, 896), np.float32)
    strip[:, 384:512] = np.where(np.arange(P)[None, :] > np.arange(P)[:, None], -1e30, 0.0)
    inv = np.zeros((P, 2, T), np.float32)
    for g, w in enumerate((2, 4, 8, 16)):
        inv[64 * (g % 2):64 * (g % 2) + 64, g // 2] = 1.0 / np.minimum(np.arange(1, T + 1), w)
    for l in range(2):
        uq = x["w_uq_2"][l]
        out[l, :, where("w_uq")][:, 0:384] = uq[0:P]
        out[l, 0:64, 384:768] = uq[P:192]
        out[l, :, where("w_ukv")] = x["w_ukv_2"][l]
        out[l, :, where("swap")] = swap
        out[l, :, where("strip")] = strip
        out[l, :, where("pool_inv")] = inv.reshape(P, -1)
        out[l, :, where("w_pool")] = x["w_pool_2"][l].reshape(2, 2, 64, 64).transpose(1, 2, 0, 3).reshape(P, P)
    return out


MASKS = ["ident", "sooner", "before", "upto", "first_lower"] + [f"level{l}" for l in range(7)]
CONSTS = [("ones", P), ("pairs", P), ("trow", T), ("seg64", T), ("seg128", T)] + [(name, P) for name in MASKS]


def constant_values():
    p = np.arange(P)
    row, one = p[:, None], p[None, :]
    same = row // 64 == one // 64
    c = {
        "ones": np.ones((P, P)),
        "ident": np.eye(P),
        "seg64": np.tile(np.arange(T) % 64 != 0, (P, 1)),
        "seg128": np.tile(np.arange(T) % 128 != 0, (P, 1)),
        "before": same & (row < one),
        "sooner": row < one,
        "upto": same & (row <= one),
        "first_lower": ((row // 2) == (one // 2)) & (row > one),
        "pairs": (p[:, None] // 64 == p[None, :] // 64),
        "trow": np.tile(np.arange(T), (P, 1)),
    }
    for l in range(7):
        c[f"level{l}"] = (row >> (l + 1) == one >> (l + 1)) & (row >> l & 1 == 0) & (one >> l & 1 == 1)
    return np.concatenate([c[name].reshape(P, n).astype(np.float32) for name, n in CONSTS], axis=1)


def device_inputs(x):
    x = {name: np.asarray(v) for name, v in x.items()}
    cols = columns(x)
    where, at = {}, 0
    for name, v in cols.items():
        where[name] = at
        at += v.shape[1]
    d = {
        "x_t": x["x"][0].T,
        "p_t": x["p"][:, 0].transpose(0, 2, 1),
        "cols": np.concatenate(list(cols.values()), axis=1),
        "consts": constant_values(),
    }
    d.update(ssm_layouts(x))
    d["small"] = small_layouts(x)
    d["positions"] = x["positions_2"]
    d["router_w"] = np.concatenate([x["router_group_w_2"], x["router_expert_w_2"]], axis=2)
    d["router_b"] = np.concatenate([x["router_group_b_2"], x["router_expert_b_2"]], axis=1)
    for name in ("w1_2", "w3_2", "w2_2"):
        d[name] = x[name]
    for name in ("w_ada_2", "w_in_2", "w_out_2"):
        d[name] = x[name]
    for name in ("w1", "w2", "a1", "a2"):
        d[f"rwkv_{name}"] = x[f"rwkv_{name}"][0]
    per_pair = [x[f"rwkv_{name}"].reshape(DC, P) for name in ("k_k", "k_a", "r_k", "lnx_g", "lnx_b")]
    per_pair += [np.zeros((DC, P), np.float32)] * 3
    d["rwkv_pairs"] = np.stack(per_pair, axis=-1)
    for name in ("conv_w_in", "conv_w_out", "ssm_w_in", "ssm_w_glu", "ssm_w_out", "rwkv_w_rkvz", "rwkv_w_out",
                 "ple_proj", "ple_gate"):
        d[name] = x[name]
    return {name: np.ascontiguousarray(v) for name, v in d.items()}, where


def build(nc, ins, out, where):
    with ExitStack() as ctx:
        k = Kernel(nc, ctx, ins, out)
        k.where = where
        tiles = {name: ctx.enter_context(nc.sbuf_tensor(f"const_{name}", [P, n], F32)) for name, n in CONSTS}
        k.ones, k.pairs, k.trow, k.ident = tiles["ones"], tiles["pairs"], tiles["trow"], tiles["ident"]
        k.seg = {64: tiles["seg64"], 128: tiles["seg128"]}
        k.mask = {name: tiles[name] for name in MASKS}
        k.const_tiles = [(tiles[name][:, :], n) for name, n in CONSTS]
        plan_weights(k)
        load_constants(k)
        for layer in range(DEPTH):
            if layer % 3 == 0:
                short_conv(k, layer // 3)
            elif layer % 3 == 1:
                ssm_mixer(k)
            else:
                rwkv_mixer(k)
            src, r = (k.B, k.A) if layer % 3 == 1 else (k.A, k.B)
            output_and_gate(k, layer, src, r)
            layer_norm(k, layer)
        modulation(k)
        for l in range(2):
            modulated_norm(k, l, 1)
            mla(k, l)
            pool_mixer(k, l)
            hgrn(k, l)
            conformer(k, l)
            mixer_output(k, l)
            mixture(k, l)
        store_output(k)


def kernel(**inputs):
    import concourse.bacc as bacc
    from concourse.bass_utils import run_bass_kernel_spmd

    nc = bacc.Bacc("TRN2", target_bir_lowering=False, num_devices=1)
    arrays, where = device_inputs(inputs)
    ins = {name: nc.dram_tensor(f"in_{name}", a.shape, mybir.dt.from_np(a.dtype), kind="ExternalInput").ap()
           for name, a in arrays.items()}
    out = nc.dram_tensor("out_t", (D, T), F32, kind="ExternalOutput").ap()
    build(nc, ins, out, where)
    r = run_bass_kernel_spmd(nc, [{f"in_{name}": a for name, a in arrays.items()}], core_ids=[0])
    return np.ascontiguousarray(r.results[0]["out_t"].T)[None]
```

```python
from contextlib import ExitStack, contextmanager

import numpy as np

import concourse.bass as bass
from concourse import mybir

F32 = mybir.dt.float32
I32 = mybir.dt.int32
ALU = mybir.AluOpType
ACT = mybir.ActivationFunctionType
AX = mybir.AxisListType

P = 128
D = 1024
DC = D // P
T = 512
TC = T // P
DEPTH = 4
ALPHA = float((2 * DEPTH) ** 0.25)
LN_EPS = 1e-5
GN_EPS = 64e-5
EPS = 1e-6
SLOTS = 6
SLOT = 4096
TWO_PI = 2.0 * np.pi
ROUND = 12582912.0
PI_A = 6.28125
PI_B = 0.0019350051879882812
PI_C = float(TWO_PI - 6.28125 - 0.0019350051879882812)


class Steps:

    def __init__(self, eng, sem, base=0):
        self.eng, self.sem, self.n, self.base = eng, sem, 0, base

    def __call__(self, ins, wait=True):
        ins.then_inc(self.sem, 1)
        self.n += 1
        if wait:
            self.eng.wait_ge(self.sem, self.base + self.n)


class Kernel:
    def __init__(self, nc, ctx, ins, out):
        self.nc, self.ctx, self.ins, self.out = nc, ctx, ins, out
        sb = lambda name, shape, dt=F32: ctx.enter_context(nc.sbuf_tensor(name, shape, dt))
        self.sb = sb
        self.ring = sb("weight_ring", [P, SLOTS, SLOT])
        self.X = sb("residual", [P, DC, T])
        self.A = sb("work_a", [P, DC, T])
        self.B = sb("work_b", [P, DC, T])
        self.C = sb("work_c", [P, DC, T])
        self.cols = sb("column_params", [P, ins["cols"].shape[1]])
        self.tmp = sb("tmp", [P, 6, T])
        self.c_act = sb("c_act", [P, DC])
        self.mod = sb("modulation", [P, 2, 48])
        self.row_w = sb("row_weights", [P, 2, TC])
        self.row_slot = sb("row_slots", [P, 2, TC])
        self.row_index = sb("row_indices", [P, 2, TC], I32)
        self.block_expert = sb("block_experts", [1, NE + FURTHER], I32)
        self.pair_count = sb("pair_count", [1, 1], I32)
        self.lb = sb("lower_bound", [P, 10])
        self.ps = ctx.enter_context(nc.psum_tensor("banks", [P, 8, 512], F32))
        sem = lambda name: ctx.enter_context(nc.semaphore(name))
        self.weights_loaded = [sem(f"weights_loaded_{i}") for i in range(SLOTS)]
        self.weights_used = sem("weights_used")
        self.dev_ready = sem("deviation_ready")
        self.rows_fetched = [sem(f"rows_fetched_{t}") for t in range(TC)]
        self.output_stored = sem("output_stored")
        self.signals = [[sem(f"stage_{h}_{i}") for i in range(16)] for h in range(2)]
        self.stage_no = 0
        self.queue = []
        self.first = {}
        self.issued = self.used = 0

    def slot(self, n):
        return self.ring[:, n % SLOTS, :]

    def want(self, name, src, kc, cols):
        self.first.setdefault(name, len(self.queue))
        self.queue.append((src, kc, cols))

    def want_halves(self, name, src, kc=DC):
        for q in range(src.shape[1] // 512):
            self.want(name, src[:, q * 512:(q + 1) * 512], kc, 512)

    def chunk(self, n):
        _, kc, cols = self.queue[n]
        return self.slot(n)[:, 0:kc * cols].rearrange("p (k n) -> p k n", k=kc)

    def feed(self, sp, consumed):
        self.used += consumed
        while self.issued < min(len(self.queue), self.used + SLOTS):
            n = self.issued
            src, kc, cols = self.queue[n]
            if src is None:
                break
            if n >= SLOTS:
                sp.wait_ge(self.weights_used, n - SLOTS + 1)
            sp.dma_start(self.chunk(n), src.rearrange("(k p) n -> p k n", p=P)).then_inc(
                self.weights_loaded[n % SLOTS], 16)
            self.issued += 1

    def loaded(self, pe, n):
        pe.wait_ge(self.weights_loaded[n % SLOTS], 16 * (n // SLOTS + 1))

    @contextmanager
    def stage(self, signals):
        mine = self.signals[self.stage_no % 2]
        other = self.signals[(self.stage_no + 1) % 2]
        self.stage_no += 1
        with self.nc.Block() as block:
            if self.stage_no > 1:
                @block.gpsimd
                def _(pool):
                    for s in other:
                        pool.sem_clear(s)
            yield (block, *mine[:signals])


def col(k, name, i, n=P):
    at = k.where[name]
    return k.cols[0:n, at + i:at + i + 1]


def plan_weights(k):
    i = k.ins
    for layer in range(DEPTH):
        j = layer // 3
        if layer % 3 == 0:
            for q in range(2):
                for part in (1, 2, 0, 3):
                    at = part * D + q * 512
                    k.want(f"conv_in{j}", i["conv_w_in"][j][:, at:at + 512], DC, 512)
            w_out = i["conv_w_out"][j]
        elif layer % 3 == 1:
            k.want_halves("ssm_in", i["ssm_w_in"][0])
            k.want_halves("ssm_glu", i["ssm_w_glu"][0])
            w_out = i["ssm_w_out"][0]
        else:
            for n in range(4):
                k.want_halves("rwkv_in", i["rwkv_w_rkvz"][0, n])
            for n in range(24):
                k.want("ada0", i["w_ada_chunks"][n] if n < 6 else None, DC, 512)
            w_out = i["rwkv_w_out"][0]
        k.want_halves(f"out{layer}", w_out)
        k.want(f"out{layer}", i["ple_proj"][layer], 2, D)
        k.want_halves(f"out{layer}", i["ple_gate"][layer])
    for l in range(2):
        plan_mixer(k, l)
        plan_experts(k, l)


def accumulate(k, pe, bank, n, m, src, kc, size=P):
    w = k.chunk(n)
    for c in range(kc):
        last = pe.matmul(bank, w[:, c, m:m + size], src[:, c, :], start=(c == 0), stop=(c == kc - 1))
    return last


def load_constants(k):
    with k.stage(1) as (block, landed):
        @block.sync
        def _(sp):
            k.feed(sp, 0)

        @block.scalar
        def _(act):
            loads = [(k.X[:, :, :], k.ins["x_t"].rearrange("(c p) t -> p c t", p=P)),
                     (k.cols[:, :], k.ins["cols"])]
            at = 0
            for dst, n in k.const_tiles:
                loads.append((dst, k.ins["consts"][:, at:at + n]))
                at += n
            for dst, src in loads:
                act.dma_start(dst, src).then_inc(landed, 16)
            act.wait_ge(landed, 16 * len(loads))


def short_conv(k, layer):
    first = k.first[f"conv_in{layer}"]
    with k.stage(6) as (block, product_ready, cg_copied, gate_ready, unit_done, dve_step, act_step):
        @block.sync
        def _(sp):
            k.feed(sp, 8)

        @block.tensor
        def _(pe):
            for q in range(2):
                for m in range(4):
                    unit = 4 * q + m
                    if unit >= 2:
                        pe.wait_ge(unit_done, unit - 1)
                    for w in range(4):
                        if m == 0:
                            k.loaded(pe, first + 4 * q + w)
                        accumulate(k, pe, k.ps[:, 4 * (unit % 2) + w, :], first + 4 * q + w, m * P, k.X, DC)\
                            .then_inc(product_ready, 1)

        @block.scalar
        def _(act):
            for unit in range(8):
                half = unit % 2
                act.wait_ge(product_ready, 4 * unit + 1)
                if unit >= 2:
                    act.wait_ge(unit_done, unit - 1)
                act.activation(k.tmp[:, 3 * half, :], k.ps[:, 4 * half, :], ACT.Copy).then_inc(cg_copied, 1)
                act.wait_ge(product_ready, 4 * unit + 4)
                act.activation(k.tmp[:, 3 * half + 1, :], k.ps[:, 4 * half + 3, :], ACT.Silu).then_inc(gate_ready, 1)

        @block.vector
        def _(dve):
            step = Steps(dve, dve_step)
            tap = [[col(k, f"conv_k{layer}_{w}", u) for u in range(DC)] for w in range(3)]
            for unit in range(8):
                half = unit % 2
                u, out = k.tmp[:, 3 * half + 2, :], k.A[:, unit, :]
                dve.wait_ge(cg_copied, unit + 1)
                dve.wait_ge(product_ready, 4 * unit + 2)
                step(dve.tensor_tensor(u, k.tmp[:, 3 * half, :], k.ps[:, 4 * half + 1, :], ALU.mult))
                step(dve.tensor_scalar(out, u, tap[2][unit], None, ALU.mult))
                step(dve.scalar_tensor_tensor(out[:, 1:T], u[:, 0:T - 1], tap[1][unit], out[:, 1:T], ALU.mult, ALU.add))
                step(dve.scalar_tensor_tensor(out[:, 2:T], u[:, 0:T - 2], tap[0][unit], out[:, 2:T], ALU.mult, ALU.add))
                dve.wait_ge(product_ready, 4 * unit + 3)
                step(dve.tensor_tensor(out, out, k.ps[:, 4 * half + 2, :], ALU.mult))
                dve.wait_ge(gate_ready, unit + 1)
                step(dve.tensor_tensor(out, out, k.tmp[:, 3 * half + 1, :], ALU.mult))
                dve.sem_inc(unit_done, 1)
                if unit % 4 == 3:
                    dve.sem_inc(k.weights_used, 4)


def output_and_gate(k, layer, src, r):
    first = k.first[f"out{layer}"]
    p_t = k.tmp[:, 4:6, :]
    with k.stage(6) as (block, p_loaded, mixed, summed, gated, gate_ready, dve_step):
        @block.sync
        def _(sp):
            sp.dma_start(p_t, k.ins["p_t"][layer].rearrange("(c p) t -> p c t", p=P)).then_inc(p_loaded, 16)
            k.feed(sp, 5)

        @block.tensor
        def _(pe):
            for m in range(DC):
                if m % 4 == 0:
                    k.loaded(pe, first + m // 4)
                if m >= 4:
                    pe.wait_ge(summed, m - 3)
                accumulate(k, pe, k.ps[:, m % 4, :], first + m // 4, m % 4 * P, src, DC).then_inc(mixed, 1)
            pe.wait_ge(p_loaded, 16)
            k.loaded(pe, first + 2)
            pe.wait_ge(summed, DC)
            for m in range(DC):
                if m % 4 == 0:
                    k.loaded(pe, first + 3 + m // 4)
                if m >= 2:
                    pe.wait_ge(summed, DC + m - 1)
                accumulate(k, pe, k.ps[:, 4 + m % 2, :], first + 3 + m // 4, m % 4 * P, r, DC).then_inc(gated, 1)
                accumulate(k, pe, k.ps[:, 6 + m % 2, :], first + 2, m * P, p_t, 2).then_inc(gated, 1)

        @block.scalar
        def _(act):
            for m in range(DC):
                act.wait_ge(gated, 2 * m + 1)
                if m >= 2:
                    act.wait_ge(summed, DC + m - 1)
                act.activation(k.tmp[:, m % 2, :], k.ps[:, 4 + m % 2, :], ACT.Sigmoid).then_inc(gate_ready, 1)

        @block.vector
        def _(dve):
            step = Steps(dve, dve_step)
            for m in range(DC):
                dve.wait_ge(mixed, m + 1)
                dve.scalar_tensor_tensor(r[:, m, :], k.X[:, m, :], ALPHA, k.ps[:, m % 4, :], ALU.mult, ALU.add)\
                    .then_inc(summed, 1)
                if m % 4 == 3:
                    dve.sem_inc(k.weights_used, 1)
            for m in range(DC):
                dve.wait_ge(gate_ready, m + 1)
                dve.wait_ge(gated, 2 * m + 2)
                step(dve.tensor_tensor(k.tmp[:, 2, :], k.tmp[:, m % 2, :], k.ps[:, 6 + m % 2, :], ALU.mult))
                step(dve.tensor_tensor(k.X[:, m, :], r[:, m, :], k.tmp[:, 2, :], ALU.add))
                dve.sem_inc(summed, 1)
            dve.sem_inc(k.weights_used, 3)


def layer_norm(k, layer):
    with k.stage(5) as (block, sums, centred, squared, deviation, dve_step):
        @block.sync
        def _(sp):
            k.feed(sp, 0)

        @block.tensor
        def _(pe):
            for c in range(DC):
                last = pe.matmul(k.ps[:, 0, :], k.ones[:, :], k.X[:, c, :], start=(c == 0), stop=(c == DC - 1))
            last.then_inc(sums, 1)
            for c in range(DC):
                pe.wait_ge(squared, c + 1)
                last = pe.matmul(k.ps[:, 1, :], k.ones[:, :], k.B[:, c, :], start=(c == 0), stop=(c == DC - 1))
            last.then_inc(sums, 1)

        @block.scalar
        def _(act):
            for c in range(DC):
                act.wait_ge(centred, c + 1)
                act.activation(k.B[:, c, :], k.A[:, c, :], ACT.Square).then_inc(squared, 1)
            act.wait_ge(sums, 2)
            act.activation(k.tmp[:, 0, :], k.ps[:, 1, :], ACT.Sqrt, bias=col(k, "ln_eps", 0), scale=1.0 / D)\
                .then_inc(deviation, 1)

        @block.vector
        def _(dve):
            step = Steps(dve, dve_step)
            dve.wait_ge(sums, 1)
            for c in range(DC):
                dve.scalar_tensor_tensor(k.A[:, c, :], k.ps[:, 0, :], -1.0 / D, k.X[:, c, :], ALU.mult, ALU.add)\
                    .then_inc(centred, 1)
            dve.wait_ge(deviation, 1)
            step(dve.reciprocal(k.tmp[:, 1, :], k.tmp[:, 0, :]))
            for c in range(DC):
                step(dve.tensor_tensor(k.A[:, c, :], k.A[:, c, :], k.tmp[:, 1, :], ALU.mult))
                step(dve.tensor_scalar(k.X[:, c, :], k.A[:, c, :], col(k, f"ln_g{layer}", c),
                                       col(k, f"ln_b{layer}", c), ALU.mult, ALU.add))


def store_output(k):
    stored = k.output_stored
    with k.stage(0) as (block,):
        @block.sync
        def _(sp):
            sp.dma_start(k.out.rearrange("(c p) t -> p c t", p=P), k.X[:, :, :]).then_inc(stored, 16)
            sp.wait_ge(stored, 16)


def reduce_angle(dve, step, angle, turns, scratch):
    step(dve.tensor_scalar(turns, angle, 1.0 / TWO_PI, ROUND, ALU.mult, ALU.add))
    step(dve.tensor_scalar(turns, turns, ROUND, None, ALU.subtract))
    step(dve.scalar_tensor_tensor(scratch, turns, -PI_A, angle, ALU.mult, ALU.add))
    step(dve.scalar_tensor_tensor(scratch, turns, -PI_B, scratch, ALU.mult, ALU.add))
    step(dve.scalar_tensor_tensor(scratch, turns, -PI_C, scratch, ALU.mult, ALU.add))
    step(dve.tensor_scalar(turns, scratch, 1.0 / TWO_PI, 0.5, ALU.mult, ALU.min))
    step(dve.tensor_scalar(turns, turns, -0.5, None, ALU.max))


TURN = 6.283185
G2 = 32


def ssm_project(k, name, halves, base, dst, func):
    first = k.first[name] + base
    with k.stage(3) as (block, product_ready, evacuated, act_step):
        @block.sync
        def _(sp):
            k.feed(sp, halves)

        @block.tensor
        def _(pe):
            for m in range(4 * halves):
                if m % 4 == 0:
                    k.loaded(pe, first + m // 4)
                if m >= 4:
                    pe.wait_ge(evacuated, m - 3)
                accumulate(k, pe, k.ps[:, m % 4, :], first + m // 4, m % 4 * P, k.X, DC).then_inc(product_ready, 1)

        @block.scalar
        def _(act):
            for m in range(4 * halves):
                act.wait_ge(product_ready, m + 1)
                act.activation(dst[:, m, :], k.ps[:, m % 4, :], func).then_inc(evacuated, 1)
                if m % 4 == 3:
                    act.sem_inc(k.weights_used, 1)


def ssm_scan(k):
    par_names = "re im dt rho turn a_re a_im den k_re k_im s0 s1".split()
    with ExitStack() as own:
        sb = lambda name, shape: own.enter_context(k.nc.sbuf_tensor(name, shape, F32))
        par = sb("ssm_params", [P, len(par_names), G2])
        raw = sb("ssm_raw", [P, 3, G2])
        bmat = sb("ssm_bmat", [P, 2, DC, P])
        cmat = sb("ssm_cmat", [P, 2, G2, 32])
        q = {name: par[:, i, :] for i, name in enumerate(par_names)}
        lr, li, log_dt = raw[:, 0, :], raw[:, 1, :], raw[:, 2, :]
        cf = k.tmp[:, 0:4, :].rearrange("p a (g h) -> p a g h", h=32)

        with k.stage(4) as (block, landed, dve_step, act_step, ready):
            @block.sync
            def _(sp):
                sp.dma_start(raw[:, :, :], k.ins["ssm_raw"].rearrange("p (a g) -> p a g", a=3)).then_inc(landed, 16)
                sp.dma_start(bmat[:, :, :, :], k.ins["ssm_b"].rearrange("p (a c n) -> p a c n", a=2, c=DC)).then_inc(landed, 16)
                sp.dma_start(cmat[:, :, :, :], k.ins["ssm_c"].rearrange("p (a g n) -> p a g n", a=2, g=G2)).then_inc(landed, 16)
                k.feed(sp, 0)

            @block.scalar
            def _(act):
                act.wait_ge(landed, 48)
                act.activation(q["dt"], log_dt, ACT.Exp).then_inc(act_step, 1)
                act.wait_ge(ready, 1)
                act.activation(q["rho"], q["re"], ACT.Exp).then_inc(act_step, 1)
                act.wait_ge(ready, 2)
                act.activation(q["s0"], q["turn"], ACT.Sin, scale=TURN).then_inc(act_step, 1)
                act.activation(q["s1"], q["k_re"], ACT.Sin, scale=-TURN, bias=col(k, "half_pi", 0)).then_inc(act_step, 1)

            @block.vector
            def _(dve):
                step = Steps(dve, dve_step)
                dve.wait_ge(act_step, 1)
                step(dve.tensor_tensor(q["re"], lr, q["dt"], ALU.mult))
                step(dve.tensor_tensor(q["im"], li, q["dt"], ALU.mult))
                dve.sem_inc(ready, 1)
                reduce_angle(dve, step, q["im"], q["turn"], q["k_re"])
                step(dve.scalar_tensor_tensor(q["k_re"], q["turn"], -1.0, q["turn"], ALU.mult, ALU.max))
                dve.sem_inc(ready, 1)
                dve.wait_ge(act_step, 4)
                step(dve.tensor_tensor(q["a_im"], q["rho"], q["s0"], ALU.mult))
                step(dve.tensor_tensor(q["a_re"], q["rho"], q["s1"], ALU.mult))
                step(dve.tensor_scalar(q["a_re"], q["a_re"], -1.0, None, ALU.add))
                step(dve.tensor_tensor(q["den"], lr, lr, ALU.mult))
                step(dve.tensor_tensor(q["s0"], li, li, ALU.mult))
                step(dve.tensor_tensor(q["den"], q["den"], q["s0"], ALU.add))
                step(dve.reciprocal(q["den"], q["den"]))
                step(dve.tensor_tensor(q["k_re"], q["a_re"], lr, ALU.mult))
                step(dve.tensor_tensor(q["s0"], q["a_im"], li, ALU.mult))
                step(dve.tensor_tensor(q["k_re"], q["k_re"], q["s0"], ALU.add))
                step(dve.tensor_tensor(q["k_re"], q["k_re"], q["den"], ALU.mult))
                step(dve.tensor_tensor(q["k_im"], q["a_im"], lr, ALU.mult))
                step(dve.tensor_tensor(q["s0"], q["a_re"], li, ALU.mult))
                step(dve.tensor_tensor(q["k_im"], q["k_im"], q["s0"], ALU.subtract))
                step(dve.tensor_tensor(q["k_im"], q["k_im"], q["den"], ALU.mult))
                for h in range(2):
                    g = slice(16 * h, 16 * h + 16)
                    kr = q["k_re"][:, g].unsqueeze(2).to_broadcast([P, 16, 32])
                    ki = q["k_im"][:, g].unsqueeze(2).to_broadcast([P, 16, 32])
                    cr, ci = cmat[:, 0, g, :], cmat[:, 1, g, :]
                    step(dve.tensor_tensor(cf[:, 0], cr, kr, ALU.mult))
                    step(dve.tensor_tensor(cf[:, 1], ci, ki, ALU.mult))
                    step(dve.tensor_tensor(cf[:, 2], cr, ki, ALU.mult))
                    step(dve.tensor_tensor(cf[:, 3], ci, kr, ALU.mult))
                    step(dve.tensor_tensor(cr, cf[:, 0], cf[:, 1], ALU.subtract))
                    step(dve.scalar_tensor_tensor(ci, cf[:, 2], -1.0, cf[:, 3], ALU.mult, ALU.subtract))

        u = k.tmp[:, 0, :]
        frac = [k.tmp[:, 1, :], k.tmp[:, 2, :]]
        size = [k.tmp[:, 3, :], k.tmp[:, 4, :]]
        sine, cosine = frac, size
        prod = k.C[:, 0:4, :]
        rot = [k.C[:, 4, :], k.C[:, 5, :]]
        scr = k.tmp[:, 5, :]
        scan = [k.C[:, 6, :], k.C[:, 7, :]]
        with ExitStack() as more:
            sb2 = lambda name, shape: more.enter_context(k.nc.sbuf_tensor(name, shape, F32))
            bc = sb2("ssm_b_chunk", [P, 2, P])
            cc = sb2("ssm_c_chunk", [P, 2, 4, 32])
            pc = sb2("ssm_param_chunk", [P, 4, 2])
            dc = sb2("ssm_d_chunk", [P, 1])
            with k.stage(10) as (block, chunk_ready, angle_ready, table_ready, bu_ready, bu_read, products_ready,
                                 products_used, y_ready, dve_step, act_step):
                STEPS = 4 * 16 + 1

                @block.sync
                def _(sp):
                    k.feed(sp, 0)

                @block.scalar
                def _(act):
                    with act.Fori(0, DC) as c:
                        act.wait_ge(y_ready, c * 2 + 1)
                        act.activation(u, k.B[:, bass.ds(c, 1), :], ACT.Copy).then_inc(chunk_ready, 1)
                        act.activation(bc[:, :, :], bmat[:, :, bass.ds(c, 1), :], ACT.Copy).then_inc(chunk_ready, 1)
                        act.activation(cc[:, :, :, :], cmat[:, :, bass.ds(c * 4, 4), :], ACT.Copy).then_inc(chunk_ready, 1)
                        act.activation(pc[:, :, 0], q["rho"][:, bass.ds(c * 4, 4)], ACT.Copy).then_inc(chunk_ready, 1)
                        act.activation(pc[:, :, 1], q["turn"][:, bass.ds(c * 4, 4)], ACT.Copy).then_inc(chunk_ready, 1)
                        act.activation(dc[:, :], k.cols[:, bass.ds(c + k.where["ssm_d"], 1)], ACT.Copy).then_inc(chunk_ready, 1)
                        for j in range(4):
                            act.wait_ge(angle_ready, c * 4 + (j + 1))
                            act.activation(sine[j % 2], frac[j % 2], ACT.Sin, scale=TURN).then_inc(table_ready, 1)
                            act.activation(cosine[j % 2], size[j % 2], ACT.Sin, scale=-TURN, bias=col(k, "half_pi", 0))\
                                .then_inc(table_ready, 1)

                @block.tensor
                def _(pe):
                    pe.sem_inc(products_used, 1)
                    with pe.Fori(0, DC) as c:
                        pe.wait_ge(chunk_ready, c * 6 + 6)

                        def inputs(j):
                            lo = 32 * j
                            for i in range(2):
                                pe.matmul(k.ps[:, 2 * (j % 2) + i, :], bc[lo:lo + 32, i, :], u[lo:lo + 32, :],
                                          start=True, stop=True).then_inc(bu_ready, 1)

                        inputs(0)
                        for j in range(4):
                            if j < 3:
                                if j >= 1:
                                    pe.wait_ge(bu_read, c * 4 + j)
                                inputs(j + 1)
                            pe.wait_ge(products_ready, c * 4 + (j + 1))
                            for i in range(4):
                                last = pe.matmul(k.ps[32 * j:32 * j + 32, 4, :], cc[:, [0, 0, 1, 1][i], j, :],
                                                 prod[:, i, :], start=(i == 0), stop=(i == 3))
                            last.then_inc(products_used, 1)

                @block.vector
                def _(dve):
                    dve.sem_inc(y_ready, 1)
                    with dve.Fori(0, DC) as c:
                        step = Steps(dve, dve_step, c * STEPS)
                        dve.wait_ge(chunk_ready, c * 6 + 6)

                        def angles(j):
                            step(dve.tensor_scalar(frac[j % 2], k.trow[:, :], pc[:, j, 1:2], None, ALU.mult))
                            step(dve.tensor_scalar(scr, frac[j % 2], ROUND, ROUND, ALU.add, ALU.subtract))
                            step(dve.tensor_tensor(frac[j % 2], frac[j % 2], scr, ALU.subtract))
                            step(dve.scalar_tensor_tensor(size[j % 2], frac[j % 2], -1.0, frac[j % 2], ALU.mult, ALU.max))
                            dve.sem_inc(angle_ready, 1)

                        angles(0)
                        for j in range(4):
                            if j < 3:
                                angles(j + 1)
                            co, si = cosine[j % 2], sine[j % 2]
                            bu = [k.ps[:, 2 * (j % 2) + i, :] for i in range(2)]
                            dve.wait_ge(table_ready, c * 8 + 2 * (j + 1))
                            dve.wait_ge(bu_ready, c * 8 + 2 * (j + 1))
                            step(dve.tensor_tensor(rot[0], co, bu[0], ALU.mult))
                            step(dve.tensor_tensor(scr, si, bu[1], ALU.mult))
                            step(dve.tensor_tensor(rot[0], rot[0], scr, ALU.add))
                            step(dve.tensor_tensor(rot[1], co, bu[1], ALU.mult))
                            step(dve.tensor_tensor(scr, si, bu[0], ALU.mult))
                            dve.sem_inc(bu_read, 1)
                            step(dve.tensor_tensor(rot[1], rot[1], scr, ALU.subtract))
                            rho = pc[:, j, 0:1].to_broadcast([P, T])
                            step(dve.tensor_tensor_scan(scan[0], rho, rot[0], 0.0, ALU.mult, ALU.add))
                            step(dve.tensor_tensor_scan(scan[1], rho, rot[1], 0.0, ALU.mult, ALU.add))
                            dve.wait_ge(products_used, c * 4 + (j + 1))
                            step(dve.tensor_tensor(prod[:, 0, :], co, scan[0], ALU.mult))
                            step(dve.scalar_tensor_tensor(prod[:, 1, :], si, -1.0, scan[1], ALU.mult, ALU.mult))
                            step(dve.tensor_tensor(prod[:, 2, :], si, scan[0], ALU.mult))
                            step(dve.tensor_tensor(prod[:, 3, :], co, scan[1], ALU.mult))
                            dve.sem_inc(products_ready, 1)
                        dve.wait_ge(products_used, c * 4 + 5)
                        dve.sem_inc(y_ready, 1)
                        step(dve.scalar_tensor_tensor(k.A[:, bass.ds(c, 1), :], u, dc[:, :], k.ps[:, 4, :], ALU.mult, ALU.add))
                        dve.sem_inc(y_ready, 1)
                        assert step.n == STEPS, step.n

    with k.stage(1) as (block, act_step):
        @block.scalar
        def _(act):
            for c in range(DC):
                act.activation(k.A[:, c, :], k.A[:, c, :], ACT.Gelu_apprx_tanh).then_inc(act_step, 1)
            act.wait_ge(act_step, DC)


def ssm_glu(k):
    first = k.first["ssm_glu"]
    with k.stage(4) as (block, product_ready, gate_ready, bank_free, dve_step):
        @block.sync
        def _(sp):
            k.feed(sp, 2)

        @block.tensor
        def _(pe):
            for m in range(DC):
                if m % 4 == 0:
                    k.loaded(pe, first + m // 4)
                if m >= 4:
                    pe.wait_ge(gate_ready, m - 3)
                accumulate(k, pe, k.ps[:, m % 4, :], first + m // 4, m % 4 * P, k.A, DC).then_inc(product_ready, 1)

        @block.scalar
        def _(act):
            for m in range(DC):
                act.wait_ge(product_ready, m + 1)
                if m >= 4:
                    act.wait_ge(bank_free, m - 3)
                act.activation(k.tmp[:, m % 4, :], k.ps[:, m % 4, :], ACT.Sigmoid, bias=col(k, "ssm_b_glu", m))\
                    .then_inc(gate_ready, 1)
                if m % 4 == 3:
                    act.sem_inc(k.weights_used, 1)

        @block.vector
        def _(dve):
            step = Steps(dve, dve_step)
            for m in range(DC):
                step(dve.tensor_tensor(k.B[:, m, :], k.A[:, m, :], k.C[:, m, :], ALU.mult))
                dve.wait_ge(gate_ready, m + 1)
                step(dve.tensor_tensor(k.B[:, m, :], k.B[:, m, :], k.tmp[:, m % 4, :], ALU.mult))
                dve.sem_inc(bank_free, 1)


def ssm_mixer(k):
    ssm_project(k, "ssm_in", 2, 0, k.B, ACT.Copy)
    ssm_scan(k)
    ssm_project(k, "ssm_in", 2, 2, k.C, ACT.Silu)
    ssm_glu(k)


class Phases:

    def __init__(self, sem, names, start=0):
        self.sem, self.names, self.told, self.start = sem, names, 0, start

    def at(self, i, name):
        return i * len(self.names) + (self.names.index(name) + 1 + self.start)

    def place(self, name):
        assert self.names[self.told] == name, (self.names[self.told], name)
        self.told += 1

    def wait(self, eng, i, name):
        eng.wait_ge(self.sem, self.at(i, name))

    def done(self, eng, name):
        self.place(name)
        eng.sem_inc(self.sem, 1)

    def last(self, ins, name):
        self.place(name)
        ins.then_inc(self.sem, 1)


HEADS = 16
L = 64
NL = T // L
DECAY = -float(np.exp(-0.5))
LEVELS = 6


def rwkv_project(k, scratch):
    first = k.first["rwkv_in"]
    with ExitStack() as own:
        sb = lambda name, shape: own.enter_context(k.nc.sbuf_tensor(name, shape, F32))
        w1 = sb("lora_down", [P, 2, DC, 64])
        w2 = sb("lora_up", [64, 2, D])
        low = sb("lora_mid", [64, T])
        xs = [k.A, k.B]
        with k.stage(10) as (block, landed, mixed, product_ready, staged, low_ready, dve_step, *stored):
            @block.sync
            def _(sp):
                k.feed(sp, 8)

            @block.vector
            def _(dve):
                step = Steps(dve, dve_step)
                for c in range(DC):
                    step(dve.tensor_tensor(k.C[:, c, 1:T], k.X[:, c, 0:T - 1], k.X[:, c, 1:T], ALU.subtract))
                    step(dve.tensor_scalar(k.C[:, c, 0:1], k.X[:, c, 0:1], -1.0, None, ALU.mult))
                for n in range(6):
                    if n >= 2:
                        dve.wait_ge(product_ready, DC * (n - 1) + (n == 5))
                    for c in range(DC):
                        step(dve.scalar_tensor_tensor(xs[n % 2][:, c, :], k.C[:, c, :], col(k, f"rwkv_mu{n}", c),
                                                      k.X[:, c, :], ALU.mult, ALU.add))
                        dve.sem_inc(mixed, 1)

            @block.tensor
            def _(pe):
                for n in range(4):
                    pe.wait_ge(mixed, DC * (n + 1))
                    for m in range(DC):
                        o = n * DC + m
                        if m % 4 == 0:
                            k.loaded(pe, first + o // 4)
                        if o >= 4:
                            pe.wait_ge(staged, o - 3)
                        accumulate(k, pe, k.ps[:, o % 4, :], first + o // 4, m % 4 * P, xs[n % 2], DC)\
                            .then_inc(product_ready, 1)
                pe.wait_ge(landed, 64)
                for n in (4, 5):
                    pe.wait_ge(mixed, DC * (n + 1))
                    if n == 5:
                        pe.wait_ge(low_ready, 1)
                    for c in range(DC):
                        last = pe.matmul(k.ps[0:64, 4, :], w1[:, n - 4, c, :], xs[n % 2][:, c, :],
                                         start=(c == 0), stop=(c == DC - 1))
                    last.then_inc(product_ready, 1)
                    pe.wait_ge(low_ready, n - 3)
                    for m in range(DC):
                        o = n * DC + m
                        pe.wait_ge(staged, o - 3)
                        pe.matmul(k.ps[:, o % 4, :], w2[:, n - 4, m * P:(m + 1) * P], low[:, :], start=True, stop=True)\
                            .then_inc(product_ready, 1)

            @block.scalar
            def _(act):
                for i, name in enumerate(("w", "a")):
                    act.dma_start(w1[:, i, :, :], k.ins[f"rwkv_{name}1"].rearrange("(c p) n -> p c n", p=P))\
                        .then_inc(landed, 16)
                    act.dma_start(w2[:, i, :], k.ins[f"rwkv_{name}2"]).then_inc(landed, 16)
                for n in range(6):
                    if n >= 4:
                        act.wait_ge(product_ready, DC * n + (n - 3))
                        act.activation(low[:, :], k.ps[0:64, 4, :], ACT.Tanh if n == 4 else ACT.Copy).then_inc(low_ready, 1)
                    for m in range(DC):
                        o = n * DC + m
                        act.wait_ge(product_ready, o + 1 + max(0, n - 3))
                        if o >= 4:
                            act.wait_ge(stored[o % 4], 16 * (o // 4))
                        if n < 4:
                            ins = act.activation(k.tmp[:, o % 4, :], k.ps[:, o % 4, :], ACT.Silu if n == 3 else ACT.Copy)
                        else:
                            ins = act.activation(k.tmp[:, o % 4, :], k.ps[:, o % 4, :], ACT.Sigmoid,
                                                 bias=col(k, "rwkv_w0" if n == 4 else "rwkv_a0", m))
                        ins.then_inc(staged, 1)
                        act.wait_ge(staged, o + 1)
                        act.dma_start(scratch[m, :, n, :], k.tmp[:, o % 4, :]).then_inc(stored[o % 4], 16)
                        if n < 4 and m % 4 == 3:
                            act.sem_inc(k.weights_used, 1)
                for s in stored:
                    act.wait_ge(s, 16 * 6 * DC // 4)


def condition(k):
    with k.stage(1) as (block, ready):
        @block.sync
        def _(sp):
            k.feed(sp, 0)

        @block.scalar
        def _(act):
            act.activation(k.c_act[:, :], k.cols[:, k.where["c"]:k.where["c"] + DC], ACT.Silu).then_inc(ready, 1)
            act.wait_ge(ready, 1)


def rwkv_heads(k, scratch):
    with ExitStack() as own:
        sb = lambda name, shape: own.enter_context(k.nc.sbuf_tensor(name, shape, F32))
        ld = sb("pair_inputs", [P, 6, T])
        hc = sb("pair_params", [P, 8])
        S = sb("state", [P, P])
        SA = sb("removed", [P, 2, 64])
        WL = sb("chunk_decay", [P, NL])
        r_, k_, v_, z_, sw, a_ = (ld[:, n, :] for n in range(6))
        k_k, k_a, r_k, gn_g, gn_b = (hc[:, n:n + 1] for n in range(5))
        bonus = sw
        alpha, beta, key, query = (k.B[:, n, :] for n in range(4))
        blocks = lambda tile: tile.rearrange("p (a b) -> p a b", b=P)
        alpha_t, beta_t, key_t, v_t = (blocks(k.B[:, 4 + n, :]) for n in range(4))
        RB = [blocks(k.C[:, 0, :]), blocks(k.C[:, 1, :])]
        RK = [blocks(k.C[:, 2, :]), blocks(k.C[:, 3, :])]
        P1T = k.C[:, 4, :]
        P2 = k.C[:, 5, :].rearrange("p (a h v) -> p a h v", h=2, v=64)
        Ti, TT = [blocks(k.C[:, 6, :]), blocks(r_)], [blocks(k.C[:, 7, :]), blocks(k_)]
        NT, AK = [blocks(k.tmp[:, 0, :]), blocks(a_)], [blocks(k.tmp[:, 3, :]), blocks(k.tmp[:, 5, :])]
        NTl, Y = [blocks(k.tmp[:, 1, :]), blocks(alpha)], [blocks(k.tmp[:, 2, :]), blocks(beta)]
        G = [k.tmp[:, 4, 256 * h:256 * h + 256].rearrange("p (a v) -> p a v", v=64) for h in range(2)]
        sum_, sum_before, e_query, e_beta, e_alpha, kk = (k.tmp[:, n, :] for n in range(6))
        square, norm = k.C[:, 6, :], k.C[:, 7, :]
        out, centred, out_sq, dev = (k.tmp[:, n, :] for n in range(4))
        bank = lambda n: k.ps[:, n, :]
        mats = lambda n: blocks(k.ps[:, n, :])
        mask = lambda name: k.mask[name][:, :].unsqueeze(1).to_broadcast([P, TC, P])

        with k.stage(6) as (block, pair_loaded, pe_done, act_done, dve_done, dve_step, act_step):
            AP_ = Phases(act_done, ["exps", "kk_sq", "kk_norm", "by_time"]
                         + [f"Y{h}{l}" for l in range(1, LEVELS) for h in range(2)]
                         + ["G0", "G1", "P20", "P21", "out", "out_sq", "dev"])
            VP = Phases(dve_done, ["sums", "kk", "bonus", "hats"]
                        + [n for h in range(2) for n in (f"made{h}", f"lvl{h}0")]
                        + [f"lvl{h}{l}" for l in range(1, LEVELS) for h in range(2)]
                        + [n for c in range(NL) for n in (f"sa{c}", f"s{c}")] + ["ada", "centred", "gated"], start=1)
            TP = Phases(pe_done, ["kk_sum", "bonus", "by_time"]
                        + ["mats0", "mats1"]
                        + [m for l in range(1, LEVELS) for m in (f"y0{l}", f"y1{l}", f"upd0{l}", f"upd1{l}")]
                        + ["g0", "g1", "p20", "p21"]
                        + [n for c in range(NL) for n in ([f"sa{c}", "ada"] if c == 6 else [f"sa{c}"]) + [f"u{c}"]] + ["mean", "var"])
            STEPS = 2 + 1 + 1 + 2 + 1 + 3 + 5 + 1 + 1 + 2 * (8 + 5 * 2 + 4) + NL * 3 + 1 + 6
            PASSES = DC // 2
            ada = k.first["ada0"]

            @block.sync
            def _(sp):
                k.feed(sp, 0)

                def load_pair(i):
                    sp.wait_ge(dve_done, i * len(VP.names) + 1)
                    sp.dma_start(ld[:, :, :], scratch[bass.ds(i, 1), :, :, :]).then_inc(pair_loaded, 16)
                    sp.dma_start(hc[:, :], k.ins["rwkv_pairs"][bass.ds(i, 1), :, :]).then_inc(pair_loaded, 16)

                with sp.Fori(0, PASSES - 1) as j:
                    for p in range(2):
                        load_pair(j * 2 + p)
                        for n in range(3):
                            at = ada + 3 * p + n
                            sp.wait_ge(k.weights_used, j * 6 + (at + 1))
                            sp.dma_start(k.slot(at).rearrange("p (k n) -> p k n", k=DC),
                                         k.ins["w_ada_chunks"][bass.ds(j * 6 + (6 + 3 * p + n), 1), :, :]
                                         .rearrange("o (k p) n -> p (o k) n", p=P)).then_inc(k.weights_loaded[at % SLOTS], 16)
                for i in (DC - 2, DC - 1):
                    load_pair(i)
                k.issued = ada + 24
                k.feed(sp, 24)

            @block.tensor
            def _(pe):
                def pair(i, j, p):
                    AP_.wait(pe, i, "kk_sq")
                    TP.last(pe.matmul(bank(0), k.pairs[:, :], square, start=True, stop=True), "kk_sum")
                    VP.wait(pe, i, "bonus")
                    TP.last(pe.matmul(bank(6), k.pairs[:, :], square, start=True, stop=True), "bonus")
                    VP.wait(pe, i, "hats")
                    for n, src in enumerate((alpha, beta, key, v_)):
                        for t in range(TC):
                            ins = pe.transpose(k.ps[:, 1 + n, t * P:(t + 1) * P], src[:, t * P:(t + 1) * P], k.ident[:, :])
                    TP.last(ins, "by_time")
                    AP_.wait(pe, i, "by_time")
                    for h in range(2):
                        lo = 64 * h
                        if h:
                            VP.wait(pe, i, "made0")
                        for n, (left, right) in enumerate(((beta, alpha), (alpha, beta), (key, alpha), (beta, query), (key, query))):
                            for t in range(TC):
                                ts = slice(t * P, (t + 1) * P)
                                ins = pe.matmul(k.ps[:, 1 + n, ts], left[lo:lo + 64, ts], right[lo:lo + 64, ts], start=True, stop=True)
                        TP.last(ins, f"mats{h}")
                    for l in range(1, LEVELS):
                        for h in range(2):
                            VP.wait(pe, i, f"lvl{h}{l - 1}")
                            for t in range(TC):
                                ins = pe.matmul(mats(6 + h)[:, t, :], NTl[h][:, t, :], Ti[h][:, t, :], start=True, stop=True)
                            TP.last(ins, f"y{h}{l}")
                        for h in range(2):
                            AP_.wait(pe, i, f"Y{h}{l}")
                            for t in range(TC):
                                pe.matmul(mats(h)[:, t, :], TT[h][:, t, :], Y[h][:, t, :], start=True, stop=True)
                            for t in range(TC):
                                ins = pe.matmul(mats(2 + h)[:, t, :], Y[h][:, t, :], TT[h][:, t, :], start=True, stop=True)
                            TP.last(ins, f"upd{h}{l}")
                    for h in range(2):
                        lo = 64 * h
                        VP.wait(pe, i, f"lvl{h}{LEVELS - 1}")
                        for t in range(TC):
                            pe.matmul(k.ps[lo:lo + 64, h, t * P:(t + 1) * P], alpha_t[:, t, lo:lo + 64], TT[h][:, t, :], start=True, stop=True)
                        for t in range(TC):
                            ins = pe.matmul(k.ps[:, 2 + h, 64 * t:64 * t + 64], AK[h][:, t, :], v_t[:, t, lo:lo + 64], start=True, stop=True)
                        TP.last(ins, f"g{h}")
                    for h in range(2):
                        AP_.wait(pe, i, f"G{h}")
                        for t in range(TC):
                            ins = pe.matmul(k.ps[:, 6 + h, 64 * t:64 * t + 64], TT[h][:, t, :], G[h][:, t, :], start=True, stop=True)
                        TP.last(ins, f"p2{h}")
                    AP_.wait(pe, i, "P21")
                    for c in range(NL):
                        t, lo = c // 2, 64 * (c % 2)
                        rows, cs = slice(lo, lo + 64), slice(64 * c, 64 * c + 64)
                        if c:
                            VP.wait(pe, i, f"s{c - 1}")
                        TP.last(pe.matmul(k.ps[rows, 4, 0:P], P1T[:, cs], S[:, :], start=True, stop=True), f"sa{c}")
                        if 1 <= c < 7:
                            for x in range(2 * (c - 1), 2 * c):
                                at = ada + 3 * p + x // 4
                                if x % 4 == 0:
                                    pe.wait_ge(k.weights_loaded[at % SLOTS], j * 16 + 16 * (at // SLOTS + 1))
                                w = k.slot(at).rearrange("p (k n) -> p k n", k=DC)
                                for d in range(DC):
                                    ins = pe.matmul(k.ps[:, 7, x:x + 1], w[:, d, x % 4 * P:(x % 4 + 1) * P], k.c_act[:, d:d + 1],
                                                    start=(d == 0), stop=(d == DC - 1))
                            if c == 6:
                                TP.last(ins, "ada")
                        VP.wait(pe, i, f"sa{c}")
                        pe.matmul(k.ps[:, 5, cs], S[:, :], query[:, cs], start=True, stop=False)
                        for h in range(2):
                            hs = slice(64 * h, 64 * h + 64)
                            pe.matmul(k.ps[hs, 5, cs], SA[rows, h, :], RB[h][rows, t, rows], start=False, stop=False)
                            pe.matmul(k.ps[hs, 5, cs], v_t[rows, t, hs], RK[h][rows, t, rows], start=False, stop=True)
                        pe.matmul(k.ps[:, 6, 0:P], beta_t[rows, t, :], SA[rows, :, :], start=True, stop=False)
                        ins = pe.matmul(k.ps[:, 6, 0:P], key_t[rows, t, :], v_t[rows, t, :], start=False, stop=True)
                        TP.last(ins, f"u{c}")
                    AP_.wait(pe, i, "out")
                    TP.last(pe.matmul(bank(0), k.pairs[:, :], out, start=True, stop=True), "mean")
                    AP_.wait(pe, i, "out_sq")
                    TP.last(pe.matmul(bank(1), k.pairs[:, :], out_sq, start=True, stop=True), "var")

                with pe.Fori(0, PASSES) as j:
                    for p in range(2):
                        TP.told = 0
                        pair(j * 2 + p, j, p)

            @block.scalar
            def _(act):
                def pair(i):
                    VP.wait(act, i, "sums")
                    act.activation(e_query, sum_, ACT.Exp, scale=DECAY)
                    act.activation(e_beta, sum_, ACT.Exp, scale=-DECAY)
                    AP_.last(act.activation(e_alpha, sum_before, ACT.Exp, scale=DECAY), "exps")
                    VP.wait(act, i, "kk")
                    AP_.last(act.activation(square, kk, ACT.Square), "kk_sq")
                    TP.wait(act, i, "kk_sum")
                    AP_.last(act.activation(norm, bank(0), ACT.Sqrt), "kk_norm")
                    TP.wait(act, i, "by_time")
                    for n in range(4):
                        ins = act.activation(k.B[:, 4 + n, :], bank(1 + n), ACT.Copy)
                    AP_.last(ins, "by_time")
                    for l in range(1, LEVELS):
                        for h in range(2):
                            TP.wait(act, i, f"y{h}{l}")
                            AP_.last(act.activation(Y[h], mats(6 + h), ACT.Copy), f"Y{h}{l}")
                    for h in range(2):
                        lo = 64 * h
                        TP.wait(act, i, f"g{h}")
                        act.activation(P1T[lo:lo + 64, :], k.ps[lo:lo + 64, h, :], ACT.Copy)
                        AP_.last(act.activation(G[h], k.ps[:, 2 + h, 0:256].rearrange("p (a v) -> p a v", v=64), ACT.Copy), f"G{h}")
                    for h in range(2):
                        TP.wait(act, i, f"p2{h}")
                        AP_.last(act.activation(P2[:, :, h, :], k.ps[:, 6 + h, 0:256].rearrange("p (a v) -> p a v", v=64), ACT.Copy), f"P2{h}")
                    TP.wait(act, i, f"u{NL - 1}")
                    AP_.last(act.activation(out, bank(5), ACT.Copy), "out")
                    VP.wait(act, i, "centred")
                    AP_.last(act.activation(out_sq, centred, ACT.Square), "out_sq")
                    TP.wait(act, i, "var")
                    AP_.last(act.activation(dev, bank(1), ACT.Sqrt, scale=1.0 / 64, bias=col(k, "gn_eps", 0)), "dev")

                with act.Fori(0, PASSES) as j:
                    for p in range(2):
                        AP_.told = 0
                        pair(j * 2 + p)

            @block.vector
            def _(dve):
                def pair(i):
                    step = Steps(dve, dve_step, i * STEPS)
                    dve.wait_ge(pair_loaded, i * 32 + 32)
                    step(dve.tensor_tensor_scan(sum_, k.seg[L][:, :], sw, 0.0, ALU.mult, ALU.add))
                    step(dve.tensor_tensor(sum_before, sum_, sw, ALU.subtract))
                    VP.done(dve, "sums")
                    step(dve.tensor_scalar(kk, k_, k_k, None, ALU.mult))
                    VP.done(dve, "kk")
                    step(dve.memset(S[:, :], 0.0))
                    step(dve.tensor_scalar(k.C[:, 0, :], a_, -1.0, k_a, ALU.add, ALU.mult))
                    step(dve.scalar_tensor_tensor(k_, k.C[:, 0, :], 1.0, k_, ALU.add, ALU.mult))
                    AP_.wait(dve, i, "kk_norm")
                    step(dve.scalar_tensor_tensor(square, r_, r_k, k_, ALU.mult, ALU.mult))
                    VP.done(dve, "bonus")
                    step(dve.tensor_scalar(norm, norm, 1e-12, None, ALU.max))
                    step(dve.reciprocal(norm, norm))
                    step(dve.tensor_tensor(kk, kk, norm, ALU.mult))
                    step(dve.scalar_tensor_tensor(alpha, kk, -1.0, e_alpha, ALU.mult, ALU.mult))
                    step(dve.tensor_tensor(beta, kk, a_, ALU.mult))
                    step(dve.tensor_tensor(beta, beta, e_beta, ALU.mult))
                    step(dve.tensor_tensor(key, k_, e_beta, ALU.mult))
                    step(dve.tensor_tensor(query, r_, e_query, ALU.mult))
                    VP.done(dve, "hats")
                    step(dve.tensor_copy(WL[:, :], e_query[:, L - 1:T:L]))
                    TP.wait(dve, i, "bonus")
                    step(dve.tensor_tensor(bonus, bank(6), v_, ALU.mult))
                    for h in range(2):
                        TP.wait(dve, i, f"mats{h}")
                        step(dve.tensor_tensor(NT[h], mats(1), mask("before"), ALU.mult))
                        step(dve.tensor_tensor(Ti[h], mats(2), mask("first_lower"), ALU.mult))
                        step(dve.tensor_tensor(AK[h], mats(3), mask("before"), ALU.mult))
                        step(dve.tensor_tensor(RB[h], mats(4), mask("upto"), ALU.mult))
                        step(dve.tensor_tensor(RK[h], mats(5), mask("upto"), ALU.mult))
                        VP.done(dve, f"made{h}")
                        step(dve.tensor_tensor(Ti[h], Ti[h], mask("ident"), ALU.add))
                        step(dve.tensor_tensor(TT[h], NT[h], mask("level0"), ALU.mult))
                        step(dve.tensor_tensor(TT[h], TT[h], mask("ident"), ALU.add))
                        step(dve.tensor_tensor(NTl[h], NT[h], mask("level1"), ALU.mult))
                        VP.done(dve, f"lvl{h}0")
                    for l in range(1, LEVELS):
                        for h in range(2):
                            if l < LEVELS - 1:
                                TP.wait(dve, i, f"y{h}{l}")
                                step(dve.tensor_tensor(NTl[h], NT[h], mask(f"level{l + 1}"), ALU.mult))
                        for h in range(2):
                            TP.wait(dve, i, f"upd{h}{l}")
                            if l < LEVELS - 1:
                                step(dve.tensor_tensor(Ti[h], Ti[h], mats(h), ALU.add))
                            step(dve.tensor_tensor(TT[h], TT[h], mats(2 + h), ALU.add))
                            VP.done(dve, f"lvl{h}{l}")
                    AP_.wait(dve, i, "P21")
                    for c in range(NL):
                        t, lo = c // 2, 64 * (c % 2)
                        rows = slice(lo, lo + 64)
                        TP.wait(dve, i, f"sa{c}")
                        step(dve.tensor_tensor(SA[rows, :, :], k.ps[rows, 4, 0:128].rearrange("p (h v) -> p h v", h=2),
                                               P2[rows, t, :, :], ALU.add))
                        VP.done(dve, f"sa{c}")
                        TP.wait(dve, i, f"u{c}")
                        step(dve.tensor_tensor(S[:, :], S[:, :], k.ps[:, 6, 0:P], ALU.add))
                        step(dve.scalar_tensor_tensor(S[:, :], S[:, :], WL[:, c:c + 1], k.pairs[:, :], ALU.mult, ALU.mult))
                        VP.done(dve, f"s{c}")
                    TP.wait(dve, i, "ada")
                    step(dve.tensor_copy(k.mod[:, :, :].rearrange("p l n -> p (l n)")[:, bass.ds(i * 12, 12)], k.ps[:, 7, 0:12]))
                    dve.sem_inc(k.weights_used, 3)
                    VP.done(dve, "ada")
                    TP.wait(dve, i, "mean")
                    step(dve.scalar_tensor_tensor(centred, bank(0), -1.0 / 64, out, ALU.mult, ALU.add))
                    VP.done(dve, "centred")
                    AP_.wait(dve, i, "dev")
                    step(dve.reciprocal(dev, dev))
                    step(dve.tensor_tensor(centred, centred, dev, ALU.mult))
                    step(dve.tensor_scalar(centred, centred, gn_g, gn_b, ALU.mult, ALU.add))
                    step(dve.tensor_tensor(centred, centred, bonus, ALU.add))
                    step(dve.tensor_tensor(k.A[:, bass.ds(i, 1), :], centred, z_, ALU.mult))
                    VP.done(dve, "gated")
                    assert step.n == STEPS, step.n

                dve.sem_inc(dve_done, 1)
                with dve.Fori(0, PASSES) as j:
                    for p in range(2):
                        VP.told = 0
                        pair(j * 2 + p)


def rwkv_mixer(k):
    scratch = k.nc.dram_tensor("rwkv_scratch", (DC, P, 6, T), F32, kind="Internal").ap()
    condition(k)
    rwkv_project(k, scratch)
    rwkv_heads(k, scratch)


MLA_H, QK, ROPE = 4, 96, 32
IN_COLS = 2144
CONV_K = 31
MOD = {"sh1": 0, "sc1": 8, "g1": 16, "sh2": 24, "sc2": 32, "g2": 40}
SMALL = {"w_uq": (0, 768), "w_ukv": (768, 512), "swap": (1280, P), "strip": (1408, 896),
         "pool_inv": (2304, 1024), "w_pool": (3328, 128)}
SMALL_COLS = 3456


def plan_mixer(k, l):
    w_in = k.ins["w_in_2"][l]
    k.want(f"small{l}", k.ins["small"][l], 1, SMALL_COLS)
    k.want(f"mla{l}", w_in[:, 0:352], DC, 352)
    k.want(f"pool{l}", w_in[:, 352:608], DC, 256)
    k.want(f"hgrn{l}", w_in[:, 608:1120], DC, 512)
    k.want(f"hgrn{l}", w_in[:, 1120:1632], DC, 512)
    k.want(f"conv{l}", w_in[:, 1632:2144], DC, 512)
    k.want_halves(f"out_2{l}", k.ins["w_out_2"][l])


def small(k, l, name):
    at, n = SMALL[name]
    return k.slot(k.first[f"small{l}"])[:, at:at + n]


def modulation(k):
    with k.stage(1) as (block, dve_step):
        @block.sync
        def _(sp):
            k.feed(sp, 0)

        @block.vector
        def _(dve):
            step = Steps(dve, dve_step)
            for l in range(2):
                at = k.where[f"b_ada{l}"]
                step(dve.tensor_tensor(k.mod[:, l, :], k.mod[:, l, :], k.cols[:, at:at + 48], ALU.add))
                for i, name in enumerate(("norm1", "norm2")):
                    g = k.cols[:, k.where[f"{name}_g{l}"]:][:, 0:DC]
                    sc = k.mod[:, l, MOD[f"sc{i + 1}"]:][:, 0:DC]
                    step(dve.scalar_tensor_tensor(sc, sc, 1.0, g, ALU.add, ALU.mult))


def mod(k, l, name, c):
    at = MOD[name] + c
    return k.mod[:, l, at:at + 1]


def modulated_norm(k, l, i):
    with k.stage(5) as (block, squared, summed, deviation, dve_step, act_step):
        @block.sync
        def _(sp):
            k.feed(sp, 0)

        @block.tensor
        def _(pe):
            for c in range(DC):
                pe.wait_ge(squared, c + 1)
                last = pe.matmul(k.ps[:, 0, :], k.ones[:, :], k.B[:, c, :], start=(c == 0), stop=(c == DC - 1))
            last.then_inc(summed, 1)

        @block.scalar
        def _(act):
            for c in range(DC):
                act.activation(k.B[:, c, :], k.X[:, c, :], ACT.Square).then_inc(squared, 1)
            act.wait_ge(summed, 1)
            act.activation(k.tmp[:, 0, :], k.ps[:, 0, :], ACT.Sqrt, bias=col(k, "eps", 0), scale=1.0 / D)\
                .then_inc(deviation, 1)

        @block.vector
        def _(dve):
            step = Steps(dve, dve_step)
            dve.wait_ge(deviation, 1)
            step(dve.reciprocal(k.tmp[:, 1, :], k.tmp[:, 0, :]))
            for c in range(DC):
                step(dve.scalar_tensor_tensor(k.A[:, c, :], k.X[:, c, :], mod(k, l, f"sc{i}", c), k.tmp[:, 1, :],
                                              ALU.mult, ALU.mult))
                step(dve.tensor_scalar(k.A[:, c, :], k.A[:, c, :], mod(k, l, f"sh{i}", c), None, ALU.add))


def mla(k, l):
    n0 = k.first[f"mla{l}"]
    tile = lambda n: k.tmp[:, n, :]
    ckv, cq = tile(2), [tile(0), k.tmp[0:64, 1, :]]
    w_uq, w_ukv, swap = small(k, l, "w_uq"), small(k, l, "w_ukv"), small(k, l, "swap")
    strip = small(k, l, "strip")
    q, key = [k.B[:, h, :] for h in range(4)], [k.B[:, 4 + h, :] for h in range(4)]
    v_t = k.tmp[:, 4:6, :].rearrange("p a b -> p (a b)").rearrange("p (t n) -> p t n", t=TC)
    with ExitStack() as own:
        rope = own.enter_context(k.nc.sbuf_tensor(f"rope{l}", [QK, 2, T], F32))

        with k.stage(7) as (block, landed, product_ready, act_done, dve_done, sums_ready, dve_step, act_step):
            AP_ = Phases(act_done, ["latents", "squares", "devs", "tables"])
            VP = Phases(dve_done, ["turns", "normed"])

            @block.sync
            def _(sp):
                sp.dma_start(k.C[0:QK, 7, :].bitcast(I32), k.ins["positions"].to_broadcast([QK, T])).then_inc(landed, 16)
                k.feed(sp, 0)

            @block.tensor
            def _(pe):
                k.loaded(pe, n0)
                w = k.chunk(n0)
                for out, lo, size in ((k.ps[:, 0, :], 0, 128), (k.ps[0:64, 1, :], 128, 64), (k.ps[:, 2, :], 192, 128),
                                      (k.ps[64:96, 3, :], 320, 32)):
                    for c in range(DC):
                        last = pe.matmul(out, w[:, c, lo:lo + size], k.A[:, c, :], start=(c == 0), stop=(c == DC - 1))
                    last.then_inc(product_ready, 1)
                AP_.wait(pe, 0, "squares")
                pe.matmul(k.ps[:, 4, :], k.ones[:, :], k.C[:, 0, :], start=True, stop=False)
                pe.matmul(k.ps[:, 4, :], k.ones[0:64, :], k.C[0:64, 1, :], start=False, stop=True)
                pe.matmul(k.ps[:, 5, :], k.ones[:, :], k.C[:, 2, :], start=True, stop=True).then_inc(sums_ready, 1)

            @block.scalar
            def _(act):
                act.wait_ge(product_ready, 3)
                act.activation(cq[0], k.ps[:, 0, :], ACT.Copy)
                act.activation(cq[1], k.ps[0:64, 1, :], ACT.Copy)
                act.activation(ckv, k.ps[:, 2, :], ACT.Copy)
                act.wait_ge(product_ready, 4)
                for h in range(MLA_H):
                    ins = act.activation(key[h][64:96, :], k.ps[64:96, 3, :], ACT.Copy)
                AP_.last(ins, "latents")
                act.activation(k.C[:, 0, :], k.ps[:, 0, :], ACT.Square)
                act.activation(k.C[0:64, 1, :], k.ps[0:64, 1, :], ACT.Square)
                AP_.last(act.activation(k.C[:, 2, :], k.ps[:, 2, :], ACT.Square), "squares")
                act.wait_ge(sums_ready, 1)
                act.activation(k.C[:, 3, :], k.ps[:, 4, :], ACT.Sqrt, bias=col(k, "eps", 0), scale=1.0 / 192)
                AP_.last(act.activation(k.C[:, 4, :], k.ps[:, 5, :], ACT.Sqrt, bias=col(k, "eps", 0), scale=1.0 / 128), "devs")
                VP.wait(act, 0, "turns")
                act.activation(rope[:, 1, :], k.C[0:QK, 5, :], ACT.Sin, scale=TURN)
                AP_.last(act.activation(rope[:, 0, :], k.C[0:QK, 6, :], ACT.Sin, scale=-TURN,
                                        bias=col(k, "half_pi", 0, QK)), "tables")

            @block.vector
            def _(dve):
                step = Steps(dve, dve_step)
                dve.wait_ge(landed, 16)
                angle, turns, scr = k.C[0:QK, 5, :], k.C[0:QK, 6, :], k.tmp[0:QK, 3, :]
                step(dve.tensor_copy(angle, k.C[0:QK, 7, :].bitcast(I32)))
                step(dve.tensor_scalar(angle, angle, col(k, "rope_freq", 0, QK), None, ALU.mult))
                reduce_angle(dve, step, angle, turns, scr)
                step(dve.tensor_scalar(angle, turns, col(k, "rope_sign", 0, QK), None, ALU.mult))
                step(dve.scalar_tensor_tensor(scr, turns, -1.0, turns, ALU.mult, ALU.max))
                step(dve.tensor_copy(turns, scr))
                VP.done(dve, "turns")
                AP_.wait(dve, 0, "devs")
                step(dve.reciprocal(k.C[:, 3, :], k.C[:, 3, :]))
                step(dve.reciprocal(k.C[:, 4, :], k.C[:, 4, :]))
                step(dve.scalar_tensor_tensor(cq[0], cq[0], col(k, f"q_a_g{l}", 0), k.C[:, 3, :], ALU.mult, ALU.mult))
                step(dve.scalar_tensor_tensor(cq[1], cq[1], col(k, f"q_a_g{l}", 1, 64), k.C[0:64, 3, :], ALU.mult, ALU.mult))
                step(dve.scalar_tensor_tensor(ckv, ckv, col(k, f"kv_a_g{l}", 0), k.C[:, 4, :], ALU.mult, ALU.mult))
                VP.done(dve, "normed")

        items = [(t, h) for h in range(MLA_H) for t in ("q", "k")]
        with k.stage(7) as (block, product_ready, copied, squared, sum_ready, dve_done, swap_ready, dve_step):
            @block.sync
            def _(sp):
                k.feed(sp, 0)

            @block.tensor
            def _(pe):
                k.loaded(pe, k.first[f"small{l}"])
                def product(i):
                    t, h = items[i]
                    if t == "q":
                        pe.matmul(k.ps[0:QK, i % 2, :], w_uq[:, QK * h:QK * (h + 1)], cq[0], start=True, stop=False)
                        ins = pe.matmul(k.ps[0:QK, i % 2, :], w_uq[0:64, 384 + QK * h:384 + QK * (h + 1)], cq[1], start=False, stop=True)
                    else:
                        ins = pe.matmul(k.ps[0:64, i % 2, :], w_ukv[:, P * h:P * h + 64], ckv, start=True, stop=True)
                    ins.then_inc(product_ready, 1)
                for i in range(8):
                    if i >= 2:
                        pe.wait_ge(copied, i - 1)
                    product(i)
                    pe.wait_ge(squared, i + 1)
                    pe.matmul(k.ps[0:QK, 2, :], k.ones[0:QK, 0:QK], k.C[0:QK, 2 + i % 2, :], start=True, stop=True)\
                        .then_inc(sum_ready, 1)
                    pe.wait_ge(dve_done, 2 * i + 1)
                    x = (q if items[i][0] == "q" else key)[items[i][1]]
                    pe.matmul(k.ps[0:QK, 3, :], swap[0:QK, 0:QK], x[0:QK, :], start=True, stop=True).then_inc(swap_ready, 1)
                    pe.wait_ge(dve_done, 2 * i + 2)
                vw = w_ukv.rearrange("p (h n) -> p h n", h=4)
                for t in range(TC):
                    ins = pe.matmul(k.ps[:, 4 + t // 2, 256 * (t % 2):256 * (t % 2) + 256], ckv[:, t * P:(t + 1) * P],
                                    vw[:, :, 64:128], start=True, stop=True)
                ins.then_inc(product_ready, 1)

            @block.scalar
            def _(act):
                for i, (t, h) in enumerate(items):
                    act.wait_ge(product_ready, i + 1)
                    if t == "q":
                        act.activation(q[h][0:QK, :], k.ps[0:QK, i % 2, :], ACT.Copy).then_inc(copied, 1)
                    else:
                        act.activation(key[h][0:64, :], k.ps[0:64, i % 2, :], ACT.Copy).then_inc(copied, 1)
                    act.wait_ge(copied, i + 1)
                    x = (q if t == "q" else key)[h]
                    act.activation(k.C[0:QK, 2 + i % 2, :], x[0:QK, :], ACT.Square).then_inc(squared, 1)
                    act.wait_ge(sum_ready, i + 1)
                    if i >= 2:
                        act.wait_ge(dve_done, 2 * i - 3)
                    act.activation(k.C[0:QK, 4 + i % 2, :], k.ps[0:QK, 2, :], ACT.Sqrt, bias=col(k, "eps", 0, QK),
                                   scale=1.0 / QK).then_inc(k.dev_ready, 1)
                act.wait_ge(product_ready, 9)
                act.activation(v_t, k.ps[:, 4:6, :].rearrange("p a b -> p (a b)").rearrange("p (t n) -> p t n", t=TC), ACT.Copy)\
                    .then_inc(copied, 1)
                act.wait_ge(copied, 9)

            @block.vector
            def _(dve):
                step = Steps(dve, dve_step)
                for i, (t, h) in enumerate(items):
                    x = (q if t == "q" else key)[h][0:QK, :]
                    rstd = k.C[0:QK, 4 + i % 2, :]
                    dve.wait_ge(k.dev_ready, 8 * l + i + 1)
                    step(dve.reciprocal(rstd, rstd))
                    step(dve.scalar_tensor_tensor(x, x, col(k, f"{t}_g{l}", 0, QK), rstd, ALU.mult, ALU.mult))
                    dve.sem_inc(dve_done, 1)
                    dve.wait_ge(swap_ready, i + 1)
                    step(dve.tensor_tensor(k.C[0:QK, 6, :], k.ps[0:QK, 3, :], rope[:, 1, :], ALU.mult))
                    step(dve.tensor_tensor(x, x, rope[:, 0, :], ALU.mult))
                    step(dve.tensor_tensor(x, x, k.C[0:QK, 6, :], ALU.add))
                    dve.sem_inc(dve_done, 1)

    with ExitStack() as own:
        mx = own.enter_context(k.nc.sbuf_tensor(f"softmax_stats{l}", [P, 2, 4], F32))
        todo = [(h, qt) for h in range(MLA_H) for qt in range(TC)]
        with k.stage(9) as (block, scores_ready, scaled, probs_ready, probs_scaled, turned, turned_copied, out_ready, dve_step, copied):
            @block.sync
            def _(sp):
                k.feed(sp, 0)

            @block.tensor
            def _(pe):
                def scores(i):
                    h, qt = todo[i]
                    if i >= 2:
                        pe.wait_ge(scaled, i - 1)
                    pe.matmul(k.ps[:, i % 2, 0:P * (qt + 1)], q[h][0:QK, qt * P:(qt + 1) * P], key[h][0:QK, 0:P * (qt + 1)],
                              start=True, stop=True).then_inc(scores_ready, 1)
                scores(0)
                for i, (h, qt) in enumerate(todo):
                    if i + 1 < len(todo):
                        scores(i + 1)
                    pe.wait_ge(probs_scaled, i + 1)
                    if i >= 2:
                        pe.wait_ge(turned_copied, i - 1)
                    for j in range(qt + 1):
                        ins = pe.transpose(k.ps[:, 2 + i % 2, j * P:(j + 1) * P], k.tmp[:, i % 2, j * P:(j + 1) * P], k.ident[:, :])
                    ins.then_inc(turned, 1)
                    pe.wait_ge(turned_copied, i + 1)
                    hs = slice(64 * (h % 2), 64 * (h % 2) + 64)
                    for j in range(qt + 1):
                        ins = pe.matmul(k.ps[hs, 4 + h // 2, qt * P:(qt + 1) * P], v_t[:, j, 64 * h:64 * h + 64],
                                        k.tmp[:, 2 + i % 2, j * P:(j + 1) * P], start=(j == 0), stop=(j == qt))
                    ins.then_inc(out_ready, 1)

            @block.scalar
            def _(act):
                def copy_turned(i):
                    act.wait_ge(turned, i + 1)
                    if i >= 2:
                        act.wait_ge(out_ready, i - 1)
                    n = P * (todo[i][1] + 1)
                    act.activation(k.tmp[:, 2 + i % 2, 0:n], k.ps[:, 2 + i % 2, 0:n], ACT.Copy).then_inc(turned_copied, 1)
                for i, (h, qt) in enumerate(todo):
                    act.wait_ge(scaled, i + 1)
                    s = k.tmp[:, i % 2, 0:P * (qt + 1)]
                    act.activation(s, s, ACT.Exp, bias=mx[:, i % 2, 0:1], accum_out=mx[:, i % 2, 1:2]).then_inc(probs_ready, 1)
                    if i:
                        copy_turned(i - 1)
                copy_turned(len(todo) - 1)
                act.wait_ge(out_ready, len(todo))
                for j in range(2):
                    act.activation(k.C[:, j, :], k.ps[:, 4 + j, :], ACT.Copy).then_inc(copied, 1)
                act.wait_ge(copied, 2)

            @block.vector
            def _(dve):
                step = Steps(dve, dve_step)
                def normalise(i):
                    dve.wait_ge(probs_ready, i + 1)
                    s = k.tmp[:, i % 2, 0:P * (todo[i][1] + 1)]
                    step(dve.reciprocal(mx[:, i % 2, 2:3], mx[:, i % 2, 1:2]))
                    step(dve.tensor_scalar(s, s, mx[:, i % 2, 2:3], None, ALU.mult))
                    dve.sem_inc(probs_scaled, 1)
                for i, (h, qt) in enumerate(todo):
                    n = P * (qt + 1)
                    dve.wait_ge(scores_ready, i + 1)
                    if i >= 2:
                        dve.wait_ge(turned, i - 1)
                    step(dve.scalar_tensor_tensor(k.tmp[:, i % 2, 0:n], k.ps[:, i % 2, 0:n], QK ** -0.5,
                                                  strip[:, 512 - n:512], ALU.mult, ALU.add))
                    step(dve.tensor_reduce(mx[:, i % 2, 0:1], k.tmp[:, i % 2, 0:n], AX.X, ALU.max, negate=True))
                    dve.sem_inc(scaled, 1)
                    if i:
                        normalise(i - 1)
                normalise(len(todo) - 1)


def pool_mixer(k, l):
    n0 = k.first[f"pool{l}"]
    inv = small(k, l, "pool_inv").rearrange("p (a t) -> p a t", a=2)
    w_pool = small(k, l, "w_pool").rearrange("p (a n) -> p a n", a=2)
    with k.stage(5) as (block, product_ready, copied, pooled_ready, mixed, dve_step):
        @block.sync
        def _(sp):
            k.feed(sp, 3)

        @block.tensor
        def _(pe):
            k.loaded(pe, n0)
            for m in range(2):
                accumulate(k, pe, k.ps[:, m, :], n0, m * P, k.A, DC).then_inc(product_ready, 1)
            pe.wait_ge(pooled_ready, 1)
            for g in range(4):
                gs = slice(64 * (g % 2), 64 * (g % 2) + 64)
                ins = pe.matmul(k.ps[gs, 2 + g // 2, :], w_pool[gs, g // 2, :], k.B[gs, g // 2, :], start=True, stop=True)
            ins.then_inc(mixed, 1)

        @block.scalar
        def _(act):
            for m in range(2):
                act.wait_ge(product_ready, m + 1)
                act.activation(k.B[:, m, :], k.ps[:, m, :], ACT.Copy).then_inc(copied, 1)

        @block.vector
        def _(dve):
            step = Steps(dve, dve_step)
            dve.wait_ge(copied, 2)

            def widen(dst, src, lag, rows):
                step(dve.tensor_copy(dst[rows, 0:lag], src[rows, 0:lag]))
                step(dve.tensor_tensor(dst[rows, lag:T], src[rows, lag:T], src[rows, 0:T - lag], ALU.add))

            tile = lambda n: k.B[:, n, :]
            every, low, high = slice(0, P), slice(0, 64), slice(64, P)
            widen(tile(2), tile(0), 1, every)
            widen(tile(4), tile(2), 2, high)
            widen(tile(3), tile(1), 1, every)
            widen(tile(5), tile(3), 2, every)
            widen(tile(6), tile(5), 4, every)
            widen(tile(7), tile(6), 8, high)
            for rows, wide, m in ((low, 2, 0), (high, 4, 0), (low, 6, 1), (high, 7, 1)):
                step(dve.tensor_tensor(k.B[rows, wide, :], k.B[rows, wide, :], inv[rows, m, :], ALU.mult))
                step(dve.tensor_tensor(k.B[rows, m, :], k.B[rows, wide, :], k.B[rows, m, :], ALU.subtract))
            dve.sem_inc(pooled_ready, 1)
            dve.wait_ge(mixed, 1)
            dve.sem_inc(k.weights_used, 3)
            for m in range(2):
                step(dve.tensor_scalar(k.C[:, 2 + m, :], k.ps[:, 2 + m, :], col(k, f"pool_scale{l}", m), None, ALU.mult))


def conformer(k, l):
    n0 = k.first[f"conv{l}"]
    with k.stage(6) as (block, product_ready, gate_ready, vector_ready, stats_ready, squared, dve_step):
        @block.sync
        def _(sp):
            k.feed(sp, 1)

        @block.tensor
        def _(pe):
            k.loaded(pe, n0)
            for m in range(4):
                accumulate(k, pe, k.ps[:, m, :], n0, m * P, k.A, DC).then_inc(product_ready, 1)
            pe.wait_ge(vector_ready, 1)
            for m in range(2):
                ins = pe.matmul(k.ps[:, 4, :], k.ones[:, :], k.B[:, 2 + m, :], start=(m == 0), stop=(m == 1))
            ins.then_inc(stats_ready, 1)
            pe.wait_ge(squared, 2)
            for m in range(2):
                ins = pe.matmul(k.ps[:, 5, :], k.ones[:, :], k.B[:, 4 + m, :], start=(m == 0), stop=(m == 1))
            ins.then_inc(stats_ready, 1)

        @block.scalar
        def _(act):
            for m in range(2):
                act.wait_ge(product_ready, m + 3)
                act.activation(k.tmp[:, m, :], k.ps[:, 2 + m, :], ACT.Sigmoid).then_inc(gate_ready, 1)
            for m in range(2):
                act.wait_ge(vector_ready, m + 2)
                act.activation(k.B[:, 4 + m, :], k.B[:, 2 + m, :], ACT.Square).then_inc(squared, 1)
            act.wait_ge(stats_ready, 2)
            act.activation(k.tmp[:, 2, :], k.ps[:, 5, :], ACT.Sqrt, bias=col(k, "eps", 0), scale=1.0 / 256).then_inc(squared, 1)
            for m in range(2):
                act.wait_ge(vector_ready, m + 4)
                act.activation(k.C[:, 6 + m, :], k.B[:, 2 + m, :], ACT.Silu).then_inc(squared, 1)
            act.wait_ge(squared, 5)

        @block.vector
        def _(dve):
            step = Steps(dve, dve_step)
            for m in range(2):
                dve.wait_ge(gate_ready, m + 1)
                step(dve.tensor_tensor(k.B[:, m, :], k.tmp[:, m, :], k.ps[:, m, :], ALU.mult))
            dve.sem_inc(k.weights_used, 1)
            taps = lambda m, j: col(k, f"dw_w{l}_{j}", m)
            for m in range(2):
                acc, u = k.B[:, 2 + m, :], k.B[:, m, :]
                step(dve.tensor_scalar(acc, u, taps(m, CONV_K - 1), col(k, f"dw_b{l}", m), ALU.mult, ALU.add))
                for lag in range(1, CONV_K):
                    step(dve.scalar_tensor_tensor(acc[:, lag:T], u[:, 0:T - lag], taps(m, CONV_K - 1 - lag), acc[:, lag:T],
                                                  ALU.mult, ALU.add))
            dve.sem_inc(vector_ready, 1)
            dve.wait_ge(stats_ready, 1)
            for m in range(2):
                step(dve.scalar_tensor_tensor(k.B[:, 2 + m, :], k.ps[:, 4, :], -1.0 / 256, k.B[:, 2 + m, :], ALU.mult, ALU.add))
                dve.sem_inc(vector_ready, 1)
            dve.wait_ge(squared, 3)
            step(dve.reciprocal(k.tmp[:, 2, :], k.tmp[:, 2, :]))
            for m in range(2):
                step(dve.tensor_tensor(k.B[:, 2 + m, :], k.B[:, 2 + m, :], k.tmp[:, 2, :], ALU.mult))
                step(dve.tensor_scalar(k.B[:, 2 + m, :], k.B[:, 2 + m, :], col(k, f"cln_g{l}", m), col(k, f"cln_b{l}", m),
                                       ALU.mult, ALU.add))
                dve.sem_inc(vector_ready, 1)


def hgrn(k, l):
    n0 = k.first[f"hgrn{l}"]
    q, key, b = k.B[:, 0:2, :], k.B[:, 2:4, :], k.B[:, 4:6, :]
    v_t = k.tmp[:, 4:6, :].rearrange("p a b -> p (a b)").rearrange("p (t n) -> p t n", t=TC)
    g = k.C[:, 6:8, :]
    blocks = lambda tile: tile.rearrange("p (a b) -> p a b", b=P)
    with k.stage(5) as (block, product_ready, act_done, dve_done, dve_step, copied):
        AP_ = Phases(act_done, ["start"] + [f"{x}{m}" for m in range(2) for x in ("e", "ln", "e2", "ln2")])
        VP = Phases(dve_done, ["bounds"] + [f"{x}{m}" for m in range(2) for x in ("z", "d")])

        @block.sync
        def _(sp):
            k.feed(sp, 2)

        @block.tensor
        def _(pe):
            k.loaded(pe, n0)
            for m in range(4):
                accumulate(k, pe, k.ps[:, m, :], n0, m * P, k.A, DC).then_inc(product_ready, 1)
            k.loaded(pe, n0 + 1)
            for m in range(2):
                accumulate(k, pe, k.ps[:, 6 + m, :], n0 + 1, 256 + m * P, k.A, DC).then_inc(product_ready, 1)
            for t in range(TC):
                for c in range(DC):
                    ins = pe.matmul(k.ps[:, 4 + t // 2, 256 * (t % 2):256 * (t % 2) + 256], k.A[:, c, t * P:(t + 1) * P],
                                    k.chunk(n0 + 1)[:, c, 0:256], start=(c == 0), stop=(c == DC - 1))
            ins.then_inc(product_ready, 1)

        @block.scalar
        def _(act):
            act.wait_ge(product_ready, 2)
            act.activation(q, k.ps[:, 0:2, :], ACT.Silu).then_inc(copied, 1)
            act.wait_ge(product_ready, 4)
            act.activation(key, k.ps[:, 2:4, :], ACT.Sigmoid, scale=-1.0).then_inc(copied, 1)
            act.wait_ge(product_ready, 6)
            act.activation(g, k.ps[:, 6:8, :], ACT.Silu).then_inc(copied, 1)
            act.wait_ge(product_ready, 7)
            act.activation(v_t, k.ps[:, 4:6, :].rearrange("p a b -> p (a b)").rearrange("p (t n) -> p t n", t=TC), ACT.Copy)\
                .then_inc(copied, 1)
            act.wait_ge(copied, 4)
            VP.wait(act, 0, "bounds")
            if l:
                act.activation(k.lb[:, 0:2], k.lb[:, 4:6], ACT.Sigmoid)
                ins = act.activation(k.lb[:, 2:4], k.lb[:, 4:6], ACT.Sigmoid, scale=-1.0)
                ins.then_inc(copied, 1)
                act.wait_ge(copied, 5)
                act.activation(k.lb[:, 6:8], k.lb[:, 2:4], ACT.Ln).then_inc(copied, 1)
                AP_.last(act.activation(k.lb[:, 8:10], k.lb[:, 0:2], ACT.Ln), "start")
            else:
                AP_.done(act, "start")
            for m in range(2):
                VP.wait(act, 0, f"z{m}")
                AP_.last(act.activation(k.tmp[:, 0, :], k.tmp[:, 0, :], ACT.Exp), f"e{m}")
                act.wait_ge(act_done, AP_.at(0, f"e{m}"))
                AP_.last(act.activation(k.tmp[:, 0, :], k.tmp[:, 0, :], ACT.Ln, bias=1.0), f"ln{m}")
                VP.wait(act, 0, f"d{m}")
                if l:
                    AP_.last(act.activation(k.tmp[:, 2, :], k.tmp[:, 2, :], ACT.Exp), f"e2{m}")
                    act.wait_ge(act_done, AP_.at(0, f"e2{m}"))
                    AP_.last(act.activation(k.tmp[:, 2, :], k.tmp[:, 2, :], ACT.Ln, bias=1.0), f"ln2{m}")
                else:
                    AP_.done(act, f"e2{m}")
                    AP_.done(act, f"ln2{m}")

        @block.vector
        def _(dve):
            step = Steps(dve, dve_step)
            at = k.where["lb_logits"]
            step(dve.tensor_tensor(k.lb[:, 4:6], k.cols[:, at + 2:at + 4], k.cols[:, at:at + 2], ALU.subtract))
            VP.done(dve, "bounds")
            dve.wait_ge(copied, 4)
            dve.sem_inc(k.weights_used, 2)
            AP_.wait(dve, 0, "start")
            for m in range(2):
                t0, t1, t2 = k.tmp[:, 0, :], k.tmp[:, 1, :], k.tmp[:, 2, :]
                z = k.ps[:, 2 + m, :]
                step(dve.tensor_copy(t1, z))
                step(dve.scalar_tensor_tensor(t0, t1, -1.0, t1, ALU.mult, ALU.min))
                VP.done(dve, f"z{m}")
                step(dve.tensor_scalar(t1, t1, 0.0, None, ALU.min))
                AP_.wait(dve, 0, f"ln{m}")
                step(dve.tensor_tensor(t1, t1, t0, ALU.subtract))
                if l:
                    step(dve.tensor_scalar(t1, t1, k.lb[:, 6 + m:7 + m], None, ALU.add))
                    step(dve.tensor_scalar(t0, t1, -1.0, k.lb[:, 8 + m:9 + m], ALU.mult, ALU.add))
                    step(dve.scalar_tensor_tensor(t2, t0, -1.0, t0, ALU.mult, ALU.min))
                    VP.done(dve, f"d{m}")
                    step(dve.scalar_tensor_tensor(t1, t0, 0.0, t1, ALU.max, ALU.add))
                    AP_.wait(dve, 0, f"ln2{m}")
                    step(dve.tensor_tensor(t1, t1, t2, ALU.add))
                    step(dve.tensor_scalar(key[:, m, :], key[:, m, :], k.lb[:, 2 + m:3 + m], None, ALU.mult))
                else:
                    VP.done(dve, f"d{m}")
                step(dve.tensor_tensor_scan(b[:, m, :], k.seg[128][:, :], t1, 0.0, ALU.mult, ALU.add))
                AP_.wait(dve, 0, f"ln2{m}")

    with ExitStack() as own:
        S = own.enter_context(k.nc.sbuf_tensor(f"hgrn_state{l}", [P, P], F32))
        last_decay = own.enter_context(k.nc.sbuf_tensor(f"hgrn_last{l}", [P, TC], F32))
        AT = [blocks(k.B[:, 6, :]), blocks(k.B[:, 7, :])]
        E, qx, kx, part = (k.tmp[:, n, :] for n in range(4))
        with k.stage(5) as (block, pe_done, act_done, dve_done, dve_step, _):
            names = lambda *n: [f"{x}{m}" for m in range(2) for x in n]
            AP_ = Phases(act_done, names(*[f"E{v}_" for v in range(7)], "inter_", "turned_", "out_", "sq_", "dev_"))
            VP = Phases(dve_done, names("diag_", *[y for v in range(7) for y in (f"d{v}_", f"x{v}_")], "inter_", "hats_", *[f"s{c}_" for c in range(TC)], "fin_"))
            TP = Phases(pe_done, names("diag_", *[f"a{v}_" for v in range(7)], "turned_", *[f"u{c}_" for c in range(TC)], "sum_"))

            @block.sync
            def _(sp):
                k.feed(sp, 0)

            @block.tensor
            def _(pe):
                def pairwise(left, right, banks):
                    for h in range(2):
                        hs = slice(64 * h, 64 * h + 64)
                        for t in range(TC):
                            ts = slice(t * P, (t + 1) * P)
                            ins = pe.matmul(k.ps[:, banks + h, ts], left[hs, ts], right[hs, ts], start=True, stop=True)
                    return ins
                for m in range(2):
                    if m:
                        VP.wait(pe, 0, "fin_0")
                    TP.last(pairwise(key[:, m, :], q[:, m, :], 0), f"diag_{m}")
                    for v in range(7):
                        VP.wait(pe, 0, f"x{v}_{m}")
                        TP.last(pairwise(kx, qx, 2 if v % 2 == 0 else 0), f"a{v}_{m}")
                    VP.wait(pe, 0, f"hats_{m}")
                    for t in range(TC):
                        ins = pe.transpose(k.ps[:, 4, t * P:(t + 1) * P], kx[:, t * P:(t + 1) * P], k.ident[:, :])
                    TP.last(ins, f"turned_{m}")
                    AP_.wait(pe, 0, f"turned_{m}")
                    kt = blocks(part)
                    for c in range(TC):
                        cs = slice(c * P, (c + 1) * P)
                        if c:
                            VP.wait(pe, 0, f"s{c - 1}_{m}")
                        pe.matmul(k.ps[:, 5, cs], S[:, :], qx[:, cs], start=True, stop=False)
                        for h in range(2):
                            pe.matmul(k.ps[64 * h:64 * h + 64, 5, cs], v_t[:, c, P * m + 64 * h:P * m + 64 * h + 64], AT[h][:, c, :],
                                      start=False, stop=True)
                        TP.last(pe.matmul(k.ps[:, 6, 0:P], kt[:, c, :], v_t[:, c, P * m:P * m + P], start=True, stop=True), f"u{c}_{m}")
                    AP_.wait(pe, 0, f"sq_{m}")
                    TP.last(pe.matmul(k.ps[:, 7, :], k.pairs[:, :], kx, start=True, stop=True), f"sum_{m}")

            @block.scalar
            def _(act):
                for m in range(2):
                    for v in range(7):
                        VP.wait(act, 0, f"d{v}_{m}")
                        AP_.last(act.activation(E, E, ACT.Exp), f"E{v}_{m}")
                    VP.wait(act, 0, f"inter_{m}")
                    act.activation(qx, b[:, m, :], ACT.Exp)
                    act.activation(last_decay[:, :], b[:, m, P - 1:T:P], ACT.Exp)
                    AP_.last(act.activation(E, E, ACT.Exp), f"inter_{m}")
                    TP.wait(act, 0, f"turned_{m}")
                    AP_.last(act.activation(part, k.ps[:, 4, :], ACT.Copy), f"turned_{m}")
                    TP.wait(act, 0, f"u{TC - 1}_{m}")
                    AP_.last(act.activation(E, k.ps[:, 5, :], ACT.Copy), f"out_{m}")
                    AP_.last(act.activation(kx, k.ps[:, 5, :], ACT.Square), f"sq_{m}")
                    TP.wait(act, 0, f"sum_{m}")
                    AP_.last(act.activation(qx, k.ps[:, 7, :], ACT.Sqrt, bias=col(k, "eps", 0), scale=1.0 / 64), f"dev_{m}")

            @block.vector
            def _(dve):
                step = Steps(dve, dve_step)
                mask = lambda name: k.mask[name][:, :].unsqueeze(1).to_broadcast([P, TC, P])
                for m in range(2):
                    step(dve.memset(S[:, :], 0.0))
                    VP.done(dve, f"diag_{m}")
                    def gather(v, bank):
                        for h in range(2):
                            step(dve.tensor_tensor(blocks(part), blocks(k.ps[:, bank + h, :]), mask(f"level{v}"), ALU.mult))
                            step(dve.tensor_tensor(AT[h], AT[h], blocks(part), ALU.add))
                    for v in range(7):
                        size = 2 ** (v + 1)
                        wide = lambda ap: ap.rearrange("p (a b) -> p a b", b=size)
                        ref = wide(b[:, m, :])[:, :, size // 2 - 1:size // 2].to_broadcast([P, T // size, size])
                        step(dve.tensor_tensor(wide(E), wide(b[:, m, :]), ref, ALU.subtract))
                        step(dve.scalar_tensor_tensor(E, E, -1.0, E, ALU.mult, ALU.min))
                        VP.done(dve, f"d{v}_{m}")
                        if v == 0:
                            TP.wait(dve, 0, f"diag_{m}")
                            for h in range(2):
                                step(dve.tensor_tensor(AT[h], blocks(k.ps[:, h, :]), mask("ident"), ALU.mult))
                        else:
                            TP.wait(dve, 0, f"a{v - 1}_{m}")
                            gather(v - 1, 2 if (v - 1) % 2 == 0 else 0)
                        AP_.wait(dve, 0, f"E{v}_{m}")
                        step(dve.tensor_tensor(qx, q[:, m, :], E, ALU.mult))
                        step(dve.tensor_tensor(kx, key[:, m, :], E, ALU.mult))
                        VP.done(dve, f"x{v}_{m}")
                    last = blocks(b[:, m, :])[:, :, P - 1:P].to_broadcast([P, TC, P])
                    step(dve.tensor_tensor(blocks(E), last, blocks(b[:, m, :]), ALU.subtract))
                    TP.wait(dve, 0, f"a6_{m}")
                    gather(6, 2)
                    VP.done(dve, f"inter_{m}")
                    AP_.wait(dve, 0, f"inter_{m}")
                    step(dve.tensor_tensor(qx, qx, q[:, m, :], ALU.mult))
                    step(dve.tensor_tensor(kx, key[:, m, :], E, ALU.mult))
                    VP.done(dve, f"hats_{m}")
                    for c in range(TC):
                        TP.wait(dve, 0, f"u{c}_{m}")
                        step(dve.scalar_tensor_tensor(S[:, :], S[:, :], last_decay[:, c:c + 1], k.ps[:, 6, 0:P], ALU.mult, ALU.add))
                        step(dve.tensor_tensor(S[:, :], S[:, :], k.pairs[:, :], ALU.mult))
                        VP.done(dve, f"s{c}_{m}")
                    AP_.wait(dve, 0, f"dev_{m}")
                    step(dve.reciprocal(qx, qx))
                    step(dve.scalar_tensor_tensor(E, E, col(k, f"hgrn_g{l}", 0), qx, ALU.mult, ALU.mult))
                    step(dve.tensor_tensor(k.C[:, 4 + m, :], E, g[:, m, :], ALU.mult))
                    VP.done(dve, f"fin_{m}")


def mixer_output(k, l):
    n0 = k.first[f"out_2{l}"]
    with k.stage(2) as (block, product_ready, dve_step):
        @block.sync
        def _(sp):
            k.feed(sp, 2)

        @block.tensor
        def _(pe):
            for m in range(DC):
                if m % 4 == 0:
                    k.loaded(pe, n0 + m // 4)
                if m >= 4:
                    pe.wait_ge(dve_step, m - 3)
                accumulate(k, pe, k.ps[:, m % 4, :], n0 + m // 4, m % 4 * P, k.C, DC).then_inc(product_ready, 1)

        @block.vector
        def _(dve):
            step = Steps(dve, dve_step)
            for m in range(DC):
                dve.wait_ge(product_ready, m + 1)
                step(dve.scalar_tensor_tensor(k.X[:, m, :], k.ps[:, m % 4, :], mod(k, l, "g1", m), k.X[:, m, :], ALU.mult, ALU.add))
                if m % 4 == 3:
                    dve.sem_inc(k.weights_used, 1)


EG, EPG = 4, 8
NE = EG * EPG
F = 512
ROWS = 64
FURTHER = 16
PAIRS = (NE + FURTHER) // 2


def plan_experts(k, l):
    for name, kc, cols in (("w1_2", DC, F), ("w3_2", DC, F), ("w2_2", F // P, D)):
        for b in range(2):
            k.want(f"experts{l}", k.ins[name][l, b], kc, cols)


def routing(k, l, rows_out):
    h_tok = k.B[:, :, :].rearrange("p a b -> p (a b)").rearrange("p (t d) -> p t d", t=TC)
    with ExitStack() as own:
        sb = lambda name, shape: own.enter_context(k.nc.sbuf_tensor(f"{name}{l}", shape, F32))
        rw = sb("router_w", [P, DC, 36])
        rb = sb("router_b", [P, 36])
        c = k.C[:, :, :].rearrange("p a b -> p (a b)")
        at = [0]

        def tile(*shape):
            n = int(np.prod(shape))
            ap = c[:, at[0]:at[0] + n]
            at[0] += n
            if len(shape) == 2:
                return ap.rearrange("p (a b) -> p a b", a=shape[0])
            if len(shape) == 3:
                return ap.rearrange("p (a b c) -> p a b c", a=shape[0], b=shape[1])
            return ap
        logit, gl_e, one_g = tile(TC, 36), tile(TC, EG), tile(TC, EG)
        small4, small8 = tile(TC, EG), tile(TC, EPG)
        stat = [tile(TC, 1) for _ in range(8)]
        by_group, sel, sel2 = tile(TC, EG, EPG), tile(TC, EPG), tile(TC, EPG)
        one = [tile(TC, EPG), tile(TC, EPG)]
        OH = [tile(TC, NE), tile(TC, NE)]
        M, R, Q, t1, t2 = (tile(TC, NE) for _ in range(5))
        cnt, nov, st, end, off = (tile(NE) for _ in range(5))
        ind, ind2 = tile(FURTHER, NE), tile(FURTHER, NE)
        eid = tile(FURTHER)
        more = tile(FURTHER // 2)
        erow = k.trow[:, 0:NE]

        with k.stage(9) as (block, filled, landed, turned, copied, logits_ready, exps, ranks, dve_step, dve_done):
            @block.sync
            def _(sp):
                sp.dma_start(rw[:, :, :], k.ins["router_w"][l].rearrange("(c p) n -> p c n", p=P)).then_inc(landed, 16)
                sp.dma_start(rb[:, :], k.ins["router_b"][l:l + 1, :].to_broadcast([P, 36])).then_inc(landed, 16)
                anything = k.X[:, 0:2, :].rearrange("p a b -> p (a b)").unsqueeze(1).to_broadcast([P, FURTHER // 2, D])
                sp.dma_start(rows_out[NE // 2:PAIRS, :, :].rearrange("b p d -> p b d"), anything).then_inc(filled, 16)
                k.feed(sp, 0)
                sp.wait_ge(filled, 16)

            @block.tensor
            def _(pe):
                pe.wait_ge(landed, 32)
                for t in range(TC):
                    for c_ in range(DC):
                        ins = pe.matmul(k.ps[:, 7, 36 * t:36 * t + 36], k.A[:, c_, t * P:(t + 1) * P], rw[:, c_, :],
                                        start=(c_ == 0), stop=(c_ == DC - 1))
                ins.then_inc(logits_ready, 1)
                for i in range(2 * TC):
                    t, half = divmod(i, 2)
                    if i >= 4:
                        pe.wait_ge(copied, i - 3)
                    for j in range(4):
                        ins = pe.transpose(k.ps[:, i % 4, j * P:(j + 1) * P], k.A[:, 4 * half + j, t * P:(t + 1) * P], k.ident[:, :])
                    ins.then_inc(turned, 1)
                pe.wait_ge(dve_done, 2)
                for t in range(TC):
                    for u in range(t):
                        pe.matmul(k.ps[:, 6, NE * t:NE * (t + 1)], k.ones[:, :], M[:, u, :], start=(u == 0), stop=False)
                    pe.matmul(k.ps[:, 6, NE * t:NE * (t + 1)], k.mask["sooner"][:, :], M[:, t, :], start=(t == 0), stop=True)
                for u in range(TC):
                    ins = pe.matmul(k.ps[:, 6, NE * TC:NE * (TC + 1)], k.ones[:, :], M[:, u, :], start=(u == 0), stop=(u == TC - 1))
                ins.then_inc(ranks, 1)

            @block.scalar
            def _(act):
                for i in range(2 * TC):
                    t, half = divmod(i, 2)
                    act.wait_ge(turned, i + 1)
                    act.activation(h_tok[:, t, 512 * half:512 * half + 512], k.ps[:, i % 4, :], ACT.Copy).then_inc(copied, 1)
                act.wait_ge(dve_done, 1)
                act.activation(gl_e, gl_e, ACT.Exp).then_inc(exps, 1)
                act.activation(stat[3], stat[3], ACT.Exp).then_inc(exps, 1)
                act.wait_ge(copied, 2 * TC)

            @block.vector
            def _(dve):
                step = Steps(dve, dve_step)
                wide = lambda ap, n: ap.to_broadcast([P, TC, n])
                row = lambda ap, n: ap.unsqueeze(1).to_broadcast([P, TC, n])

                def first_of(x, top, n, scratch, out):
                    step(dve.tensor_tensor(scratch, x, wide(top, n), ALU.is_equal))
                    step(dve.tensor_scalar(scratch, scratch, -64.0, 64.0, ALU.mult, ALU.add))
                    step(dve.tensor_tensor(scratch, scratch, row(k.trow[:, 0:n], n), ALU.add))
                    step(dve.tensor_reduce(stat[7], scratch, AX.X, ALU.min))
                    step(dve.tensor_tensor(out, row(k.trow[:, 0:n], n), wide(stat[7], n), ALU.is_equal))

                dve.wait_ge(logits_ready, 1)
                step(dve.tensor_tensor(logit, k.ps[:, 7, 0:36 * TC].rearrange("p (t n) -> p t n", t=TC), row(rb[:, :], 36), ALU.add))
                gl = logit[:, :, 0:EG]
                step(dve.tensor_reduce(stat[0], gl, AX.X, ALU.max))
                first_of(gl, stat[0], EG, small4, one_g)
                step(dve.tensor_tensor(gl_e, gl, wide(stat[0], EG), ALU.subtract))
                el = logit[:, :, EG:36].rearrange("p t (g e) -> p t g e", g=EG)
                for g in range(EG):
                    step(dve.tensor_tensor(by_group[:, :, g, :], el[:, :, g, :], wide(one_g[:, :, g:g + 1], EPG), ALU.mult))
                step(dve.tensor_tensor(sel, by_group[:, :, 0, :], by_group[:, :, 1, :], ALU.add))
                step(dve.tensor_tensor(sel, sel, by_group[:, :, 2, :], ALU.add))
                step(dve.tensor_tensor(sel, sel, by_group[:, :, 3, :], ALU.add))
                step(dve.tensor_reduce(stat[1], sel, AX.X, ALU.max))
                first_of(sel, stat[1], EPG, small8, one[0])
                step(dve.scalar_tensor_tensor(sel2, one[0], -1e30, sel, ALU.mult, ALU.add))
                step(dve.tensor_reduce(stat[2], sel2, AX.X, ALU.max))
                first_of(sel2, stat[2], EPG, small8, one[1])
                step(dve.tensor_tensor(stat[3], stat[2], stat[1], ALU.subtract))
                dve.sem_inc(dve_done, 1)
                for i in range(2):
                    for g in range(EG):
                        step(dve.tensor_tensor(OH[i][:, :, EPG * g:EPG * (g + 1)], one[i], wide(one_g[:, :, g:g + 1], EPG), ALU.mult))
                step(dve.tensor_tensor(M, OH[0], OH[1], ALU.add))
                dve.sem_inc(dve_done, 1)
                dve.wait_ge(exps, 2)
                step(dve.tensor_reduce(stat[4], gl_e, AX.X, ALU.add))
                step(dve.tensor_scalar(stat[5], stat[3], 1.0, None, ALU.add))
                step(dve.tensor_tensor(stat[4], stat[4], stat[5], ALU.mult))
                step(dve.reciprocal(stat[4], stat[4]))
                step(dve.tensor_copy(k.row_w[:, 0, :].unsqueeze(2), stat[4]))
                step(dve.tensor_tensor(k.row_w[:, 1, :].unsqueeze(2), stat[4], stat[3], ALU.mult))
                dve.wait_ge(ranks, 1)
                step(dve.tensor_copy(R, k.ps[:, 6, 0:NE * TC].rearrange("p (t e) -> p t e", t=TC)))
                step(dve.tensor_copy(cnt, k.ps[:, 6, NE * TC:NE * (TC + 1)]))
                for x, y, cmp in ((R, Q, ALU.is_ge), (cnt, nov, ALU.is_gt)):
                    step(dve.tensor_scalar(y, x, float(ROWS), None, cmp))
                    for edge in range(2, T // ROWS):
                        step(dve.scalar_tensor_tensor(y, x, float(edge * ROWS), y, cmp, ALU.add))
                step(dve.tensor_tensor_scan(end, k.ones[:, 0:NE], nov, 0.0, ALU.mult, ALU.add))
                step(dve.tensor_tensor(st, end, nov, ALU.subtract))
                step(dve.tensor_tensor(off, st, erow, ALU.subtract))
                step(dve.tensor_scalar(off, off, float(NE - 1), None, ALU.add))
                step(dve.tensor_tensor(t1, Q, row(off, NE), ALU.add))
                step(dve.scalar_tensor_tensor(t1, Q, 0.0, t1, ALU.is_gt, ALU.mult))
                step(dve.tensor_tensor(t1, t1, row(erow, NE), ALU.add))
                step(dve.scalar_tensor_tensor(t1, t1, float(ROWS), R, ALU.mult, ALU.add))
                step(dve.scalar_tensor_tensor(t1, Q, -float(ROWS), t1, ALU.mult, ALU.add))
                for i in range(2):
                    step(dve.tensor_tensor(t2, t1, OH[i], ALU.mult))
                    step(dve.tensor_reduce(k.row_slot[:, i, :].unsqueeze(2), t2, AX.X, ALU.add))
                step(dve.tensor_copy(k.row_index[:, :, :], k.row_slot[:, :, :]))
                wide_e = lambda ap: ap.unsqueeze(1).to_broadcast([P, FURTHER, NE])
                jcol = k.trow[:, 0:FURTHER].unsqueeze(2).to_broadcast([P, FURTHER, NE])
                step(dve.tensor_tensor(ind, wide_e(st), jcol, ALU.is_le))
                step(dve.tensor_tensor(ind2, wide_e(end), jcol, ALU.is_gt))
                step(dve.tensor_tensor(ind, ind, ind2, ALU.mult))
                step(dve.tensor_tensor(ind, ind, wide_e(erow), ALU.mult))
                step(dve.tensor_reduce(eid, ind, AX.X, ALU.add))
                step(dve.tensor_copy(k.block_expert[:, 0:NE], erow[0:1, :]))
                step(dve.tensor_copy(k.block_expert[:, NE:NE + FURTHER], eid[0:1, :]))
                step(dve.tensor_scalar(more, k.trow[:, 0:FURTHER // 2], 2.0, None, ALU.mult))
                step(dve.tensor_tensor(more, more, end[:, NE - 1:NE].to_broadcast([P, FURTHER // 2]), ALU.is_lt))
                step(dve.tensor_reduce(eid[:, 0:1], more, AX.X, ALU.add))
                step(dve.tensor_scalar(k.pair_count[:, :], eid[0:1, 0:1], float(NE // 2), None, ALU.add))


def experts(k, l, rows_out):
    n0 = k.first[f"experts{l}"]
    h_tok = k.B[:, :, :].rearrange("p a b -> p (a b)").rearrange("p (t d) -> p t d", t=TC)
    flat = lambda lo: k.C[:, lo:lo + 2, :].rearrange("p a b -> p (a b)")
    xb = flat(0).rearrange("p (c r) -> p c r", c=DC)
    yb = flat(4)
    pick, gate, hidden, hidden_t, row_no = (k.tmp[:, n, :] for n in (0, 1, 2, 3, 4))
    blocks = lambda ap: ap.rearrange("p (a b) -> p a b", b=P)
    pair_count = lambda eng: eng.value_load(k.pair_count[0:1, 0:1], min_val=NE // 2, max_val=PAIRS)
    with k.stage(16) as (block, picked, gathered, x_ready, up_ready, gate_ready, hidden_ready, turned, turned_copied,
                         y_ready, y_copied, stored, dve_step, w1_loaded, w3_loaded, w2_loaded, pair_used):
        kinds = [("w1_2", DC, w1_loaded), ("w3_2", DC, w3_loaded), ("w2_2", F // P, w2_loaded)]
        slots = [[k.slot(n0 + 2 * j + h).rearrange("p (k n) -> p k n", k=kinds[j][1]) for h in range(2)] for j in range(3)]
        side = [slice(0, ROWS), slice(ROWS, P)]

        @block.sync
        def _(sp):
            count = pair_count(sp)
            k.feed(sp, 0)
            for j in range(3):
                for h in range(2):
                    k.loaded(sp, n0 + 2 * j + h)
                sp.sem_inc(kinds[j][2], 32)
            with sp.Fori(1, count) as i:
                expert = [sp.value_load(k.block_expert[0:1, bass.ds(i * 2 + h, 1)], min_val=0, max_val=NE - 1) for h in range(2)]
                for j, (name, kc, loaded) in enumerate(kinds):
                    sp.wait_ge(pair_used, i * 6 + (2 * j - 4))
                    for h in range(2):
                        src = k.ins[name][l][bass.ds(expert[h], 1), :, :].rearrange("o (k p) n -> p (o k) n", p=P)
                        sp.dma_start(slots[j][h], src).then_inc(loaded, 16)

        @block.tensor
        def _(pe):
            def gather(i):
                pe.wait_ge(picked, i + 1)
                for half in range(2):
                    for c in range(4):
                        for t in range(TC):
                            ins = pe.matmul(k.ps[:, half, c * P:(c + 1) * P], h_tok[:, t, (4 * half + c) * P:(4 * half + c + 1) * P],
                                            pick[:, t * P:(t + 1) * P], start=(t == 0), stop=(t == TC - 1))
                    ins.then_inc(gathered, 1)

            def up(i):
                pe.wait_ge(x_ready, i * 2 + 2)
                pe.wait_ge(hidden_ready, i + 1)
                for j in range(2):
                    pe.wait_ge(kinds[j][2], i * 32 + 32)
                    for c in range(DC):
                        for h in range(2):
                            ins = pe.matmul(k.ps[side[h], 2 + j, :], xb[:, c, side[h]], slots[j][h][:, c, :],
                                            start=(c == 0), stop=(c == DC - 1))
                    ins.then_inc(up_ready, 1)

            def down(i):
                pe.wait_ge(hidden_ready, i + 2)
                for j in range(4):
                    ins = pe.transpose(k.ps[:, 4, j * P:(j + 1) * P], hidden[:, j * P:(j + 1) * P], k.ident[:, :])
                ins.then_inc(turned, 1)
                pe.wait_ge(w2_loaded, i * 32 + 32)
                pe.wait_ge(y_copied, i * 2 + 1)
                pe.wait_ge(turned_copied, i + 1)
                for half in range(2):
                    for f in range(F // P):
                        for h in range(2):
                            ins = pe.matmul(k.ps[side[h], 5 + half, :], hidden_t[:, f * P + ROWS * h:f * P + ROWS * h + ROWS],
                                            slots[2][h][:, f, 512 * half:512 * half + 512], start=(f == 0), stop=(f == F // P - 1))
                    ins.then_inc(y_ready, 1)

            count = pair_count(pe)
            pe.sem_inc(turned, 1)
            pe.sem_inc(y_ready, 1)
            gather(0)
            with pe.Fori(0, count) as i:
                up(i)
                gather(i + 1)
                down(i)

        @block.scalar
        def _(act):
            def take(i):
                for half in range(2):
                    act.wait_ge(gathered, i * 2 + (half + 1))
                    act.activation(xb[:, 4 * half:4 * half + 4, :], blocks(k.ps[:, half, :]), ACT.Copy).then_inc(x_ready, 1)

            def gates(i):
                act.wait_ge(up_ready, i * 2 + 1)
                act.sem_inc(pair_used, 2)
                act.wait_ge(hidden_ready, i + 1)
                act.activation(gate, k.ps[:, 2, :], ACT.Silu).then_inc(gate_ready, 1)
                act.wait_ge(up_ready, i * 2 + 2)
                act.sem_inc(pair_used, 2)

            def finish(i):
                act.wait_ge(turned, i + 2)
                act.wait_ge(y_ready, i * 2 + 1)
                act.activation(hidden_t, k.ps[:, 4, :], ACT.Copy).then_inc(turned_copied, 1)
                act.wait_ge(stored, i * 16 + 16)
                for half in range(2):
                    act.wait_ge(y_ready, i * 2 + (half + 2))
                    if half:
                        act.sem_inc(pair_used, 2)
                    act.activation(yb[:, 512 * half:512 * half + 512], k.ps[:, 5 + half, :], ACT.Copy).then_inc(y_copied, 1)
                act.wait_ge(y_copied, i * 2 + 3)
                act.dma_start(rows_out[bass.ds(i, 1), :, :].rearrange("o p d -> p (o d)"), yb).then_inc(stored, 16)

            count = pair_count(act)
            act.sem_inc(y_copied, 1)
            act.sem_inc(stored, 16)
            take(0)
            with act.Fori(0, count) as i:
                gates(i)
                take(i + 1)
                finish(i)
            act.wait_ge(stored, count * 16 + 16)
            act.sem_inc(k.weights_used, 6)

        @block.vector
        def _(dve):
            of_token = lambda i: k.row_slot[:, i, :].unsqueeze(2).to_broadcast([P, TC, P])
            rows = row_no[:, 0:P].unsqueeze(1).to_broadcast([P, TC, P])
            other = k.tmp[:, 5, :]

            def choose(step, i, first=False):
                step(dve.tensor_tensor(blocks(other), rows, of_token(0), ALU.is_equal))
                if not first:
                    dve.wait_ge(gathered, i * 2)
                step(dve.tensor_tensor(blocks(pick), rows, of_token(1), ALU.is_equal))
                step(dve.tensor_tensor(pick, pick, other, ALU.add))
                dve.sem_inc(picked, 1)
                step(dve.tensor_scalar(row_no[:, 0:P], row_no[:, 0:P], float(P), None, ALU.add))

            def hide(step, i):
                dve.wait_ge(gate_ready, i + 1)
                dve.wait_ge(up_ready, i * 2 + 2)
                dve.wait_ge(turned, i + 1)
                step(dve.tensor_tensor(hidden, gate, k.ps[:, 3, :], ALU.mult))
                dve.sem_inc(hidden_ready, 1)

            count = pair_count(dve)
            step = Steps(dve, dve_step)
            step(dve.tensor_copy(row_no[:, 0:P], k.trow[:, 0:P]))
            dve.sem_inc(hidden_ready, 1)
            choose(step, 0, first=True)
            done = step.n
            with dve.Fori(0, count) as i:
                step = Steps(dve, dve_step, i * 5 + done)
                choose(step, i + 1)
                hide(step, i)
                assert step.n == 5


def combine(k, l, rows_out):
    row = [k.A[:, :, :].rearrange("p a b -> p (a b)").rearrange("p (t d) -> p t d", t=TC),
           k.C[:, :, :].rearrange("p a b -> p (a b)").rearrange("p (t d) -> p t d", t=TC)]
    source = rows_out.rearrange("b p d -> (b p) d")
    fetched = k.rows_fetched
    with k.stage(3) as (block, mixed, turned, dve_step):
        @block.sync
        def _(sp):
            for t in range(TC):
                sp.wait_ge(fetched[t], 32 * (l + 1))
            k.feed(sp, 6)

        @block.gpsimd
        def _(pool):
            for t in range(TC):
                for i in range(2):
                    pool.indirect_dma_start(row[i][:, t, :], None, source,
                                            bass.IndirectOffsetOnAxis(ap=k.row_index[:, i, t:t + 1], axis=0)).then_inc(fetched[t], 16)

        @block.vector
        def _(dve):
            step = Steps(dve, dve_step)
            for t in range(TC):
                dve.wait_ge(fetched[t], 32 * (l + 1))
                step(dve.tensor_scalar(row[0][:, t, :], row[0][:, t, :], k.row_w[:, 0, t:t + 1], None, ALU.mult))
                step(dve.scalar_tensor_tensor(row[0][:, t, :], row[1][:, t, :], k.row_w[:, 1, t:t + 1], row[0][:, t, :],
                                              ALU.mult, ALU.add))
            dve.sem_inc(mixed, 1)
            for c in range(DC):
                dve.wait_ge(turned, c + 1)
                step(dve.scalar_tensor_tensor(k.X[:, c, :], k.ps[:, c % 4, :], mod(k, l, "g2", c), k.X[:, c, :], ALU.mult, ALU.add))

        @block.tensor
        def _(pe):
            pe.wait_ge(mixed, 1)
            for c in range(DC):
                if c >= 4:
                    pe.wait_ge(dve_step, 2 * TC + c - 3)
                for t in range(TC):
                    ins = pe.transpose(k.ps[:, c % 4, t * P:(t + 1) * P], row[0][:, t, c * P:(c + 1) * P], k.ident[:, :])
                ins.then_inc(turned, 1)


def mixture(k, l):
    modulated_norm(k, l, 2)
    rows_out = k.nc.dram_tensor(f"expert_rows{l}", (PAIRS, P, D), F32, kind="Internal").ap()
    routing(k, l, rows_out)
    experts(k, l, rows_out)
    combine(k, l, rows_out)


def columns(x):
    out = {}

    def put(name, v):
        v = np.asarray(v).reshape(-1)
        pad = -len(v) % P
        if pad:
            v = np.concatenate([v, np.zeros(pad, v.dtype)])
        out[name] = v.reshape(-1, P).T

    for j in range(2):
        for w in range(3):
            put(f"conv_k{j}_{w}", x["conv_k"][j, w])
    for i in range(DEPTH):
        put(f"ln_g{i}", x["ln_g"][i])
        put(f"ln_b{i}", x["ln_b"][i])
    for n in range(6):
        put(f"rwkv_mu{n}", x["rwkv_mu"][0, n])
    put("rwkv_w0", x["rwkv_w0"])
    put("rwkv_a0", x["rwkv_a0"])
    put("c", x["c_2"])
    put("eps", np.full(P, EPS, np.float32))
    half = ROPE // 2
    freq = np.zeros(P, np.float32)
    freq[64:96] = np.tile((np.float32(10000.0) ** (-np.arange(half, dtype=np.float32) / half)).astype(np.float32), 2)
    put("rope_freq", freq)
    put("rope_sign", np.where(np.arange(P) < 80, -1.0, 1.0).astype(np.float32))
    put("lb_logits", x["hgrn_lb_logits_2"])
    for l in range(2):
        for name, key in (("b_ada", "b_ada"), ("norm1_g", "norm1_g"), ("norm2_g", "norm2_g"), ("q_a_g", "q_a_norm_g"),
                          ("kv_a_g", "kv_a_norm_g"), ("q_g", "q_norm_g"), ("k_g", "k_norm_g"), ("pool_scale", "pool_scale"),
                          ("dw_b", "conv_dw_b"), ("cln_g", "conv_ln_g"), ("cln_b", "conv_ln_b")):
            put(f"{name}{l}", x[f"{key}_2"][l])
        put(f"hgrn_g{l}", np.tile(x["hgrn_out_norm_g_2"][l], 2))
        for j in range(CONV_K):
            put(f"dw_w{l}_{j}", x["conv_dw_w_2"][l, j])
    put("gn_eps", np.full(P, GN_EPS, np.float32))
    put("ssm_d", x["ssm_d"])
    put("ssm_b_glu", x["ssm_b_glu"])
    put("half_pi", np.full(P, np.pi / 2, np.float32))
    put("ln_eps", np.full(P, LN_EPS, np.float32))
    return out


def ssm_layouts(x):
    tile = lambda v: np.asarray(v)[0].reshape(32, P).T
    log_dt = np.broadcast_to(x["ssm_log_dt"][0][:, None], (64, 64))
    raw = [tile(x["ssm_lam_re"]), tile(x["ssm_lam_im"]), log_dt.reshape(32, P).T]
    b = np.zeros((P, 2, DC, P), np.float32)
    c = np.zeros((P, 2, 32, 32), np.float32)
    for part, (bn, cn) in enumerate((("ssm_b_re", "ssm_c_re"), ("ssm_b_im", "ssm_c_im"))):
        for g in range(64):
            j, half = divmod(g, 2)
            row = 32 * (j % 4) + 16 * half
            b[row:row + 16, part, j // 4, 64 * half:64 * half + 64] = x[bn][0, g].T
            c[64 * half:64 * half + 64, part, j, 16 * half:16 * half + 16] = x[cn][0, g].T
    return {"ssm_raw": np.concatenate(raw, axis=1), "ssm_b": b.reshape(P, -1), "ssm_c": c.reshape(P, -1)}


def small_layouts(x):
    out = np.zeros((2, P, SMALL_COLS), np.float32)
    where = lambda name: slice(SMALL[name][0], SMALL[name][0] + SMALL[name][1])
    swap = np.zeros((P, P), np.float32)
    for i in range(64, 80):
        swap[i, i + 16] = swap[i + 16, i] = 1.0
    strip = np.zeros((P, 896), np.float32)
    strip[:, 384:512] = np.where(np.arange(P)[None, :] > np.arange(P)[:, None], -1e30, 0.0)
    inv = np.zeros((P, 2, T), np.float32)
    for g, w in enumerate((2, 4, 8, 16)):
        inv[64 * (g % 2):64 * (g % 2) + 64, g // 2] = 1.0 / np.minimum(np.arange(1, T + 1), w)
    for l in range(2):
        uq = x["w_uq_2"][l]
        out[l, :, where("w_uq")][:, 0:384] = uq[0:P]
        out[l, 0:64, 384:768] = uq[P:192]
        out[l, :, where("w_ukv")] = x["w_ukv_2"][l]
        out[l, :, where("swap")] = swap
        out[l, :, where("strip")] = strip
        out[l, :, where("pool_inv")] = inv.reshape(P, -1)
        out[l, :, where("w_pool")] = x["w_pool_2"][l].reshape(2, 2, 64, 64).transpose(1, 2, 0, 3).reshape(P, P)
    return out


MASKS = ["ident", "sooner", "before", "upto", "first_lower"] + [f"level{l}" for l in range(7)]
CONSTS = [("ones", P), ("pairs", P), ("trow", T), ("seg64", T), ("seg128", T)] + [(name, P) for name in MASKS]


def constant_values():
    p = np.arange(P)
    row, one = p[:, None], p[None, :]
    same = row // 64 == one // 64
    c = {
        "ones": np.ones((P, P)),
        "ident": np.eye(P),
        "seg64": np.tile(np.arange(T) % 64 != 0, (P, 1)),
        "seg128": np.tile(np.arange(T) % 128 != 0, (P, 1)),
        "before": same & (row < one),
        "sooner": row < one,
        "upto": same & (row <= one),
        "first_lower": ((row // 2) == (one // 2)) & (row > one),
        "pairs": (p[:, None] // 64 == p[None, :] // 64),
        "trow": np.tile(np.arange(T), (P, 1)),
    }
    for l in range(7):
        c[f"level{l}"] = (row >> (l + 1) == one >> (l + 1)) & (row >> l & 1 == 0) & (one >> l & 1 == 1)
    return np.concatenate([c[name].reshape(P, n).astype(np.float32) for name, n in CONSTS], axis=1)


def device_inputs(x):
    x = {name: np.asarray(v) for name, v in x.items()}
    cols = columns(x)
    where, at = {}, 0
    for name, v in cols.items():
        where[name] = at
        at += v.shape[1]
    d = {
        "x_t": x["x"][0].T,
        "p_t": x["p"][:, 0].transpose(0, 2, 1),
        "cols": np.concatenate(list(cols.values()), axis=1),
        "consts": constant_values(),
    }
    d.update(ssm_layouts(x))
    d["small"] = small_layouts(x)
    d["positions"] = x["positions_2"]
    d["router_w"] = np.concatenate([x["router_group_w_2"], x["router_expert_w_2"]], axis=2)
    d["router_b"] = np.concatenate([x["router_group_b_2"], x["router_expert_b_2"]], axis=1)
    for name in ("w1_2", "w3_2", "w2_2"):
        d[name] = x[name]
    d["w_ada_chunks"] = x["w_ada_2"].reshape(2, D, 12, 512).transpose(0, 2, 1, 3).reshape(24, D, 512)
    for name in ("w_in_2", "w_out_2"):
        d[name] = x[name]
    for name in ("w1", "w2", "a1", "a2"):
        d[f"rwkv_{name}"] = x[f"rwkv_{name}"][0]
    per_pair = [x[f"rwkv_{name}"].reshape(DC, P) for name in ("k_k", "k_a", "r_k", "lnx_g", "lnx_b")]
    per_pair += [np.zeros((DC, P), np.float32)] * 3
    d["rwkv_pairs"] = np.stack(per_pair, axis=-1)
    for name in ("conv_w_in", "conv_w_out", "ssm_w_in", "ssm_w_glu", "ssm_w_out", "rwkv_w_rkvz", "rwkv_w_out",
                 "ple_proj", "ple_gate"):
        d[name] = x[name]
    return {name: np.ascontiguousarray(v) for name, v in d.items()}, where


def build(nc, ins, out, where):
    with ExitStack() as ctx:
        k = Kernel(nc, ctx, ins, out)
        k.where = where
        tiles = {name: ctx.enter_context(nc.sbuf_tensor(f"const_{name}", [P, n], F32)) for name, n in CONSTS}
        k.ones, k.pairs, k.trow, k.ident = tiles["ones"], tiles["pairs"], tiles["trow"], tiles["ident"]
        k.seg = {64: tiles["seg64"], 128: tiles["seg128"]}
        k.mask = {name: tiles[name] for name in MASKS}
        k.const_tiles = [(tiles[name][:, :], n) for name, n in CONSTS]
        plan_weights(k)
        load_constants(k)
        for layer in range(DEPTH):
            if layer % 3 == 0:
                short_conv(k, layer // 3)
            elif layer % 3 == 1:
                ssm_mixer(k)
            else:
                rwkv_mixer(k)
            src, r = (k.B, k.A) if layer % 3 == 1 else (k.A, k.B)
            output_and_gate(k, layer, src, r)
            layer_norm(k, layer)
        modulation(k)
        for l in range(2):
            modulated_norm(k, l, 1)
            mla(k, l)
            pool_mixer(k, l)
            hgrn(k, l)
            conformer(k, l)
            mixer_output(k, l)
            mixture(k, l)
        store_output(k)


def kernel(**inputs):
    import concourse.bacc as bacc
    from concourse.bass_utils import run_bass_kernel_spmd

    nc = bacc.Bacc("TRN2", target_bir_lowering=False, num_devices=1)
    arrays, where = device_inputs(inputs)
    ins = {name: nc.dram_tensor(f"in_{name}", a.shape, mybir.dt.from_np(a.dtype), kind="ExternalInput").ap()
           for name, a in arrays.items()}
    out = nc.dram_tensor("out_t", (D, T), F32, kind="ExternalOutput").ap()
    build(nc, ins, out, where)
    r = run_bass_kernel_spmd(nc, [{f"in_{name}": a for name, a in arrays.items()}], core_ids=[0])
    return np.ascontiguousarray(r.results[0]["out_t"].T)[None]
```

```python
from contextlib import ExitStack, contextmanager

import numpy as np

import concourse.bass as bass
from concourse import mybir

F32 = mybir.dt.float32
I32 = mybir.dt.int32
ALU = mybir.AluOpType
ACT = mybir.ActivationFunctionType
AX = mybir.AxisListType
PE = mybir.EngineType.PE

P = 128
D = 1024
DC = D // P
T = 512
TC = T // P
DEPTH = 4
ALPHA = float((2 * DEPTH) ** 0.25)
LN_EPS = 1e-5
GN_EPS = 64e-5
EPS = 1e-6
SLOTS = 6
SLOT = 4096
TWO_PI = 2.0 * np.pi
ROUND = 12582912.0
PI_A = 6.28125
PI_B = 0.0019350051879882812
PI_C = float(TWO_PI - 6.28125 - 0.0019350051879882812)


class Steps:

    def __init__(self, eng, sem, base=0):
        self.eng, self.sem, self.n, self.base = eng, sem, 0, base

    def __call__(self, ins, wait=True):
        ins.then_inc(self.sem, 1)
        self.n += 1
        if wait:
            self.eng.wait_ge(self.sem, self.base + self.n)


class Kernel:
    def __init__(self, nc, ctx, ins, out):
        self.nc, self.ctx, self.ins, self.out = nc, ctx, ins, out
        sb = lambda name, shape, dt=F32: ctx.enter_context(nc.sbuf_tensor(name, shape, dt))
        self.sb = sb
        self.ring = sb("weight_ring", [P, SLOTS, SLOT])
        self.X = sb("residual", [P, DC, T])
        self.A = sb("work_a", [P, DC, T])
        self.B = sb("work_b", [P, DC, T])
        self.C = sb("work_c", [P, DC, T])
        self.cols = sb("column_params", [P, ins["cols"].shape[1]])
        self.tmp = sb("tmp", [P, 6, T])
        self.mod = sb("modulation", [P, 2, 48])
        self.row_w = sb("row_weights", [P, 2, TC])
        self.row_slot = sb("row_slots", [P, 2, TC])
        self.row_index = sb("row_indices", [P, 2, TC], I32)
        self.block_expert = sb("block_experts", [1, NE + FURTHER], I32)
        self.pair_count = sb("pair_count", [1, 1], I32)
        self.lb = sb("lower_bound", [P, 10])
        self.ps = ctx.enter_context(nc.psum_tensor("banks", [P, 8, 512], F32))
        sem = lambda name: ctx.enter_context(nc.semaphore(name))
        self.weights_loaded = [sem(f"weights_loaded_{i}") for i in range(SLOTS)]
        self.weights_used = sem("weights_used")
        self.dev_ready = sem("deviation_ready")
        self.rows_fetched = [sem(f"rows_fetched_{t}") for t in range(TC)]
        self.output_stored = sem("output_stored")
        self.signals = [[sem(f"stage_{h}_{i}") for i in range(16)] for h in range(2)]
        self.stage_no = 0
        self.queue = []
        self.first = {}
        self.issued = self.used = 0

    def slot(self, n):
        return self.ring[:, n % SLOTS, :]

    def want(self, name, src, kc, cols):
        self.first.setdefault(name, len(self.queue))
        self.queue.append((src, kc, cols))

    def want_halves(self, name, src, kc=DC):
        for q in range(src.shape[1] // 512):
            self.want(name, src[:, q * 512:(q + 1) * 512], kc, 512)

    def chunk(self, n):
        _, kc, cols = self.queue[n]
        return self.slot(n)[:, 0:kc * cols].rearrange("p (k n) -> p k n", k=kc)

    def feed(self, sp, consumed, limit=10 ** 6):
        self.used += consumed
        while self.issued < min(len(self.queue), self.used + SLOTS, limit):
            n = self.issued
            src, kc, cols = self.queue[n]
            if src is None:
                break
            if n >= SLOTS:
                sp.wait_ge(self.weights_used, n - SLOTS + 1)
            sp.dma_start(self.chunk(n), src.rearrange("(k p) n -> p k n", p=P)).then_inc(
                self.weights_loaded[n % SLOTS], 16)
            self.issued += 1

    def loaded(self, pe, n):
        pe.wait_ge(self.weights_loaded[n % SLOTS], 16 * (n // SLOTS + 1))

    @contextmanager
    def stage(self, signals):
        mine = self.signals[self.stage_no % 2]
        other = self.signals[(self.stage_no + 1) % 2]
        self.stage_no += 1
        with self.nc.Block() as block:
            if self.stage_no > 1:
                @block.gpsimd
                def _(pool):
                    for s in other:
                        pool.sem_clear(s)
            yield (block, *mine[:signals])


def col(k, name, i, n=P):
    at = k.where[name]
    return k.cols[0:n, at + i:at + i + 1]


def plan_weights(k):
    i = k.ins
    for layer in range(DEPTH):
        j = layer // 3
        if layer % 3 == 0:
            for q in range(2):
                for part in (1, 2, 0, 3):
                    at = part * D + q * 512
                    k.want(f"conv_in{j}", i["conv_w_in"][j][:, at:at + 512], DC, 512)
            w_out = i["conv_w_out"][j]
        elif layer % 3 == 1:
            k.want_halves("ssm_in", i["ssm_w_in"][0])
            k.want_halves("ssm_glu", i["ssm_w_glu"][0])
            w_out = i["ssm_w_out"][0]
        else:
            for n in range(4):
                k.want_halves("rwkv_in", i["rwkv_w_rkvz"][0, n])
            for n in range(6):
                k.want("ada0", i["w_ada_chunks"][n] if n < 3 else None, DC, 512)
            w_out = i["rwkv_w_out"][0]
        k.want_halves(f"out{layer}", w_out)
        k.want(f"out{layer}", i["ple_proj"][layer], 2, D)
        k.want_halves(f"out{layer}", i["ple_gate"][layer])
    for l in range(2):
        plan_mixer(k, l)
        plan_experts(k, l)


def accumulate(k, pe, bank, n, m, src, kc, size=P):
    w = k.chunk(n)
    for c in range(kc):
        last = pe.matmul(bank, w[:, c, m:m + size], src[:, c, :], start=(c == 0), stop=(c == kc - 1))
    return last


def load_constants(k):
    with k.stage(1) as (block, landed):
        @block.sync
        def _(sp):
            k.feed(sp, 0, limit=1)

        @block.scalar
        def _(act):
            loads = [(k.X[:, :, :], k.ins["x_t"].rearrange("(c p) t -> p c t", p=P)),
                     (k.cols[:, :], k.ins["cols"])]
            at = 0
            for dst, n in k.const_tiles:
                loads.append((dst, k.ins["consts"][:, at:at + n]))
                at += n
            for dst, src in loads:
                act.dma_start(dst, src).then_inc(landed, 16)
            act.wait_ge(landed, 16 * len(loads))


def short_conv(k, layer):
    first = k.first[f"conv_in{layer}"]
    with k.stage(6) as (block, product_ready, cg_copied, gate_ready, unit_done, dve_step, act_step):
        @block.sync
        def _(sp):
            k.feed(sp, 8)

        @block.tensor
        def _(pe):
            for q in range(2):
                for m in range(4):
                    unit = 4 * q + m
                    if unit >= 2:
                        pe.wait_ge(unit_done, unit - 1)
                    for w in range(4):
                        if m == 0:
                            k.loaded(pe, first + 4 * q + w)
                        accumulate(k, pe, k.ps[:, 4 * (unit % 2) + w, :], first + 4 * q + w, m * P, k.X, DC)\
                            .then_inc(product_ready, 1)

        @block.scalar
        def _(act):
            for unit in range(8):
                half = unit % 2
                act.wait_ge(product_ready, 4 * unit + 1)
                if unit >= 2:
                    act.wait_ge(unit_done, unit - 1)
                act.activation(k.tmp[:, 3 * half, :], k.ps[:, 4 * half, :], ACT.Copy).then_inc(cg_copied, 1)
                act.wait_ge(product_ready, 4 * unit + 4)
                act.activation(k.tmp[:, 3 * half + 1, :], k.ps[:, 4 * half + 3, :], ACT.Silu).then_inc(gate_ready, 1)

        @block.vector
        def _(dve):
            step = Steps(dve, dve_step)
            tap = [[col(k, f"conv_k{layer}_{w}", u) for u in range(DC)] for w in range(3)]
            for unit in range(8):
                half = unit % 2
                u, out = k.tmp[:, 3 * half + 2, :], k.A[:, unit, :]
                dve.wait_ge(cg_copied, unit + 1)
                dve.wait_ge(product_ready, 4 * unit + 2)
                step(dve.tensor_tensor(u, k.tmp[:, 3 * half, :], k.ps[:, 4 * half + 1, :], ALU.mult))
                step(dve.tensor_scalar(out, u, tap[2][unit], None, ALU.mult))
                step(dve.scalar_tensor_tensor(out[:, 1:T], u[:, 0:T - 1], tap[1][unit], out[:, 1:T], ALU.mult, ALU.add))
                step(dve.scalar_tensor_tensor(out[:, 2:T], u[:, 0:T - 2], tap[0][unit], out[:, 2:T], ALU.mult, ALU.add))
                dve.wait_ge(product_ready, 4 * unit + 3)
                step(dve.tensor_tensor(out, out, k.ps[:, 4 * half + 2, :], ALU.mult))
                dve.wait_ge(gate_ready, unit + 1)
                step(dve.tensor_tensor(out, out, k.tmp[:, 3 * half + 1, :], ALU.mult))
                dve.sem_inc(unit_done, 1)
                if unit % 4 == 3:
                    dve.sem_inc(k.weights_used, 4)


def output_and_gate(k, layer, src, r):
    first = k.first[f"out{layer}"]
    p_t = k.tmp[:, 4:6, :]
    with k.stage(6) as (block, p_loaded, mixed, summed, gated, gate_ready, dve_step):
        @block.sync
        def _(sp):
            sp.dma_start(p_t, k.ins["p_t"][layer].rearrange("(c p) t -> p c t", p=P)).then_inc(p_loaded, 16)
            k.feed(sp, 5)

        @block.tensor
        def _(pe):
            for m in range(DC):
                if m % 4 == 0:
                    k.loaded(pe, first + m // 4)
                if m >= 4:
                    pe.wait_ge(summed, m - 3)
                accumulate(k, pe, k.ps[:, m % 4, :], first + m // 4, m % 4 * P, src, DC).then_inc(mixed, 1)
            pe.wait_ge(p_loaded, 16)
            k.loaded(pe, first + 2)
            pe.wait_ge(summed, DC)
            for m in range(DC):
                if m % 4 == 0:
                    k.loaded(pe, first + 3 + m // 4)
                if m >= 2:
                    pe.wait_ge(summed, DC + m - 1)
                accumulate(k, pe, k.ps[:, 4 + m % 2, :], first + 3 + m // 4, m % 4 * P, r, DC).then_inc(gated, 1)
                accumulate(k, pe, k.ps[:, 6 + m % 2, :], first + 2, m * P, p_t, 2).then_inc(gated, 1)

        @block.scalar
        def _(act):
            for m in range(DC):
                act.wait_ge(gated, 2 * m + 1)
                if m >= 2:
                    act.wait_ge(summed, DC + m - 1)
                act.activation(k.tmp[:, m % 2, :], k.ps[:, 4 + m % 2, :], ACT.Sigmoid).then_inc(gate_ready, 1)

        @block.vector
        def _(dve):
            step = Steps(dve, dve_step)
            for m in range(DC):
                dve.wait_ge(mixed, m + 1)
                dve.scalar_tensor_tensor(r[:, m, :], k.X[:, m, :], ALPHA, k.ps[:, m % 4, :], ALU.mult, ALU.add)\
                    .then_inc(summed, 1)
                if m % 4 == 3:
                    dve.sem_inc(k.weights_used, 1)
            for m in range(DC):
                dve.wait_ge(gate_ready, m + 1)
                dve.wait_ge(gated, 2 * m + 2)
                step(dve.tensor_tensor(k.tmp[:, 2, :], k.tmp[:, m % 2, :], k.ps[:, 6 + m % 2, :], ALU.mult))
                step(dve.tensor_tensor(k.X[:, m, :], r[:, m, :], k.tmp[:, 2, :], ALU.add))
                dve.sem_inc(summed, 1)
            dve.sem_inc(k.weights_used, 3)


def layer_norm(k, layer):
    with k.stage(5) as (block, sums, centred, squared, deviation, dve_step):
        @block.sync
        def _(sp):
            k.feed(sp, 0)

        @block.tensor
        def _(pe):
            for c in range(DC):
                last = pe.matmul(k.ps[:, 0, :], k.ones[:, :], k.X[:, c, :], start=(c == 0), stop=(c == DC - 1))
            last.then_inc(sums, 1)
            for c in range(DC):
                pe.wait_ge(squared, c + 1)
                last = pe.matmul(k.ps[:, 1, :], k.ones[:, :], k.B[:, c, :], start=(c == 0), stop=(c == DC - 1))
            last.then_inc(sums, 1)

        @block.scalar
        def _(act):
            for c in range(DC):
                act.wait_ge(centred, c + 1)
                act.activation(k.B[:, c, :], k.A[:, c, :], ACT.Square).then_inc(squared, 1)
            act.wait_ge(sums, 2)
            act.activation(k.tmp[:, 0, :], k.ps[:, 1, :], ACT.Sqrt, bias=col(k, "ln_eps", 0), scale=1.0 / D)\
                .then_inc(deviation, 1)

        @block.vector
        def _(dve):
            step = Steps(dve, dve_step)
            dve.wait_ge(sums, 1)
            for c in range(DC):
                dve.scalar_tensor_tensor(k.A[:, c, :], k.ps[:, 0, :], -1.0 / D, k.X[:, c, :], ALU.mult, ALU.add)\
                    .then_inc(centred, 1)
            dve.wait_ge(deviation, 1)
            step(dve.reciprocal(k.tmp[:, 1, :], k.tmp[:, 0, :]))
            for c in range(DC):
                step(dve.tensor_tensor(k.A[:, c, :], k.A[:, c, :], k.tmp[:, 1, :], ALU.mult))
                step(dve.tensor_scalar(k.X[:, c, :], k.A[:, c, :], col(k, f"ln_g{layer}", c),
                                       col(k, f"ln_b{layer}", c), ALU.mult, ALU.add))


def store_output(k):
    stored = k.output_stored
    with k.stage(0) as (block,):
        @block.sync
        def _(sp):
            sp.dma_start(k.out.rearrange("(c p) t -> p c t", p=P), k.X[:, :, :]).then_inc(stored, 16)
            sp.wait_ge(stored, 16)


def reduce_angle(dve, step, angle, turns, scratch):
    step(dve.tensor_scalar(turns, angle, 1.0 / TWO_PI, ROUND, ALU.mult, ALU.add))
    step(dve.tensor_scalar(turns, turns, ROUND, None, ALU.subtract))
    step(dve.scalar_tensor_tensor(scratch, turns, -PI_A, angle, ALU.mult, ALU.add))
    step(dve.scalar_tensor_tensor(scratch, turns, -PI_B, scratch, ALU.mult, ALU.add))
    step(dve.scalar_tensor_tensor(scratch, turns, -PI_C, scratch, ALU.mult, ALU.add))
    step(dve.tensor_scalar(turns, scratch, 1.0 / TWO_PI, 0.5, ALU.mult, ALU.min))
    step(dve.tensor_scalar(turns, turns, -0.5, None, ALU.max))


TURN = 6.283185
G2 = 32


def ssm_project(k, name, halves, base, dst, func):
    first = k.first[name] + base
    with k.stage(3) as (block, product_ready, evacuated, act_step):
        @block.sync
        def _(sp):
            k.feed(sp, halves)

        @block.tensor
        def _(pe):
            for m in range(4 * halves):
                if m % 4 == 0:
                    k.loaded(pe, first + m // 4)
                if m >= 4:
                    pe.wait_ge(evacuated, m - 3)
                accumulate(k, pe, k.ps[:, m % 4, :], first + m // 4, m % 4 * P, k.X, DC).then_inc(product_ready, 1)

        @block.scalar
        def _(act):
            for m in range(4 * halves):
                act.wait_ge(product_ready, m + 1)
                act.activation(dst[:, m, :], k.ps[:, m % 4, :], func).then_inc(evacuated, 1)
                if m % 4 == 3:
                    act.sem_inc(k.weights_used, 1)


def ssm_scan(k):
    par_names = "rho turn re im dt a_re a_im den k_re k_im s0 s1".split()
    with ExitStack() as own:
        sb = lambda name, shape: own.enter_context(k.nc.sbuf_tensor(name, shape, F32))
        kept = sb("ssm_params", [P, 2, G2])
        par = k.tmp[:, 4, :].rearrange("p (a g) -> p a g", g=G2)
        raw = k.tmp[:, 5, 0:3 * G2].rearrange("p (a g) -> p a g", g=G2)
        bmat = sb("ssm_bmat", [P, 2, DC, P])
        cmat = sb("ssm_cmat", [P, 2, G2, 32])
        q = {name: (kept if i < 2 else par)[:, i, :] for i, name in enumerate(par_names)}
        lr, li, log_dt = raw[:, 0, :], raw[:, 1, :], raw[:, 2, :]
        cf = k.tmp[:, 0:4, :].rearrange("p a (g h) -> p a g h", h=32)

        with k.stage(4) as (block, landed, dve_step, act_step, ready):
            @block.sync
            def _(sp):
                sp.dma_start(raw[:, :, :], k.ins["ssm_raw"].rearrange("p (a g) -> p a g", a=3)).then_inc(landed, 16)
                sp.dma_start(bmat[:, :, :, :], k.ins["ssm_b"].rearrange("p (a c n) -> p a c n", a=2, c=DC)).then_inc(landed, 16)
                sp.dma_start(cmat[:, :, :, :], k.ins["ssm_c"].rearrange("p (a g n) -> p a g n", a=2, g=G2)).then_inc(landed, 16)
                k.feed(sp, 0)

            @block.scalar
            def _(act):
                act.wait_ge(landed, 48)
                act.activation(q["dt"], log_dt, ACT.Exp).then_inc(act_step, 1)
                act.wait_ge(ready, 1)
                act.activation(q["rho"], q["re"], ACT.Exp).then_inc(act_step, 1)
                act.wait_ge(ready, 2)
                act.activation(q["s0"], q["turn"], ACT.Sin, scale=TURN).then_inc(act_step, 1)
                act.activation(q["s1"], q["k_re"], ACT.Sin, scale=-TURN, bias=col(k, "half_pi", 0)).then_inc(act_step, 1)

            @block.vector
            def _(dve):
                step = Steps(dve, dve_step)
                dve.wait_ge(act_step, 1)
                step(dve.tensor_tensor(q["re"], lr, q["dt"], ALU.mult))
                step(dve.tensor_tensor(q["im"], li, q["dt"], ALU.mult))
                dve.sem_inc(ready, 1)
                reduce_angle(dve, step, q["im"], q["turn"], q["k_re"])
                step(dve.scalar_tensor_tensor(q["k_re"], q["turn"], -1.0, q["turn"], ALU.mult, ALU.max))
                dve.sem_inc(ready, 1)
                dve.wait_ge(act_step, 4)
                step(dve.tensor_tensor(q["a_im"], q["rho"], q["s0"], ALU.mult))
                step(dve.tensor_tensor(q["a_re"], q["rho"], q["s1"], ALU.mult))
                step(dve.tensor_scalar(q["a_re"], q["a_re"], -1.0, None, ALU.add))
                step(dve.tensor_tensor(q["den"], lr, lr, ALU.mult))
                step(dve.tensor_tensor(q["s0"], li, li, ALU.mult))
                step(dve.tensor_tensor(q["den"], q["den"], q["s0"], ALU.add))
                step(dve.reciprocal(q["den"], q["den"]))
                step(dve.tensor_tensor(q["k_re"], q["a_re"], lr, ALU.mult))
                step(dve.tensor_tensor(q["s0"], q["a_im"], li, ALU.mult))
                step(dve.tensor_tensor(q["k_re"], q["k_re"], q["s0"], ALU.add))
                step(dve.tensor_tensor(q["k_re"], q["k_re"], q["den"], ALU.mult))
                step(dve.tensor_tensor(q["k_im"], q["a_im"], lr, ALU.mult))
                step(dve.tensor_tensor(q["s0"], q["a_re"], li, ALU.mult))
                step(dve.tensor_tensor(q["k_im"], q["k_im"], q["s0"], ALU.subtract))
                step(dve.tensor_tensor(q["k_im"], q["k_im"], q["den"], ALU.mult))
                for h in range(2):
                    g = slice(16 * h, 16 * h + 16)
                    kr = q["k_re"][:, g].unsqueeze(2).to_broadcast([P, 16, 32])
                    ki = q["k_im"][:, g].unsqueeze(2).to_broadcast([P, 16, 32])
                    cr, ci = cmat[:, 0, g, :], cmat[:, 1, g, :]
                    step(dve.tensor_tensor(cf[:, 0], cr, kr, ALU.mult))
                    step(dve.tensor_tensor(cf[:, 1], ci, ki, ALU.mult))
                    step(dve.tensor_tensor(cf[:, 2], cr, ki, ALU.mult))
                    step(dve.tensor_tensor(cf[:, 3], ci, kr, ALU.mult))
                    step(dve.tensor_tensor(cr, cf[:, 0], cf[:, 1], ALU.subtract))
                    step(dve.scalar_tensor_tensor(ci, cf[:, 2], -1.0, cf[:, 3], ALU.mult, ALU.subtract))

        frac = [k.tmp[:, 1, :], k.tmp[:, 2, :]]
        size = [k.tmp[:, 3, :], k.tmp[:, 4, :]]
        sine, cosine = frac, size
        prod = k.C[:, 0:4, :]
        rot = [k.C[:, 4, :], k.C[:, 5, :]]
        scr = k.tmp[:, 5, :]
        scan = [k.C[:, 6, :], k.C[:, 7, :]]
        with ExitStack() as more:
            sb2 = lambda name, shape: more.enter_context(k.nc.sbuf_tensor(name, shape, F32))
            u = k.tmp[:, 0, :]
            bc = sb2("ssm_b_chunk", [P, 2, P])
            cc = sb2("ssm_c_chunk", [P, 2, 2, 4, 32])
            pc = sb2("ssm_param_chunk", [P, 2, 4, 2])
            dc = sb2("ssm_d_chunk", [P, 2, 1])
            with k.stage(11) as (block, chunk_ready, turns_ready, angle_ready, table_ready, bu_ready, bu_read,
                                 products_ready, products_used, y_read, dve_step, act_step):
                STEPS = 4 * 13 + 1

                def passes(eng, run):
                    run(0, 0, first=True)
                    with eng.Fori(0, DC // 2 - 1) as i:
                        for q_ in (1, 0):
                            run(i * 2 + (2 - q_), q_)
                    run(DC - 1, 1, last=True)

                @block.sync
                def _(sp):
                    k.feed(sp, 0)

                @block.scalar
                def _(act):
                    def operands(c, p, wait_inputs=True):
                        act.activation(pc[:, p, :, 0], q["rho"][:, bass.ds(c * 4, 4)], ACT.Copy).then_inc(chunk_ready, 1)
                        act.activation(pc[:, p, :, 1], q["turn"][:, bass.ds(c * 4, 4)], ACT.Copy).then_inc(chunk_ready, 1)
                        if wait_inputs:
                            act.wait_ge(bu_ready, c * 8)
                        act.activation(u, k.B[:, bass.ds(c, 1), :], ACT.Copy).then_inc(chunk_ready, 1)
                        act.activation(bc[:, :, :], bmat[:, :, bass.ds(c, 1), :], ACT.Copy).then_inc(chunk_ready, 1)
                        act.activation(cc[:, p, :, :, :], cmat[:, :, bass.ds(c * 4, 4), :], ACT.Copy).then_inc(chunk_ready, 1)
                        act.activation(dc[:, p, :], k.cols[:, bass.ds(c + k.where["ssm_d"], 1)], ACT.Copy).then_inc(chunk_ready, 1)
                        act.wait_ge(chunk_ready, c * 6 + 6)

                    def turns(c, p, j, start=False):
                        act.activation(frac[j % 2], k.trow[:, :], ACT.Copy, scale=pc[:, p, j, 1:2]).then_inc(act_step, 1)
                        act.wait_ge(act_step, c * 8 + (2 * j + 1))
                        if not start:
                            act.wait_ge(angle_ready, c * 4 + j)
                        act.activation(scr, frac[j % 2], ACT.Identity, bias=col(k, "round", 0)).then_inc(turns_ready, 1)

                    def run(c, p, first=False, last=False):
                        for j in range(4):
                            act.wait_ge(angle_ready, c * 4 + (j + 1))
                            act.activation(size[j % 2], frac[j % 2], ACT.Abs).then_inc(act_step, 1)
                            act.wait_ge(act_step, c * 8 + (2 * j + 2))
                            act.activation(sine[j % 2], frac[j % 2], ACT.Sin, scale=-TURN).then_inc(table_ready, 1)
                            act.activation(cosine[j % 2], size[j % 2], ACT.Sin, scale=-TURN, bias=col(k, "half_pi", 0))\
                                .then_inc(table_ready, 1)
                            if not (first and j == 0):
                                act.wait_ge(products_ready, c * 4 + j)
                            if j < 3:
                                turns(c, p, j + 1)
                            elif not last:
                                act.wait_ge(y_read, c + 1)
                                operands(c + 1, 1 - p)
                                turns(c + 1, 1 - p, 0)

                    operands(0, 0, wait_inputs=False)
                    turns(0, 0, 0, start=True)
                    passes(act, run)

                @block.tensor
                def _(pe):
                    def inputs(j):
                        lo = 32 * j
                        for i in range(2):
                            pe.matmul(k.ps[:, 2 * (j % 2) + i, :], bc[lo:lo + 32, i, :], u[lo:lo + 32, :],
                                      start=True, stop=True).then_inc(bu_ready, 1)

                    def run(c, p, first=False, last=False):
                        for j in range(4):
                            if not (last and j == 3):
                                if not (first and j == 0):
                                    pe.wait_ge(bu_read, c * 4 + j)
                                if j < 3:
                                    inputs(j + 1)
                                else:
                                    pe.wait_ge(chunk_ready, c * 6 + 12)
                                    inputs(0)
                            pe.wait_ge(products_ready, c * 4 + (j + 1))
                            if j == 0 and not first:
                                pe.wait_ge(y_read, c)
                            for i in range(4):
                                ins = pe.matmul(k.ps[32 * j:32 * j + 32, 4 + p, :], cc[:, p, [0, 0, 1, 1][i], j, :],
                                                prod[:, i, :], start=(i == 0), stop=(i == 3))
                            ins.then_inc(products_used, 1)

                    pe.wait_ge(chunk_ready, 6)
                    inputs(0)
                    passes(pe, run)

                @block.vector
                def _(dve):
                    def angles(step, c, j):
                        dve.wait_ge(turns_ready, c * 4 + (j + 1))
                        step(dve.scalar_tensor_tensor(frac[j % 2], scr, ROUND, frac[j % 2], ALU.subtract, ALU.subtract))
                        dve.sem_inc(angle_ready, 1)

                    def output(step, c, p):
                        dve.wait_ge(products_used, c * 4 + 4)
                        step(dve.scalar_tensor_tensor(k.A[:, bass.ds(c, 1), :], k.B[:, bass.ds(c, 1), :], dc[:, p, :], k.ps[:, 4 + p, :], ALU.mult, ALU.add))
                        dve.sem_inc(y_read, 1)

                    def run(step, c, p, first=False, last=False):
                        dve.wait_ge(chunk_ready, c * 6 + 6)
                        for j in range(4):
                            co, si = cosine[j % 2], sine[j % 2]
                            bu = [k.ps[:, 2 * (j % 2) + i, :] for i in range(2)]
                            dve.wait_ge(table_ready, c * 8 + 2 * (j + 1))
                            dve.wait_ge(bu_ready, c * 8 + 2 * (j + 1))
                            step(dve.tensor_tensor(rot[0], co, bu[0], ALU.mult), wait=False)
                            step(dve.tensor_tensor(scan[0], si, bu[1], ALU.mult), wait=False)
                            step(dve.tensor_tensor(rot[1], co, bu[1], ALU.mult), wait=False)
                            step(dve.tensor_tensor(scan[1], si, bu[0], ALU.mult))
                            dve.sem_inc(bu_read, 1)
                            step(dve.tensor_tensor(rot[0], rot[0], scan[0], ALU.add), wait=False)
                            step(dve.tensor_tensor(rot[1], rot[1], scan[1], ALU.subtract))
                            rho = pc[:, p, j, 0:1].to_broadcast([P, T])
                            if j < 3:
                                angles(step, c, j + 1)
                            elif not last:
                                angles(step, c + 1, 0)
                            step(dve.tensor_tensor_scan(scan[0], rho, rot[0], 0.0, ALU.mult, ALU.add), wait=False)
                            step(dve.tensor_tensor_scan(scan[1], rho, rot[1], 0.0, ALU.mult, ALU.add))
                            if j == 0 and not first:
                                output(step, c - 1, 1 - p)
                            if not (first and j == 0):
                                dve.wait_ge(products_used, c * 4 + j)
                            step(dve.tensor_tensor(prod[:, 0, :], co, scan[0], ALU.mult), wait=False)
                            step(dve.scalar_tensor_tensor(prod[:, 1, :], si, -1.0, scan[1], ALU.mult, ALU.mult), wait=False)
                            step(dve.tensor_tensor(prod[:, 2, :], si, scan[0], ALU.mult), wait=False)
                            step(dve.tensor_tensor(prod[:, 3, :], co, scan[1], ALU.mult))
                            dve.sem_inc(products_ready, 1)

                    dve.sem_inc(y_read, 1)
                    step = Steps(dve, dve_step)
                    angles(step, 0, 0)
                    run(step, 0, 0, first=True)
                    done = step.n
                    with dve.Fori(0, DC // 2 - 1) as i:
                        for p in (1, 0):
                            step = Steps(dve, dve_step, i * (2 * STEPS) + (done + (1 - p) * STEPS))
                            run(step, i * 2 + (2 - p), p)
                            assert step.n == STEPS, step.n
                    step = Steps(dve, dve_step, done + (DC - 2) * STEPS)
                    run(step, DC - 1, 1, last=True)
                    output(step, DC - 1, 1)

    with k.stage(1) as (block, act_step):
        @block.scalar
        def _(act):
            for c in range(DC):
                act.activation(k.A[:, c, :], k.A[:, c, :], ACT.Gelu_apprx_tanh).then_inc(act_step, 1)
            act.wait_ge(act_step, DC)


def ssm_glu(k):
    first = k.first["ssm_glu"]
    with k.stage(4) as (block, product_ready, gate_ready, bank_free, dve_step):
        @block.sync
        def _(sp):
            k.feed(sp, 2)

        @block.tensor
        def _(pe):
            for m in range(DC):
                if m % 4 == 0:
                    k.loaded(pe, first + m // 4)
                if m >= 4:
                    pe.wait_ge(gate_ready, m - 3)
                accumulate(k, pe, k.ps[:, m % 4, :], first + m // 4, m % 4 * P, k.A, DC).then_inc(product_ready, 1)

        @block.scalar
        def _(act):
            for m in range(DC):
                act.wait_ge(product_ready, m + 1)
                if m >= 4:
                    act.wait_ge(bank_free, m - 3)
                act.activation(k.tmp[:, m % 4, :], k.ps[:, m % 4, :], ACT.Sigmoid, bias=col(k, "ssm_b_glu", m))\
                    .then_inc(gate_ready, 1)
                if m % 4 == 3:
                    act.sem_inc(k.weights_used, 1)

        @block.vector
        def _(dve):
            step = Steps(dve, dve_step)
            for m in range(DC):
                step(dve.tensor_tensor(k.B[:, m, :], k.A[:, m, :], k.C[:, m, :], ALU.mult))
                dve.wait_ge(gate_ready, m + 1)
                step(dve.tensor_tensor(k.B[:, m, :], k.B[:, m, :], k.tmp[:, m % 4, :], ALU.mult))
                dve.sem_inc(bank_free, 1)


def ssm_mixer(k):
    ssm_project(k, "ssm_in", 2, 0, k.B, ACT.Copy)
    ssm_scan(k)
    ssm_project(k, "ssm_in", 2, 2, k.C, ACT.Silu)
    ssm_glu(k)


class Phases:

    def __init__(self, sem, names, start=0):
        self.sem, self.names, self.told, self.start = sem, names, 0, start

    def at(self, i, name):
        return i * len(self.names) + (self.names.index(name) + 1 + self.start)

    def place(self, name):
        assert self.names[self.told] == name, (self.names[self.told], name)
        self.told += 1

    def wait(self, eng, i, name):
        eng.wait_ge(self.sem, self.at(i, name))

    def done(self, eng, name):
        self.place(name)
        eng.sem_inc(self.sem, 1)

    def last(self, ins, name):
        self.place(name)
        ins.then_inc(self.sem, 1)


HEADS = 16
L = 64
NL = T // L
DECAY = -float(np.exp(-0.5))
LEVELS = 6


def rwkv_project(k, scratch):
    first = k.first["rwkv_in"]
    with ExitStack() as own:
        sb = lambda name, shape: own.enter_context(k.nc.sbuf_tensor(name, shape, F32))
        w1 = sb("lora_down", [P, 2, DC, 64])
        w2 = sb("lora_up", [64, 2, D])
        low = sb("lora_mid", [64, T])
        xs = [k.A, k.B]
        with k.stage(10) as (block, landed, mixed, product_ready, staged, low_ready, dve_step, *stored):
            @block.sync
            def _(sp):
                k.feed(sp, 8)

            @block.vector
            def _(dve):
                step = Steps(dve, dve_step)
                for c in range(DC):
                    step(dve.tensor_tensor(k.C[:, c, 1:T], k.X[:, c, 0:T - 1], k.X[:, c, 1:T], ALU.subtract))
                    step(dve.tensor_scalar(k.C[:, c, 0:1], k.X[:, c, 0:1], -1.0, None, ALU.mult))
                for n in range(6):
                    if n >= 2:
                        dve.wait_ge(product_ready, DC * (n - 1) + (n == 5))
                    for c in range(DC):
                        step(dve.scalar_tensor_tensor(xs[n % 2][:, c, :], k.C[:, c, :], col(k, f"rwkv_mu{n}", c),
                                                      k.X[:, c, :], ALU.mult, ALU.add))
                        dve.sem_inc(mixed, 1)

            @block.tensor
            def _(pe):
                for n in range(4):
                    pe.wait_ge(mixed, DC * (n + 1))
                    for m in range(DC):
                        o = n * DC + m
                        if m % 4 == 0:
                            k.loaded(pe, first + o // 4)
                        if o >= 4:
                            pe.wait_ge(staged, o - 3)
                        accumulate(k, pe, k.ps[:, o % 4, :], first + o // 4, m % 4 * P, xs[n % 2], DC)\
                            .then_inc(product_ready, 1)
                pe.wait_ge(landed, 64)
                for n in (4, 5):
                    pe.wait_ge(mixed, DC * (n + 1))
                    if n == 5:
                        pe.wait_ge(low_ready, 1)
                    for c in range(DC):
                        last = pe.matmul(k.ps[0:64, 4, :], w1[:, n - 4, c, :], xs[n % 2][:, c, :],
                                         start=(c == 0), stop=(c == DC - 1))
                    last.then_inc(product_ready, 1)
                    pe.wait_ge(low_ready, n - 3)
                    for m in range(DC):
                        o = n * DC + m
                        pe.wait_ge(staged, o - 3)
                        pe.matmul(k.ps[:, o % 4, :], w2[:, n - 4, m * P:(m + 1) * P], low[:, :], start=True, stop=True)\
                            .then_inc(product_ready, 1)

            @block.scalar
            def _(act):
                for i, name in enumerate(("w", "a")):
                    act.dma_start(w1[:, i, :, :], k.ins[f"rwkv_{name}1"].rearrange("(c p) n -> p c n", p=P))\
                        .then_inc(landed, 16)
                    act.dma_start(w2[:, i, :], k.ins[f"rwkv_{name}2"]).then_inc(landed, 16)
                for n in range(6):
                    if n >= 4:
                        act.wait_ge(product_ready, DC * n + (n - 3))
                        act.activation(low[:, :], k.ps[0:64, 4, :], ACT.Tanh if n == 4 else ACT.Copy).then_inc(low_ready, 1)
                    for m in range(DC):
                        o = n * DC + m
                        act.wait_ge(product_ready, o + 1 + max(0, n - 3))
                        if o >= 4:
                            act.wait_ge(stored[o % 4], 16 * (o // 4))
                        if n < 4:
                            ins = act.activation(k.tmp[:, o % 4, :], k.ps[:, o % 4, :], ACT.Silu if n == 3 else ACT.Copy)
                        else:
                            ins = act.activation(k.tmp[:, o % 4, :], k.ps[:, o % 4, :], ACT.Sigmoid,
                                                 bias=col(k, "rwkv_w0" if n == 4 else "rwkv_a0", m))
                        ins.then_inc(staged, 1)
                        act.wait_ge(staged, o + 1)
                        act.dma_start(scratch[m, :, n, :], k.tmp[:, o % 4, :]).then_inc(stored[o % 4], 16)
                        if n < 4 and m % 4 == 3:
                            act.sem_inc(k.weights_used, 1)
                for s in stored:
                    act.wait_ge(s, 16 * 6 * DC // 4)


def rwkv_heads(k, scratch):
    with ExitStack() as own:
        sb = lambda name, shape: own.enter_context(k.nc.sbuf_tensor(name, shape, F32))
        ada = k.first["ada0"]
        spare = [k.slot(ada + 3 + n).rearrange("p (a t) -> p a t", t=T) for n in range(3)]
        hc = sb("pair_params", [P, 2, 8])
        c_wide = spare[2][:, 0, 0:256].rearrange("p (c n) -> p c n", c=DC)
        ada_row = spare[2][:, 1, :]
        S = sb("state", [P, P])
        SA = sb("removed", [P, 2, 64])
        WL = sb("chunk_decay", [P, 2, NL])
        alpha, beta, key = (k.B[:, n, :] for n in range(3))
        query_of = [k.B[:, 3, :], spare[2][:, 5, :]]
        blocks = lambda tile: tile.rearrange("p (a b) -> p a b", b=P)
        alpha_t, beta_t, key_t, v_t = (blocks(k.B[:, 4 + n, :]) for n in range(4))
        RB = [blocks(k.C[:, 0, :]), blocks(k.C[:, 1, :])]
        RK = [blocks(k.C[:, 2, :]), blocks(k.C[:, 3, :])]
        P1T = k.C[:, 4, :]
        P2 = k.C[:, 5, :].rearrange("p (a h v) -> p a h v", h=2, v=64)
        Ti, TT = [blocks(k.C[:, 6, :]), blocks(spare[2][:, 2, :])], [blocks(k.C[:, 7, :]), blocks(spare[2][:, 3, :])]
        NT, AK = [blocks(k.tmp[:, 0, :]), blocks(spare[2][:, 4, :])], [blocks(k.tmp[:, 3, :]), blocks(k.tmp[:, 5, :])]
        NTl, Y = [blocks(k.tmp[:, 1, :]), blocks(spare[2][:, 6, :])], [blocks(k.tmp[:, 2, :]), blocks(spare[2][:, 7, :])]
        G = [k.tmp[:, 4, 256 * h:256 * h + 256].rearrange("p (a v) -> p a v", v=64) for h in range(2)]
        sum_, sum_before, e_query, e_beta, e_alpha, kk = (k.tmp[:, n, :] for n in range(6))
        square, norm = k.C[:, 6, :], k.C[:, 7, :]
        out, centred, out_sq, dev = (spare[n // 2][:, 6 + n % 2, :] for n in range(4))
        bank = lambda n: k.ps[:, n, :]
        mats = lambda n: blocks(k.ps[:, n, :])
        mask = lambda name: k.mask[name][:, :].unsqueeze(1).to_broadcast([P, TC, P])

        inputs = lambda p: (spare[p][:, n, :] for n in range(6))
        params = lambda p: (hc[:, p, n:n + 1] for n in range(5))

        with k.stage(14) as (block, pair_loaded0, pair_loaded1, ada_loaded, c_ready, pe_head, act_head, dve_head,
                             pe_main, act_main, dve_main, pe_tail, act_tail, dve_tail, dve_step):
            pair_loaded = [pair_loaded0, pair_loaded1]
            HP = Phases(pe_head, ["kk_sum", "bonus"])
            HA = Phases(act_head, ["exps", "kk_sq", "kk_norm"])
            HV = Phases(dve_head, ["sums", "kk", "bonus", "hats"])
            MP = Phases(pe_main, ["by_time"] + [f"mats{n}" for n in range(5)]
                        + [m for l in range(1, LEVELS) for m in (f"y0{l}", f"y1{l}", f"upd0{l}", f"upd1{l}")]
                        + ["g0", "g1", "p20", "p21"]
                        + [n for c in range(NL) for n in ([f"sa{c}", "ada"] if c == NL - 1 else [f"sa{c}"]) + [f"u{c}"]])
            MA = Phases(act_main, ["by_time"] + [f"Y{h}{l}" for l in range(1, LEVELS) for h in range(2)] + ["G0", "G1", "P20", "P21"])
            MV = Phases(dve_main, ["made0", "made1", "lvl00", "lvl10", "made2", "made3", "made4"]
                        + [f"lvl{h}{l}" for l in range(1, LEVELS) for h in range(2)]
                        + [n for c in range(NL) for n in (f"sa{c}", f"s{c}")])
            EP = Phases(pe_tail, ["mean", "ada_turned", "var"])
            EA = Phases(act_tail, ["ada_row", "out", "out_sq", "dev"])
            EV = Phases(dve_tail, ["centred", "ada", "gated"])
            MATS = [(1, 2), (3, 4), (5, 0), (1, 2), (3, 4)]
            STEPS = 1 + 1 + 2 * 9 + 1 + (6 * (LEVELS - 2) + 2) + 5 + 3 * NL + 16

            def restart():
                for phases in (HP, HA, HV, MP, MA, MV, EP, EA, EV):
                    if phases.told == len(phases.names):
                        phases.told = 0

            def passes(eng, run):
                run(0, 0, first=True)
                with eng.Fori(0, DC // 2 - 1) as j:
                    for p in (1, 0):
                        run(j * 2 + (2 - p), p)
                run(DC - 1, 1, last=True)

            @block.sync
            def _(sp):
                k.feed(sp, 0)

                def load_pair(i, p):
                    sp.dma_start(spare[p][:, 0:6, :], scratch[bass.ds(i, 1), :, :, :]).then_inc(pair_loaded[p], 16)
                    sp.dma_start(hc[:, p, :], k.ins["rwkv_pairs"][bass.ds(i, 1), :, :]).then_inc(pair_loaded[p], 16)

                def load_ada(i):
                    MP.wait(sp, i - 1, "ada")
                    for n in range(3):
                        sp.dma_start(k.slot(ada + n).rearrange("p (k n) -> p k n", k=DC),
                                     k.ins["w_ada_chunks"][bass.ds(i * 3 + n, 1), :, :]
                                     .rearrange("o (k p) n -> p (o k) n", p=P)).then_inc(ada_loaded, 16)

                for p in range(2):
                    load_pair(p, p)
                for n in range(3):
                    k.loaded(sp, ada + n)
                    sp.sem_inc(k.weights_loaded[(ada + 3 + n) % SLOTS], 16)
                sp.sem_inc(ada_loaded, 48)
                with sp.Fori(0, DC // 2 - 1) as j:
                    for p in range(2):
                        load_ada(j * 2 + (p + 1))
                        EV.wait(sp, j * 2 + p, "gated")
                        load_pair(j * 2 + (p + 2), p)
                load_ada(DC - 1)
                k.issued = ada + 6
                k.feed(sp, 6)

            @block.tensor
            def _(pe):
                def head_sum(i, name):
                    if name == "kk_sum":
                        HA.wait(pe, i, "kk_sq")
                    else:
                        HV.wait(pe, i, "bonus")
                    HP.last(pe.matmul(bank(0 if name == "kk_sum" else 1), k.pairs[:, :], square, start=True, stop=True), name)

                def turn_modulation(i):
                    EA.wait(pe, i, "ada_row")
                    for n in range(4):
                        ins = pe.transpose(k.ps[:, 7, n * P:(n + 1) * P], ada_row[:, n * P:(n + 1) * P], k.ident[:, :])
                    EP.last(ins, "ada_turned")

                def variance(i):
                    EA.wait(pe, i, "out_sq")
                    EP.last(pe.matmul(bank(6), k.pairs[:, :], out_sq, start=True, stop=True), "var")

                def matrices(i, p, first):
                    v_, query = spare[p][:, 2, :], query_of[p]
                    HV.wait(pe, i, "hats")
                    for n, src in enumerate((alpha, beta, key, v_)):
                        for t in range(TC):
                            ins = pe.transpose(k.ps[:, 1 + n, t * P:(t + 1) * P], src[:, t * P:(t + 1) * P], k.ident[:, :])
                    MP.last(ins, "by_time")
                    if not first:
                        turn_modulation(i - 1)
                    MA.wait(pe, i, "by_time")
                    for n, (left, right) in enumerate(((beta, alpha), (alpha, beta), (key, alpha), (beta, query), (key, query))):
                        if n == 2 and not first:
                            EV.wait(pe, i - 1, "centred")
                        if n >= 3:
                            MV.wait(pe, i, f"made{n - 3}")
                        for t in range(TC):
                            ts = slice(t * P, (t + 1) * P)
                            for h in range(2):
                                hs = slice(64 * h, 64 * h + 64)
                                ins = pe.matmul(k.ps[:, MATS[n][h], ts], left[hs, ts], right[hs, ts], start=True, stop=True)
                        MP.last(ins, f"mats{n}")
                        if n == 2 and not first:
                            variance(i - 1)

                def inverses(i, first):
                    if not first:
                        EA.wait(pe, i - 1, "dev")
                        EV.wait(pe, i - 1, "ada")
                    for l in range(1, LEVELS):
                        for h in range(2):
                            MV.wait(pe, i, f"lvl{h}{l - 1}")
                            for t in range(TC):
                                ins = pe.matmul(mats(6 + h)[:, t, :], NTl[h][:, t, :], Ti[h][:, t, :], start=True, stop=True)
                            MP.last(ins, f"y{h}{l}")
                        if l == 1:
                            MV.wait(pe, i, "made4")
                        for h in range(2):
                            MA.wait(pe, i, f"Y{h}{l}")
                            for t in range(TC):
                                pe.matmul(mats(h)[:, t, :], TT[h][:, t, :], Y[h][:, t, :], start=True, stop=True)
                            for t in range(TC):
                                ins = pe.matmul(mats(2 + h)[:, t, :], Y[h][:, t, :], TT[h][:, t, :], start=True, stop=True)
                            MP.last(ins, f"upd{h}{l}")
                    for h in range(2):
                        lo = 64 * h
                        MV.wait(pe, i, f"lvl{h}{LEVELS - 1}")
                        for t in range(TC):
                            pe.matmul(k.ps[lo:lo + 64, h, t * P:(t + 1) * P], alpha_t[:, t, lo:lo + 64], TT[h][:, t, :], start=True, stop=True)
                        for t in range(TC):
                            ins = pe.matmul(k.ps[:, 2 + h, 64 * t:64 * t + 64], AK[h][:, t, :], v_t[:, t, lo:lo + 64], start=True, stop=True)
                        MP.last(ins, f"g{h}")
                    for h in range(2):
                        MA.wait(pe, i, f"G{h}")
                        for t in range(TC):
                            ins = pe.matmul(k.ps[:, 6 + h, 64 * t:64 * t + 64], TT[h][:, t, :], G[h][:, t, :], start=True, stop=True)
                        MP.last(ins, f"p2{h}")

                def recurrence(i, p, last):
                    query = query_of[p]
                    MA.wait(pe, i, "P21")
                    for c in range(NL):
                        t, lo = c // 2, 64 * (c % 2)
                        rows, cs = slice(lo, lo + 64), slice(64 * c, 64 * c + 64)
                        if c:
                            MV.wait(pe, i, f"s{c - 1}")
                        MP.last(pe.matmul(k.ps[rows, 4, 0:P], P1T[:, cs], S[:, :], start=True, stop=True), f"sa{c}")
                        if c == 0:
                            pe.wait_ge(ada_loaded, i * 48 + 48)
                        for n in range(4):
                            w = k.slot(ada + min(n, 2)).rearrange("p (k n) -> p k n", k=DC)
                            ins = pe.matmul(k.ps[32 * n:32 * n + 32, 7, :], c_wide[:, c, :], w[:, c, :],
                                            start=(c == 0), stop=(c == DC - 1))
                        if c == NL - 1:
                            MP.last(ins, "ada")
                        MV.wait(pe, i, f"sa{c}")
                        pe.matmul(k.ps[:, 5, cs], S[:, :], query[:, cs], start=True, stop=False)
                        for h in range(2):
                            hs = slice(64 * h, 64 * h + 64)
                            pe.matmul(k.ps[hs, 5, cs], SA[rows, h, :], RB[h][rows, t, rows], start=False, stop=False)
                            pe.matmul(k.ps[hs, 5, cs], v_t[rows, t, hs], RK[h][rows, t, rows], start=False, stop=True)
                        pe.matmul(k.ps[:, 6, 0:P], beta_t[rows, t, :], SA[rows, :, :], start=True, stop=False)
                        ins = pe.matmul(k.ps[:, 6, 0:P], key_t[rows, t, :], v_t[rows, t, :], start=False, stop=True)
                        MP.last(ins, f"u{c}")
                        if not last and c == 3:
                            head_sum(i + 1, "kk_sum")
                        if not last and c == 6:
                            head_sum(i + 1, "bonus")
                    EA.wait(pe, i, "out")
                    EP.last(pe.matmul(bank(0), k.pairs[:, :], out, start=True, stop=True), "mean")

                def run(i, p, first=False, last=False):
                    matrices(i, p, first)
                    restart()
                    inverses(i, first)
                    recurrence(i, p, last)
                    restart()

                pe.wait_ge(c_ready, 1)
                head_sum(0, "kk_sum")
                head_sum(0, "bonus")
                restart()
                passes(pe, run)
                turn_modulation(DC - 1)
                variance(DC - 1)

            @block.scalar
            def _(act):
                def head(i):
                    HV.wait(act, i, "sums")
                    act.activation(e_query, sum_, ACT.Exp, scale=DECAY)
                    act.activation(e_beta, sum_, ACT.Exp, scale=-DECAY)
                    HA.last(act.activation(e_alpha, sum_before, ACT.Exp, scale=DECAY), "exps")
                    HV.wait(act, i, "kk")
                    HA.last(act.activation(square, kk, ACT.Square), "kk_sq")
                    HP.wait(act, i, "kk_sum")
                    HA.last(act.activation(norm, bank(0), ACT.Sqrt), "kk_norm")

                def square_out(i):
                    EV.wait(act, i, "centred")
                    EA.last(act.activation(out_sq, centred, ACT.Square), "out_sq")

                def deviation(i):
                    EP.wait(act, i, "var")
                    EA.last(act.activation(dev, bank(6), ACT.Sqrt, scale=1.0 / 64, bias=col(k, "gn_eps", 0)), "dev")

                def run(i, p, first=False, last=False):
                    if not first:
                        square_out(i - 1)
                    MP.wait(act, i, "by_time")
                    for n in range(4):
                        ins = act.activation(k.B[:, 4 + n, :], bank(1 + n), ACT.Copy)
                    MA.last(ins, "by_time")
                    if not first:
                        deviation(i - 1)
                    restart()
                    for l in range(1, LEVELS):
                        for h in range(2):
                            MP.wait(act, i, f"y{h}{l}")
                            MA.last(act.activation(Y[h], mats(6 + h), ACT.Copy), f"Y{h}{l}")
                    for h in range(2):
                        lo = 64 * h
                        MP.wait(act, i, f"g{h}")
                        act.activation(P1T[lo:lo + 64, :], k.ps[lo:lo + 64, h, :], ACT.Copy)
                        MA.last(act.activation(G[h], k.ps[:, 2 + h, 0:256].rearrange("p (a v) -> p a v", v=64), ACT.Copy), f"G{h}")
                    for h in range(2):
                        MP.wait(act, i, f"p2{h}")
                        MA.last(act.activation(P2[:, :, h, :], k.ps[:, 6 + h, 0:256].rearrange("p (a v) -> p a v", v=64), ACT.Copy), f"P2{h}")
                    if not last:
                        head(i + 1)
                    MP.wait(act, i, "ada")
                    EA.last(act.activation(ada_row, bank(7), ACT.Copy), "ada_row")
                    MP.wait(act, i, f"u{NL - 1}")
                    EA.last(act.activation(out, bank(5), ACT.Copy), "out")
                    restart()

                c_col = k.cols[:, k.where["c"]:k.where["c"] + DC]
                act.activation(c_wide, c_col.unsqueeze(2).to_broadcast([P, DC, 32]), ACT.Silu).then_inc(c_ready, 1)
                head(0)
                restart()
                passes(act, run)
                square_out(DC - 1)
                deviation(DC - 1)

            @block.vector
            def _(dve):
                def head(step, i, p, part):
                    r_, k_, v_, z_, sw, a_ = inputs(p)
                    k_k, k_a, r_k, gn_g, gn_b = params(p)
                    if part == 0:
                        dve.wait_ge(pair_loaded[p], i * 16 + (32 - 16 * p))
                        step(dve.tensor_tensor_scan(sum_, k.seg[L][:, :], sw, 0.0, ALU.mult, ALU.add))
                        step(dve.tensor_tensor(sum_before, sum_, sw, ALU.subtract))
                        HV.done(dve, "sums")
                    elif part == 1:
                        step(dve.tensor_scalar(kk, k_, k_k, None, ALU.mult), wait=False)
                        step(dve.tensor_scalar(norm, a_, -1.0, k_a, ALU.add, ALU.mult))
                    elif part == 2:
                        step(dve.scalar_tensor_tensor(k_, norm, 1.0, k_, ALU.add, ALU.mult))
                        HV.done(dve, "kk")
                    elif part == 4:
                        HA.wait(dve, i, "kk_norm")
                        step(dve.scalar_tensor_tensor(square, r_, r_k, k_, ALU.mult, ALU.mult))
                        HV.done(dve, "bonus")
                        step(dve.tensor_scalar(norm, norm, 1e-12, None, ALU.max))
                    elif part == 5:
                        step(dve.reciprocal(norm, norm))
                    elif part == 6:
                        step(dve.tensor_tensor(kk, kk, norm, ALU.mult))
                        step(dve.scalar_tensor_tensor(alpha, kk, -1.0, e_alpha, ALU.mult, ALU.mult), wait=False)
                        step(dve.tensor_tensor(beta, kk, a_, ALU.mult))
                        step(dve.tensor_tensor(beta, beta, e_beta, ALU.mult))
                    elif part == 7:
                        step(dve.tensor_tensor(key, k_, e_beta, ALU.mult), wait=False)
                        step(dve.tensor_tensor(query_of[p], r_, e_query, ALU.mult), wait=False)
                        step(dve.tensor_copy(WL[:, p, :], e_query[:, L - 1:T:L]), wait=False)
                        HP.wait(dve, i, "bonus")
                        step(dve.tensor_tensor(sw, bank(1), v_, ALU.mult))
                        HV.done(dve, "hats")

                def tail(step, i, p, part):
                    r_, k_, v_, z_, bonus, a_ = inputs(p)
                    k_k, k_a, r_k, gn_g, gn_b = params(p)
                    if part == "centre":
                        EP.wait(dve, i, "mean")
                        step(dve.scalar_tensor_tensor(centred, bank(0), -1.0 / 64, out, ALU.mult, ALU.add))
                        EV.done(dve, "centred")
                    elif part == "modulation":
                        EP.wait(dve, i, "ada_turned")
                        rows = k.ps[:, 7, :].rearrange("p (c r n) -> p r c n", c=4, r=4)[:, 0:3, :, 0:1]
                        step(dve.tensor_copy(k.mod[:, :, :].rearrange("p l n -> p (l n)")[:, bass.ds(i * 12, 12)]
                                             .rearrange("p (r c n) -> p r c n", r=3, n=1), rows))
                        EV.done(dve, "ada")
                    elif part == 1:
                        EA.wait(dve, i, "dev")
                        step(dve.reciprocal(dev, dev))
                    elif part == 2:
                        step(dve.tensor_tensor(centred, centred, dev, ALU.mult))
                        step(dve.tensor_scalar(centred, centred, gn_g, gn_b, ALU.mult, ALU.add))
                    elif part == 3:
                        step(dve.tensor_tensor(centred, centred, bonus, ALU.add))
                        step(dve.tensor_tensor(k.A[:, bass.ds(i, 1), :], centred, z_, ALU.mult))
                        EV.done(dve, "gated")

                def main(step, i, p, first, last):
                    step(dve.memset(S[:, :], 0.0), wait=False)
                    if not first:
                        tail(step, i - 1, 1 - p, "centre")
                    for n, (dst, name) in enumerate(((NT, "before"), (Ti, "first_lower"), (AK, "before"), (RB, "upto"), (RK, "upto"))):
                        MP.wait(dve, i, f"mats{n}")
                        for h in range(2):
                            step(dve.tensor_tensor(dst[h], mats(MATS[n][h]), mask(name), ALU.mult), wait=(h == 1))
                        MV.done(dve, f"made{n}")
                        if n == 0:
                            for h in range(2):
                                step(dve.tensor_tensor(TT[h], NT[h], mask("level0"), ALU.mult), wait=False)
                            for h in range(2):
                                step(dve.tensor_tensor(NTl[h], NT[h], mask("level1"), ALU.mult), wait=(h == 1))
                        elif n == 1:
                            for h in range(2):
                                step(dve.tensor_tensor(Ti[h], Ti[h], mask("ident"), ALU.add), wait=False)
                            for h in range(2):
                                step(dve.tensor_tensor(TT[h], TT[h], mask("ident"), ALU.add), wait=(h == 1))
                            MV.done(dve, "lvl00")
                            MV.done(dve, "lvl10")
                        elif n == 2 and not first:
                            tail(step, i - 1, 1 - p, "modulation")
                    for l in range(1, LEVELS):
                        for h in range(2):
                            if l < LEVELS - 1:
                                MP.wait(dve, i, f"y{h}{l}")
                                step(dve.tensor_tensor(NTl[h], NT[h], mask(f"level{l + 1}"), ALU.mult))
                        for h in range(2):
                            MP.wait(dve, i, f"upd{h}{l}")
                            if l < LEVELS - 1:
                                step(dve.tensor_tensor(Ti[h], Ti[h], mats(h), ALU.add), wait=False)
                            step(dve.tensor_tensor(TT[h], TT[h], mats(2 + h), ALU.add))
                            MV.done(dve, f"lvl{h}{l}")
                        if not first:
                            tail(step, i - 1, 1 - p, l)
                    MA.wait(dve, i, "P21")
                    restart()
                    for c in range(NL):
                        t, lo = c // 2, 64 * (c % 2)
                        rows = slice(lo, lo + 64)
                        MP.wait(dve, i, f"sa{c}")
                        step(dve.tensor_tensor(SA[rows, :, :], k.ps[rows, 4, 0:128].rearrange("p (h v) -> p h v", h=2),
                                               P2[rows, t, :, :], ALU.add))
                        MV.done(dve, f"sa{c}")
                        if not last:
                            head(step, i + 1, 1 - p, c)
                        MP.wait(dve, i, f"u{c}")
                        step(dve.tensor_tensor(S[:, :], S[:, :], k.ps[:, 6, 0:P], ALU.add))
                        step(dve.scalar_tensor_tensor(S[:, :], S[:, :], WL[:, p, c:c + 1], k.pairs[:, :], ALU.mult, ALU.mult))
                        MV.done(dve, f"s{c}")
                    restart()

                step = Steps(dve, dve_step)
                for part in range(NL):
                    head(step, 0, 0, part)
                restart()
                main(step, 0, 0, first=True, last=False)
                done = step.n
                with dve.Fori(0, DC // 2 - 1) as j:
                    for p in (1, 0):
                        step = Steps(dve, dve_step, j * (2 * STEPS) + (done + (1 - p) * STEPS))
                        main(step, j * 2 + (2 - p), p, first=False, last=False)
                        assert step.n == STEPS, step.n
                step = Steps(dve, dve_step, done + (DC - 2) * STEPS)
                main(step, DC - 1, 1, first=False, last=True)
                for part in ("centre", "modulation", 1, 2, 3):
                    tail(step, DC - 1, 1, part)
                dve.sem_inc(k.weights_used, 6)


def rwkv_mixer(k):
    scratch = k.nc.dram_tensor("rwkv_scratch", (DC, P, 6, T), F32, kind="Internal").ap()
    rwkv_project(k, scratch)
    rwkv_heads(k, scratch)


MLA_H, QK, ROPE = 4, 96, 32
IN_COLS = 2144
CONV_K = 31
MOD = {"sh1": 0, "sc1": 8, "g1": 16, "sh2": 24, "sc2": 32, "g2": 40}
SMALL = {"w_uq": (0, 768), "w_ukv": (768, 512), "swap": (1280, P), "strip": (1408, 896),
         "pool_inv": (2304, 1024), "w_pool": (3328, 128)}
SMALL_COLS = 3456


def plan_mixer(k, l):
    w_in = k.ins["w_in_2"][l]
    k.want(f"small{l}", k.ins["small"][l], 1, SMALL_COLS)
    k.want(f"mla{l}", w_in[:, 0:352], DC, 352)
    k.want(f"pool{l}", w_in[:, 352:608], DC, 256)
    k.want(f"conv{l}", w_in[:, 1632:2144], DC, 512)
    k.want(f"hgrn{l}", w_in[:, 608:1120], DC, 512)
    k.want(f"hgrn{l}", w_in[:, 1120:1632], DC, 512)
    k.want_halves(f"out_2{l}", k.ins["w_out_2"][l])


def small(k, l, name):
    at, n = SMALL[name]
    return k.slot(k.first[f"small{l}"])[:, at:at + n]


def modulation(k):
    with k.stage(1) as (block, dve_step):
        @block.sync
        def _(sp):
            k.feed(sp, 0)

        @block.vector
        def _(dve):
            step = Steps(dve, dve_step)
            for l in range(2):
                at = k.where[f"b_ada{l}"]
                step(dve.tensor_tensor(k.mod[:, l, :], k.mod[:, l, :], k.cols[:, at:at + 48], ALU.add))
                for i, name in enumerate(("norm1", "norm2")):
                    g = k.cols[:, k.where[f"{name}_g{l}"]:][:, 0:DC]
                    sc = k.mod[:, l, MOD[f"sc{i + 1}"]:][:, 0:DC]
                    step(dve.scalar_tensor_tensor(sc, sc, 1.0, g, ALU.add, ALU.mult))


def mod(k, l, name, c):
    at = MOD[name] + c
    return k.mod[:, l, at:at + 1]


def modulated_norm(k, l, i):
    with k.stage(5) as (block, squared, summed, deviation, dve_step, act_step):
        @block.sync
        def _(sp):
            k.feed(sp, 0)

        @block.tensor
        def _(pe):
            for c in range(DC):
                pe.wait_ge(squared, c + 1)
                last = pe.matmul(k.ps[:, 0, :], k.ones[:, :], k.B[:, c, :], start=(c == 0), stop=(c == DC - 1))
            last.then_inc(summed, 1)

        @block.scalar
        def _(act):
            for c in range(DC):
                act.activation(k.B[:, c, :], k.X[:, c, :], ACT.Square).then_inc(squared, 1)
            act.wait_ge(summed, 1)
            act.activation(k.tmp[:, 0, :], k.ps[:, 0, :], ACT.Sqrt, bias=col(k, "eps", 0), scale=1.0 / D)\
                .then_inc(deviation, 1)

        @block.vector
        def _(dve):
            step = Steps(dve, dve_step)
            dve.wait_ge(deviation, 1)
            step(dve.reciprocal(k.tmp[:, 1, :], k.tmp[:, 0, :]))
            for c in range(DC):
                step(dve.scalar_tensor_tensor(k.A[:, c, :], k.X[:, c, :], mod(k, l, f"sc{i}", c), k.tmp[:, 1, :],
                                              ALU.mult, ALU.mult))
                step(dve.tensor_scalar(k.A[:, c, :], k.A[:, c, :], mod(k, l, f"sh{i}", c), None, ALU.add))


def mla(k, l):
    n0 = k.first[f"mla{l}"]
    tile = lambda n: k.tmp[:, n, :]
    ckv, cq = tile(2), [tile(0), k.tmp[0:64, 1, :]]
    w_uq, w_ukv, swap = small(k, l, "w_uq"), small(k, l, "w_ukv"), small(k, l, "swap")
    strip = small(k, l, "strip")
    q, key = [k.B[:, h, :] for h in range(4)], [k.B[:, 4 + h, :] for h in range(4)]
    v_t = k.tmp[:, 4:6, :].rearrange("p a b -> p (a b)").rearrange("p (t n) -> p t n", t=TC)
    with ExitStack() as own:
        rope = own.enter_context(k.nc.sbuf_tensor(f"rope{l}", [QK, 2, T], F32))

        with k.stage(7) as (block, landed, product_ready, act_done, dve_done, sums_ready, dve_step, act_step):
            AP_ = Phases(act_done, ["latents", "squares", "devs", "tables"])
            VP = Phases(dve_done, ["turns", "normed"])

            @block.sync
            def _(sp):
                sp.dma_start(k.C[0:QK, 7, :].bitcast(I32), k.ins["positions"].to_broadcast([QK, T])).then_inc(landed, 16)
                k.feed(sp, 0)

            @block.tensor
            def _(pe):
                k.loaded(pe, n0)
                w = k.chunk(n0)
                for out, lo, size in ((k.ps[:, 0, :], 0, 128), (k.ps[0:64, 1, :], 128, 64), (k.ps[:, 2, :], 192, 128),
                                      (k.ps[64:96, 3, :], 320, 32)):
                    for c in range(DC):
                        last = pe.matmul(out, w[:, c, lo:lo + size], k.A[:, c, :], start=(c == 0), stop=(c == DC - 1))
                    last.then_inc(product_ready, 1)
                AP_.wait(pe, 0, "squares")
                pe.matmul(k.ps[:, 4, :], k.ones[:, :], k.C[:, 0, :], start=True, stop=False)
                pe.matmul(k.ps[:, 4, :], k.ones[0:64, :], k.C[0:64, 1, :], start=False, stop=True)
                pe.matmul(k.ps[:, 5, :], k.ones[:, :], k.C[:, 2, :], start=True, stop=True).then_inc(sums_ready, 1)

            @block.scalar
            def _(act):
                act.wait_ge(product_ready, 3)
                act.activation(cq[0], k.ps[:, 0, :], ACT.Copy)
                act.activation(cq[1], k.ps[0:64, 1, :], ACT.Copy)
                act.activation(ckv, k.ps[:, 2, :], ACT.Copy)
                act.wait_ge(product_ready, 4)
                for h in range(MLA_H):
                    ins = act.activation(key[h][64:96, :], k.ps[64:96, 3, :], ACT.Copy)
                AP_.last(ins, "latents")
                act.activation(k.C[:, 0, :], k.ps[:, 0, :], ACT.Square)
                act.activation(k.C[0:64, 1, :], k.ps[0:64, 1, :], ACT.Square)
                AP_.last(act.activation(k.C[:, 2, :], k.ps[:, 2, :], ACT.Square), "squares")
                act.wait_ge(sums_ready, 1)
                act.activation(k.C[:, 3, :], k.ps[:, 4, :], ACT.Sqrt, bias=col(k, "eps", 0), scale=1.0 / 192)
                AP_.last(act.activation(k.C[:, 4, :], k.ps[:, 5, :], ACT.Sqrt, bias=col(k, "eps", 0), scale=1.0 / 128), "devs")
                VP.wait(act, 0, "turns")
                act.activation(rope[:, 1, :], k.C[0:QK, 5, :], ACT.Sin, scale=TURN)
                AP_.last(act.activation(rope[:, 0, :], k.C[0:QK, 6, :], ACT.Sin, scale=-TURN,
                                        bias=col(k, "half_pi", 0, QK)), "tables")

            @block.vector
            def _(dve):
                step = Steps(dve, dve_step)
                dve.wait_ge(landed, 16)
                angle, turns, scr = k.C[0:QK, 5, :], k.C[0:QK, 6, :], k.tmp[0:QK, 3, :]
                step(dve.tensor_copy(angle, k.C[0:QK, 7, :].bitcast(I32)))
                step(dve.tensor_scalar(angle, angle, col(k, "rope_freq", 0, QK), None, ALU.mult))
                reduce_angle(dve, step, angle, turns, scr)
                step(dve.tensor_scalar(angle, turns, col(k, "rope_sign", 0, QK), None, ALU.mult))
                step(dve.scalar_tensor_tensor(scr, turns, -1.0, turns, ALU.mult, ALU.max))
                step(dve.tensor_copy(turns, scr))
                VP.done(dve, "turns")
                AP_.wait(dve, 0, "devs")
                step(dve.reciprocal(k.C[:, 3, :], k.C[:, 3, :]))
                step(dve.reciprocal(k.C[:, 4, :], k.C[:, 4, :]))
                step(dve.scalar_tensor_tensor(cq[0], cq[0], col(k, f"q_a_g{l}", 0), k.C[:, 3, :], ALU.mult, ALU.mult))
                step(dve.scalar_tensor_tensor(cq[1], cq[1], col(k, f"q_a_g{l}", 1, 64), k.C[0:64, 3, :], ALU.mult, ALU.mult))
                step(dve.scalar_tensor_tensor(ckv, ckv, col(k, f"kv_a_g{l}", 0), k.C[:, 4, :], ALU.mult, ALU.mult))
                VP.done(dve, "normed")

        items = [(t, h) for h in range(MLA_H) for t in ("q", "k")]
        with k.stage(9) as (block, product_ready, values_ready, copied, squared, sum_ready, normed, swap_ready, rotated, dve_step):
            def of(i):
                t, h = items[i]
                return t, h, (q if t == "q" else key)[h][0:QK, :]

            @block.sync
            def _(sp):
                k.feed(sp, 0)

            @block.tensor
            def _(pe):
                k.loaded(pe, k.first[f"small{l}"])

                def product(i):
                    t, h, _ = of(i)
                    if i >= 2:
                        pe.wait_ge(copied, i - 1)
                    if t == "q":
                        pe.matmul(k.ps[0:QK, i % 2, :], w_uq[:, QK * h:QK * (h + 1)], cq[0], start=True, stop=False)
                        ins = pe.matmul(k.ps[0:QK, i % 2, :], w_uq[0:64, 384 + QK * h:384 + QK * (h + 1)], cq[1], start=False, stop=True)
                    else:
                        ins = pe.matmul(k.ps[0:64, i % 2, :], w_ukv[:, P * h:P * h + 64], ckv, start=True, stop=True)
                    ins.then_inc(product_ready, 1)

                def swapped(i):
                    pe.wait_ge(normed, i + 1)
                    if i >= 2:
                        pe.wait_ge(rotated, i - 1)
                    pe.matmul(k.ps[0:QK, 6 + i % 2, :], swap[0:QK, 0:QK], of(i)[2], start=True, stop=True).then_inc(swap_ready, 1)

                product(0)
                product(1)
                vw = w_ukv.rearrange("p (h n) -> p h n", h=4)
                for t in range(TC):
                    ins = pe.matmul(k.ps[:, 4 + t // 2, 256 * (t % 2):256 * (t % 2) + 256], ckv[:, t * P:(t + 1) * P],
                                    vw[:, :, 64:128], start=True, stop=True)
                ins.then_inc(values_ready, 1)
                for i in range(8):
                    pe.wait_ge(squared, i + 1)
                    if i >= 2:
                        pe.wait_ge(k.dev_ready, 8 * l + i - 1)
                    pe.matmul(k.ps[0:QK, 2 + i % 2, :], k.ones[0:QK, 0:QK], k.C[0:QK, 2 + i % 2, :], start=True, stop=True)\
                        .then_inc(sum_ready, 1)
                    if i + 2 < 8:
                        product(i + 2)
                    if i:
                        swapped(i - 1)
                swapped(7)

            @block.scalar
            def _(act):
                def take(i):
                    t, h, x = of(i)
                    act.wait_ge(product_ready, i + 1)
                    n = QK if t == "q" else 64
                    act.activation(x[0:n, :], k.ps[0:n, i % 2, :], ACT.Copy).then_inc(copied, 1)
                    act.wait_ge(copied, i + 1)
                    if i >= 2:
                        act.wait_ge(sum_ready, i - 1)
                    act.activation(k.C[0:QK, 2 + i % 2, :], x, ACT.Square).then_inc(squared, 1)

                take(0)
                for i in range(8):
                    if i + 1 < 8:
                        take(i + 1)
                    act.wait_ge(sum_ready, i + 1)
                    if i >= 2:
                        act.wait_ge(normed, i - 1)
                    act.activation(k.C[0:QK, 4 + i % 2, :], k.ps[0:QK, 2 + i % 2, :], ACT.Sqrt, bias=col(k, "eps", 0, QK),
                                   scale=1.0 / QK).then_inc(k.dev_ready, 1)
                act.wait_ge(values_ready, 1)
                act.activation(v_t, k.ps[:, 4:6, :].rearrange("p a b -> p (a b)").rearrange("p (t n) -> p t n", t=TC), ACT.Copy)\
                    .then_inc(copied, 1)
                act.wait_ge(copied, 9)

            @block.vector
            def _(dve):
                step = Steps(dve, dve_step)

                def rotate(i):
                    x = of(i)[2]
                    dve.wait_ge(swap_ready, i + 1)
                    step(dve.tensor_tensor(k.C[0:QK, 6, :], k.ps[0:QK, 6 + i % 2, :], rope[:, 1, :], ALU.mult), wait=False)
                    step(dve.tensor_tensor(x, x, rope[:, 0, :], ALU.mult))
                    step(dve.tensor_tensor(x, x, k.C[0:QK, 6, :], ALU.add))
                    dve.sem_inc(rotated, 1)

                for i in range(8):
                    t, h, x = of(i)
                    rstd = k.C[0:QK, 4 + i % 2, :]
                    dve.wait_ge(k.dev_ready, 8 * l + i + 1)
                    step(dve.reciprocal(rstd, rstd))
                    step(dve.scalar_tensor_tensor(x, x, col(k, f"{t}_g{l}", 0, QK), rstd, ALU.mult, ALU.mult))
                    dve.sem_inc(normed, 1)
                    if i:
                        rotate(i - 1)
                rotate(7)

    with ExitStack() as own:
        mx = own.enter_context(k.nc.sbuf_tensor(f"softmax_stats{l}", [P, 2, 4], F32))
        todo = [(h, qt) for h in range(MLA_H) for qt in range(TC)]
        with k.stage(9) as (block, scores_ready, scaled, probs_ready, probs_scaled, turned, turned_copied, out_ready, dve_step, copied):
            @block.sync
            def _(sp):
                k.feed(sp, 0)

            @block.tensor
            def _(pe):
                def scores(i):
                    h, qt = todo[i]
                    if i >= 2:
                        pe.wait_ge(scaled, i - 1)
                    pe.matmul(k.ps[:, i % 2, 0:P * (qt + 1)], q[h][0:QK, qt * P:(qt + 1) * P], key[h][0:QK, 0:P * (qt + 1)],
                              start=True, stop=True).then_inc(scores_ready, 1)

                def weigh(i):
                    h, qt = todo[i]
                    pe.wait_ge(turned_copied, i + 1)
                    hs = slice(64 * (h % 2), 64 * (h % 2) + 64)
                    for j in range(qt + 1):
                        ins = pe.matmul(k.ps[hs, 4 + h // 2, qt * P:(qt + 1) * P], v_t[:, j, 64 * h:64 * h + 64],
                                        k.tmp[:, 2 + i % 2, j * P:(j + 1) * P], start=(j == 0), stop=(j == qt))
                    ins.then_inc(out_ready, 1)

                scores(0)
                for i, (h, qt) in enumerate(todo):
                    if i + 1 < len(todo):
                        scores(i + 1)
                    pe.wait_ge(probs_scaled, i + 1)
                    if i >= 2:
                        pe.wait_ge(turned_copied, i - 1)
                    for j in range(qt + 1):
                        ins = pe.transpose(k.ps[:, 2 + i % 2, j * P:(j + 1) * P], k.tmp[:, i % 2, j * P:(j + 1) * P], k.ident[:, :])
                    ins.then_inc(turned, 1)
                    if i:
                        weigh(i - 1)
                weigh(len(todo) - 1)

            @block.scalar
            def _(act):
                def copy_turned(i):
                    act.wait_ge(turned, i + 1)
                    if i >= 2:
                        act.wait_ge(out_ready, i - 1)
                    n = P * (todo[i][1] + 1)
                    act.activation(k.tmp[:, 2 + i % 2, 0:n], k.ps[:, 2 + i % 2, 0:n], ACT.Copy).then_inc(turned_copied, 1)
                for i, (h, qt) in enumerate(todo):
                    act.wait_ge(scaled, i + 1)
                    s = k.tmp[:, i % 2, 0:P * (qt + 1)]
                    act.activation(s, s, ACT.Exp, bias=mx[:, i % 2, 0:1], accum_out=mx[:, i % 2, 1:2]).then_inc(probs_ready, 1)
                    if i:
                        copy_turned(i - 1)
                copy_turned(len(todo) - 1)
                act.wait_ge(out_ready, len(todo))
                for j in range(2):
                    act.activation(k.C[:, j, :], k.ps[:, 4 + j, :], ACT.Copy).then_inc(copied, 1)
                act.wait_ge(copied, 2)

            @block.vector
            def _(dve):
                step = Steps(dve, dve_step)
                def normalise(i):
                    dve.wait_ge(probs_ready, i + 1)
                    s = k.tmp[:, i % 2, 0:P * (todo[i][1] + 1)]
                    step(dve.reciprocal(mx[:, i % 2, 2:3], mx[:, i % 2, 1:2]))
                    step(dve.tensor_scalar(s, s, mx[:, i % 2, 2:3], None, ALU.mult))
                    dve.sem_inc(probs_scaled, 1)
                for i, (h, qt) in enumerate(todo):
                    n = P * (qt + 1)
                    dve.wait_ge(scores_ready, i + 1)
                    if i >= 2:
                        dve.wait_ge(turned, i - 1)
                    step(dve.scalar_tensor_tensor(k.tmp[:, i % 2, 0:n], k.ps[:, i % 2, 0:n], QK ** -0.5,
                                                  strip[:, 512 - n:512], ALU.mult, ALU.add))
                    step(dve.tensor_reduce(mx[:, i % 2, 0:1], k.tmp[:, i % 2, 0:n], AX.X, ALU.max, negate=True))
                    dve.sem_inc(scaled, 1)
                    if i:
                        normalise(i - 1)
                normalise(len(todo) - 1)


def pool_mixer(k, l):
    n0 = k.first[f"pool{l}"]
    inv = small(k, l, "pool_inv").rearrange("p (a t) -> p a t", a=2)
    w_pool = small(k, l, "w_pool").rearrange("p (a n) -> p a n", a=2)
    with k.stage(5) as (block, product_ready, copied, pooled_ready, mixed, dve_step):
        @block.sync
        def _(sp):
            k.feed(sp, 3)

        @block.tensor
        def _(pe):
            k.loaded(pe, n0)
            for m in range(2):
                accumulate(k, pe, k.ps[:, m, :], n0, m * P, k.A, DC).then_inc(product_ready, 1)
            pe.wait_ge(pooled_ready, 1)
            for g in range(4):
                gs = slice(64 * (g % 2), 64 * (g % 2) + 64)
                ins = pe.matmul(k.ps[gs, 2 + g // 2, :], w_pool[gs, g // 2, :], k.B[gs, g // 2, :], start=True, stop=True)
            ins.then_inc(mixed, 1)

        @block.scalar
        def _(act):
            for m in range(2):
                act.wait_ge(product_ready, m + 1)
                act.activation(k.B[:, m, :], k.ps[:, m, :], ACT.Copy).then_inc(copied, 1)

        @block.vector
        def _(dve):
            step = Steps(dve, dve_step)
            dve.wait_ge(copied, 2)

            def widen(dst, src, lag, rows):
                step(dve.tensor_copy(dst[rows, 0:lag], src[rows, 0:lag]))
                step(dve.tensor_tensor(dst[rows, lag:T], src[rows, lag:T], src[rows, 0:T - lag], ALU.add))

            tile = lambda n: k.B[:, n, :]
            every, low, high = slice(0, P), slice(0, 64), slice(64, P)
            widen(tile(2), tile(0), 1, every)
            widen(tile(4), tile(2), 2, high)
            widen(tile(3), tile(1), 1, every)
            widen(tile(5), tile(3), 2, every)
            widen(tile(6), tile(5), 4, every)
            widen(tile(7), tile(6), 8, high)
            for rows, wide, m in ((low, 2, 0), (high, 4, 0), (low, 6, 1), (high, 7, 1)):
                step(dve.tensor_tensor(k.B[rows, wide, :], k.B[rows, wide, :], inv[rows, m, :], ALU.mult))
                step(dve.tensor_tensor(k.B[rows, m, :], k.B[rows, wide, :], k.B[rows, m, :], ALU.subtract))
            dve.sem_inc(pooled_ready, 1)
            dve.wait_ge(mixed, 1)
            dve.sem_inc(k.weights_used, 3)
            for m in range(2):
                step(dve.tensor_scalar(k.C[:, 2 + m, :], k.ps[:, 2 + m, :], col(k, f"pool_scale{l}", m), None, ALU.mult))


def conformer_and_gates(k, l, g):
    n0, n1 = k.first[f"conv{l}"], k.first[f"hgrn{l}"]
    q, key, b = k.B[:, 0:2, :], k.B[:, 2:4, :], k.B[:, 4:6, :]
    v_t = k.tmp[:, 4:6, :].rearrange("p a b -> p (a b)").rearrange("p (t n) -> p t n", t=TC)
    u, acc, dev = k.B[:, 6:8, :], k.C[:, 6:8, :], k.tmp[:, 3, :]
    with k.stage(10) as (block, conv_product, gate_ready, vector_ready, stats_ready, squared,
                         product_ready, copied, act_done, dve_done, dve_step):
        AP_ = Phases(act_done, ["start"] + [f"{x}{m}" for m in range(2) for x in ("e", "ln", "e2", "ln2")])
        VP = Phases(dve_done, ["bounds"] + [f"{x}{m}" for m in range(2) for x in ("z", "d")])

        @block.sync
        def _(sp):
            k.feed(sp, 3)

        @block.tensor
        def _(pe):
            k.loaded(pe, n0)
            for m in (2, 0, 3, 1):
                accumulate(k, pe, k.ps[:, 4 + m, :], n0, m * P, k.A, DC).then_inc(conv_product, 1)
            k.loaded(pe, n1)
            for m in range(4):
                accumulate(k, pe, k.ps[:, m, :], n1, m * P, k.A, DC).then_inc(product_ready, 1)
            k.loaded(pe, n1 + 1)
            pe.wait_ge(vector_ready, 1)
            for m in range(2):
                accumulate(k, pe, k.ps[:, 6 + m, :], n1 + 1, 256 + m * P, k.A, DC).then_inc(product_ready, 1)
            for t in range(TC):
                for c in range(DC):
                    ins = pe.matmul(k.ps[:, 4 + t // 2, 256 * (t % 2):256 * (t % 2) + 256], k.A[:, c, t * P:(t + 1) * P],
                                    k.chunk(n1 + 1)[:, c, 0:256], start=(c == 0), stop=(c == DC - 1))
            ins.then_inc(product_ready, 1)
            pe.wait_ge(vector_ready, 2)
            pe.wait_ge(copied, 1)
            for m in range(2):
                ins = pe.matmul(k.ps[:, 0, :], k.ones[:, :], acc[:, m, :], start=(m == 0), stop=(m == 1))
            ins.then_inc(stats_ready, 1)
            pe.wait_ge(squared, 2)
            for m in range(2):
                ins = pe.matmul(k.ps[:, 1, :], k.ones[:, :], u[:, m, :], start=(m == 0), stop=(m == 1))
            ins.then_inc(stats_ready, 1)

        @block.scalar
        def _(act):
            for m in range(2):
                act.wait_ge(conv_product, 2 * m + 1)
                act.activation(k.tmp[:, m, :], k.ps[:, 6 + m, :], ACT.Sigmoid).then_inc(gate_ready, 1)
            act.wait_ge(product_ready, 2)
            act.activation(q, k.ps[:, 0:2, :], ACT.Silu).then_inc(copied, 1)
            act.wait_ge(product_ready, 4)
            act.activation(key, k.ps[:, 2:4, :], ACT.Sigmoid, scale=-1.0).then_inc(copied, 1)
            VP.wait(act, 0, "bounds")
            if l:
                act.activation(k.lb[:, 0:2], k.lb[:, 4:6], ACT.Sigmoid).then_inc(copied, 1)
                act.activation(k.lb[:, 2:4], k.lb[:, 4:6], ACT.Sigmoid, scale=-1.0).then_inc(copied, 1)
                act.wait_ge(copied, 4)
                act.activation(k.lb[:, 6:8], k.lb[:, 2:4], ACT.Ln).then_inc(copied, 1)
                AP_.last(act.activation(k.lb[:, 8:10], k.lb[:, 0:2], ACT.Ln), "start")
            else:
                AP_.done(act, "start")
            for m in range(2):
                VP.wait(act, 0, f"z{m}")
                AP_.last(act.activation(k.tmp[:, 0, :], k.tmp[:, 0, :], ACT.Exp), f"e{m}")
                act.wait_ge(act_done, AP_.at(0, f"e{m}"))
                AP_.last(act.activation(k.tmp[:, 0, :], k.tmp[:, 0, :], ACT.Ln, bias=1.0), f"ln{m}")
                VP.wait(act, 0, f"d{m}")
                if l:
                    AP_.last(act.activation(k.tmp[:, 2, :], k.tmp[:, 2, :], ACT.Exp), f"e2{m}")
                    act.wait_ge(act_done, AP_.at(0, f"e2{m}"))
                    AP_.last(act.activation(k.tmp[:, 2, :], k.tmp[:, 2, :], ACT.Ln, bias=1.0), f"ln2{m}")
                else:
                    AP_.done(act, f"e2{m}")
                    AP_.done(act, f"ln2{m}")
            at = 5 if l else 2
            act.wait_ge(product_ready, 6)
            act.activation(g[:, :, :], k.ps[:, 6:8, :], ACT.Silu).then_inc(copied, 1)
            act.wait_ge(product_ready, 7)
            act.activation(v_t, k.ps[:, 4:6, :].rearrange("p a b -> p (a b)").rearrange("p (t n) -> p t n", t=TC), ACT.Copy)\
                .then_inc(copied, 1)
            act.wait_ge(copied, at + 2)
            for m in range(2):
                act.wait_ge(vector_ready, m + 3)
                act.activation(u[:, m, :], acc[:, m, :], ACT.Square).then_inc(squared, 1)
            act.wait_ge(stats_ready, 2)
            act.activation(dev, k.ps[:, 1, :], ACT.Sqrt, bias=col(k, "eps", 0), scale=1.0 / 256).then_inc(squared, 1)
            for m in range(2):
                act.wait_ge(vector_ready, m + 5)
                act.activation(acc[:, m, :], acc[:, m, :], ACT.Silu).then_inc(squared, 1)
            act.wait_ge(squared, 5)

        @block.vector
        def _(dve):
            step = Steps(dve, dve_step)
            at = k.where["lb_logits"]
            step(dve.tensor_tensor(k.lb[:, 4:6], k.cols[:, at + 2:at + 4], k.cols[:, at:at + 2], ALU.subtract))
            VP.done(dve, "bounds")
            for m in range(2):
                dve.wait_ge(gate_ready, m + 1)
                dve.wait_ge(conv_product, 2 * m + 2)
                step(dve.tensor_tensor(u[:, m, :], k.tmp[:, m, :], k.ps[:, 4 + m, :], ALU.mult))
            dve.sem_inc(vector_ready, 1)
            dve.sem_inc(k.weights_used, 1)
            taps = lambda m, j: col(k, f"dw_w{l}_{j}", m)
            for m in range(2):
                step(dve.tensor_scalar(acc[:, m, :], u[:, m, :], taps(m, CONV_K - 1), col(k, f"dw_b{l}", m), ALU.mult, ALU.add),
                     wait=(m == 1))
            for lag in range(1, CONV_K):
                for m in range(2):
                    step(dve.scalar_tensor_tensor(acc[:, m, lag:T], u[:, m, 0:T - lag], taps(m, CONV_K - 1 - lag), acc[:, m, lag:T],
                                                  ALU.mult, ALU.add), wait=(m == 1))
            dve.sem_inc(vector_ready, 1)
            dve.wait_ge(copied, 2)
            AP_.wait(dve, 0, "start")
            for m in range(2):
                t0, t1, t2 = k.tmp[:, 0, :], k.tmp[:, 1, :], k.tmp[:, 2, :]
                z = k.ps[:, 2 + m, :]
                step(dve.tensor_copy(t1, z))
                step(dve.scalar_tensor_tensor(t0, t1, -1.0, t1, ALU.mult, ALU.min))
                VP.done(dve, f"z{m}")
                step(dve.tensor_scalar(t1, t1, 0.0, None, ALU.min))
                AP_.wait(dve, 0, f"ln{m}")
                step(dve.tensor_tensor(t1, t1, t0, ALU.subtract))
                if l:
                    step(dve.tensor_scalar(t1, t1, k.lb[:, 6 + m:7 + m], None, ALU.add))
                    step(dve.tensor_scalar(t0, t1, -1.0, k.lb[:, 8 + m:9 + m], ALU.mult, ALU.add))
                    step(dve.scalar_tensor_tensor(t2, t0, -1.0, t0, ALU.mult, ALU.min))
                    VP.done(dve, f"d{m}")
                    step(dve.scalar_tensor_tensor(t1, t0, 0.0, t1, ALU.max, ALU.add))
                    AP_.wait(dve, 0, f"ln2{m}")
                    step(dve.tensor_tensor(t1, t1, t2, ALU.add))
                    step(dve.tensor_scalar(key[:, m, :], key[:, m, :], k.lb[:, 2 + m:3 + m], None, ALU.mult))
                else:
                    VP.done(dve, f"d{m}")
                step(dve.tensor_tensor_scan(b[:, m, :], k.seg[128][:, :], t1, 0.0, ALU.mult, ALU.add))
                AP_.wait(dve, 0, f"ln2{m}")
            dve.wait_ge(stats_ready, 1)
            for m in range(2):
                step(dve.scalar_tensor_tensor(acc[:, m, :], k.ps[:, 0, :], -1.0 / 256, acc[:, m, :], ALU.mult, ALU.add))
                dve.sem_inc(vector_ready, 1)
            dve.sem_inc(k.weights_used, 2)
            dve.wait_ge(squared, 3)
            step(dve.reciprocal(dev, dev))
            for m in range(2):
                step(dve.tensor_tensor(acc[:, m, :], acc[:, m, :], dev, ALU.mult))
                step(dve.tensor_scalar(acc[:, m, :], acc[:, m, :], col(k, f"cln_g{l}", m), col(k, f"cln_b{l}", m),
                                       ALU.mult, ALU.add))
                dve.sem_inc(vector_ready, 1)


def hgrn(k, l, g):
    q, key, b = k.B[:, 0:2, :], k.B[:, 2:4, :], k.B[:, 4:6, :]
    v_t = k.tmp[:, 4:6, :].rearrange("p a b -> p (a b)").rearrange("p (t n) -> p t n", t=TC)
    blocks = lambda tile: tile.rearrange("p (a b) -> p a b", b=P)
    with ExitStack() as own:
        S = own.enter_context(k.nc.sbuf_tensor(f"hgrn_state{l}", [P, 2, P], F32))
        last_decay = own.enter_context(k.nc.sbuf_tensor(f"hgrn_last{l}", [P, 2, TC], F32))
        second = own.enter_context(k.nc.sbuf_tensor(f"hgrn_second{l}", [P, 6, T], F32))
        E, qx, kx, part = ([k.tmp[:, n, :], second[:, n, :]] for n in range(4))
        AT = [[blocks(k.B[:, 6, :]), blocks(k.B[:, 7, :])], [blocks(second[:, 4, :]), blocks(second[:, 5, :])]]
        bank = lambda m, n: k.ps[:, 4 * m + n, :]
        with k.stage(4) as (block, pe_done, act_done, dve_done, dve_step):
            both = lambda *names: [f"{x}{m}" for x in names for m in range(2)]
            AP_ = Phases(act_done, both(*[f"E{v}_" for v in range(7)], "inter_", "turned_") + [f"{x}{m}" for m in range(2) for x in ("out_", "sq_")]
                         + both("dev_"))
            VP = Phases(dve_done, both(*[y for v in range(7) for y in (f"d{v}_", f"x{v}_")], "inter_", "hats_", *[f"s{c}_" for c in range(TC)], "fin_"))
            TP = Phases(pe_done, both("diag_", *[f"a{v}_" for v in range(7)], "turned_", *[f"u{c}_" for c in range(TC)], "sum_"))

            @block.sync
            def _(sp):
                k.feed(sp, 0)

            @block.tensor
            def _(pe):
                def pairwise(m, left, right, banks):
                    for t in range(TC):
                        ts = slice(t * P, (t + 1) * P)
                        for h in range(2):
                            hs = slice(64 * h, 64 * h + 64)
                            ins = pe.matmul(bank(m, banks + h)[:, ts], left[hs, ts], right[hs, ts], start=True, stop=True)
                    return ins
                for m in range(2):
                    TP.last(pairwise(m, key[:, m, :], q[:, m, :], 0), f"diag_{m}")
                for v in range(7):
                    for m in range(2):
                        VP.wait(pe, 0, f"x{v}_{m}")
                        TP.last(pairwise(m, kx[m], qx[m], 2 if v % 2 == 0 else 0), f"a{v}_{m}")
                for m in range(2):
                    VP.wait(pe, 0, f"hats_{m}")
                    for t in range(TC):
                        ins = pe.transpose(bank(m, 0)[:, t * P:(t + 1) * P], kx[m][:, t * P:(t + 1) * P], k.ident[:, :])
                    TP.last(ins, f"turned_{m}")
                for c in range(TC):
                    cs = slice(c * P, (c + 1) * P)
                    for m in range(2):
                        if c:
                            VP.wait(pe, 0, f"s{c - 1}_{m}")
                        else:
                            AP_.wait(pe, 0, f"turned_{m}")
                        pe.matmul(bank(m, 1)[:, cs], S[:, m, :], qx[m][:, cs], start=True, stop=False)
                        for h in range(2):
                            pe.matmul(k.ps[64 * h:64 * h + 64, 4 * m + 1, cs], v_t[:, c, P * m + 64 * h:P * m + 64 * h + 64],
                                      AT[m][h][:, c, :], start=False, stop=True)
                        TP.last(pe.matmul(bank(m, 2)[:, 0:P], blocks(part[m])[:, c, :], v_t[:, c, P * m:P * m + P],
                                          start=True, stop=True), f"u{c}_{m}")
                for m in range(2):
                    AP_.wait(pe, 0, f"sq_{m}")
                    TP.last(pe.matmul(bank(m, 3), k.pairs[:, :], kx[m], start=True, stop=True), f"sum_{m}")

            @block.scalar
            def _(act):
                for v in range(7):
                    for m in range(2):
                        VP.wait(act, 0, f"d{v}_{m}")
                        AP_.last(act.activation(E[m], E[m], ACT.Exp), f"E{v}_{m}")
                for m in range(2):
                    VP.wait(act, 0, f"inter_{m}")
                    act.activation(qx[m], b[:, m, :], ACT.Exp)
                    act.activation(last_decay[:, m, :], b[:, m, P - 1:T:P], ACT.Exp)
                    AP_.last(act.activation(E[m], E[m], ACT.Exp), f"inter_{m}")
                for m in range(2):
                    TP.wait(act, 0, f"turned_{m}")
                    AP_.last(act.activation(part[m], bank(m, 0), ACT.Copy), f"turned_{m}")
                for m in range(2):
                    TP.wait(act, 0, f"u{TC - 1}_{m}")
                    AP_.last(act.activation(E[m], bank(m, 1), ACT.Copy), f"out_{m}")
                    AP_.last(act.activation(kx[m], bank(m, 1), ACT.Square), f"sq_{m}")
                for m in range(2):
                    TP.wait(act, 0, f"sum_{m}")
                    AP_.last(act.activation(qx[m], bank(m, 3), ACT.Sqrt, bias=col(k, "eps", 0), scale=1.0 / 64), f"dev_{m}")

            @block.vector
            def _(dve):
                step = Steps(dve, dve_step)
                mask = lambda name: k.mask[name][:, :].unsqueeze(1).to_broadcast([P, TC, P])

                def gather(m, v, banks):
                    for h in range(2):
                        step(dve.tensor_tensor(blocks(part[m]), blocks(bank(m, banks + h)), mask(f"level{v}"), ALU.mult))
                        step(dve.tensor_tensor(AT[m][h], AT[m][h], blocks(part[m]), ALU.add))

                def distance(m, v):
                    size = 2 ** (v + 1)
                    wide = lambda ap: ap.rearrange("p (a b) -> p a b", b=size)
                    ref = wide(b[:, m, :])[:, :, size // 2 - 1:size // 2].to_broadcast([P, T // size, size])
                    step(dve.tensor_tensor(wide(E[m]), wide(b[:, m, :]), ref, ALU.subtract))
                    step(dve.scalar_tensor_tensor(E[m], E[m], -1.0, E[m], ALU.mult, ALU.min))
                    VP.done(dve, f"d{v}_{m}")

                step(dve.memset(S[:, :, :], 0.0))
                for v in range(7):
                    for m in range(2):
                        distance(m, v)
                    for m in range(2):
                        if v == 0:
                            TP.wait(dve, 0, f"diag_{m}")
                            for h in range(2):
                                step(dve.tensor_tensor(AT[m][h], blocks(bank(m, h)), mask("ident"), ALU.mult))
                        else:
                            TP.wait(dve, 0, f"a{v - 1}_{m}")
                            gather(m, v - 1, 2 if (v - 1) % 2 == 0 else 0)
                        AP_.wait(dve, 0, f"E{v}_{m}")
                        step(dve.tensor_tensor(qx[m], q[:, m, :], E[m], ALU.mult), wait=False)
                        step(dve.tensor_tensor(kx[m], key[:, m, :], E[m], ALU.mult))
                        VP.done(dve, f"x{v}_{m}")
                for m in range(2):
                    last = blocks(b[:, m, :])[:, :, P - 1:P].to_broadcast([P, TC, P])
                    step(dve.tensor_tensor(blocks(E[m]), last, blocks(b[:, m, :]), ALU.subtract))
                    TP.wait(dve, 0, f"a6_{m}")
                    gather(m, 6, 2)
                    VP.done(dve, f"inter_{m}")
                for m in range(2):
                    AP_.wait(dve, 0, f"inter_{m}")
                    step(dve.tensor_tensor(qx[m], qx[m], q[:, m, :], ALU.mult), wait=False)
                    step(dve.tensor_tensor(kx[m], key[:, m, :], E[m], ALU.mult))
                    VP.done(dve, f"hats_{m}")
                for c in range(TC):
                    for m in range(2):
                        TP.wait(dve, 0, f"u{c}_{m}")
                        step(dve.scalar_tensor_tensor(S[:, m, :], S[:, m, :], last_decay[:, m, c:c + 1], bank(m, 2)[:, 0:P], ALU.mult, ALU.add))
                        step(dve.tensor_tensor(S[:, m, :], S[:, m, :], k.pairs[:, :], ALU.mult))
                        VP.done(dve, f"s{c}_{m}")
                for m in range(2):
                    AP_.wait(dve, 0, f"dev_{m}")
                    step(dve.reciprocal(qx[m], qx[m]))
                    step(dve.scalar_tensor_tensor(E[m], E[m], col(k, f"hgrn_g{l}", 0), qx[m], ALU.mult, ALU.mult))
                    step(dve.tensor_tensor(k.C[:, 4 + m, :], E[m], g[:, m, :], ALU.mult))
                    VP.done(dve, f"fin_{m}")


def mixer_output(k, l):
    n0 = k.first[f"out_2{l}"]
    with k.stage(2) as (block, product_ready, dve_step):
        @block.sync
        def _(sp):
            k.feed(sp, 2)

        @block.tensor
        def _(pe):
            for m in range(DC):
                if m % 4 == 0:
                    k.loaded(pe, n0 + m // 4)
                if m >= 4:
                    pe.wait_ge(dve_step, m - 3)
                accumulate(k, pe, k.ps[:, m % 4, :], n0 + m // 4, m % 4 * P, k.C, DC).then_inc(product_ready, 1)

        @block.vector
        def _(dve):
            step = Steps(dve, dve_step)
            for m in range(DC):
                dve.wait_ge(product_ready, m + 1)
                step(dve.scalar_tensor_tensor(k.X[:, m, :], k.ps[:, m % 4, :], mod(k, l, "g1", m), k.X[:, m, :], ALU.mult, ALU.add))
                if m % 4 == 3:
                    dve.sem_inc(k.weights_used, 1)


def conformer_and_hgrn(k, l):
    with k.nc.sbuf_tensor(f"hgrn_gate{l}", [P, 2, T], F32) as g:
        conformer_and_gates(k, l, g)
        hgrn(k, l, g)


EG, EPG = 4, 8
NE = EG * EPG
F = 512
ROWS = 64
FURTHER = 16
PAIRS = (NE + FURTHER) // 2


def plan_experts(k, l):
    for name, kc, cols in (("w1_2", DC, F), ("w3_2", DC, F), ("w2_2", F // P, D)):
        for b in range(2):
            k.want(f"experts{l}", k.ins[name][l, b], kc, cols)


def routing(k, l, rows_out):
    h_tok = k.B[:, :, :].rearrange("p a b -> p (a b)").rearrange("p (t d) -> p t d", t=TC)
    with ExitStack() as own:
        sb = lambda name, shape: own.enter_context(k.nc.sbuf_tensor(f"{name}{l}", shape, F32))
        rw = sb("router_w", [P, DC, 36])
        rb = sb("router_b", [P, 36])
        c = k.C[:, :, :].rearrange("p a b -> p (a b)")
        at = [0]

        def tile(*shape):
            n = int(np.prod(shape))
            ap = c[:, at[0]:at[0] + n]
            at[0] += n
            if len(shape) == 2:
                return ap.rearrange("p (a b) -> p a b", a=shape[0])
            if len(shape) == 3:
                return ap.rearrange("p (a b c) -> p a b c", a=shape[0], b=shape[1])
            return ap
        logit, gl_e, one_g = tile(TC, 36), tile(TC, EG), tile(TC, EG)
        small4, small8 = tile(TC, EG), tile(TC, EPG)
        stat = [tile(TC, 1) for _ in range(8)]
        by_group, sel, sel2 = tile(TC, EG, EPG), tile(TC, EPG), tile(TC, EPG)
        one = [tile(TC, EPG), tile(TC, EPG)]
        OH = [tile(TC, NE), tile(TC, NE)]
        M, R, Q, t1, t2 = (tile(TC, NE) for _ in range(5))
        cnt, nov, st, end, off = (tile(NE) for _ in range(5))
        ind, ind2 = tile(FURTHER, NE), tile(FURTHER, NE)
        eid = tile(FURTHER)
        more = tile(FURTHER // 2)
        erow = k.trow[:, 0:NE]

        with k.stage(9) as (block, filled, landed, turned, copied, logits_ready, exps, ranks, dve_step, dve_done):
            @block.sync
            def _(sp):
                sp.dma_start(rw[:, :, :], k.ins["router_w"][l].rearrange("(c p) n -> p c n", p=P)).then_inc(landed, 16)
                sp.dma_start(rb[:, :], k.ins["router_b"][l:l + 1, :].to_broadcast([P, 36])).then_inc(landed, 16)
                anything = k.X[:, 0:2, :].rearrange("p a b -> p (a b)").unsqueeze(1).to_broadcast([P, FURTHER // 2, D])
                sp.dma_start(rows_out[NE // 2:PAIRS, :, :].rearrange("b p d -> p b d"), anything).then_inc(filled, 16)
                k.feed(sp, 0)
                sp.wait_ge(filled, 16)

            @block.tensor
            def _(pe):
                pe.wait_ge(landed, 32)
                for t in range(TC):
                    for c_ in range(DC):
                        ins = pe.matmul(k.ps[:, 7, 36 * t:36 * t + 36], k.A[:, c_, t * P:(t + 1) * P], rw[:, c_, :],
                                        start=(c_ == 0), stop=(c_ == DC - 1))
                ins.then_inc(logits_ready, 1)
                for i in range(2 * TC):
                    t, half = divmod(i, 2)
                    if i >= 4:
                        pe.wait_ge(copied, i - 3)
                    for j in range(4):
                        ins = pe.transpose(k.ps[:, i % 4, j * P:(j + 1) * P], k.A[:, 4 * half + j, t * P:(t + 1) * P], k.ident[:, :])
                    ins.then_inc(turned, 1)
                pe.wait_ge(dve_done, 2)
                for t in range(TC):
                    for u in range(t):
                        pe.matmul(k.ps[:, 6, NE * t:NE * (t + 1)], k.ones[:, :], M[:, u, :], start=(u == 0), stop=False)
                    pe.matmul(k.ps[:, 6, NE * t:NE * (t + 1)], k.mask["sooner"][:, :], M[:, t, :], start=(t == 0), stop=True)
                for u in range(TC):
                    ins = pe.matmul(k.ps[:, 6, NE * TC:NE * (TC + 1)], k.ones[:, :], M[:, u, :], start=(u == 0), stop=(u == TC - 1))
                ins.then_inc(ranks, 1)

            @block.scalar
            def _(act):
                for i in range(2 * TC):
                    t, half = divmod(i, 2)
                    act.wait_ge(turned, i + 1)
                    act.activation(h_tok[:, t, 512 * half:512 * half + 512], k.ps[:, i % 4, :], ACT.Copy).then_inc(copied, 1)
                act.wait_ge(dve_done, 1)
                act.activation(gl_e, gl_e, ACT.Exp).then_inc(exps, 1)
                act.activation(stat[3], stat[3], ACT.Exp).then_inc(exps, 1)
                act.wait_ge(copied, 2 * TC)

            @block.vector
            def _(dve):
                step = Steps(dve, dve_step)
                wide = lambda ap, n: ap.to_broadcast([P, TC, n])
                row = lambda ap, n: ap.unsqueeze(1).to_broadcast([P, TC, n])

                def first_of(x, top, n, scratch, out):
                    step(dve.tensor_tensor(scratch, x, wide(top, n), ALU.is_equal))
                    step(dve.tensor_scalar(scratch, scratch, -64.0, 64.0, ALU.mult, ALU.add))
                    step(dve.tensor_tensor(scratch, scratch, row(k.trow[:, 0:n], n), ALU.add))
                    step(dve.tensor_reduce(stat[7], scratch, AX.X, ALU.min))
                    step(dve.tensor_tensor(out, row(k.trow[:, 0:n], n), wide(stat[7], n), ALU.is_equal))

                dve.wait_ge(logits_ready, 1)
                step(dve.tensor_tensor(logit, k.ps[:, 7, 0:36 * TC].rearrange("p (t n) -> p t n", t=TC), row(rb[:, :], 36), ALU.add))
                gl = logit[:, :, 0:EG]
                step(dve.tensor_reduce(stat[0], gl, AX.X, ALU.max))
                first_of(gl, stat[0], EG, small4, one_g)
                step(dve.tensor_tensor(gl_e, gl, wide(stat[0], EG), ALU.subtract))
                el = logit[:, :, EG:36].rearrange("p t (g e) -> p t g e", g=EG)
                for g in range(EG):
                    step(dve.tensor_tensor(by_group[:, :, g, :], el[:, :, g, :], wide(one_g[:, :, g:g + 1], EPG), ALU.mult))
                step(dve.tensor_tensor(sel, by_group[:, :, 0, :], by_group[:, :, 1, :], ALU.add))
                step(dve.tensor_tensor(sel, sel, by_group[:, :, 2, :], ALU.add))
                step(dve.tensor_tensor(sel, sel, by_group[:, :, 3, :], ALU.add))
                step(dve.tensor_reduce(stat[1], sel, AX.X, ALU.max))
                first_of(sel, stat[1], EPG, small8, one[0])
                step(dve.scalar_tensor_tensor(sel2, one[0], -1e30, sel, ALU.mult, ALU.add))
                step(dve.tensor_reduce(stat[2], sel2, AX.X, ALU.max))
                first_of(sel2, stat[2], EPG, small8, one[1])
                step(dve.tensor_tensor(stat[3], stat[2], stat[1], ALU.subtract))
                dve.sem_inc(dve_done, 1)
                for i in range(2):
                    for g in range(EG):
                        step(dve.tensor_tensor(OH[i][:, :, EPG * g:EPG * (g + 1)], one[i], wide(one_g[:, :, g:g + 1], EPG), ALU.mult))
                step(dve.tensor_tensor(M, OH[0], OH[1], ALU.add))
                dve.sem_inc(dve_done, 1)
                dve.wait_ge(exps, 2)
                step(dve.tensor_reduce(stat[4], gl_e, AX.X, ALU.add))
                step(dve.tensor_scalar(stat[5], stat[3], 1.0, None, ALU.add))
                step(dve.tensor_tensor(stat[4], stat[4], stat[5], ALU.mult))
                step(dve.reciprocal(stat[4], stat[4]))
                step(dve.tensor_copy(k.row_w[:, 0, :].unsqueeze(2), stat[4]))
                step(dve.tensor_tensor(k.row_w[:, 1, :].unsqueeze(2), stat[4], stat[3], ALU.mult))
                dve.wait_ge(ranks, 1)
                step(dve.tensor_copy(R, k.ps[:, 6, 0:NE * TC].rearrange("p (t e) -> p t e", t=TC)))
                step(dve.tensor_copy(cnt, k.ps[:, 6, NE * TC:NE * (TC + 1)]))
                for x, y, cmp in ((R, Q, ALU.is_ge), (cnt, nov, ALU.is_gt)):
                    step(dve.tensor_scalar(y, x, float(ROWS), None, cmp))
                    for edge in range(2, T // ROWS):
                        step(dve.scalar_tensor_tensor(y, x, float(edge * ROWS), y, cmp, ALU.add))
                step(dve.tensor_tensor_scan(end, k.ones[:, 0:NE], nov, 0.0, ALU.mult, ALU.add))
                step(dve.tensor_tensor(st, end, nov, ALU.subtract))
                step(dve.tensor_tensor(off, st, erow, ALU.subtract))
                step(dve.tensor_scalar(off, off, float(NE - 1), None, ALU.add))
                step(dve.tensor_tensor(t1, Q, row(off, NE), ALU.add))
                step(dve.scalar_tensor_tensor(t1, Q, 0.0, t1, ALU.is_gt, ALU.mult))
                step(dve.tensor_tensor(t1, t1, row(erow, NE), ALU.add))
                step(dve.scalar_tensor_tensor(t1, t1, float(ROWS), R, ALU.mult, ALU.add))
                step(dve.scalar_tensor_tensor(t1, Q, -float(ROWS), t1, ALU.mult, ALU.add))
                for i in range(2):
                    step(dve.tensor_tensor(t2, t1, OH[i], ALU.mult))
                    step(dve.tensor_reduce(k.row_slot[:, i, :].unsqueeze(2), t2, AX.X, ALU.add))
                step(dve.tensor_copy(k.row_index[:, :, :], k.row_slot[:, :, :]))
                wide_e = lambda ap: ap.unsqueeze(1).to_broadcast([P, FURTHER, NE])
                jcol = k.trow[:, 0:FURTHER].unsqueeze(2).to_broadcast([P, FURTHER, NE])
                step(dve.tensor_tensor(ind, wide_e(st), jcol, ALU.is_le))
                step(dve.tensor_tensor(ind2, wide_e(end), jcol, ALU.is_gt))
                step(dve.tensor_tensor(ind, ind, ind2, ALU.mult))
                step(dve.tensor_tensor(ind, ind, wide_e(erow), ALU.mult))
                step(dve.tensor_reduce(eid, ind, AX.X, ALU.add))
                step(dve.tensor_copy(k.block_expert[:, 0:NE], erow[0:1, :]))
                step(dve.tensor_copy(k.block_expert[:, NE:NE + FURTHER], eid[0:1, :]))
                step(dve.tensor_scalar(more, k.trow[:, 0:FURTHER // 2], 2.0, None, ALU.mult))
                step(dve.tensor_tensor(more, more, end[:, NE - 1:NE].to_broadcast([P, FURTHER // 2]), ALU.is_lt))
                step(dve.tensor_reduce(eid[:, 0:1], more, AX.X, ALU.add))
                step(dve.tensor_scalar(k.pair_count[:, :], eid[0:1, 0:1], float(NE // 2), None, ALU.add))


def experts(k, l, rows_out):
    n0 = k.first[f"experts{l}"]
    h_tok = k.B[:, :, :].rearrange("p a b -> p (a b)").rearrange("p (t d) -> p t d", t=TC)
    flat = lambda lo: k.C[:, lo:lo + 2, :].rearrange("p a b -> p (a b)")
    xb = flat(0).rearrange("p (c r) -> p c r", c=DC)
    yb = flat(4)
    pick, gate, hidden, hidden_t, row_no = (k.tmp[:, n, :] for n in (0, 1, 2, 3, 4))
    blocks = lambda ap: ap.rearrange("p (a b) -> p a b", b=P)
    pair_count = lambda eng: eng.value_load(k.pair_count[0:1, 0:1], min_val=NE // 2, max_val=PAIRS)
    with k.stage(16) as (block, picked, gathered, x_ready, up_ready, gate_ready, hidden_ready, turned, turned_copied,
                         y_ready, y_copied, stored, dve_step, w1_loaded, w3_loaded, w2_loaded, pair_used):
        kinds = [("w1_2", DC, w1_loaded), ("w3_2", DC, w3_loaded), ("w2_2", F // P, w2_loaded)]
        slots = [[k.slot(n0 + 2 * j + h).rearrange("p (k n) -> p k n", k=kinds[j][1]) for h in range(2)] for j in range(3)]
        side = [slice(0, ROWS), slice(ROWS, P)]

        @block.sync
        def _(sp):
            count = pair_count(sp)
            k.feed(sp, 0)
            for j in range(3):
                for h in range(2):
                    k.loaded(sp, n0 + 2 * j + h)
                sp.sem_inc(kinds[j][2], 32)
            with sp.Fori(1, count) as i:
                expert = [sp.value_load(k.block_expert[0:1, bass.ds(i * 2 + h, 1)], min_val=0, max_val=NE - 1) for h in range(2)]
                for j, (name, kc, loaded) in enumerate(kinds):
                    sp.wait_ge(pair_used, i * 6 + (2 * j - 4))
                    for h in range(2):
                        src = k.ins[name][l][bass.ds(expert[h], 1), :, :].rearrange("o (k p) n -> p (o k) n", p=P)
                        sp.dma_start(slots[j][h], src).then_inc(loaded, 16)

        @block.tensor
        def _(pe):
            def gather(i):
                pe.wait_ge(picked, i + 1)
                for half in range(2):
                    for c in range(4):
                        for t in range(TC):
                            ins = pe.matmul(k.ps[:, half, c * P:(c + 1) * P], h_tok[:, t, (4 * half + c) * P:(4 * half + c + 1) * P],
                                            pick[:, t * P:(t + 1) * P], start=(t == 0), stop=(t == TC - 1))
                    ins.then_inc(gathered, 1)

            def up(i):
                pe.wait_ge(x_ready, i * 2 + 2)
                pe.wait_ge(hidden_ready, i + 1)
                for j in range(2):
                    pe.wait_ge(kinds[j][2], i * 32 + 32)
                    for c in range(DC):
                        for h in range(2):
                            ins = pe.matmul(k.ps[side[h], 2 + j, :], xb[:, c, side[h]], slots[j][h][:, c, :],
                                            start=(c == 0), stop=(c == DC - 1))
                    ins.then_inc(up_ready, 1)

            def down(i):
                pe.wait_ge(hidden_ready, i + 2)
                for j in range(4):
                    ins = pe.transpose(k.ps[:, 4, j * P:(j + 1) * P], hidden[:, j * P:(j + 1) * P], k.ident[:, :])
                ins.then_inc(turned, 1)
                pe.wait_ge(w2_loaded, i * 32 + 32)
                pe.wait_ge(y_copied, i * 2 + 1)
                pe.wait_ge(turned_copied, i + 1)
                for half in range(2):
                    for f in range(F // P):
                        for h in range(2):
                            ins = pe.matmul(k.ps[side[h], 5 + half, :], hidden_t[:, f * P + ROWS * h:f * P + ROWS * h + ROWS],
                                            slots[2][h][:, f, 512 * half:512 * half + 512], start=(f == 0), stop=(f == F // P - 1))
                    ins.then_inc(y_ready, 1)

            count = pair_count(pe)
            pe.sem_inc(turned, 1)
            pe.sem_inc(y_ready, 1)
            gather(0)
            with pe.Fori(0, count) as i:
                up(i)
                gather(i + 1)
                down(i)

        @block.scalar
        def _(act):
            def take(i):
                for half in range(2):
                    act.wait_ge(gathered, i * 2 + (half + 1))
                    act.activation(xb[:, 4 * half:4 * half + 4, :], blocks(k.ps[:, half, :]), ACT.Copy).then_inc(x_ready, 1)

            def gates(i):
                act.wait_ge(up_ready, i * 2 + 1)
                act.sem_inc(pair_used, 2)
                act.wait_ge(hidden_ready, i + 1)
                act.activation(gate, k.ps[:, 2, :], ACT.Silu).then_inc(gate_ready, 1)
                act.wait_ge(up_ready, i * 2 + 2)
                act.sem_inc(pair_used, 2)

            def finish(i):
                act.wait_ge(turned, i + 2)
                act.wait_ge(y_ready, i * 2 + 1)
                act.activation(hidden_t, k.ps[:, 4, :], ACT.Copy).then_inc(turned_copied, 1)
                act.wait_ge(stored, i * 16 + 16)
                for half in range(2):
                    act.wait_ge(y_ready, i * 2 + (half + 2))
                    if half:
                        act.sem_inc(pair_used, 2)
                    act.activation(yb[:, 512 * half:512 * half + 512], k.ps[:, 5 + half, :], ACT.Copy).then_inc(y_copied, 1)
                act.wait_ge(y_copied, i * 2 + 3)
                act.dma_start(rows_out[bass.ds(i, 1), :, :].rearrange("o p d -> p (o d)"), yb).then_inc(stored, 16)

            count = pair_count(act)
            act.sem_inc(y_copied, 1)
            act.sem_inc(stored, 16)
            take(0)
            with act.Fori(0, count) as i:
                gates(i)
                take(i + 1)
                finish(i)
            act.wait_ge(stored, count * 16 + 16)
            act.sem_inc(k.weights_used, 6)

        @block.vector
        def _(dve):
            of_token = lambda i: k.row_slot[:, i, :].unsqueeze(2).to_broadcast([P, TC, P])
            rows = row_no[:, 0:P].unsqueeze(1).to_broadcast([P, TC, P])
            other = k.tmp[:, 5, :]

            def choose(step, i, first=False):
                step(dve.tensor_tensor(blocks(other), rows, of_token(0), ALU.is_equal))
                if not first:
                    dve.wait_ge(gathered, i * 2)
                step(dve.tensor_tensor(blocks(pick), rows, of_token(1), ALU.is_equal))
                step(dve.tensor_tensor(pick, pick, other, ALU.add))
                dve.sem_inc(picked, 1)
                step(dve.tensor_scalar(row_no[:, 0:P], row_no[:, 0:P], float(P), None, ALU.add))

            def hide(step, i):
                dve.wait_ge(gate_ready, i + 1)
                dve.wait_ge(up_ready, i * 2 + 2)
                dve.wait_ge(turned, i + 1)
                step(dve.tensor_tensor(hidden, gate, k.ps[:, 3, :], ALU.mult))
                dve.sem_inc(hidden_ready, 1)

            count = pair_count(dve)
            step = Steps(dve, dve_step)
            step(dve.tensor_copy(row_no[:, 0:P], k.trow[:, 0:P]))
            dve.sem_inc(hidden_ready, 1)
            choose(step, 0, first=True)
            done = step.n
            with dve.Fori(0, count) as i:
                step = Steps(dve, dve_step, i * 5 + done)
                choose(step, i + 1)
                hide(step, i)
                assert step.n == 5


def combine(k, l, rows_out):
    row = [k.A[:, :, :].rearrange("p a b -> p (a b)").rearrange("p (t d) -> p t d", t=TC),
           k.C[:, :, :].rearrange("p a b -> p (a b)").rearrange("p (t d) -> p t d", t=TC)]
    source = rows_out.rearrange("b p d -> (b p) d")
    fetched = k.rows_fetched
    with k.stage(3) as (block, mixed, turned, dve_step):
        @block.sync
        def _(sp):
            for t in range(TC):
                sp.wait_ge(fetched[t], 32 * (l + 1))
            k.feed(sp, 6)

        @block.gpsimd
        def _(pool):
            for t in range(TC):
                for i in range(2):
                    pool.indirect_dma_start(row[i][:, t, :], None, source,
                                            bass.IndirectOffsetOnAxis(ap=k.row_index[:, i, t:t + 1], axis=0)).then_inc(fetched[t], 16)

        @block.vector
        def _(dve):
            step = Steps(dve, dve_step)
            for t in range(TC):
                dve.wait_ge(fetched[t], 32 * (l + 1))
                step(dve.tensor_scalar(row[0][:, t, :], row[0][:, t, :], k.row_w[:, 0, t:t + 1], None, ALU.mult))
                step(dve.scalar_tensor_tensor(row[0][:, t, :], row[1][:, t, :], k.row_w[:, 1, t:t + 1], row[0][:, t, :],
                                              ALU.mult, ALU.add))
            dve.sem_inc(mixed, 1)
            for c in range(DC):
                dve.wait_ge(turned, c + 1)
                step(dve.scalar_tensor_tensor(k.X[:, c, :], k.ps[:, c % 4, :], mod(k, l, "g2", c), k.X[:, c, :], ALU.mult, ALU.add))

        @block.tensor
        def _(pe):
            pe.wait_ge(mixed, 1)
            for c in range(DC):
                if c >= 4:
                    pe.wait_ge(dve_step, 2 * TC + c - 3)
                for t in range(TC):
                    ins = pe.transpose(k.ps[:, c % 4, t * P:(t + 1) * P], row[0][:, t, c * P:(c + 1) * P], k.ident[:, :])
                ins.then_inc(turned, 1)


def mixture(k, l):
    modulated_norm(k, l, 2)
    rows_out = k.nc.dram_tensor(f"expert_rows{l}", (PAIRS, P, D), F32, kind="Internal").ap()
    routing(k, l, rows_out)
    experts(k, l, rows_out)
    combine(k, l, rows_out)


def columns(x):
    out = {}

    def put(name, v):
        v = np.asarray(v).reshape(-1)
        pad = -len(v) % P
        if pad:
            v = np.concatenate([v, np.zeros(pad, v.dtype)])
        out[name] = v.reshape(-1, P).T

    for j in range(2):
        for w in range(3):
            put(f"conv_k{j}_{w}", x["conv_k"][j, w])
    for i in range(DEPTH):
        put(f"ln_g{i}", x["ln_g"][i])
        put(f"ln_b{i}", x["ln_b"][i])
    for n in range(6):
        put(f"rwkv_mu{n}", x["rwkv_mu"][0, n])
    put("rwkv_w0", x["rwkv_w0"])
    put("rwkv_a0", x["rwkv_a0"])
    put("c", x["c_2"])
    put("eps", np.full(P, EPS, np.float32))
    half = ROPE // 2
    freq = np.zeros(P, np.float32)
    freq[64:96] = np.tile((np.float32(10000.0) ** (-np.arange(half, dtype=np.float32) / half)).astype(np.float32), 2)
    put("rope_freq", freq)
    put("rope_sign", np.where(np.arange(P) < 80, -1.0, 1.0).astype(np.float32))
    put("lb_logits", x["hgrn_lb_logits_2"])
    for l in range(2):
        for name, key in (("b_ada", "b_ada"), ("norm1_g", "norm1_g"), ("norm2_g", "norm2_g"), ("q_a_g", "q_a_norm_g"),
                          ("kv_a_g", "kv_a_norm_g"), ("q_g", "q_norm_g"), ("k_g", "k_norm_g"), ("pool_scale", "pool_scale"),
                          ("dw_b", "conv_dw_b"), ("cln_g", "conv_ln_g"), ("cln_b", "conv_ln_b")):
            put(f"{name}{l}", x[f"{key}_2"][l])
        put(f"hgrn_g{l}", np.tile(x["hgrn_out_norm_g_2"][l], 2))
        for j in range(CONV_K):
            put(f"dw_w{l}_{j}", x["conv_dw_w_2"][l, j])
    put("gn_eps", np.full(P, GN_EPS, np.float32))
    put("ssm_d", x["ssm_d"])
    put("ssm_b_glu", x["ssm_b_glu"])
    put("half_pi", np.full(P, np.pi / 2, np.float32))
    put("round", np.full(P, ROUND, np.float32))
    put("ln_eps", np.full(P, LN_EPS, np.float32))
    return out


def ssm_layouts(x):
    tile = lambda v: np.asarray(v)[0].reshape(32, P).T
    log_dt = np.broadcast_to(x["ssm_log_dt"][0][:, None], (64, 64))
    raw = [tile(x["ssm_lam_re"]), tile(x["ssm_lam_im"]), log_dt.reshape(32, P).T]
    b = np.zeros((P, 2, DC, P), np.float32)
    c = np.zeros((P, 2, 32, 32), np.float32)
    for part, (bn, cn) in enumerate((("ssm_b_re", "ssm_c_re"), ("ssm_b_im", "ssm_c_im"))):
        for g in range(64):
            j, half = divmod(g, 2)
            row = 32 * (j % 4) + 16 * half
            b[row:row + 16, part, j // 4, 64 * half:64 * half + 64] = x[bn][0, g].T
            c[64 * half:64 * half + 64, part, j, 16 * half:16 * half + 16] = x[cn][0, g].T
    return {"ssm_raw": np.concatenate(raw, axis=1), "ssm_b": b.reshape(P, -1), "ssm_c": c.reshape(P, -1)}


def small_layouts(x):
    out = np.zeros((2, P, SMALL_COLS), np.float32)
    where = lambda name: slice(SMALL[name][0], SMALL[name][0] + SMALL[name][1])
    swap = np.zeros((P, P), np.float32)
    for i in range(64, 80):
        swap[i, i + 16] = swap[i + 16, i] = 1.0
    strip = np.zeros((P, 896), np.float32)
    strip[:, 384:512] = np.where(np.arange(P)[None, :] > np.arange(P)[:, None], -1e30, 0.0)
    inv = np.zeros((P, 2, T), np.float32)
    for g, w in enumerate((2, 4, 8, 16)):
        inv[64 * (g % 2):64 * (g % 2) + 64, g // 2] = 1.0 / np.minimum(np.arange(1, T + 1), w)
    for l in range(2):
        uq = x["w_uq_2"][l]
        out[l, :, where("w_uq")][:, 0:384] = uq[0:P]
        out[l, 0:64, 384:768] = uq[P:192]
        out[l, :, where("w_ukv")] = x["w_ukv_2"][l]
        out[l, :, where("swap")] = swap
        out[l, :, where("strip")] = strip
        out[l, :, where("pool_inv")] = inv.reshape(P, -1)
        out[l, :, where("w_pool")] = x["w_pool_2"][l].reshape(2, 2, 64, 64).transpose(1, 2, 0, 3).reshape(P, P)
    return out


MASKS = ["ident", "sooner", "before", "upto", "first_lower"] + [f"level{l}" for l in range(7)]
CONSTS = [("ones", P), ("pairs", P), ("trow", T), ("seg64", T), ("seg128", T)] + [(name, P) for name in MASKS]


def constant_values():
    p = np.arange(P)
    row, one = p[:, None], p[None, :]
    same = row // 64 == one // 64
    c = {
        "ones": np.ones((P, P)),
        "ident": np.eye(P),
        "seg64": np.tile(np.arange(T) % 64 != 0, (P, 1)),
        "seg128": np.tile(np.arange(T) % 128 != 0, (P, 1)),
        "before": same & (row < one),
        "sooner": row < one,
        "upto": same & (row <= one),
        "first_lower": ((row // 2) == (one // 2)) & (row > one),
        "pairs": (p[:, None] // 64 == p[None, :] // 64),
        "trow": np.tile(np.arange(T), (P, 1)),
    }
    for l in range(7):
        c[f"level{l}"] = (row >> (l + 1) == one >> (l + 1)) & (row >> l & 1 == 0) & (one >> l & 1 == 1)
    return np.concatenate([c[name].reshape(P, n).astype(np.float32) for name, n in CONSTS], axis=1)


def device_inputs(x):
    x = {name: np.asarray(v) for name, v in x.items()}
    cols = columns(x)
    where, at = {}, 0
    for name, v in cols.items():
        where[name] = at
        at += v.shape[1]
    d = {
        "x_t": x["x"][0].T,
        "p_t": x["p"][:, 0].transpose(0, 2, 1),
        "cols": np.concatenate(list(cols.values()), axis=1),
        "consts": constant_values(),
    }
    d.update(ssm_layouts(x))
    d["small"] = small_layouts(x)
    d["positions"] = x["positions_2"]
    d["router_w"] = np.concatenate([x["router_group_w_2"], x["router_expert_w_2"]], axis=2)
    d["router_b"] = np.concatenate([x["router_group_b_2"], x["router_expert_b_2"]], axis=1)
    for name in ("w1_2", "w3_2", "w2_2"):
        d[name] = x[name]
    d["w_ada_chunks"] = x["w_ada_2"].reshape(2, D, 12, 512).transpose(0, 2, 1, 3).reshape(24, D, 512)
    for name in ("w_in_2", "w_out_2"):
        d[name] = x[name]
    for name in ("w1", "w2", "a1", "a2"):
        d[f"rwkv_{name}"] = x[f"rwkv_{name}"][0]
    per_pair = [x[f"rwkv_{name}"].reshape(DC, P) for name in ("k_k", "k_a", "r_k", "lnx_g", "lnx_b")]
    per_pair += [np.zeros((DC, P), np.float32)] * 3
    d["rwkv_pairs"] = np.stack(per_pair, axis=-1)
    for name in ("conv_w_in", "conv_w_out", "ssm_w_in", "ssm_w_glu", "ssm_w_out", "rwkv_w_rkvz", "rwkv_w_out",
                 "ple_proj", "ple_gate"):
        d[name] = x[name]
    return {name: np.ascontiguousarray(v) for name, v in d.items()}, where


def build(nc, ins, out, where):
    with ExitStack() as ctx:
        k = Kernel(nc, ctx, ins, out)
        k.where = where
        tiles = {name: ctx.enter_context(nc.sbuf_tensor(f"const_{name}", [P, n], F32)) for name, n in CONSTS}
        k.ones, k.pairs, k.trow, k.ident = tiles["ones"], tiles["pairs"], tiles["trow"], tiles["ident"]
        k.seg = {64: tiles["seg64"], 128: tiles["seg128"]}
        k.mask = {name: tiles[name] for name in MASKS}
        k.const_tiles = [(tiles[name][:, :], n) for name, n in CONSTS]
        plan_weights(k)
        load_constants(k)
        for layer in range(DEPTH):
            if layer % 3 == 0:
                short_conv(k, layer // 3)
            elif layer % 3 == 1:
                ssm_mixer(k)
            else:
                rwkv_mixer(k)
            src, r = (k.B, k.A) if layer % 3 == 1 else (k.A, k.B)
            output_and_gate(k, layer, src, r)
            layer_norm(k, layer)
        modulation(k)
        for l in range(2):
            modulated_norm(k, l, 1)
            mla(k, l)
            pool_mixer(k, l)
            conformer_and_hgrn(k, l)
            mixer_output(k, l)
            mixture(k, l)
        store_output(k)


def kernel(**inputs):
    import concourse.bacc as bacc
    from concourse.bass_utils import run_bass_kernel_spmd

    nc = bacc.Bacc("TRN2", target_bir_lowering=False, num_devices=1)
    arrays, where = device_inputs(inputs)
    ins = {name: nc.dram_tensor(f"in_{name}", a.shape, mybir.dt.from_np(a.dtype), kind="ExternalInput").ap()
           for name, a in arrays.items()}
    out = nc.dram_tensor("out_t", (D, T), F32, kind="ExternalOutput").ap()
    build(nc, ins, out, where)
    r = run_bass_kernel_spmd(nc, [{f"in_{name}": a for name, a in arrays.items()}], core_ids=[0])
    return np.ascontiguousarray(r.results[0]["out_t"].T)[None]
```
